# Optimizing a Trainium2 kernel written in Bass

```python
import jax
import jax.numpy as jnp
from jax import lax
import numpy as np
import math
import jax, jax.numpy as jnp

D_MODEL = 1024
BATCH = 1
SEQ = 256
DEPTH = 2

GRID_W = 64
CTX_LEN = 256
EPS = 1e-6
N_BRANCH = 4
MIX_W = D_MODEL // 4

ML_HEADS = 4
ML_W = MIX_W
ML_DH = ML_W // ML_HEADS
ML_CHUNK = 64
ML_CONV = 3
ML_STATE_COLS = 3 * ML_W + 4 * ML_HEADS
ML_COLS = ML_STATE_COLS + ML_W
GM_GROUPS = 4
GM_CHUNK = 128
GM_W = MIX_W
GM_DG = GM_W // GM_GROUPS
CV_W = MIX_W
CV_K = 31
FT_GROUPS = 4
FT_W = MIX_W
FT_DG = FT_W // FT_GROUPS
GM_OFF = ML_COLS
CV_OFF = GM_OFF + 2 * GM_W
FT_OFF = CV_OFF + 2 * CV_W
GATE_OFF = FT_OFF + FT_W
IN_COLS = GATE_OFF + N_BRANCH * D_MODEL
PEER_HEADS = 8
PEER_TOPK = 16
N_KEYS = 128
N_EXPERTS = N_KEYS * N_KEYS
PEER_DQ = 256
PEER_DK_HALF = PEER_DQ // 2
PEER_BLOCK = 128


def _rmsnorm(x, g):
    xf = x.astype(jnp.float32)
    y = xf * lax.rsqrt(jnp.mean(xf * xf, axis=-1, keepdims=True) + EPS)
    return (y * g.astype(jnp.float32)).astype(x.dtype)

def _layernorm(x, g, b):
    xf = x.astype(jnp.float32)
    mu = jnp.mean(xf, axis=-1, keepdims=True)
    xc = xf - mu
    y = xc * lax.rsqrt(jnp.mean(xc * xc, axis=-1, keepdims=True) + EPS)
    return (y * g.astype(jnp.float32) + b.astype(jnp.float32)).astype(x.dtype)

def _modulate(h, shift, scale):
    return h * (1 + scale) + shift

def _dwconv(x, w, b):
    k, ch = w.shape
    y = lax.conv_general_dilated(x, w[:, None, :].astype(x.dtype), window_strides=(1,),
                                 padding=((k // 2, k // 2),),
                                 dimension_numbers=('NWC', 'WIO', 'NWC'),
                                 feature_group_count=ch)
    return y + b

def _grid_sincos(n_tok, d):
    rows = n_tok // GRID_W
    n_freq = d // 4
    freq = 1.0 / (10000.0 ** (jnp.arange(n_freq, dtype=jnp.float32) / n_freq))
    r = jnp.repeat(jnp.arange(rows, dtype=jnp.float32), GRID_W)
    cc = jnp.tile(jnp.arange(GRID_W, dtype=jnp.float32), rows)
    ar = r[:, None] * freq[None, :]
    ac = cc[:, None] * freq[None, :]
    return jnp.concatenate([jnp.sin(ar), jnp.cos(ar), jnp.sin(ac), jnp.cos(ac)], axis=-1)

def _zero_state(b_sz):
    g = 2 * ML_HEADS
    return (jnp.zeros((b_sz, g, ML_DH, ML_DH), jnp.float32),
            jnp.zeros((b_sz, g, ML_DH), jnp.float32),
            jnp.zeros((b_sz, g), jnp.float32))

def _mlstm_scan(q, k, v, li, lf, state, need_out):
    b_sz, g, t_len, dh = q.shape
    nc = t_len // ML_CHUNK

    def chunks(a):
        a = a.reshape((b_sz, g, nc, ML_CHUNK) + a.shape[3:])
        return jnp.moveaxis(a, 2, 0)

    tril = jnp.tril(jnp.ones((ML_CHUNK, ML_CHUNK), dtype=bool))

    def step(carry, inp):
        c_st, n_st, m_st = carry
        qc, kc, vc, lic, lfc = inp
        bcum = jnp.cumsum(lfc, axis=-1)
        b_last = bcum[..., -1]
        w = b_last[..., None] - bcum + lic
        m_new = jnp.maximum(b_last + m_st, jnp.max(w, axis=-1))
        ws = jnp.exp(w - m_new[..., None])
        decay = jnp.exp(b_last + m_st - m_new)
        c_new = decay[..., None, None] * c_st + jnp.einsum('bgs,bgsd,bgse->bgde', ws, kc, vc)
        n_new = decay[..., None] * n_st + jnp.einsum('bgs,bgsd->bgd', ws, kc)
        if not need_out:
            return (c_new, n_new, m_new), None
        dlog = jnp.where(tril, bcum[..., :, None] - bcum[..., None, :] + lic[..., None, :], -jnp.inf)
        inter = bcum + m_st[..., None]
        m_t = jnp.maximum(inter, jnp.max(dlog, axis=-1))
        s = jnp.einsum('bgtd,bgsd->bgts', qc, kc) * jnp.exp(dlog - m_t[..., None])
        gi = jnp.exp(inter - m_t)
        num = gi[..., None] * jnp.einsum('bgtd,bgde->bgte', qc, c_st) + jnp.einsum('bgts,bgse->bgte', s, vc)
        den = gi * jnp.einsum('bgtd,bgd->bgt', qc, n_st) + jnp.sum(s, axis=-1)
        h = num / jnp.maximum(jnp.abs(den), jnp.exp(-m_t))[..., None]
        return (c_new, n_new, m_new), h

    state, h = lax.scan(step, state, (chunks(q), chunks(k), chunks(v), chunks(li), chunks(lf)))
    if need_out:
        h = jnp.moveaxis(h, 0, 2).reshape(b_sz, g, t_len, dh)
    return h, state

def _mlstm_branch(p, conv_w, conv_b, gate_b, norm_g, state, need_out):
    b_sz, t_len, _ = p.shape
    qk = jax.nn.silu(_dwconv(p[..., :2 * ML_W], conv_w, conv_b))

    def heads(a):
        return a.astype(jnp.float32).reshape(b_sz, t_len, ML_HEADS, ML_DH).transpose(0, 2, 1, 3)

    q = heads(qk[..., :ML_W])
    k = heads(qk[..., ML_W:]) * (ML_DH ** -0.5)
    v = heads(p[..., 2 * ML_W:3 * ML_W])
    gates = (p[..., 3 * ML_W:ML_STATE_COLS] + gate_b).astype(jnp.float32).transpose(0, 2, 1)
    li = gates[:, :2 * ML_HEADS]
    lf = jax.nn.log_sigmoid(gates[:, 2 * ML_HEADS:])

    def both(a):
        return jnp.concatenate([a, jnp.flip(a, axis=2)], axis=1)

    def dirs(a):
        return jnp.concatenate([a[:, :ML_HEADS], jnp.flip(a[:, ML_HEADS:], axis=2)], axis=1)

    h2, state = _mlstm_scan(both(q), both(k), both(v), dirs(li), dirs(lf), state, need_out)
    if not need_out:
        return None, state
    h = h2[:, :ML_HEADS] + jnp.flip(h2[:, ML_HEADS:], axis=2)
    h = h * lax.rsqrt(jnp.mean(h * h, axis=-1, keepdims=True) + EPS) * norm_g.astype(jnp.float32)[None, :, None, :]
    h = h.transpose(0, 2, 1, 3).reshape(b_sz, t_len, ML_W)
    o = jax.nn.sigmoid(p[..., ML_STATE_COLS:ML_COLS].astype(jnp.float32))
    return (h * o).astype(p.dtype), state

def _gmlp_branch(p, ln_g, ln_b, w_s, b_s):
    b_sz, t_len, _ = p.shape
    z = jax.nn.gelu(p)
    u, v = z[..., :GM_W], z[..., GM_W:]
    v = _layernorm(v, ln_g, ln_b).reshape(b_sz, t_len // GM_CHUNK, GM_CHUNK, GM_GROUPS, GM_DG)
    s = jnp.einsum('gts,bnsgc->bntgc', w_s, v) + b_s.T[:, :, None]
    return u * s.reshape(b_sz, t_len, GM_W)

def _conv_branch(p, dw_w, dw_b, ln_g, ln_b):
    z = p[..., :CV_W] * jax.nn.sigmoid(p[..., CV_W:])
    z = _dwconv(z, dw_w, dw_b)
    return jax.nn.silu(_layernorm(z, ln_g, ln_b))

def _fourier_branch(p):
    b_sz, t_len, _ = p.shape
    z = p.astype(jnp.float32).reshape(b_sz, t_len, FT_GROUPS, FT_DG)
    z = jnp.fft.fft2(z, axes=(1, 3), norm='ortho').real
    return z.reshape(b_sz, t_len, FT_W).astype(p.dtype)

def _mixer_merge(p, ml_out, gm_ln_g, gm_ln_b, gm_w_s, gm_b_s, cv_dw_w, cv_dw_b, cv_ln_g, cv_ln_b, w_branch, w_out):
    branches = (ml_out,
                _gmlp_branch(p[..., GM_OFF:CV_OFF], gm_ln_g, gm_ln_b, gm_w_s, gm_b_s),
                _conv_branch(p[..., CV_OFF:FT_OFF], cv_dw_w, cv_dw_b, cv_ln_g, cv_ln_b),
                _fourier_branch(p[..., FT_OFF:GATE_OFF]))
    y = None
    for i, z in enumerate(branches):
        gate = jax.nn.sigmoid(p[..., GATE_OFF + i * D_MODEL:GATE_OFF + (i + 1) * D_MODEL])
        term = gate * (z @ w_branch[i])
        y = term if y is None else y + term
    return y @ w_out

def _peer(h, w_q, keys, u_tab, v_tab):
    b_sz, t_len, d = h.shape
    hb_all = h.reshape(-1, PEER_BLOCK, d)

    def block(hb):
        n = hb.shape[0]
        q = (hb @ w_q).reshape(n, PEER_HEADS, 2, PEER_DK_HALF)
        s = jnp.einsum('nhpk,pek->nhpe', q, keys)
        v_top, i_top = lax.top_k(s, PEER_TOPK)
        cand = (v_top[:, :, 0, :, None] + v_top[:, :, 1, None, :]).reshape(n, PEER_HEADS, PEER_TOPK * PEER_TOPK)
        sc, pos = lax.top_k(cand, PEER_TOPK)
        i1 = jnp.take_along_axis(i_top[:, :, 0], pos // PEER_TOPK, axis=-1)
        i2 = jnp.take_along_axis(i_top[:, :, 1], pos % PEER_TOPK, axis=-1)
        e = i1 * N_KEYS + i2
        g = jax.nn.softmax(sc.astype(jnp.float32), axis=-1).astype(hb.dtype)
        a = jax.nn.gelu(jnp.einsum('nhkd,nd->nhk', u_tab[e], hb)) * g
        return jnp.einsum('nhk,nhkd->nd', a, v_tab[e])

    return lax.map(block, hb_all).reshape(b_sz, t_len, d)

def first_inputs(seed: int = 0) -> dict:
    key = jax.random.key(seed)
    ks = jax.random.split(key, 32)
    f32 = jnp.float32
    L, D = DEPTH, D_MODEL

    def nrm(k, shape, s):
        return jax.random.normal(k, shape, f32) * s

    def gain(k, shape):
        return 1.0 + nrm(k, shape, 0.02)

    ml_gate_b = jnp.concatenate([nrm(ks[11], (L, 2 * ML_HEADS), 0.1),
                                 jax.random.uniform(ks[12], (L, 2 * ML_HEADS), f32, 3.0, 6.0)], axis=-1)
    return {
        'x': nrm(ks[0], (BATCH, SEQ, D), 1.0),
        'c': nrm(ks[1], (BATCH, D), 1.0),
        'ctx': nrm(ks[2], (BATCH, CTX_LEN, D), 1.0),
        'c_ctx': nrm(ks[3], (D,), 1.0),
        'w_ada': nrm(ks[4], (L, D, 6 * D), 0.5 * D ** -0.5),
        'b_ada': nrm(ks[5], (L, 6 * D), 0.02),
        'norm1_g': gain(ks[6], (L, D)),
        'norm2_g': gain(ks[7], (L, D)),
        'w_in': nrm(ks[8], (L, D, IN_COLS), D ** -0.5),
        'ml_conv_w': nrm(ks[9], (L, ML_CONV, 2 * ML_W), ML_CONV ** -0.5),
        'ml_conv_b': nrm(ks[10], (L, 2 * ML_W), 0.02),
        'ml_gate_b': ml_gate_b,
        'ml_norm_g': gain(ks[13], (L, ML_HEADS, ML_DH)),
        'gm_ln_g': gain(ks[14], (L, GM_W)),
        'gm_ln_b': nrm(ks[15], (L, GM_W), 0.02),
        'gm_w_s': nrm(ks[16], (L, GM_GROUPS, GM_CHUNK, GM_CHUNK), GM_CHUNK ** -0.5),
        'gm_b_s': gain(ks[17], (L, GM_GROUPS, GM_CHUNK)),
        'cv_dw_w': nrm(ks[18], (L, CV_K, CV_W), CV_K ** -0.5),
        'cv_dw_b': nrm(ks[19], (L, CV_W), 0.02),
        'cv_ln_g': gain(ks[20], (L, CV_W)),
        'cv_ln_b': nrm(ks[21], (L, CV_W), 0.02),
        'w_branch': nrm(ks[22], (L, N_BRANCH, MIX_W, D), MIX_W ** -0.5),
        'w_out': nrm(ks[23], (L, D, D), D ** -0.5),
        'peer_w_q': nrm(ks[24], (L, D, PEER_HEADS * PEER_DQ), D ** -0.5),
        'peer_keys': nrm(ks[25], (L, 2, N_KEYS, PEER_DK_HALF), PEER_DK_HALF ** -0.5),
        'peer_u': nrm(ks[26], (L, N_EXPERTS, D), D ** -0.5),
        'peer_v': nrm(ks[27], (L, N_EXPERTS, D), PEER_HEADS ** -0.5),
        'final_norm_g': gain(ks[28], (D,)),
    }

def first_block(x, c, ctx, c_ctx, w_ada, b_ada, norm1_g, norm2_g, w_in, ml_conv_w, ml_conv_b, ml_gate_b,
              ml_norm_g, gm_ln_g, gm_ln_b, gm_w_s, gm_b_s, cv_dw_w, cv_dw_b, cv_ln_g, cv_ln_b, w_branch,
              w_out, peer_w_q, peer_keys, peer_u, peer_v, final_norm_g):
    b_sz, n_tok, d = x.shape
    x = x + _grid_sincos(n_tok, d).astype(x.dtype)[None]
    xc = ctx
    s_lat = jax.nn.silu(c)[:, None, :]
    s_ctx = jax.nn.silu(c_ctx)
    for l in range(DEPTH):
        last = l == DEPTH - 1
        mod = jnp.split(s_lat @ w_ada[l] + b_ada[l], 6, axis=-1)
        modc = jnp.split(s_ctx @ w_ada[l] + b_ada[l], 6, axis=-1)
        h = _modulate(_rmsnorm(x, norm1_g[l]), mod[0], mod[1])
        hc = _modulate(_rmsnorm(xc, norm1_g[l]), modc[0], modc[1])
        p = h @ w_in[l]
        pc = hc @ (w_in[l][:, :ML_STATE_COLS] if last else w_in[l])
        ml_args = (ml_conv_w[l], ml_conv_b[l], ml_gate_b[l], ml_norm_g[l])
        ml_c, state = _mlstm_branch(pc, *ml_args, _zero_state(b_sz), not last)
        ml_x, _ = _mlstm_branch(p, *ml_args, state, True)
        mix_args = (gm_ln_g[l], gm_ln_b[l], gm_w_s[l], gm_b_s[l], cv_dw_w[l], cv_dw_b[l],
                    cv_ln_g[l], cv_ln_b[l], w_branch[l], w_out[l])
        x = x + mod[2] * _mixer_merge(p, ml_x, *mix_args)
        peer_args = (peer_w_q[l], peer_keys[l], peer_u[l], peer_v[l])
        h = _modulate(_rmsnorm(x, norm2_g[l]), mod[3], mod[4])
        x = x + mod[5] * _peer(h, *peer_args)
        if not last:
            xc = xc + modc[2] * _mixer_merge(pc, ml_c, *mix_args)
            hc = _modulate(_rmsnorm(xc, norm2_g[l]), modc[3], modc[4])
            xc = xc + modc[5] * _peer(hc, *peer_args)
    return _rmsnorm(x, final_norm_g)


N_MIXERS = 2
HEAD_DIM = 128
GDN_HEADS = D_MODEL // HEAD_DIM
GDN_CONV = 4
GDN_CHUNK = 64
NSA_Q_HEADS = D_MODEL // HEAD_DIM
NSA_KV_HEADS = NSA_Q_HEADS // 4
CMP_LEN = 32
CMP_STRIDE = 16
SLC_BLOCK = 64
SLC_TOPK = 16
WINDOW = 512
NSA_Q_BLOCK = 64
MEM_TOKENS = 256
MEM_HEADS = 4
NUM_BUCKETS = 32
MAX_DISTANCE = 128
D_FF = ((8 * D_MODEL // 3 + 255) // 256) * 256
FFN_CONV = 3
MEM_WIDTH = MEM_HEADS * HEAD_DIM
MIX_WIDTH = D_MODEL + MEM_WIDTH
GDN_COLS = 4 * GDN_HEADS * HEAD_DIM + 2 * GDN_HEADS
NSA_KV_WIDTH = NSA_KV_HEADS * HEAD_DIM
NSA_COLS = NSA_Q_HEADS * HEAD_DIM + 6 * NSA_KV_WIDTH + 3 * NSA_Q_HEADS
N_GDN = (DEPTH + 1) // 2
N_NSA = DEPTH // 2


def rms_norm(x, w):
    xf = x.astype(jnp.float32)
    y = xf * lax.rsqrt(jnp.mean(xf * xf, axis=-1, keepdims=True) + EPS)
    return (y * w.astype(jnp.float32)).astype(x.dtype)

def l2norm(x):
    xf = x.astype(jnp.float32)
    return xf * lax.rsqrt(jnp.sum(xf * xf, axis=-1, keepdims=True) + EPS)

def causal_dwconv(x, w):
    K = w.shape[0]
    S = x.shape[1]
    xp = jnp.pad(x, ((0, 0), (K - 1, 0), (0, 0)))
    y = xp[:, 0:S] * w[0]
    for j in range(1, K):
        y = y + xp[:, j:j + S] * w[j]
    return y

def t5_bucket(dist):
    n = jnp.maximum(dist, 0)
    max_exact = NUM_BUCKETS // 2
    logv = jnp.log(jnp.maximum(n, 1).astype(jnp.float32) / max_exact) / math.log(MAX_DISTANCE / max_exact)
    large = max_exact + (logv * (NUM_BUCKETS - max_exact)).astype(jnp.int32)
    large = jnp.minimum(large, NUM_BUCKETS - 1)
    return jnp.where(n < max_exact, n, large)

def masked_softmax(s, mask):
    s = jnp.where(mask, s.astype(jnp.float32), -jnp.inf)
    m = jnp.max(s, axis=-1, keepdims=True)
    m = jnp.where(jnp.isfinite(m), m, 0.0)
    p = jnp.where(mask, jnp.exp(s - m), 0.0)
    return p / jnp.maximum(jnp.sum(p, axis=-1, keepdims=True), 1e-30)

def gated_delta_rule_chunked(q, k, v, g, beta):
    f32 = jnp.float32
    B, H, S, dk = q.shape
    dv = v.shape[-1]
    C = GDN_CHUNK
    N = S // C
    q = (q.astype(f32) * dk ** -0.5).reshape(B, H, N, C, dk)
    k = k.astype(f32).reshape(B, H, N, C, dk)
    v = v.astype(f32).reshape(B, H, N, C, dv)
    beta = beta.astype(f32).reshape(B, H, N, C)
    gc = jnp.cumsum(g.astype(f32).reshape(B, H, N, C), axis=-1)
    incl = jnp.tril(jnp.ones((C, C), bool))
    strict = jnp.tril(jnp.ones((C, C), bool), -1)
    diff = gc[..., :, None] - gc[..., None, :]
    decay = jnp.where(incl, jnp.exp(jnp.where(incl, diff, 0.0)), 0.0)
    kb = k * beta[..., None]
    L = jnp.where(strict, jnp.einsum('bhnid,bhnjd->bhnij', kb, k) * decay, 0.0)
    eye = jnp.eye(C, dtype=f32)
    T = lax.linalg.triangular_solve(eye + L, jnp.broadcast_to(eye, L.shape),
                                    left_side=True, lower=True, unit_diagonal=True)
    u = jnp.einsum('bhnij,bhnjd->bhnid', T, v * beta[..., None])
    w = jnp.einsum('bhnij,bhnjd->bhnid', T, kb * jnp.exp(gc)[..., None])
    a_intra = jnp.where(incl, jnp.einsum('bhnid,bhnjd->bhnij', q, k) * decay, 0.0)
    q_dec = q * jnp.exp(gc)[..., None]
    k_dec = k * jnp.exp(gc[..., -1:] - gc)[..., None]
    g_last = jnp.exp(gc[..., -1])

    def chunk_step(state, xs):
        u_n, w_n, a_n, qd_n, kd_n, gl_n = xs
        v_new = u_n - jnp.einsum('bhcd,bhde->bhce', w_n, state)
        o_n = jnp.einsum('bhcd,bhde->bhce', qd_n, state) + jnp.einsum('bhij,bhje->bhie', a_n, v_new)
        state = state * gl_n[..., None, None] + jnp.einsum('bhcd,bhce->bhde', kd_n, v_new)
        return state, o_n

    to_n = lambda t: jnp.moveaxis(t, 2, 0)
    state0 = jnp.zeros((B, H, dk, dv), f32)
    _, o = lax.scan(chunk_step, state0,
                    (to_n(u), to_n(w), to_n(a_intra), to_n(q_dec), to_n(k_dec), to_n(g_last)))
    return jnp.moveaxis(o, 0, 2).reshape(B, H, S, dv)

def gdn_mixer(cols, conv_w, a_log, dt_bias, norm_w):
    B, S, _ = cols.shape
    H, dh = GDN_HEADS, HEAD_DIM
    wd = H * dh
    qkv = jax.nn.silu(causal_dwconv(cols[..., :3 * wd], conv_w)).reshape(B, S, 3, H, dh)
    q, k, v = qkv[:, :, 0], qkv[:, :, 1], qkv[:, :, 2]
    z = cols[..., 3 * wd:4 * wd].reshape(B, S, H, dh)
    b = cols[..., 4 * wd:4 * wd + H]
    a = cols[..., 4 * wd + H:4 * wd + 2 * H]
    beta = jax.nn.sigmoid(b.astype(jnp.float32))
    g = -jnp.exp(a_log.astype(jnp.float32)) * jax.nn.softplus(a.astype(jnp.float32) + dt_bias.astype(jnp.float32))
    heads = lambda t: jnp.swapaxes(t, 1, 2)
    o = gated_delta_rule_chunked(heads(l2norm(q)), heads(l2norm(k)), heads(v.astype(jnp.float32)),
                                 heads(g), heads(beta))
    o = jnp.swapaxes(o, 1, 2)
    o = rms_norm(o, norm_w) * jax.nn.silu(z.astype(jnp.float32))
    return o.reshape(B, S, wd).astype(cols.dtype)

def compress_blocks(t, pos_emb, w1, w2):
    B, S, G, dh = t.shape
    n_cmp = (S - CMP_LEN) // CMP_STRIDE + 1
    idx = (np.arange(n_cmp, dtype=np.int32)[:, None] * CMP_STRIDE
           + np.arange(CMP_LEN, dtype=np.int32)[None, :])
    blk = t[:, idx] + pos_emb[:, None, :]
    flat = jnp.transpose(blk, (0, 3, 1, 2, 4)).reshape(B, G, n_cmp, CMP_LEN * dh)
    return jax.nn.silu(flat @ w1) @ w2

def nsa_mixer(cols, rel_bias, pos_k, w1_k, w2_k, pos_v, w1_v, w2_v):
    B, S, _ = cols.shape
    HQ, G, dh = NSA_Q_HEADS, NSA_KV_HEADS, HEAD_DIM
    R = HQ // G
    Q = NSA_Q_BLOCK
    scale = dh ** -0.5
    qw = HQ * dh
    q = cols[..., :qw]
    kvs = [cols[..., qw + j * NSA_KV_WIDTH:qw + (j + 1) * NSA_KV_WIDTH].reshape(B, S, G, dh) for j in range(6)]
    k_cmp, v_cmp, k_slc, v_slc, k_win, v_win = kvs
    gates = jax.nn.sigmoid(cols[..., qw + 6 * NSA_KV_WIDTH:].astype(jnp.float32)).reshape(B, S, HQ, 3)

    n_q = S // Q
    n_cmp = (S - CMP_LEN) // CMP_STRIDE + 1
    n_slc = S // SLC_BLOCK
    n_sel = min(SLC_TOPK, n_slc)

    kc = compress_blocks(k_cmp, pos_k, w1_k, w2_k)
    vc = compress_blocks(v_cmp, pos_v, w1_v, w2_v)
    c_start = np.arange(n_cmp, dtype=np.int32) * CMP_STRIDE
    c_end = c_start + CMP_LEN - 1
    s_start = np.arange(n_slc, dtype=np.int32) * SLC_BLOCK
    sel_map = ((c_start[:, None] < s_start[None, :] + SLC_BLOCK)
               & (s_start[None, :] <= c_end[:, None])).astype(np.float32)
    to_blocks = lambda t: jnp.swapaxes(t, 1, 2).reshape(B, G, n_slc, SLC_BLOCK, dh)
    ks, vs = to_blocks(k_slc), to_blocks(v_slc)
    pad = lambda t: jnp.pad(jnp.swapaxes(t, 1, 2), ((0, 0), (0, 0), (WINDOW, 0), (0, 0)))
    kw, vw = pad(k_win), pad(v_win)
    tab = rel_bias.reshape(NUM_BUCKETS, G, R)
    c_end_j = jnp.asarray(c_end)
    bi = jnp.arange(B)[:, None, None, None]
    gi = jnp.arange(G)[None, :, None, None]

    def head_bias(dist):
        return jnp.moveaxis(tab[t5_bucket(dist)], (-2, -1), (0, 1))

    qh = jnp.moveaxis(q.reshape(B, S, G, R, dh).transpose(0, 2, 3, 1, 4).reshape(B, G, R, n_q, Q, dh), 3, 0)
    gh = jnp.moveaxis(gates.reshape(B, S, G, R, 3).transpose(0, 2, 3, 1, 4).reshape(B, G, R, n_q, Q, 3), 3, 0)

    def step(args):
        qi, qb, gb = args
        s0 = qi * Q
        t = s0 + jnp.arange(Q, dtype=jnp.int32)
        dist_c = t[:, None] - c_end_j[None, :]
        sc = jnp.einsum('bgrqd,bgcd->bgrqc', qb, kc).astype(jnp.float32) * scale + head_bias(dist_c)
        p_c = masked_softmax(sc, dist_c >= 0)
        o_c = jnp.einsum('bgrqc,bgcd->bgrqd', p_c, vc.astype(jnp.float32))
        imp = jnp.einsum('bgqc,cs->bgqs', jnp.sum(p_c, axis=2), sel_map)
        jb = jnp.arange(n_slc, dtype=jnp.int32)[None, :]
        tb = (t // SLC_BLOCK)[:, None]
        forced = (jb == 0) | (jb == tb) | (jb == tb - 1)
        score = jnp.where(jb <= tb, jnp.where(forced, jnp.inf, imp), -jnp.inf)
        vals, idx = lax.top_k(score, n_sel)
        ok = vals > -jnp.inf
        kg = ks[bi, gi, idx].reshape(B, G, Q, n_sel * SLC_BLOCK, dh)
        vg = vs[bi, gi, idx].reshape(B, G, Q, n_sel * SLC_BLOCK, dh)
        pos = idx[..., None] * SLC_BLOCK + jnp.arange(SLC_BLOCK, dtype=jnp.int32)
        dist_s = t[:, None, None] - pos
        mask_s = (ok[..., None] & (dist_s >= 0)).reshape(B, G, Q, n_sel * SLC_BLOCK)
        bias_s = jnp.moveaxis(tab[t5_bucket(dist_s).reshape(B, G, Q, n_sel * SLC_BLOCK), gi], -1, 2)
        ss = jnp.einsum('bgrqd,bgqkd->bgrqk', qb, kg).astype(jnp.float32) * scale + bias_s
        p_s = masked_softmax(ss, mask_s[:, :, None])
        o_s = jnp.einsum('bgrqk,bgqkd->bgrqd', p_s, vg.astype(jnp.float32))
        kwb = lax.dynamic_slice_in_dim(kw, s0, Q + WINDOW, axis=2)
        vwb = lax.dynamic_slice_in_dim(vw, s0, Q + WINDOW, axis=2)
        kpos = s0 - WINDOW + jnp.arange(Q + WINDOW, dtype=jnp.int32)
        dist_w = t[:, None] - kpos[None, :]
        mask_w = (dist_w >= 0) & (dist_w < WINDOW) & (kpos[None, :] >= 0)
        sw = jnp.einsum('bgrqd,bgkd->bgrqk', qb, kwb).astype(jnp.float32) * scale + head_bias(dist_w)
        p_w = masked_softmax(sw, mask_w)
        o_w = jnp.einsum('bgrqk,bgkd->bgrqd', p_w, vwb.astype(jnp.float32))
        o = gb[..., 0:1] * o_c + gb[..., 1:2] * o_s + gb[..., 2:3] * o_w
        return o.astype(cols.dtype)

    out = lax.map(step, (jnp.arange(n_q, dtype=jnp.int32), qh, gh))
    return jnp.transpose(out, (1, 0, 4, 2, 3, 5)).reshape(B, S, HQ * dh)

def memory_attention(qm, mem_n, w_kv):
    B, S = qm.shape[:2]
    kv = (mem_n @ w_kv).reshape(B, -1, 2, MEM_HEADS, HEAD_DIM)
    k, v = kv[:, :, 0], kv[:, :, 1]
    s = jnp.einsum('bshd,bmhd->bhsm', qm, k).astype(jnp.float32) * HEAD_DIM ** -0.5
    p = jax.nn.softmax(s, axis=-1)
    o = jnp.einsum('bhsm,bmhd->bshd', p, v.astype(jnp.float32))
    return o.reshape(B, S, MEM_WIDTH).astype(qm.dtype)

def conv_glu(h, w_up, conv_w, conv_b, w_down):
    gate, val = jnp.split(h @ w_up, 2, axis=-1)
    gate = causal_dwconv(gate, conv_w) + conv_b
    return (jax.nn.silu(gate) * val) @ w_down

def second_inputs(seed: int = 0) -> dict:
    key = jax.random.key(seed)
    ks = iter(jax.random.split(key, 32))
    f32 = jnp.float32
    nrm = lambda shape, scale: scale * jax.random.normal(next(ks), shape, f32)
    gain = lambda shape: 1.0 + nrm(shape, 0.02)
    x = nrm((BATCH, SEQ, D_MODEL), 1.0)
    mem = nrm((BATCH, MEM_TOKENS, D_MODEL), 1.0)
    rel_bias = nrm((NUM_BUCKETS, NSA_Q_HEADS), 0.2)
    norm_mix_w = gain((DEPTH, D_MODEL))
    norm_ffn_w = gain((DEPTH, D_MODEL))
    final_norm_w = gain((D_MODEL,))
    mem_norm_w = gain((DEPTH, D_MODEL))
    mem_w_kv = nrm((DEPTH, D_MODEL, 2 * MEM_WIDTH), D_MODEL ** -0.5)
    w_out = nrm((DEPTH, MIX_WIDTH, D_MODEL), MIX_WIDTH ** -0.5)
    gdn_w_in = nrm((N_GDN, D_MODEL, GDN_COLS + MEM_WIDTH), D_MODEL ** -0.5)
    gdn_conv_w = nrm((N_GDN, GDN_CONV, 3 * GDN_HEADS * HEAD_DIM), GDN_CONV ** -0.5)
    gdn_a_log = jnp.log(jax.random.uniform(next(ks), (N_GDN, GDN_HEADS), f32, 1.0, 16.0))
    dt = jnp.exp(jax.random.uniform(next(ks), (N_GDN, GDN_HEADS), f32, math.log(1e-3), math.log(1e-1)))
    gdn_dt_bias = dt + jnp.log(-jnp.expm1(-dt))
    gdn_norm_w = gain((N_GDN, HEAD_DIM))
    nsa_w_in = nrm((N_NSA, D_MODEL, NSA_COLS + MEM_WIDTH), D_MODEL ** -0.5)
    nsa_cmp_pos_k = nrm((N_NSA, CMP_LEN, HEAD_DIM), 0.1)
    nsa_cmp_w1_k = nrm((N_NSA, CMP_LEN * HEAD_DIM, HEAD_DIM), (CMP_LEN * HEAD_DIM) ** -0.5)
    nsa_cmp_w2_k = nrm((N_NSA, HEAD_DIM, HEAD_DIM), HEAD_DIM ** -0.5)
    nsa_cmp_pos_v = nrm((N_NSA, CMP_LEN, HEAD_DIM), 0.1)
    nsa_cmp_w1_v = nrm((N_NSA, CMP_LEN * HEAD_DIM, HEAD_DIM), (CMP_LEN * HEAD_DIM) ** -0.5)
    nsa_cmp_w2_v = nrm((N_NSA, HEAD_DIM, HEAD_DIM), HEAD_DIM ** -0.5)
    ffn_w_up = nrm((DEPTH, D_MODEL, 2 * D_FF), D_MODEL ** -0.5)
    ffn_conv_w = nrm((DEPTH, FFN_CONV, D_FF), FFN_CONV ** -0.5)
    ffn_conv_b = nrm((DEPTH, D_FF), 0.02)
    ffn_w_down = nrm((DEPTH, D_FF, D_MODEL), D_FF ** -0.5)
    return {'x': x, 'mem': mem, 'rel_bias': rel_bias, 'norm_mix_w': norm_mix_w,
            'norm_ffn_w': norm_ffn_w, 'final_norm_w': final_norm_w, 'mem_norm_w': mem_norm_w,
            'mem_w_kv': mem_w_kv, 'w_out': w_out, 'gdn_w_in': gdn_w_in, 'gdn_conv_w': gdn_conv_w,
            'gdn_a_log': gdn_a_log, 'gdn_dt_bias': gdn_dt_bias, 'gdn_norm_w': gdn_norm_w,
            'nsa_w_in': nsa_w_in, 'nsa_cmp_pos_k': nsa_cmp_pos_k, 'nsa_cmp_w1_k': nsa_cmp_w1_k,
            'nsa_cmp_w2_k': nsa_cmp_w2_k, 'nsa_cmp_pos_v': nsa_cmp_pos_v, 'nsa_cmp_w1_v': nsa_cmp_w1_v,
            'nsa_cmp_w2_v': nsa_cmp_w2_v, 'ffn_w_up': ffn_w_up, 'ffn_conv_w': ffn_conv_w,
            'ffn_conv_b': ffn_conv_b, 'ffn_w_down': ffn_w_down}

def second_block(x, mem, rel_bias, norm_mix_w, norm_ffn_w, final_norm_w, mem_norm_w, mem_w_kv, w_out,
              gdn_w_in, gdn_conv_w, gdn_a_log, gdn_dt_bias, gdn_norm_w, nsa_w_in, nsa_cmp_pos_k,
              nsa_cmp_w1_k, nsa_cmp_w2_k, nsa_cmp_pos_v, nsa_cmp_w1_v, nsa_cmp_w2_v, ffn_w_up,
              ffn_conv_w, ffn_conv_b, ffn_w_down):
    B, S, _ = x.shape
    for i in range(DEPTH):
        h = rms_norm(x, norm_mix_w[i])
        mem_n = rms_norm(mem, mem_norm_w[i])
        j = i // N_MIXERS
        if i % N_MIXERS == 0:
            proj = h @ gdn_w_in[j]
            mix = gdn_mixer(proj[..., :GDN_COLS], gdn_conv_w[j], gdn_a_log[j], gdn_dt_bias[j], gdn_norm_w[j])
            qm = proj[..., GDN_COLS:]
        else:
            proj = h @ nsa_w_in[j]
            mix = nsa_mixer(proj[..., :NSA_COLS], rel_bias, nsa_cmp_pos_k[j], nsa_cmp_w1_k[j],
                            nsa_cmp_w2_k[j], nsa_cmp_pos_v[j], nsa_cmp_w1_v[j], nsa_cmp_w2_v[j])
            qm = proj[..., NSA_COLS:]
        mo = memory_attention(qm.reshape(B, S, MEM_HEADS, HEAD_DIM), mem_n, mem_w_kv[i])
        x = x + jnp.concatenate([mix, mo], axis=-1) @ w_out[i]
        x = x + conv_glu(rms_norm(x, norm_ffn_w[i]), ffn_w_up[i], ffn_conv_w[i], ffn_conv_b[i], ffn_w_down[i])
    return rms_norm(x, final_norm_w)


def setup_inputs(seed=0):
    out = dict(first_inputs(seed))
    for name, value in second_inputs(seed + 1).items():
        if name != "x":
            out[name + "_2"] = value
    return out


def reference(
    x, c, ctx, c_ctx, w_ada, b_ada, norm1_g, norm2_g, w_in, ml_conv_w, ml_conv_b, ml_gate_b,
    ml_norm_g, gm_ln_g, gm_ln_b, gm_w_s, gm_b_s, cv_dw_w, cv_dw_b, cv_ln_g, cv_ln_b, w_branch,
    w_out, peer_w_q, peer_keys, peer_u, peer_v, final_norm_g, mem_2, rel_bias_2, norm_mix_w_2,
    norm_ffn_w_2, final_norm_w_2, mem_norm_w_2, mem_w_kv_2, w_out_2, gdn_w_in_2, gdn_conv_w_2,
    gdn_a_log_2, gdn_dt_bias_2, gdn_norm_w_2, nsa_w_in_2, nsa_cmp_pos_k_2, nsa_cmp_w1_k_2,
    nsa_cmp_w2_k_2, nsa_cmp_pos_v_2, nsa_cmp_w1_v_2, nsa_cmp_w2_v_2, ffn_w_up_2, ffn_conv_w_2,
    ffn_conv_b_2, ffn_w_down_2,
):
    x = first_block(
        x, c, ctx, c_ctx, w_ada, b_ada, norm1_g, norm2_g, w_in, ml_conv_w, ml_conv_b, ml_gate_b,
        ml_norm_g, gm_ln_g, gm_ln_b, gm_w_s, gm_b_s, cv_dw_w, cv_dw_b, cv_ln_g, cv_ln_b,
        w_branch, w_out, peer_w_q, peer_keys, peer_u, peer_v, final_norm_g,
    )
    return second_block(
        x, mem_2, rel_bias_2, norm_mix_w_2, norm_ffn_w_2, final_norm_w_2, mem_norm_w_2,
        mem_w_kv_2, w_out_2, gdn_w_in_2, gdn_conv_w_2, gdn_a_log_2, gdn_dt_bias_2, gdn_norm_w_2,
        nsa_w_in_2, nsa_cmp_pos_k_2, nsa_cmp_w1_k_2, nsa_cmp_w2_k_2, nsa_cmp_pos_v_2,
        nsa_cmp_w1_v_2, nsa_cmp_w2_v_2, ffn_w_up_2, ffn_conv_w_2, ffn_conv_b_2, ffn_w_down_2,
    )


_drawn_inputs = setup_inputs


def setup_inputs(seed=0):
    import zlib

    import numpy as np

    out = dict(_drawn_inputs(seed))
    spreads = {}
    factors = {'norm1_g': 4.612,
     'norm2_g': 4.021,
     'ml_conv_b': 46.9,
     'ml_norm_g': 8.0,
     'gm_ln_g': 8.0,
     'gm_ln_b': 8.0,
     'gm_b_s': 8.0,
     'cv_dw_b': 6.868,
     'cv_ln_g': 8.0,
     'cv_ln_b': 8.0,
     'rel_bias_2': 3.03,
     'norm_mix_w_2': 3.091,
     'norm_ffn_w_2': 2.884,
     'final_norm_w_2': 8.287,
     'mem_norm_w_2': 8.0,
     'gdn_norm_w_2': 5.701,
     'nsa_cmp_pos_k_2': 21.455,
     'nsa_cmp_pos_v_2': 23.211,
     'ffn_conv_b_2': 4.271}
    for name, (base, spread) in spreads.items():
        noise = np.random.default_rng([zlib.crc32(name.encode()), seed]).standard_normal(out[name].shape)
        drawn = base * np.exp(spread * noise) if base else spread * noise
        out[name] = jnp.asarray(drawn.astype(out[name].dtype))
    for name, factor in factors.items():
        out[name] = (out[name] * factor).astype(out[name].dtype)
    return out
```

```python
import numpy as np
from contextlib import ExitStack, contextmanager

import concourse.bass as bass
from concourse import mybir

F32 = mybir.dt.float32
U32 = mybir.dt.uint32
ALU = mybir.AluOpType
ACT = mybir.ActivationFunctionType
AX = mybir.AxisListType
ds = bass.ds

P = 128
D = 1024
KD = D // P
T1 = 256
CTX = 256
TALL = T1 + CTX
DEPTH = 2
EPS = 1e-6
MASKED = -1e30
MIX = D // 4
HEADS = 4
DH = MIX // HEADS
V_OFF, GATE_OFF_ML, O_OFF = 2 * MIX, 3 * MIX, 3 * MIX + 16
GM_OFF = 4 * MIX + 16
CV_OFF = GM_OFF + 2 * MIX
FT_OFF = CV_OFF + 2 * MIX
BR_OFF = FT_OFF + MIX
CV_K = 31
PAD = CV_K // 2
PH, TOPK, NKEYS = 8, 16, 128
NEXP = NKEYS * NKEYS
GH = D // P
KV_W = 256
MEM_W = 512
MEM_H = 4
CAT = D + MEM_W
D_FF = 2816
N_CMP = (T1 - 32) // 16 + 1
NB = 4
SCALE = float(P) ** -0.5


SEMS = 16


@contextmanager
def stage(K, *names):
    nc = K.nc
    turn = K.stages % 2
    K.stages += 1
    sems = K.sems[turn][0:len(names)]
    retired = K.sems[1 - turn]
    with nc.Block(no_gpsimd_drain=True) as block:
        @block.gpsimd
        def _(pool):
            pool.sem_clear(range(retired[0].num, retired[-1].num + 1))
        yield (block, *sems)


class Core:

    def __init__(self, nc, dram, dense, skew, out):
        self.nc, self.dram, self.dense, self.skew, self.out = nc, dram, dense, skew, out


class Chain:

    def __init__(self, engine, sem):
        self.engine, self.sem, self.count = engine, sem, 0

    def __call__(self, instruction):
        self.count += 1
        instruction.then_inc(self.sem, 1)
        self.engine.wait_ge(self.sem, self.count)


def load(K, *pairs):
    with stage(K, "loaded") as (block, loaded):
        @block.sync
        def _(sp):
            for dst, src in pairs:
                sp.dma_start(dst, src).then_inc(loaded, 16)
            sp.wait_ge(loaded, 16 * len(pairs))


def project(K, weights, k_tiles, acts, jobs, width=512, ring=2, engine="scalar"):
    nc = K.nc
    items = []
    for n, (c0, cw, by_channel, where, evacuate) in enumerate(jobs):
        if by_channel:
            items += [(n, o, min(P, cw - o), None) for o in range(0, cw, P)]
        else:
            items += [(n, 0, cw, t) for t in where]
    ends = [max(i for i, it in enumerate(items) if it[0] == n) + 1 for n in range(len(jobs))]
    names = ["psum_ready", "psum_free", "step"] + [f"weights{r}" for r in range(ring)]
    K.uid += 1
    with nc.sbuf_tensor(f"wring{K.uid}", [P, ring, k_tiles, width], F32) as wt, stage(K, *names) as (block, ready, free, step, *loaded):
        @block.sync
        def _(sp):
            for n, (c0, cw, _b, _w, _e) in enumerate(jobs):
                if n >= ring:
                    sp.wait_ge(ready, ends[n - ring])
                sp.dma_start(wt[:, n % ring, :, 0:cw],
                             weights[:, c0:c0 + cw].rearrange("(k p) n -> p k n", p=P)).then_inc(loaded[n % ring], 16)

        @block.tensor
        def _(pe):
            for i, (n, o, w, t) in enumerate(items):
                slot = n % ring
                pe.wait_ge(loaded[slot], 16 * (n // ring + 1))
                if i >= NB:
                    pe.wait_ge(free, i - NB + 1)
                bank = K.ps[i % NB]
                for k in range(k_tiles):
                    if t is None:
                        t0, t1 = jobs[n][3]
                        last = pe.matmul(bank[0:w, 0:t1 - t0], wt[:, slot, k, o:o + w], acts[:, k, t0:t1],
                                         start=k == 0, stop=k == k_tiles - 1)
                    else:
                        last = pe.matmul(bank[:, 0:w], acts[:, k, t * P:(t + 1) * P], wt[:, slot, k, 0:w],
                                         start=k == 0, stop=k == k_tiles - 1)
                last.then_inc(ready, 1)

        def reader(eng):
            chain = Chain(eng, step)
            for i, (n, o, w, t) in enumerate(items):
                eng.wait_ge(ready, i + 1)
                if i and engine == "vector":
                    eng.wait_ge(free, i)
                if t is None:
                    t0, t1 = jobs[n][3]
                    tile = K.ps[i % NB][0:w, 0:t1 - t0]
                else:
                    tile = K.ps[i % NB][:, 0:w]
                jobs[n][4](eng, chain, tile, o, t).then_inc(free, 1)

        if engine == "scalar":
            block.scalar(reader)
        else:
            block.vector(reader)


def transpose(K, groups):
    nc = K.nc
    with stage(K, "turned", "free_even", "free_odd") as (block, turned, free_even, free_odd):
        frees = (free_even, free_odd)

        def bank(i):
            ins, out = groups[i]
            f, n, p = out.shape
            return K.ps[i % NB][0:f, 0:n * p].rearrange("f (n p) -> f n p", n=n)

        @block.tensor
        def _(pe):
            for i, (ins, out) in enumerate(groups):
                if i >= NB:
                    pe.wait_ge(frees[i % 2], i // 2 - 1)
                for j, a in enumerate(ins):
                    p = a.shape[0]
                    last = pe.transpose(bank(i)[:, j, :], a, K.ident[0:p, 0:p])
                last.then_inc(turned, 1)

        @block.scalar
        def _(act):
            for i in range(0, len(groups), 2):
                act.wait_ge(turned, i + 1)
                act.activation(groups[i][1], bank(i), ACT.Copy).then_inc(free_even, 1)

        @block.vector
        def _(dve):
            for i in range(1, len(groups), 2):
                dve.wait_ge(turned, i + 1)
                dve.tensor_copy(groups[i][1], bank(i)).then_inc(free_odd, 1)


def rows_to_channels(K, rows, out, tiles, channels):
    groups = []
    for t in tiles:
        for c in range(0, channels // P, 4):
            n = min(4, channels // P - c)
            groups.append(([rows[:, t, (c + j) * P:(c + j + 1) * P] for j in range(n)],
                           out[:, c:c + n, t * P:(t + 1) * P]))
    transpose(K, groups)


def inverse_root(K, values, add):
    with stage(K, "shifted", "rooted") as (block, shifted, rooted):
        @block.vector
        def _(dve):
            dve.tensor_scalar_add(values, values, add).then_inc(shifted, 1)
            dve.wait_ge(rooted, 1)
            dve.reciprocal(values, values)

        @block.scalar
        def _(act):
            act.wait_ge(shifted, 1)
            act.activation(values, values, ACT.Sqrt).then_inc(rooted, 1)


def rms_norm(K, rows, tiles, gain_of, shift_of, out, chans=None):
    nc = K.nc
    ss = K.small[:, 0:len(tiles)]
    with stage(K, "squared") as (block, squared):
        @block.scalar
        def _(act):
            for i, t in enumerate(tiles):
                if i >= 1:
                    act.wait_ge(squared, i)
                act.activation(K.junk[:, 0:D], rows[:, t, :], ACT.Square, scale=D ** -0.5,
                               accum_out=ss[:, i:i + 1]).then_inc(squared, 1)
    inverse_root(K, ss, EPS)
    with stage(K, "scaled", "shifted") as (block, scaled, shifted):
        @block.vector
        def _(dve):
            for i, t in enumerate(tiles):
                dve.scalar_tensor_tensor(out=out[:, t, :], in0=rows[:, t, :], scalar=ss[:, i:i + 1], in1=gain_of(t),
                                         op0=ALU.mult, op1=ALU.mult).then_inc(scaled, 1)

        @block.gpsimd
        def _(pool):
            if shift_of:
                for i, t in enumerate(tiles):
                    pool.wait_ge(scaled, i + 1)
                    pool.tensor_tensor(out[:, t, :], out[:, t, :], shift_of(t), ALU.add).then_inc(shifted, 1)
                pool.wait_ge(shifted, len(tiles))
    if chans is not None:
        rows_to_channels(K, out, chans, tiles, D)


def layer_norm(K, rows, tiles, width, gain, bias, silu=False):
    nc = K.nc
    n = len(tiles)
    stats = K.small[:, 32:32 + 6 * n].rearrange("p (n s) -> p n s", s=6)
    mv = K.small[:, 0:2 * n].rearrange("p (n s) -> p n s", s=2)
    with stage(K, "step") as (block, step):
        @block.vector
        def _(dve):
            chain = Chain(dve, step)
            for i, t in enumerate(tiles):
                chain(dve.bn_stats(stats[:, i, :], rows[:, t, :]))
            for i, t in enumerate(tiles):
                dve.bn_aggr(mv[:, i, :], stats[:, i, :])
    inverse_root(K, mv[:, :, 1], EPS)
    with stage(K, "step", "normed") as (block, step, normed):
        @block.vector
        def _(dve):
            chain = Chain(dve, step)
            for i, t in enumerate(tiles):
                chain(dve.tensor_scalar(rows[:, t, :], rows[:, t, :], mv[:, i, 0:1], mv[:, i, 1:2],
                                        ALU.subtract, ALU.mult))
                chain(dve.tensor_tensor(rows[:, t, :], rows[:, t, :], gain, ALU.mult))
                dve.tensor_tensor(rows[:, t, :], rows[:, t, :], bias, ALU.add).then_inc(normed, 1)

        @block.scalar
        def _(act):
            if silu:
                for i, t in enumerate(tiles):
                    act.wait_ge(normed, i + 1)
                    act.activation(rows[:, t, :], rows[:, t, :], ACT.Silu)



def modulation(K, l, s_cols, mod):
    nc = K.nc
    w = K.dram["w_ada"][l]
    n_chunks = 6 * D // 512
    with nc.sbuf_tensor(f"ada_w{l}", [P, 2, KD, 512], F32) as wt, nc.sbuf_tensor(f"ada_b{l}", [2, 6 * D], F32) as ball, \
            nc.sbuf_tensor(f"ada_row{l}", [2, 2, 512], F32) as row, nc.sbuf_tensor(f"ada_g{l}", [P, 2, D], F32) as gains:
        load(K, (ball[:, :], K.dram["b_ada"][l:l + 1, :].broadcast_to([2, 6 * D])),
             (gains[:, 0, :], K.dram["norm1_g"][l:l + 1, :].broadcast_to([P, D])),
             (gains[:, 1, :], K.dram["norm2_g"][l:l + 1, :].broadcast_to([P, D])))
        with stage(K, "w0", "w1", "row_ready", "row_sum", "spread", "copied") as (block, w0, w1, row_ready, row_sum, spread, copied):
            loaded = (w0, w1)

            @block.sync
            def _(sp):
                for n in range(n_chunks):
                    if n >= 2:
                        sp.wait_ge(row_ready, n - 1)
                    sp.dma_start(wt[:, n % 2, :, :], w[:, n * 512:(n + 1) * 512].rearrange("(k p) n -> p k n", p=P))\
                      .then_inc(loaded[n % 2], 16)

            @block.tensor
            def _(pe):
                def spread_row(n):
                    pe.wait_ge(row_sum, n + 1)
                    if n >= 1:
                        pe.wait_ge(copied, n)
                    for s in range(2):
                        last = pe.matmul(K.ps[2 + s][:, :], K.pick2[0:2, s, :], row[0:2, n % 2, :], start=True, stop=True)
                    last.then_inc(spread, 1)

                for n in range(n_chunks):
                    pe.wait_ge(loaded[n % 2], 16 * (n // 2 + 1))
                    if n >= 2:
                        pe.wait_ge(row_sum, n - 1)
                    for k in range(KD):
                        last = pe.matmul(K.ps[n % 2][0:2, :], s_cols[:, k, :], wt[:, n % 2, k, :], start=k == 0, stop=k == KD - 1)
                    last.then_inc(row_ready, 1)
                    if n >= 1:
                        spread_row(n - 1)
                spread_row(n_chunks - 1)

            @block.vector
            def _(dve):
                for n in range(n_chunks):
                    dve.wait_ge(row_ready, n + 1)
                    if n >= 2:
                        dve.wait_ge(spread, n - 1)
                    dve.tensor_tensor(row[0:2, n % 2, :], K.ps[n % 2][0:2, :], ball[0:2, n * 512:(n + 1) * 512],
                                      ALU.add).then_inc(row_sum, 1)

            @block.scalar
            def _(act):
                for n in range(n_chunks):
                    act.wait_ge(spread, n + 1)
                    c, half = divmod(n, 2)
                    act.activation(mod[c][:, 0, half * 512:(half + 1) * 512], K.ps[2][:, :], ACT.Copy)
                    act.activation(mod[c][:, 1, half * 512:(half + 1) * 512], K.ps[3][:, :], ACT.Copy).then_inc(copied, 1)
        with stage(K) as (block,):
            @block.vector
            def _(dve):
                for s in range(2):
                    for c, g in ((1, 0), (4, 1)):
                        dve.scalar_tensor_tensor(out=mod[c][:, s, :], in0=mod[c][:, s, :], scalar=1.0, in1=gains[:, g, :],
                                                 op0=ALU.add, op1=ALU.mult)


def copy_to(dst_of, func=ACT.Copy):
    def evacuate(eng, chain, psum, o, t):
        return eng.activation(dst_of(o, t), psum, func)
    return evacuate


def mlstm(K, l, hT, zT, n_lat_only, vones, gates, osig):
    nc = K.nc
    out_tiles = [2, 3] if n_lat_only else [0, 1, 2, 3]
    q0 = CTX if n_lat_only else 0
    with ExitStack() as mem:
        def sb(name, shape):
            return mem.enter_context(nc.sbuf_tensor(f"ml_{name}{l}", shape, F32))
        gcol = sb("gcol", [P, 2, 4, 2, 4])
        neg_run = sb("neg_run", [4, 2, TALL])
        qk = sb("qk", [P, 4, TALL])
        cw = sb("cw", [P, 4, 3])
        cb = sb("cb", [P, 4])
        gb = sb("gb", [P, 16])
        ng = sb("ng", [P, MIX])
        early = ExitStack()
        padded = early.enter_context(nc.sbuf_tensor(f"ml_padded{l}", [P, 4, 2, CTX + 2], F32))
        with stage(K) as (block,):
            @block.vector
            def _(dve):
                dve.memset(padded[:, :, :, 0:1], 0.0)
                dve.memset(padded[:, :, :, CTX + 1:CTX + 2], 0.0)
        load(K, (cw[:, :, :], K.dram["ml_conv_w"][l]), (cb[:, :], K.dram["ml_conv_b"][l]),
             (gb[:, :], K.dram["ml_gate_b"][l:l + 1, :].broadcast_to([P, 16])),
             (ng[:, :], K.dram["ml_norm_g"][l:l + 1, :].broadcast_to([P, MIX])))
        project(K, K.dram["w_in"][l], KD, hT, [
            (0, 512, True, (0, TALL), lambda eng, chain, psum, o, t: eng.activation(
                padded[:, o // P, :, 1:CTX + 1], psum.rearrange("p (s t) -> p s t", s=2), ACT.Copy))])
        with stage(K, "step", "conved") as (block, step, conved):
            @block.vector
            def _(dve):
                chain = Chain(dve, step)
                for j in range(4):
                    dst = qk[:, j, :].rearrange("p (s t) -> p s t", s=2)
                    chain(dve.tensor_scalar(dst, padded[:, j, :, 0:CTX], cw[:, j, 0:1], cb[:, j:j + 1], ALU.mult, ALU.add))
                    chain(dve.scalar_tensor_tensor(out=dst, in0=padded[:, j, :, 1:CTX + 1], scalar=cw[:, j, 1:2], in1=dst,
                                                   op0=ALU.mult, op1=ALU.add))
                    dve.scalar_tensor_tensor(out=dst, in0=padded[:, j, :, 2:CTX + 2], scalar=cw[:, j, 2:3], in1=dst,
                                             op0=ALU.mult, op1=ALU.add).then_inc(conved, 1)

            @block.scalar
            def _(act):
                for j in range(4):
                    act.wait_ge(conved, j + 1)
                    act.activation(qk[:, j, :], qk[:, j, :], ACT.Silu)
        early.close()
        early = ExitStack()

        def sb_early(name, shape):
            return early.enter_context(nc.sbuf_tensor(f"ml_{name}{l}", shape, F32))
        lf = sb_early("lf", [P, 4, 8])
        soft = sb_early("soft", [P, 4, 8])
        with stage(K, "step", "to_act", "softened") as (block, step, to_act, softened):
            @block.vector
            def _(dve):
                chain = Chain(dve, step)
                chain(dve.tensor_tensor(gates[:, :, :], gates[:, :, :], gb[:, None, :].broadcast_to([P, 4, 16]), ALU.add))
                dve.tensor_single_scalar(lf[:, :, :], gates[:, :, 8:16], 0.0, ALU.min).then_inc(to_act, 1)
                dve.wait_ge(softened, 3)
                dve.wait_ge(to_act, 1)
                dve.tensor_tensor(lf[:, :, :], lf[:, :, :], soft[:, :, :], ALU.subtract)

            @block.scalar
            def _(act):
                act.wait_ge(to_act, 1)
                chain = Chain(act, softened)
                chain(act.activation(soft[:, :, :], gates[:, :, 8:16], ACT.Abs))
                chain(act.activation(soft[:, :, :], soft[:, :, :], ACT.Exp, scale=-1.0))
                chain(act.activation(soft[:, :, :], soft[:, :, :], ACT.Ln, bias=1.0))
        li_r, lf_r = sb_early("li_r", [4, 2, TALL]), sb_early("lf_r", [4, 2, TALL])
        cum, run = sb_early("cum", [4, 2, TALL]), sb_early("run", [4, 2, TALL])
        gsrc = sb_early("gsrc", [4, 2, 2, TALL])
        with stage(K, "turned", "copied") as (block, turned, copied):
            @block.tensor
            def _(pe):
                for t in range(4):
                    for b, src in enumerate((gates, lf)):
                        for d in range(2):
                            last = pe.transpose(K.ps[t][0:4, (2 * b + d) * P:(2 * b + d + 1) * P],
                                                src[:, t, 4 * d:4 * d + 4], K.ident[:, :])
                last.then_inc(turned, 1)

            @block.vector
            def _(dve):
                dve.wait_ge(turned, 1)
                for t in range(4):
                    for b, dst in enumerate((li_r, lf_r)):
                        dve.tensor_copy(dst[:, 0, t * P:(t + 1) * P], K.ps[t][0:4, 2 * b * P:(2 * b + 1) * P])
                        at = (t // 2) * CTX + (1 - t % 2) * P
                        rev = dst[:, 1, at:at + P]
                        dve.tensor_copy(rev, K.ps[t][0:4, (2 * b + 1) * P:(2 * b + 2) * P][:, ::-1])
        with stage(K, "step") as (block, step):
            @block.vector
            def _(dve):
                chain = Chain(dve, step)
                for d in range(2):
                    chain(dve.tensor_tensor_scan(cum[:, d, :], K.ones4[0:4, :], lf_r[:, d, :], 0.0, ALU.mult, ALU.add))
                chain(dve.tensor_tensor(li_r[:, :, :], li_r[:, :, :], cum[:, :, :], ALU.subtract))
                for d in range(2):
                    chain(dve.tensor_tensor_scan(run[:, d, :], li_r[:, d, :], li_r[:, d, :], 0.0, ALU.max, ALU.max))
                chain(dve.tensor_tensor(cum[:, :, :], cum[:, :, :], run[:, :, :], ALU.add))
                for src, dst, sign in ((li_r, gsrc[:, 0], 1.0), (cum, gsrc[:, 1], -1.0), (run, neg_run, -1.0)):
                    dve.tensor_single_scalar(dst[:, 0, :], src[:, 0, :], sign, ALU.mult)
                    for s in range(2):
                        dve.tensor_single_scalar(dst[:, 1, s * CTX:(s + 1) * CTX],
                                                 src[:, 1, s * CTX:(s + 1) * CTX][:, ::-1], sign, ALU.mult)
        with stage(K, "turned") as (block, turned):
            @block.tensor
            def _(pe):
                for d in range(2):
                    for t in range(4):
                        for b in range(2):
                            c = ((d * 4 + t) * 2 + b) * 4
                            last = pe.transpose(K.ps[0][:, c:c + 4], gsrc[:, b, d, t * P:(t + 1) * P], K.ident[0:4, 0:4])
                last.then_inc(turned, 1)

            @block.scalar
            def _(act):
                act.wait_ge(turned, 1)
                view = K.ps[0][:, 0:64].rearrange("p (a b h) -> p a b h", b=2, h=4)
                dst = gcol[:, :, :, :, :].rearrange("p d t b h -> p (d t) b h")
                act.activation(dst[:, :, 0, :], view[:, :, 0, :], ACT.Copy)
                act.activation(dst[:, :, 1, :], view[:, :, 1, :], ACT.Exp)
        early.close()
        hacc = sb("hacc", [P, 4, MIX])
        wts = sb("wts", [P, 2, 4, TALL])
        prod = sb("prod", [P, 2, 4, TALL])
        den = sb("den", [P, 2, 4])
        tmp = sb("tmp", [P, 4, DH])
        mask = sb("mask", [P, 2, 4, TALL])
        load(K, (mask[:, :, :, :], K.dram["ml_mask"]))
        n_it = 2 * HEADS
        begin = [q0, q0, CTX, CTX]

        def sources(qt, d):
            if qt < 2:
                return [s for s in (0, 1) if (s <= qt if d == 0 else s >= qt)]
            return [0, 1] + [s for s in (2, 3) if (s <= qt if d == 0 else s >= qt)]

        with stage(K, "scores", "spread", "gated", "exped", "weighted", "summed", "step", "out_read") as \
                (block, scores, spread, gated, exped, weighted, summed, step, out_read):
            @block.tensor
            def _(pe):
                def sums(i):
                    h, d = divmod(i, 2)
                    pe.wait_ge(weighted, i + 1)
                    if i >= 2:
                        pe.wait_ge(out_read, i - 1)
                    for qt in out_tiles:
                        src = sources(qt, d)
                        for s in src:
                            last = pe.matmul(K.ps[6 + i % 2][:, qt * 65:qt * 65 + 65], prod[:, i % 2, s, qt * P:(qt + 1) * P],
                                             vones[:, s, h, :], start=s == src[0], stop=s == src[-1])
                    last.then_inc(summed, 1)

                for i in range(n_it):
                    h, d = divmod(i, 2)
                    r = (h % 2) * DH
                    if d == 0:
                        if i:
                            pe.wait_ge(weighted, i)
                        for s in range(4):
                            last = pe.matmul(K.ps[s][:, begin[s]:TALL], qk[r:r + DH, 2 + h // 2, s * P:(s + 1) * P],
                                             qk[r:r + DH, h // 2, begin[s]:TALL], start=True, stop=True)
                        last.then_inc(scores, 1)
                    if i >= 2:
                        pe.wait_ge(gated, i - 1)
                    pe.matmul(K.ps[4 + i % 2][:, :], K.pick4[0:4, h, :], neg_run[:, d, :], start=True, stop=True).then_inc(spread, 1)
                    if i:
                        sums(i - 1)
                sums(n_it - 1)

            @block.scalar
            def _(act):
                for i in range(n_it):
                    act.wait_ge(gated, i + 1)
                    for s in range(4):
                        last = act.activation(wts[:, i % 2, s, begin[s]:TALL], wts[:, i % 2, s, begin[s]:TALL], ACT.Exp)
                    last.then_inc(exped, 1)

            @block.vector
            def _(dve):
                chain = Chain(dve, step)

                def collect(i):
                    h, d = divmod(i, 2)
                    dve.wait_ge(summed, i + 1)
                    o = K.ps[6 + i % 2][:, 0:260].rearrange("p (t c) -> p t c", c=65)
                    lo, n = out_tiles[0], len(out_tiles)
                    o = o[:, lo:4, :]
                    chain(dve.tensor_tensor(den[:, 0, lo:4], o[:, :, 64], gcol[:, d, lo:4, 1, h], ALU.max))
                    chain(dve.scalar_tensor_tensor(out=den[:, 1, lo:4], in0=o[:, :, 64], scalar=-1.0, in1=den[:, 0, lo:4],
                                                   op0=ALU.mult, op1=ALU.max))
                    chain(dve.reciprocal(den[:, 1, lo:4], den[:, 1, lo:4]))
                    rd = den[:, 1, lo:4][:, :, None].broadcast_to([P, n, DH])
                    dst = hacc[:, lo:4, h * DH:(h + 1) * DH]
                    if d == 0:
                        ins = dve.tensor_tensor(dst, o[:, :, 0:64], rd, ALU.mult)
                        ins.then_inc(out_read, 1)
                        dve.wait_ge(out_read, i + 1)
                    else:
                        dve.tensor_tensor(tmp[:, lo:4, :], o[:, :, 0:64], rd, ALU.mult).then_inc(out_read, 1)
                        dve.wait_ge(out_read, i + 1)
                        chain(dve.tensor_tensor(dst, dst, tmp[:, lo:4, :], ALU.add))

                for i in range(n_it):
                    h, d = divmod(i, 2)
                    dve.wait_ge(spread, i + 1)
                    for s in range(4):
                        b = begin[s]
                        last = dve.scalar_tensor_tensor(out=wts[:, i % 2, s, b:TALL], in0=K.ps[4 + i % 2][:, b:TALL],
                                                        scalar=gcol[:, d, s, 0, h:h + 1],
                                                        in1=mask[:, d, s, b:TALL],
                                                        op0=ALU.add, op1=ALU.min)
                    last.then_inc(gated, 1)
                    if i:
                        collect(i - 1)
                    dve.wait_ge(exped, i + 1)
                    dve.wait_ge(scores, h + 1)
                    if i >= 2:
                        dve.wait_ge(summed, i - 1)
                    for s in range(4):
                        b = begin[s]
                        last = dve.scalar_tensor_tensor(out=prod[:, i % 2, s, b:TALL], in0=K.ps[s][:, b:TALL],
                                                        scalar=DH ** -0.5, in1=wts[:, i % 2, s, b:TALL],
                                                        op0=ALU.mult, op1=ALU.mult)
                    last.then_inc(weighted, 1)
                collect(n_it - 1)
        lo, n = out_tiles[0], len(out_tiles)
        ss = sb("ss", [P, 4, 4])
        sq = sb("sq", [P, 4, MIX])
        hv = hacc[:, lo:4, :].rearrange("p t (h d) -> p t h d", h=4)
        with stage(K, "step") as (block, step):
            @block.vector
            def _(dve):
                chain = Chain(dve, step)
                chain(dve.tensor_tensor(sq[:, lo:4, :], hacc[:, lo:4, :], hacc[:, lo:4, :], ALU.mult))
                chain(dve.tensor_reduce(ss[:, lo:4, :], sq[:, lo:4, :].rearrange("p t (h d) -> p t h d", h=4), AX.X, ALU.add))
                dve.tensor_single_scalar(ss[:, lo:4, :], ss[:, lo:4, :], 1.0 / DH, ALU.mult)
        inverse_root(K, ss[:, lo:4, :], EPS)
        with stage(K, "step") as (block, step):
            @block.vector
            def _(dve):
                chain = Chain(dve, step)
                for t in out_tiles:
                    v = hacc[:, t, :].rearrange("p (h d) -> p h d", h=4)
                    chain(dve.tensor_tensor(v, v, ss[:, t, :][:, :, None].broadcast_to([P, 4, DH]), ALU.mult))
                chain(dve.tensor_tensor(hacc[:, lo:4, :], hacc[:, lo:4, :], ng[:, None, :].broadcast_to([P, n, MIX]), ALU.mult))
                dve.tensor_tensor(hacc[:, lo:4, :], hacc[:, lo:4, :], osig[:, lo:4, :], ALU.mult)
        rows_to_channels(K, hacc, zT, out_tiles, MIX)


def gmlp(K, l, zT, gm, tiles):
    nc = K.nc
    lo, n = tiles[0], len(tiles)
    with ExitStack() as mem:
        def sb(name, shape):
            return mem.enter_context(nc.sbuf_tensor(f"gm_{name}{l}", shape, F32))
        ln = sb("ln", [P, 2, MIX])
        ws = sb("ws", [P, 4, P])
        bs = sb("bs", [P, 4])
        mixed = sb("mixed", [P, 4, MIX])
        load(K, (ln[:, 0, :], K.dram["gm_ln_g"][l:l + 1, :].broadcast_to([P, MIX])),
             (ln[:, 1, :], K.dram["gm_ln_b"][l:l + 1, :].broadcast_to([P, MIX])),
             (ws[:, :, :], K.dram["gm_w_s"][l]), (bs[:, :], K.dram["gm_b_s"][l]))
        v = gm[:, :, MIX:2 * MIX]
        layer_norm(K, v, tiles, MIX, ln[:, 0, :], ln[:, 1, :])
        with stage(K, "mixed_s", "step") as (block, done, step):
            @block.tensor
            def _(pe):
                for t in tiles:
                    for g in range(4):
                        last = pe.matmul(K.ps[t][:, g * DH:(g + 1) * DH], ws[:, g, :], v[:, t, g * DH:(g + 1) * DH],
                                         start=True, stop=True)
                    last.then_inc(done, 1)

            @block.vector
            def _(dve):
                chain = Chain(dve, step)
                for i, t in enumerate(tiles):
                    dve.wait_ge(done, i + 1)
                    chain(dve.tensor_tensor(mixed[:, t, :].rearrange("p (g c) -> p g c", g=4),
                                            K.ps[t][:, 0:MIX].rearrange("p (g c) -> p g c", g=4),
                                            bs[:, :][:, :, None].broadcast_to([P, 4, DH]), ALU.add))
                    dve.tensor_tensor(mixed[:, t, :], mixed[:, t, :], gm[:, t, 0:MIX], ALU.mult)
        rows_to_channels(K, mixed, zT, tiles, MIX)


def conv_branch(K, l, hT, zT, streams):
    nc = K.nc
    s0, ns = streams[0], len(streams)
    t0 = s0 * CTX
    tiles = list(range(2 * s0, 4))
    with ExitStack() as mem:
        def sb(name, shape):
            return mem.enter_context(nc.sbuf_tensor(f"cv_{name}{l}", shape, F32))
        a = sb("a", [P, 2, 2, CTX + 2 * PAD])
        b = sb("b", [P, 2, 2, CTX])
        y = sb("y", [P, 2, TALL])
        rows = sb("rows", [P, 4, MIX])
        w = sb("w", [P, 2, CV_K])
        wb = sb("wb", [P, 2])
        ln = sb("ln", [P, 2, MIX])
        with stage(K) as (block,):
            @block.vector
            def _(dve):
                dve.memset(a[:, :, :, :], 0.0)
        load(K, (w[:, :, :], K.dram["cv_dw_w"][l]), (wb[:, :], K.dram["cv_dw_b"][l]),
             (ln[:, 0, :], K.dram["cv_ln_g"][l:l + 1, :].broadcast_to([P, MIX])),
             (ln[:, 1, :], K.dram["cv_ln_b"][l:l + 1, :].broadcast_to([P, MIX])))

        def evac(eng, chain, psum, o, t):
            j = o // P
            src = psum.rearrange("p (s t) -> p s t", s=ns)
            if j < 2:
                return eng.activation(a[:, j, s0:2, PAD:PAD + CTX], src, ACT.Copy)
            return eng.activation(b[:, j - 2, s0:2, :], src, ACT.Sigmoid)
        project(K, K.dram["w_in"][l], KD, hT, [(CV_OFF, 512, True, (t0, TALL), evac)])
        with stage(K, "step", "glu") as (block, step, glu):
            @block.gpsimd
            def _(pool):
                for j in range(2):
                    pool.tensor_tensor(a[:, j, s0:2, PAD:PAD + CTX], a[:, j, s0:2, PAD:PAD + CTX], b[:, j, s0:2, :],
                                       ALU.mult).then_inc(glu, 1)

            @block.vector
            def _(dve):
                chain = Chain(dve, step)
                for j in range(2):
                    dst = y[:, j, t0:TALL].rearrange("p (s t) -> p s t", s=ns)
                    dve.wait_ge(glu, j + 1)
                    chain(dve.tensor_scalar(dst, a[:, j, s0:2, 0:CTX], w[:, j, 0:1], wb[:, j:j + 1], ALU.mult, ALU.add))
                    for tap in range(1, CV_K):
                        chain(dve.scalar_tensor_tensor(out=dst, in0=a[:, j, s0:2, tap:tap + CTX], scalar=w[:, j, tap:tap + 1],
                                                       in1=dst, op0=ALU.mult, op1=ALU.add))
        transpose(K, [([y[:, j, t * P:(t + 1) * P] for j in range(2)],
                       rows[:, t, :].rearrange("p (j c) -> p j c", j=2)) for t in tiles])
        layer_norm(K, rows, tiles, MIX, ln[:, 0, :], ln[:, 1, :], silu=True)
        rows_to_channels(K, rows, zT, tiles, MIX)


def fourier(K, l, zT, ft, streams):
    nc = K.nc
    with nc.sbuf_tensor(f"ft_mid{l}", [P, 2, 2, CTX], F32) as mid, nc.sbuf_tensor(f"ft_t{l}", [P, 2, 2, CTX], F32) as dft_t, \
            nc.sbuf_tensor(f"ft_c{l}", [P, 2, P], F32) as dft_c:
        load(K, (dft_t[:, :, :, :], K.dram["dft_t"]), (dft_c[:, :, :], K.dram["dft_c"]))
        with stage(K, "timed", "copied", "done", "out_copied") as (block, timed, copied, done, out_copied):
            @block.tensor
            def _(pe):
                for i, s in enumerate(streams):
                    if i:
                        pe.wait_ge(copied, i)
                    for c in range(2):
                        for m in range(2):
                            for k in range(2):
                                last = pe.matmul(K.ps[2 * c + m][:, 0:CTX], ft[:, 2 * s + k, c * P:(c + 1) * P],
                                                 dft_t[:, m, k, :], start=k == 0, stop=k == 1)
                    last.then_inc(timed, 1)
                    pe.wait_ge(copied, i + 1)
                    if i:
                        pe.wait_ge(out_copied, i)
                    for c in range(2):
                        for m in range(2):
                            last = pe.matmul(K.ps[4 + c][:, 0:CTX], dft_c[:, m, :], mid[:, c, m, :], start=m == 0, stop=m == 1)
                    last.then_inc(done, 1)

            @block.scalar
            def _(act):
                for i, s in enumerate(streams):
                    act.wait_ge(timed, i + 1)
                    if i:
                        act.wait_ge(done, i)
                    for c in range(2):
                        for m in range(2):
                            last = act.activation(mid[:, c, m, :], K.ps[2 * c + m][:, 0:CTX], ACT.Copy)
                    last.then_inc(copied, 1)

            @block.vector
            def _(dve):
                for i, s in enumerate(streams):
                    dve.wait_ge(done, i + 1)
                    for c in range(2):
                        last = dve.tensor_copy(zT[:, c, s * CTX:(s + 1) * CTX], K.ps[4 + c][:, 0:CTX])
                    last.then_inc(out_copied, 1)


def merge(K, l, hT, zTs, yT, t0):
    nc = K.nc
    tw = TALL - t0
    jobs = [(b, c) for b in range(4) for c in range(2)]
    with ExitStack() as mem:
        wg = mem.enter_context(nc.sbuf_tensor(f"mg_wg{l}", [P, 2, KD, 512], F32))
        wb = mem.enter_context(nc.sbuf_tensor(f"mg_wb{l}", [P, 2, 2, 512], F32))
        gate = mem.enter_context(nc.sbuf_tensor(f"mg_gate{l}", [P, 2, tw], F32))
        term = mem.enter_context(nc.sbuf_tensor(f"mg_term{l}", [P, 2, tw], F32))
        with stage(K, "w0", "w1", "gate_psum", "branch_psum", "gate_done", "termed", "added") as \
                (block, w0, w1, gate_psum, branch_psum, gate_done, termed, added):
            loaded = (w0, w1)

            @block.sync
            def _(sp):
                for n, (b, c) in enumerate(jobs):
                    if n >= 2:
                        sp.wait_ge(branch_psum, 4 * (n - 1))
                    at = BR_OFF + b * D + c * 512
                    sp.dma_start(wg[:, n % 2, :, :], K.dram["w_in"][l][:, at:at + 512].rearrange("(k p) n -> p k n", p=P)).then_inc(loaded[n % 2], 16)
                    sp.dma_start(wb[:, n % 2, :, :], K.dram["w_branch"][l][b * MIX:(b + 1) * MIX, c * 512:(c + 1) * 512]
                                 .rearrange("(k p) n -> p k n", p=P)).then_inc(loaded[n % 2], 16)

            @block.tensor
            def _(pe):
                for n, (b, c) in enumerate(jobs):
                    pe.wait_ge(loaded[n % 2], 32 * (n // 2 + 1))
                    for j in range(4):
                        i = 4 * n + j
                        if i >= 2:
                            pe.wait_ge(gate_done, i - 1)
                        for k in range(KD):
                            last = pe.matmul(K.ps[i % 2][:, 0:tw], wg[:, n % 2, k, j * P:(j + 1) * P], hT[:, k, t0:TALL],
                                             start=k == 0, stop=k == KD - 1)
                        last.then_inc(gate_psum, 1)
                        if i >= 2:
                            pe.wait_ge(termed, i - 1)
                        for k in range(2):
                            last = pe.matmul(K.ps[2 + i % 2][:, 0:tw], wb[:, n % 2, k, j * P:(j + 1) * P],
                                             zTs[:, b, k, t0:TALL], start=k == 0, stop=k == 1)
                        last.then_inc(branch_psum, 1)

            @block.scalar
            def _(act):
                for i in range(4 * len(jobs)):
                    act.wait_ge(gate_psum, i + 1)
                    if i >= 2:
                        act.wait_ge(termed, i - 1)
                    act.activation(gate[:, i % 2, :], K.ps[i % 2][:, 0:tw], ACT.Sigmoid).then_inc(gate_done, 1)

            @block.vector
            def _(dve):
                for i in range(4 * len(jobs)):
                    n, j = divmod(i, 4)
                    b, c = jobs[n]
                    dve.wait_ge(gate_done, i + 1)
                    dve.wait_ge(branch_psum, i + 1)
                    dst = yT[:, 4 * c + j, t0:TALL]
                    if b == 0:
                        dve.tensor_tensor(dst, K.ps[2 + i % 2][:, 0:tw], gate[:, i % 2, :], ALU.mult).then_inc(termed, 1)
                    else:
                        if i >= 10:
                            dve.wait_ge(added, i - 9)
                        dve.tensor_tensor(term[:, i % 2, :], K.ps[2 + i % 2][:, 0:tw], gate[:, i % 2, :], ALU.mult).then_inc(termed, 1)
                        dve.wait_ge(termed, i + 1)
                        dve.tensor_tensor(dst, dst, term[:, i % 2, :], ALU.add).then_inc(added, 1)


def add_scaled(K, x, scale_of, width=512):
    def evacuate_at(c0):
        def evacuate(eng, chain, psum, o, t):
            w = psum.shape[1]
            if scale_of is None:
                return eng.tensor_tensor(x[:, t, c0:c0 + w], x[:, t, c0:c0 + w], psum, ALU.add)
            chain(eng.tensor_tensor(K.junk[:, 0:w], psum, scale_of(t)[:, c0:c0 + w], ALU.mult))
            return eng.tensor_tensor(x[:, t, c0:c0 + w], x[:, t, c0:c0 + w], K.junk[:, 0:w], ALU.add)
        return evacuate
    return evacuate_at


def expert_choice(K, l, qT, tiles, choice):
    nc = K.nc
    with ExitStack() as mem:
        def sb(name, shape, dt=F32):
            return mem.enter_context(nc.sbuf_tensor(f"pc_{name}{l}", shape, dt))
        keys = sb("keys", [P, 2, NKEYS])
        sc = sb("sc", [P, 16, NKEYS])
        sc2 = sb("sc2", [P, 16, NKEYS])
        top = sb("top", [P, 16, TOPK])
        topi = sb("topi", [P, 16, TOPK], U32)
        topf = sb("topf", [P, 16, TOPK])
        best = sb("best", [P, PH, TOPK])
        pos = sb("pos", [P, PH, TOPK], U32)
        half = sb("half", [P, 2, PH, TOPK], U32)
        halff = sb("halff", [P, 2, PH, TOPK])
        rows = sb("rows", [P, 3, P])
        tot = sb("tot", [P, 2, PH])
        cand = sc[:, :, :].rearrange("p (h a) n -> p h (a n)", a=2)
        cand2 = sc2[:, :, :].rearrange("p (h a) n -> p h (a n)", a=2)
        hot = sc2[:, :, :].rearrange("p a n -> p (a n)").rearrange("p (q j) -> p q j", j=TOPK)
        load(K, (keys[:, :, :], K.dram["peer_keys"][l]))
        for t in tiles:
            with stage(K, "scored", "copied", "step", "shifted", "exped", "rows_done", "turned") as \
                    (block, scored, copied, step, shifted, exped, rows_done, turned):
                @block.tensor
                def _(pe):
                    for b in range(4):
                        for j in range(4):
                            hp = 4 * b + j
                            last = pe.matmul(K.ps[b][:, j * P:(j + 1) * P], qT[:, hp, t * P:(t + 1) * P], keys[:, hp % 2, :],
                                             start=True, stop=True)
                        last.then_inc(scored, 1)
                    pe.wait_ge(rows_done, 1)
                    for r in range(3):
                        last = pe.transpose(K.ps[4][:, r * P:(r + 1) * P], rows[:, r, :], K.ident[:, :])
                    last.then_inc(turned, 1)

                @block.scalar
                def _(act):
                    for b in range(4):
                        act.wait_ge(scored, b + 1)
                        act.activation(sc[:, 4 * b:4 * b + 4, :], K.ps[b][:, :].rearrange("p (j n) -> p j n", j=4), ACT.Copy).then_inc(copied, 1)
                    act.wait_ge(shifted, 1)
                    act.activation(rows[:, 2, :], rows[:, 2, :], ACT.Exp).then_inc(exped, 1)
                    act.wait_ge(turned, 1)
                    act.activation(choice[:, :, t * P:(t + 1) * P], K.ps[4][:, 0:3 * P].rearrange("p (r n) -> p r n", r=3), ACT.Copy)

                @block.vector
                def _(dve):
                    chain = Chain(dve, step)

                    def top16(vals, idx, src, scratch, n):
                        for i in range(n):
                            last = dve.max(vals[:, i, 0:8], src[:, i, :])
                        chain(last)
                        for i in range(n):
                            dve.max_index(idx[:, i, 0:8], vals[:, i, 0:8], src[:, i, :])
                            last = dve.match_replace(scratch[:, i, :], vals[:, i, 0:8], src[:, i, :], -3e38)
                        chain(last)
                        for i in range(n):
                            last = dve.max(vals[:, i, 8:16], scratch[:, i, :])
                        chain(last)
                        for i in range(n):
                            last = dve.max_index(idx[:, i, 8:16], vals[:, i, 8:16], scratch[:, i, :])
                        chain(last)

                    dve.wait_ge(copied, 4)
                    top16(top, topi, sc, sc2, 16)
                    chain(dve.tensor_copy(topf[:, :, :], topi[:, :, :]))
                    for h in range(PH):
                        last = dve.tensor_tensor(cand[:, h, :].rearrange("p (a b) -> p a b", a=TOPK),
                                                 top[:, 2 * h, :][:, :, None].broadcast_to([P, TOPK, TOPK]),
                                                 top[:, 2 * h + 1, :][:, None, :].broadcast_to([P, TOPK, TOPK]), ALU.add)
                    chain(last)
                    top16(best, pos, cand, cand2, PH)
                    dve.tensor_single_scalar(half[:, 0, :, :], pos[:, :, :], 4, ALU.logical_shift_right)
                    chain(dve.tensor_single_scalar(half[:, 1, :, :], pos[:, :, :], TOPK - 1, ALU.bitwise_and))
                    chain(dve.tensor_copy(halff[:, :, :, :], half[:, :, :, :]))
                    tf = topf[:, :, :].rearrange("p (h a) j -> p h a j", a=2)
                    for a in range(2):
                        chain(dve.tensor_tensor(hot, halff[:, a, :, :].rearrange("p h k -> p (h k)")[:, :, None].broadcast_to([P, P, TOPK]),
                                                K.iota[:, None, 0:TOPK].broadcast_to([P, P, TOPK]), ALU.is_equal))
                        for h in range(PH):
                            hh = hot[:, h * TOPK:(h + 1) * TOPK, :]
                            last = dve.tensor_tensor(hh, hh, tf[:, h, a, :][:, None, :].broadcast_to([P, TOPK, TOPK]), ALU.mult)
                        chain(last)
                        chain(dve.tensor_reduce(rows[:, a, :], hot, AX.X, ALU.add))
                    g = rows[:, 2, :].rearrange("p (h k) -> p h k", h=PH)
                    dve.tensor_tensor(g, best[:, :, :], best[:, :, 0:1].broadcast_to([P, PH, TOPK]), ALU.subtract).then_inc(shifted, 1)
                    dve.wait_ge(exped, 1)
                    chain(dve.tensor_reduce(tot[:, 0, :], g, AX.X, ALU.add))
                    chain(dve.reciprocal(tot[:, 1, :], tot[:, 0, :]))
                    dve.tensor_tensor(g, g, tot[:, 1, :][:, :, None].broadcast_to([P, PH, TOPK]), ALU.mult).then_inc(rows_done, 1)


def spread_choice(K, l, choice, t0, tw):
    nc = K.nc
    rounds = tw // 128
    with ExitStack() as mem:
        first = mem.enter_context(nc.sbuf_tensor(f"sp_a{l}", [P, 2, 4, P], F32))
        second = mem.enter_context(nc.sbuf_tensor(f"sp_b{l}", [P, 2, 4, P], F32))
        buf = mem.enter_context(nc.sbuf_tensor(f"sp_buf{l}", [P, 2, P, 64], F32))
        with stage(K, "hot", "paired", "copied", "stored0", "stored1") as \
                (block, hot, paired, copied, stored0, stored1):
            stored = (stored0, stored1)

            def groups(eng, work, before_slot=None):
                with eng.Fori(0, rounds) as i:
                    for slot in range(2):
                        if before_slot:
                            before_slot(i, slot)
                        with eng.Fori(0, 8) as g:
                            for u in range(2):
                                work(i * 32 + slot * 16 + g * 2 + u, u, slot, g * 2 + u)

            @block.vector
            def _(dve):
                def work(n, u, slot, q0):
                    dve.wait_ge(copied, n + 1)
                    for q in range(4):
                        t = n * 4 + q + t0
                        dve.tensor_scalar(first[:, u, q, :], K.iota[:, :], choice[:, 0, ds(t, 1)],
                                          choice[:, 2, ds(t, 1)], ALU.is_equal, ALU.mult)
                        last = dve.tensor_scalar(second[:, u, q, :], K.iota[:, :], choice[:, 1, ds(t, 1)], None, ALU.is_equal)
                    last.then_inc(hot, 1)
                groups(dve, work)

            @block.tensor
            def _(pe):
                def work(n, u, slot, q0):
                    pe.wait_ge(hot, n + 1)
                    for q in range(4):
                        last = pe.matmul(K.ps[u][:, q * P:(q + 1) * P], second[:, u, q, :], first[:, u, q, :], start=True, stop=True)
                    last.then_inc(paired, 1)
                groups(pe, work)

            @block.scalar
            def _(act):
                act.sem_inc(copied, 2)

                def work(n, u, slot, q0):
                    act.wait_ge(paired, n + 1)
                    act.activation(buf[:, slot, :, ds(q0 * 4, 4)], K.ps[u][:, :].rearrange("p (q i) -> p i q", q=4),
                                   ACT.Copy).then_inc(copied, 1)
                groups(act, work, lambda i, slot: act.wait_ge(stored[slot], i * 16 + 16))

            @block.sync
            def _(sp):
                for slot in range(2):
                    sp.sem_inc(stored[slot], 16)
                with sp.Fori(0, rounds) as i:
                    for slot in range(2):
                        sp.wait_ge(copied, i * 32 + (slot * 16 + 18))
                        sp.dma_start(K.dense[ds(i * 2 + slot, 1), :, :].rearrange("b j n -> (b j) n"),
                                     buf[:, slot, :, :].rearrange("p i t -> p (i t)")).then_inc(stored[slot], 16)
                for slot in range(2):
                    sp.wait_ge(stored[slot], 16 * (rounds + 1))


def experts(K, l, hT, acc, t0, tw):
    nc = K.nc
    step_e = 512
    n_steps = NEXP // step_e
    outs = tw // P * 2
    nb = tw // 64
    with ExitStack() as mem:
        def sb(name, shape):
            return mem.enter_context(nc.sbuf_tensor(f"ex_{name}{l}", shape, F32))
        u = sb("u", [P, 2, KD, step_e])
        v = sb("v", [P, 2, 4, D])
        g = sb("g", [P, 2, nb, 4 * 64])
        a = sb("a", [P, 2, 4, tw])
        with stage(K, "u0", "u1", "v0", "v1", "g0", "g1", "scored", "gelued", "weighted", "outed", "added") as \
                (block, u0, u1, v0, v1, g0, g1, scored, gelued, weighted, outed, added):
            us, vs, gs = (u0, u1), (v0, v1), (g0, g1)
            half = n_steps // 2

            def steps(eng, first, second=None):
                first(0, 0, True)
                first(1, 1, True)
                if second:
                    second(0, 0, True)
                with eng.Fori(1, half) as i:
                    first(i * 2, 0, False)
                    if second:
                        second(i * 2 - 1, 1, False)
                    first(i * 2 + 1, 1, False)
                    if second:
                        second(i * 2, 0, False)
                if second:
                    second(n_steps - 1, 1, False)

            @block.sync
            def _(sp):
                def fetch(n, s, fresh):
                    if not fresh:
                        sp.wait_ge(scored, n * 4 - 4)
                    sp.dma_start(u[:, s, :, :], K.dram["peer_u"][l][:, ds(n * step_e, step_e)].rearrange("(k p) e -> p k e", p=P)).then_inc(us[s], 16)
                    if not fresh:
                        sp.wait_ge(weighted, n * 4 - 4)
                    sp.dma_start(g[:, s, :, :], K.dense[0:nb, :, ds(n * 256, 256)].rearrange("b j n -> j b n")).then_inc(gs[s], 16)
                    if not fresh:
                        sp.wait_ge(outed, n * outs - outs)
                    sp.dma_start(v[:, s, :, :], K.dram["peer_v"][l][ds(n * step_e, step_e), :].rearrange("(k p) d -> p k d", p=P)).then_inc(vs[s], 16)
                steps(sp, fetch)

            @block.tensor
            def _(pe):
                def score(n, s, fresh):
                    pe.wait_ge(us[s], (n - s) * 8 + 16)
                    for e in range(4):
                        if not (fresh and s == 0 and e < 2):
                            pe.wait_ge(gelued, n * 4 + (e - 1))
                        for k in range(KD):
                            last = pe.matmul(K.ps[e % 2][:, 0:tw], u[:, s, k, e * P:(e + 1) * P], hT[:, k, t0:t0 + tw],
                                             start=k == 0, stop=k == KD - 1)
                        last.then_inc(scored, 1)

                def combine(n, s, fresh):
                    pe.wait_ge(vs[s], (n - s) * 8 + 16)
                    pe.wait_ge(weighted, n * 4 + 4)
                    for o in range(outs):
                        t, c = divmod(o, 2)
                        if not (fresh and o < 4):
                            pe.wait_ge(added, n * outs + (o - 3))
                        for e in range(4):
                            last = pe.matmul(K.ps[2 + o % 4][:, :], a[:, s, e, t * P:(t + 1) * P], v[:, s, e, c * 512:(c + 1) * 512],
                                             start=e == 0, stop=e == 3)
                        last.then_inc(outed, 1)
                steps(pe, score, combine)

            @block.scalar
            def _(act):
                def gelu(n, s, fresh):
                    if not fresh:
                        act.wait_ge(outed, n * outs - outs)
                    for e in range(4):
                        act.wait_ge(scored, n * 4 + (e + 1))
                        act.activation(a[:, s, e, :], K.ps[e % 2][:, 0:tw], ACT.Gelu_apprx_tanh).then_inc(gelued, 1)
                steps(act, gelu)

            @block.vector
            def _(dve):
                def weigh(n, s, fresh):
                    dve.wait_ge(gs[s], (n - s) * 8 + 16)
                    for e in range(4):
                        dve.wait_ge(gelued, n * 4 + (e + 1))
                        av = a[:, s, e, :].rearrange("p (b t) -> p b t", t=64)
                        dve.tensor_tensor(av, av, g[:, s, :, e * 64:(e + 1) * 64], ALU.mult).then_inc(weighted, 1)

                def gather(n, s, fresh):
                    for o in range(outs):
                        t, c = divmod(o, 2)
                        dve.wait_ge(outed, n * outs + (o + 1))
                        dst = acc[:, t, c * 512:(c + 1) * 512]
                        if fresh:
                            dve.tensor_copy(dst, K.ps[2 + o % 4][:, :]).then_inc(added, 1)
                        else:
                            dve.wait_ge(added, n * outs + (o + 1 - outs))
                            dve.tensor_tensor(dst, dst, K.ps[2 + o % 4][:, :], ALU.add).then_inc(added, 1)
                steps(dve, weigh, gather)


def first_layer(K, l, x, s_cols):
    nc = K.nc
    last = l == DEPTH - 1
    all_tiles = [0, 1, 2, 3]
    tiles = [2, 3] if last else all_tiles
    streams = [1] if last else [0, 1]
    t0 = tiles[0] * P
    with ExitStack() as mem:
        def sb(name, shape, scope=mem):
            return scope.enter_context(nc.sbuf_tensor(f"{name}_l{l}", shape, F32))
        mod25 = sb("mod25", [P, 2, 2, D])
        hT = sb("hT", [P, KD, TALL])
        late = ExitStack()
        mod34 = sb("mod34", [P, 2, 2, D], late)
        with nc.sbuf_tensor(f"mod01_l{l}", [P, 2, 2, D], F32) as mod01, nc.sbuf_tensor(f"h_l{l}", [P, 4, D], F32) as h:
            mod = [mod01[:, 0], mod01[:, 1], mod25[:, 0], mod34[:, 0], mod34[:, 1], mod25[:, 1]]
            modulation(K, l, s_cols, mod)
            rms_norm(K, x, all_tiles, lambda t: mod[1][:, t // 2, :], lambda t: mod[0][:, t // 2, :], h, hT)
        mix = ExitStack()
        yT = sb("yT", [P, KD, TALL], mix)
        with ExitStack() as branch:
            zTs = sb("zTs", [P, 4, 2, TALL], branch)
            with ExitStack() as rows:
                vones = sb("vones", [P, 4, 4, DH + 1], rows)
                gates = sb("gates", [P, 4, 16], rows)
                osig = sb("osig", [P, 4, MIX], rows)
                gm = sb("gm", [P, 4, 2 * MIX], rows)
                ft = sb("ft", [P, 4, MIX], rows)
                with stage(K) as (block,):
                    @block.vector
                    def _(dve):
                        dve.memset(vones[:, :, :, DH:DH + 1], 1.0)

                def v_and_gates(eng, chain, psum, o, t):
                    eng.activation(vones[:, t, :, 0:DH], psum[:, 0:MIX].rearrange("p (h d) -> p h d", h=4), ACT.Copy)
                    return eng.activation(gates[:, t, :], psum[:, MIX:MIX + 16], ACT.Copy)
                project(K, K.dram["w_in"][l], KD, hT, [
                    (V_OFF, MIX + 16, False, all_tiles, v_and_gates),
                    (O_OFF, MIX, False, tiles, copy_to(lambda o, t: osig[:, t, :], ACT.Sigmoid)),
                    (GM_OFF, 2 * MIX, False, tiles, copy_to(lambda o, t: gm[:, t, :], ACT.Gelu_apprx_tanh)),
                    (FT_OFF, MIX, False, tiles, copy_to(lambda o, t: ft[:, t, :]))])
                gmlp(K, l, zTs[:, 1], gm, tiles)
                fourier(K, l, zTs[:, 3], ft, streams)
                mlstm(K, l, hT, zTs[:, 0], last, vones, gates, osig)
            conv_branch(K, l, hT, zTs[:, 2], streams)
            merge(K, l, hT, zTs, yT, t0)
        jobs = [(c * 512, 512, False, tiles, add_scaled(K, x, lambda t: mod[2][:, t // 2, :])(c * 512)) for c in range(2)]
        project(K, K.dram["w_out"][l], KD, yT, jobs, engine="vector")
        mix.close()
        with nc.sbuf_tensor(f"h2_l{l}", [P, 4, D], F32) as h:
            rms_norm(K, x, tiles, lambda t: mod[4][:, t // 2, :], lambda t: mod[3][:, t // 2, :], h, hT)
        late.close()
        with nc.sbuf_tensor(f"choice_l{l}", [P, 3, TALL], F32) as choice:
            with nc.sbuf_tensor(f"qT_l{l}", [P, 16, TALL], F32) as qT:
                project(K, K.dram["peer_w_q"][l], KD, hT, [
                    (c * 512, 512, True, (t0, TALL), copy_to(lambda o, t, c=c: qT[:, c * 4 + o // P, t0:TALL])) for c in range(4)])
                expert_choice(K, l, qT, tiles, choice)
            spread_choice(K, l, choice, t0, TALL - t0)
        with nc.sbuf_tensor(f"peer_l{l}", [P, len(tiles), D], F32) as acc:
            experts(K, l, hT, acc, t0, TALL - t0)
            with stage(K, "step") as (block, step):
                @block.vector
                def _(dve):
                    chain = Chain(dve, step)
                    for i, t in enumerate(tiles):
                        chain(dve.tensor_tensor(acc[:, i, :], acc[:, i, :], mod[5][:, t // 2, :], ALU.mult))
                        dve.tensor_tensor(x[:, t, :], x[:, t, :], acc[:, i, :], ALU.add)



def products(K, jobs, evacuate):
    with stage(K, "done", "step") as (block, done, step):
        @block.tensor
        def _(pe):
            for i, (lhsT, rhs) in enumerate(jobs):
                last = pe.matmul(K.ps[i // 4][:, (i % 4) * P:(i % 4 + 1) * P], lhsT, rhs, start=True, stop=True)
                if i % 4 == 3:
                    last.then_inc(done, 1)

        @block.vector
        def _(dve):
            chain = Chain(dve, step)
            for half in range(len(jobs) // 4):
                dve.wait_ge(done, half + 1)
                evacuate(dve, chain, half, K.ps[half][:, :].rearrange("p (h c) -> p h c", h=4))


def gated_delta(K, j, qkv, ba, z, cat):
    nc = K.nc
    with ExitStack() as mem:
        def sb(name, shape, scope=mem):
            return scope.enter_context(nc.sbuf_tensor(f"gd_{name}", shape, F32))
        beta, g = sb("beta", [P, 2, GH]), sb("g", [P, 2, GH])
        par = sb("par", [P, 3, GH])
        soft = sb("soft", [P, 2, GH])
        gcs = sb("gcs", [P, 2, 2, GH])
        eg = sb("eg", [P, 2, GH])
        kd = sb("kd", [P, 2, GH])
        gain = sb("gain", [P, P])
        load(K, (par[:, 0, :], K.dram["gdn_a_log"][j:j + 1, :].broadcast_to([P, GH])),
             (par[:, 1, :], K.dram["gdn_dt_bias"][j:j + 1, :].broadcast_to([P, GH])),
             (gain[:, :], K.dram["gdn_norm_w"][j:j + 1, :].broadcast_to([P, P])))
        with stage(K, "step", "biased", "act_step") as (block, step, biased, act_step):
            @block.vector
            def _(dve):
                chain = Chain(dve, step)
                dve.tensor_tensor(g[:, :, :], ba[:, :, GH:2 * GH], par[:, 1, :][:, None, :].broadcast_to([P, 2, GH]), ALU.add).then_inc(biased, 1)
                dve.wait_ge(act_step, 5)
                chain(dve.tensor_single_scalar(g[:, :, :], g[:, :, :], 0.0, ALU.max))
                chain(dve.tensor_tensor(g[:, :, :], g[:, :, :], soft[:, :, :], ALU.add))
                chain(dve.tensor_tensor(g[:, :, :], g[:, :, :], par[:, 2, :][:, None, :].broadcast_to([P, 2, GH]), ALU.mult))
                dve.tensor_single_scalar(g[:, :, :], g[:, :, :], -1.0, ALU.mult)

            @block.scalar
            def _(act):
                chain = Chain(act, act_step)
                chain(act.activation(beta[:, :, :], ba[:, :, 0:GH], ACT.Sigmoid))
                chain(act.activation(par[:, 2, :], par[:, 0, :], ACT.Exp))
                act.wait_ge(biased, 1)
                chain(act.activation(soft[:, :, :], g[:, :, :], ACT.Abs))
                chain(act.activation(soft[:, :, :], soft[:, :, :], ACT.Exp, scale=-1.0))
                chain(act.activation(soft[:, :, :], soft[:, :, :], ACT.Ln, bias=1.0))
        with nc.sbuf_tensor("gd_sq", [P, 16, T1], F32) as sq:
            with stage(K, "squared", "summed") as (block, squared, summed):
                @block.scalar
                def _(act):
                    for i in range(16):
                        act.activation(sq[:, i, :], qkv[:, i, :], ACT.Square).then_inc(squared, 1)

                @block.tensor
                def _(pe):
                    for i in range(8):
                        pe.wait_ge(squared, 2 * i + 2)
                        for u in range(2):
                            last = pe.matmul(K.ps[i][:, u * T1:(u + 1) * T1], K.ones[:, :], sq[:, 2 * i + u, :], start=True, stop=True)
                        last.then_inc(summed, 1)

                @block.vector
                def _(dve):
                    for i in range(8):
                        dve.wait_ge(summed, i + 1)
                        dve.tensor_copy(sq[:, 2 * i:2 * i + 2, :], K.ps[i][:, :].rearrange("p (u t) -> p u t", u=2))
            inverse_root(K, sq[:, :, :], EPS)
            with stage(K) as (block,):
                @block.vector
                def _(dve):
                    for i in range(4):
                        dve.tensor_tensor(qkv[:, 4 * i:4 * i + 4, :], qkv[:, 4 * i:4 * i + 4, :], sq[:, 4 * i:4 * i + 4, :], ALU.mult)
        ktok, vtok = sb("ktok", [P, 2, GH, P]), sb("vtok", [P, 2, GH, P])
        transpose(K, [([qkv[:, base + 4 * q + i, t * P:(t + 1) * P] for i in range(4)], dst[:, t, 4 * q:4 * q + 4, :])
                      for base, dst in ((GH, ktok), (2 * GH, vtok)) for t in range(2) for q in range(2)])
        with stage(K, "summed", "copied") as (block, summed, copied):
            @block.tensor
            def _(pe):
                for t in range(2):
                    pe.matmul(K.ps[0][:, t * GH:(t + 1) * GH], K.tri[:, :], g[:, t, :], start=True, stop=True)
                    last = pe.matmul(K.ps[0][:, (2 + t) * GH:(3 + t) * GH], K.ones[:, :], g[:, t, :], start=True, stop=True)
                last.then_inc(summed, 1)

            @block.vector
            def _(dve):
                dve.wait_ge(summed, 1)
                dve.tensor_copy(gcs[:, :, :, :], K.ps[0][:, 0:4 * GH].rearrange("p (a t h) -> p a t h", a=2, t=2)).then_inc(copied, 1)
                dve.wait_ge(copied, 1)
                dve.tensor_tensor(kd[:, :, :], gcs[:, 1, :, :], gcs[:, 0, :, :], ALU.subtract).then_inc(copied, 1)

            @block.scalar
            def _(act):
                act.wait_ge(copied, 2)
                act.activation(eg[:, :, :], gcs[:, 0, :, :], ACT.Exp)
                act.activation(kd[:, :, :], kd[:, :, :], ACT.Exp)
        low, att = sb("low", [P, 4, 4, P]), sb("att", [P, 4, 4, P])
        masks = sb("masks", [P, 2, P])
        load(K, (masks[:, :, :], K.dram["gd_masks"]))
        with stage(K, "pe_done", "ranged", "exped", "read") as (block, pe_done, ranged, exped, read):
            @block.tensor
            def _(pe):
                for n in range(4):
                    t, hg = divmod(n, 2)
                    if n >= 2:
                        pe.wait_ge(read, n - 1)
                    b = 3 * (n % 2)
                    for i in range(4):
                        h = 4 * hg + i
                        cols = slice(i * P, (i + 1) * P)
                        kT, qT = qkv[:, GH + h, t * P:(t + 1) * P], qkv[:, h, t * P:(t + 1) * P]
                        pe.matmul(K.ps[b][:, cols], g[:, t, h:h + 1].broadcast_to([P, P]), K.tri[:, :], start=True, stop=True)
                        pe.matmul(K.ps[b + 1][:, cols], kT, kT, start=True, stop=True)
                        last = pe.matmul(K.ps[b + 2][:, cols], kT, qT, start=True, stop=True)
                    last.then_inc(pe_done, 1)

            @block.vector
            def _(dve):
                for n in range(4):
                    t, hg = divmod(n, 2)
                    dve.wait_ge(pe_done, n + 1)
                    b = 3 * (n % 2)
                    for i in range(4):
                        h = 4 * hg + i
                        row = K.ps[b][:, i * P:(i + 1) * P]
                        dve.scalar_tensor_tensor(out=low[:, n, i, :], in0=row, scalar=gcs[:, 0, t, h:h + 1], in1=masks[:, 0, :],
                                                 op0=ALU.subtract, op1=ALU.max)
                        last = dve.scalar_tensor_tensor(out=att[:, n, i, :], in0=row, scalar=gcs[:, 0, t, h:h + 1], in1=masks[:, 1, :],
                                                        op0=ALU.subtract, op1=ALU.min)
                    last.then_inc(ranged, 1)
                    dve.wait_ge(exped, n + 1)
                    view = [K.ps[b + 1 + i][:, :].rearrange("p (h c) -> p h c", h=4) for i in range(2)]
                    dve.tensor_tensor(low[:, n, :, :], low[:, n, :, :], view[0], ALU.mult)
                    dve.scalar_tensor_tensor(out=att[:, n, :, :], in0=view[1], scalar=SCALE, in1=att[:, n, :, :],
                                             op0=ALU.mult, op1=ALU.mult).then_inc(read, 1)
                    dve.wait_ge(read, n + 1)
                    dve.tensor_tensor(low[:, n, :, :], low[:, n, :, :],
                                      beta[:, t, 4 * hg:4 * hg + 4][:, :, None].broadcast_to([P, 4, P]), ALU.mult)

            @block.scalar
            def _(act):
                for n in range(4):
                    act.wait_ge(ranged, n + 1)
                    act.activation(low[:, n, :, :], low[:, n, :, :], ACT.Exp, scale=-1.0)
                    act.activation(att[:, n, :, :], att[:, n, :, :], ACT.Exp).then_inc(exped, 1)
        inv_t = sb("inv_t", [P, 4, 4, P])
        with ExitStack() as solve:
            inv = sb("inv", [P, 4, 4, P], solve)
            part, mid = sb("part", [P, 4, 4, P], solve), sb("mid", [P, 4, 4, P], solve)
            level = sb("level", [P, 7, P], solve)
            load(K, (level[:, :, :], K.dram["gd_levels"]))
            with stage(K) as (block,):
                @block.vector
                def _(dve):
                    for n in range(4):
                        dve.tensor_copy(inv[:, n, :, :], K.ident[:, None, :].broadcast_to([P, 4, P]))

                @block.scalar
                def _(act):
                    for n in range(4):
                        act.activation(inv_t[:, n, :, :], K.ident[:, None, :].broadcast_to([P, 4, P]), ACT.Copy)
            with stage(K, "parted", "mid_psum", "mid_copied", "joined", "subbed") as (block, parted, mid_psum, mid_copied, joined, subbed):
                @block.gpsimd
                def _(pool):
                    for m in range(28):
                        lv, n = divmod(m, 4)
                        if m >= 4:
                            pool.wait_ge(mid_psum, m - 3)
                        pool.tensor_tensor(part[:, n, :, :], low[:, n, :, :], level[:, lv, :][:, None, :].broadcast_to([P, 4, P]),
                                           ALU.mult).then_inc(parted, 1)

                @block.tensor
                def _(pe):
                    for lv in range(7):
                        for n in range(4):
                            m = 4 * lv + n
                            pe.wait_ge(parted, m + 1)
                            if m >= 4:
                                pe.wait_ge(subbed, m - 3)
                            for i in range(4):
                                last = pe.matmul(K.ps[n][:, i * P:(i + 1) * P], part[:, n, i, :], inv_t[:, n, i, :], start=True, stop=True)
                            last.then_inc(mid_psum, 1)
                        for n in range(4):
                            m = 4 * lv + n
                            pe.wait_ge(mid_copied, m + 1)
                            if m >= 2:
                                pe.wait_ge(subbed, m - 1)
                            b = 4 + 2 * (n % 2)
                            for i in range(4):
                                pe.matmul(K.ps[b][:, i * P:(i + 1) * P], inv[:, n, i, :], mid[:, n, i, :], start=True, stop=True)
                                last = pe.matmul(K.ps[b + 1][:, i * P:(i + 1) * P], mid[:, n, i, :], inv[:, n, i, :], start=True, stop=True)
                            last.then_inc(joined, 1)

                @block.scalar
                def _(act):
                    for m in range(28):
                        n = m % 4
                        act.wait_ge(mid_psum, m + 1)
                        if m >= 4:
                            act.wait_ge(joined, m - 3)
                        act.activation(mid[:, n, :, :], K.ps[n][:, :].rearrange("p (h c) -> p h c", h=4), ACT.Copy).then_inc(mid_copied, 1)

                @block.vector
                def _(dve):
                    for m in range(28):
                        n = m % 4
                        b = 4 + 2 * (n % 2)
                        dve.wait_ge(joined, m + 1)
                        if m >= 4:
                            dve.wait_ge(subbed, m - 3)
                        dve.tensor_tensor(inv_t[:, n, :, :], inv_t[:, n, :, :], K.ps[b][:, :].rearrange("p (h c) -> p h c", h=4), ALU.subtract)
                        dve.tensor_tensor(inv[:, n, :, :], inv[:, n, :, :], K.ps[b + 1][:, :].rearrange("p (h c) -> p h c", h=4),
                                          ALU.subtract).then_inc(subbed, 1)
        vb, vnew = sb("vb", [P, 2, GH, P]), sb("vnew", [P, 2, GH, P])
        state = sb("state", [P, GH, P])
        o = sb("o", [P, 2, GH, P])

        def over(ap, half):
            return ap[:, 4 * half:4 * half + 4][:, :, None].broadcast_to([P, 4, P])
        with stage(K) as (block,):
            @block.vector
            def _(dve):
                for half in range(2):
                    hs = slice(4 * half, 4 * half + 4)
                    dve.tensor_tensor(vb[:, 0, hs, :], vtok[:, 0, hs, :], over(beta[:, 0, :], half), ALU.mult)
                    dve.tensor_tensor(ktok[:, 0, hs, :], ktok[:, 0, hs, :], over(kd[:, 0, :], half), ALU.mult)

        def copy_into(dst):
            def evacuate(dve, chain, half, psum):
                dve.tensor_copy(dst[:, 4 * half:4 * half + 4, :], psum)
            return evacuate
        heads = range(GH)
        products(K, [(inv_t[:, h // 4, h % 4, :], vb[:, 0, h, :]) for h in heads], copy_into(vnew[:, 0]))
        products(K, [(ktok[:, 0, h, :], vnew[:, 0, h, :]) for h in heads], copy_into(state))

        def residual(dve, chain, half, psum):
            hs = slice(4 * half, 4 * half + 4)
            r = vb[:, 1, hs, :]
            chain(dve.tensor_tensor(r, psum, over(eg[:, 1, :], half), ALU.mult))
            chain(dve.tensor_tensor(r, vtok[:, 1, hs, :], r, ALU.subtract))
            chain(dve.tensor_tensor(r, r, over(beta[:, 1, :], half), ALU.mult))
        products(K, [(qkv[:, GH + h, P:2 * P], state[:, h, :]) for h in heads], residual)
        products(K, [(inv_t[:, 2 + h // 4, h % 4, :], vb[:, 1, h, :]) for h in heads], copy_into(vnew[:, 1]))
        for t in range(2):
            products(K, [(att[:, 2 * t + h // 4, h % 4, :], vnew[:, t, h, :]) for h in heads], copy_into(o[:, t]))

        def from_state(dve, chain, half, psum):
            hs = slice(4 * half, 4 * half + 4)
            chain(dve.scalar_tensor_tensor(out=vb[:, 0, hs, :], in0=psum, scalar=SCALE, in1=over(eg[:, 1, :], half),
                                           op0=ALU.mult, op1=ALU.mult))
            dve.tensor_tensor(o[:, 1, hs, :], o[:, 1, hs, :], vb[:, 0, hs, :], ALU.add)
        products(K, [(qkv[:, h, P:2 * P], state[:, h, :]) for h in heads], from_state)
        ss = K.small[:, 0:16].rearrange("p (t h) -> p t h", t=2)
        with stage(K, "step") as (block, step):
            @block.vector
            def _(dve):
                chain = Chain(dve, step)
                for t in range(2):
                    chain(dve.tensor_tensor(vb[:, t, :, :], o[:, t, :, :], o[:, t, :, :], ALU.mult))
                    chain(dve.tensor_reduce(ss[:, t, :], vb[:, t, :, :], AX.X, ALU.add))
                dve.tensor_single_scalar(ss[:, :, :], ss[:, :, :], 1.0 / P, ALU.mult)
        inverse_root(K, K.small[:, 0:16], EPS)
        with stage(K, "step") as (block, step):
            @block.vector
            def _(dve):
                chain = Chain(dve, step)
                for t in range(2):
                    ov = o[:, t, :, :]
                    chain(dve.tensor_tensor(ov, ov, ss[:, t, :][:, :, None].broadcast_to([P, GH, P]), ALU.mult))
                    chain(dve.tensor_tensor(ov, ov, gain[:, None, :].broadcast_to([P, GH, P]), ALU.mult))
                    dve.tensor_tensor(cat[:, t, 0:D].rearrange("p (h c) -> p h c", h=GH), ov,
                                      z[:, t, :].rearrange("p (h c) -> p h c", h=GH), ALU.mult)


def attend(K, items, scale):
    nc = K.nc
    N = len(items)
    K.uid += 1
    with ExitStack() as mem:
        def sb(name, shape):
            return mem.enter_context(nc.sbuf_tensor(f"at_{name}{K.uid}", shape, F32))
        sc, pr, pt = sb("sc", [P, 2, T1]), sb("pr", [P, 2, T1]), sb("pt", [P, 2, T1])
        neg_max, total, weight = sb("max", [P, N]), sb("total", [P, N]), sb("weight", [P, N])
        out_tmp = sb("tmp", [P, 2, P])
        with stage(K, "scored", "scaled", "maxed", "exped", "turned", "pt_ready", "outed", "finished", "step") as \
                (block, scored, scaled, maxed, exped, turned, pt_ready, outed, finished, step):
            @block.tensor
            def _(pe):
                def score(n):
                    q, k = items[n][0:2]
                    if n >= 2:
                        pe.wait_ge(scaled, n - 1)
                    pe.matmul(K.ps[n % 2][:, 0:k.shape[1]], q, k, start=True, stop=True).then_inc(scored, 1)

                score(0)
                for n in range(N):
                    if n + 1 < N:
                        score(n + 1)
                    width = items[n][1].shape[1]
                    pe.wait_ge(exped, n + 1)
                    if n >= 2:
                        pe.wait_ge(pt_ready, n - 1)
                    for c in range(width // P):
                        last = pe.transpose(K.ps[2 + n % 2][:, c * P:(c + 1) * P], pr[:, n % 2, c * P:(c + 1) * P], K.ident[:, :])
                    last.then_inc(turned, 1)
                    pe.wait_ge(pt_ready, n + 1)
                    if n >= 2:
                        pe.wait_ge(finished, n - 1)
                    for c, v in enumerate(items[n][3]):
                        last = pe.matmul(K.ps[4 + n % 2][:, 0:P], pt[:, n % 2, c * P:(c + 1) * P], v, start=c == 0, stop=c == width // P - 1)
                    last.then_inc(outed, 1)

            @block.scalar
            def _(act):
                for n in range(N):
                    width = items[n][1].shape[1]
                    act.wait_ge(maxed, n + 1)
                    if n >= 2:
                        act.wait_ge(turned, n - 1)
                    act.activation(pr[:, n % 2, 0:width], sc[:, n % 2, 0:width], ACT.Exp, bias=neg_max[:, n:n + 1],
                                   accum_out=total[:, n:n + 1]).then_inc(exped, 1)
                    act.wait_ge(turned, n + 1)
                    if n >= 2:
                        act.wait_ge(outed, n - 1)
                    act.activation(pt[:, n % 2, 0:width], K.ps[2 + n % 2][:, 0:width], ACT.Copy).then_inc(pt_ready, 1)

            @block.vector
            def _(dve):
                chain = Chain(dve, step)

                def head(n):
                    bias = items[n][2]
                    width = items[n][1].shape[1]
                    dve.wait_ge(scored, n + 1)
                    if n >= 2:
                        dve.wait_ge(exped, n - 1)
                    s = sc[:, n % 2, 0:width]
                    if bias is None:
                        dve.tensor_single_scalar(s, K.ps[n % 2][:, 0:width], scale, ALU.mult).then_inc(scaled, 1)
                    else:
                        dve.scalar_tensor_tensor(out=s, in0=K.ps[n % 2][:, 0:width], scalar=scale, in1=bias,
                                                 op0=ALU.mult, op1=ALU.add).then_inc(scaled, 1)
                    dve.wait_ge(scaled, n + 1)
                    dve.tensor_reduce(neg_max[:, n:n + 1], s, AX.X, ALU.max, negate=True).then_inc(maxed, 1)

                head(0)
                for n in range(N):
                    if n + 1 < N:
                        head(n + 1)
                    out, gate, add = items[n][4:7]
                    dve.wait_ge(outed, n + 1)
                    chain(dve.reciprocal(weight[:, n:n + 1], total[:, n:n + 1]))
                    if gate is not None:
                        chain(dve.tensor_tensor(weight[:, n:n + 1], weight[:, n:n + 1], gate, ALU.mult))
                    if add:
                        dve.scalar_tensor_tensor(out=out, in0=K.ps[4 + n % 2][:, 0:P], scalar=weight[:, n:n + 1], in1=out,
                                                 op0=ALU.mult, op1=ALU.add).then_inc(finished, 1)
                    else:
                        dve.tensor_scalar(out, K.ps[4 + n % 2][:, 0:P], weight[:, n:n + 1], None, ALU.mult).then_inc(finished, 1)


def memory_attention(K, l, mem_rows, qmT, cat):
    nc = K.nc
    with ExitStack() as mem:
        def sb(name, shape):
            return mem.enter_context(nc.sbuf_tensor(f"ma_{name}{l}", shape, F32))
        mT = sb("mT", [P, KD, T1])
        with nc.sbuf_tensor(f"ma_gain{l}", [P, D], F32) as gain, nc.sbuf_tensor(f"ma_h{l}", [P, 2, D], F32) as h:
            load(K, (gain[:, :], K.dram["mem_norm_w"][l:l + 1, :].broadcast_to([P, D])))
            rms_norm(K, mem_rows, [0, 1], lambda t: gain[:, :], None, h, mT)
        kT, v = sb("kT", [P, MEM_H, T1]), sb("v", [P, 2, MEM_W])
        project(K, K.dram["mem_w_kv"][l], KD, mT, [
            (0, MEM_W, True, (0, T1), copy_to(lambda o, t: kT[:, o // P, :])),
            (MEM_W, MEM_W, False, [0, 1], copy_to(lambda o, t: v[:, t, :]))])
        attend(K, [(qmT[:, h, t * P:(t + 1) * P], kT[:, h, :], None, [v[:, m, h * P:(h + 1) * P] for m in range(2)],
                    cat[:, t, D + h * P:D + (h + 1) * P], None, False) for h in range(MEM_H) for t in range(2)], SCALE)


def gdn_layer(K, l, j, hT, cat, qmT):
    nc = K.nc
    with ExitStack() as mem:
        def sb(name, shape, scope=mem):
            return scope.enter_context(nc.sbuf_tensor(f"gl_{name}", shape, F32))
        qkv = sb("qkv", [P, 3 * GH, T1])
        ba, z = sb("ba", [P, 2, 2 * GH]), sb("z", [P, 2, D])
        with ExitStack() as conv:
            padded = sb("padded", [P, 3 * GH, T1 + 3], conv)
            w = sb("w", [P, 3 * GH, 4], conv)
            load(K, (w[:, :, :], K.dram["gdn_conv_w"][j]))
            with stage(K) as (block,):
                @block.vector
                def _(dve):
                    dve.memset(padded[:, :, 0:3], 0.0)
            project(K, K.dram["gdn_w_in"][j], KD, hT,
                    [(c * 512, 512, True, (0, T1), copy_to(lambda o, t, c=c: padded[:, 4 * c + o // P, 3:T1 + 3])) for c in range(6)] +
                    [(3 * D + c * 512, 512, False, [0, 1], copy_to(lambda o, t, c=c: z[:, t, c * 512:(c + 1) * 512], ACT.Silu)) for c in range(2)] +
                    [(4 * D, 2 * GH, False, [0, 1], copy_to(lambda o, t: ba[:, t, :])),
                     (4 * D + 2 * GH, MEM_W, True, (0, T1), copy_to(lambda o, t: qmT[:, o // P, :]))])
            with stage(K, "step", "conved") as (block, step, conved):
                @block.vector
                def _(dve):
                    chain = Chain(dve, step)
                    for i in range(3 * GH):
                        dst = qkv[:, i, :]
                        chain(dve.tensor_scalar(dst, padded[:, i, 0:T1], w[:, i, 0:1], None, ALU.mult))
                        for tap in range(1, 4):
                            ins = dve.scalar_tensor_tensor(out=dst, in0=padded[:, i, tap:tap + T1], scalar=w[:, i, tap:tap + 1], in1=dst,
                                                           op0=ALU.mult, op1=ALU.add)
                            if tap < 3:
                                chain(ins)
                        ins.then_inc(conved, 1)

                @block.scalar
                def _(act):
                    for i in range(3 * GH):
                        act.wait_ge(conved, i + 1)
                        act.activation(qkv[:, i, :], qkv[:, i, :], ACT.Silu)
        gated_delta(K, j, qkv, ba, z, cat)


def sparse_attention(K, j, hT, cat, qmT):
    nc = K.nc
    with ExitStack() as mem:
        def sb(name, shape, scope=mem):
            return scope.enter_context(nc.sbuf_tensor(f"ns_{name}", shape, F32))
        qT = sb("qT", [P, GH, T1])
        kvT = sb("kvT", [P, 4, 2, T1])
        vtok = sb("vtok", [P, 2, 2, KV_W])
        gates = sb("gates", [P, 2, 3 * GH])

        def kv(n):
            return copy_to(lambda o, t: kvT[:, n, o // P, :])
        base = D
        project(K, K.dram["nsa_w_in"][j], KD, hT,
                [(c * 512, 512, True, (0, T1), copy_to(lambda o, t, c=c: qT[:, 4 * c + o // P, :])) for c in range(2)] +
                [(base + i * KV_W, KV_W, True, (0, T1), kv(n)) for i, n in ((0, 0), (1, 1), (2, 2), (4, 3))] +
                [(base + 3 * KV_W, KV_W, False, [0, 1], copy_to(lambda o, t: vtok[:, 0, t, :])),
                 (base + 5 * KV_W, KV_W, False, [0, 1], copy_to(lambda o, t: vtok[:, 1, t, :])),
                 (base + 6 * KV_W, 3 * GH, False, [0, 1], copy_to(lambda o, t: gates[:, t, :], ACT.Sigmoid)),
                 (base + 6 * KV_W + 3 * GH, MEM_W, True, (0, T1), copy_to(lambda o, t: qmT[:, o // P, :]))])
        rel = sb("rel", [32, GH])
        bias = sb("bias", [P, GH, T1])
        W = 3 * P
        with ExitStack() as tmp:
            hot = sb("hot", [32, W], tmp)
            wide = sb("wide", [P, GH, W], tmp)
            causal = sb("causal", [P, P], tmp)
            load(K, (rel[:, :], K.dram["rel_bias"]), (hot[:, :], K.dram["bucket_rev"]), (causal[:, :], K.dram["causal"]))
            with stage(K, "spread", "copied", "stored", "skewed") as (block, spread, copied, stored, skewed):
                @block.tensor
                def _(pe):
                    for h in range(GH):
                        pe.matmul(K.ps[h][:, 0:W], rel[:, h:h + 1].broadcast_to([32, P]), hot[:, :], start=True, stop=True).then_inc(spread, 1)

                @block.scalar
                def _(act):
                    for h in range(GH):
                        act.wait_ge(spread, h + 1)
                        act.activation(wide[:, h, :], K.ps[h][:, 0:W], ACT.Copy).then_inc(copied, 1)

                @block.sync
                def _(sp):
                    sp.wait_ge(copied, GH)
                    sp.dma_start(K.skew.rearrange("h p w -> p h w"), wide[:, :, :]).then_inc(stored, 16)
                    sp.wait_ge(stored, 16)
                    sp.dma_start(bias[:, :, :], bass.AP(K.skew.tensor, P - 1, [[W - 1, P], [P * W, GH], [1, T1]])).then_inc(skewed, 16)
                    sp.wait_ge(skewed, 16)

                @block.vector
                def _(dve):
                    dve.wait_ge(skewed, 16)
                    dve.tensor_tensor(bias[:, :, P:T1], bias[:, :, P:T1], causal[:, None, :].broadcast_to([P, GH, P]), ALU.add)
        kcT, vc = sb("kcT", [P, 2, N_CMP]), sb("vc", [N_CMP, 2, P])
        for which, (pos_in, w1_in, w2_in) in enumerate(((K.dram["pos_k"], K.dram["w1_k"], K.dram["w2_k"]), (K.dram["pos_v"], K.dram["w1_v"], K.dram["w2_v"]))):
            with ExitStack() as tmp:
                pos, w2 = sb(f"pos{which}", [P, 32], tmp), sb(f"w2{which}", [P, P], tmp)
                w1 = sb(f"w1{which}", [P, 32, P], tmp)
                blk = sb(f"blk{which}", [P, 2, 2, 16, N_CMP], tmp)
                hid = sb(f"hid{which}", [P, 2, N_CMP], tmp)
                load(K, (pos[:, :], pos_in[j]), (w2[:, :], w2_in[j]), (w1[:, :, :], w1_in[j].rearrange("(i p) n -> p i n", p=P)))
                with stage(K, "blocked", "hidden", "acted", "done") as (block, blocked, hidden, acted, done):
                    @block.vector
                    def _(dve):
                        for g in range(2):
                            src = kvT[:, which, g, :].rearrange("p (n i) -> p i n", i=16)
                            for a in range(2):
                                last = dve.tensor_tensor(blk[:, g, a, :, :], src[:, :, a:a + N_CMP],
                                                         pos[:, 16 * a:16 * a + 16][:, :, None].broadcast_to([P, 16, N_CMP]), ALU.add)
                        last.then_inc(blocked, 1)
                        dve.wait_ge(done, 1)
                        if which == 0:
                            dve.tensor_copy(kcT[:, :, :], K.ps[1][:, 0:2 * N_CMP].rearrange("p (g n) -> p g n", g=2))
                        else:
                            dve.tensor_copy(vc[:, :, :], K.ps[1][0:N_CMP, 0:2 * P].rearrange("p (g n) -> p g n", g=2))

                    @block.tensor
                    def _(pe):
                        pe.wait_ge(blocked, 1)
                        for g in range(2):
                            for i in range(32):
                                last = pe.matmul(K.ps[0][:, g * N_CMP:(g + 1) * N_CMP], w1[:, i, :], blk[:, g, i // 16, i % 16, :],
                                                 start=i == 0, stop=i == 31)
                        last.then_inc(hidden, 1)
                        pe.wait_ge(acted, 1)
                        for g in range(2):
                            if which == 0:
                                last = pe.matmul(K.ps[1][:, g * N_CMP:(g + 1) * N_CMP], w2[:, :], hid[:, g, :], start=True, stop=True)
                            else:
                                last = pe.matmul(K.ps[1][0:N_CMP, g * P:(g + 1) * P], hid[:, g, :], w2[:, :], start=True, stop=True)
                        last.then_inc(done, 1)

                    @block.scalar
                    def _(act):
                        act.wait_ge(hidden, 1)
                        act.activation(hid[:, :, :], K.ps[0][:, 0:2 * N_CMP].rearrange("p (g n) -> p g n", g=2), ACT.Silu).then_inc(acted, 1)
        with ExitStack() as tmp:
            hot = sb("chot", [32, 2, N_CMP, P], tmp)
            cm = sb("cmask", [P, 2, 2, N_CMP], tmp)
            s = sb("cs", [P, 2, GH, 16], tmp)
            bc = sb("cb", [P, 2, GH, N_CMP], tmp)
            red = sb("cred", [P, 3, 2, GH], tmp)
            pT = sb("cpT", [N_CMP, 16, P], tmp)
            load(K, (hot[:, :, :, :], K.dram["bucket_cmp"]), (cm[:, :, :, :], K.dram["cmp_masks"]))
            with stage(K, "scored", "shifted", "exped", "step", "weighted", "turned", "copied", "outed") as \
                    (block, scored, shifted, exped, step, weighted, turned, copied, outed):
                @block.tensor
                def _(pe):
                    for t in range(2):
                        for h in range(GH):
                            c = (t * GH + h) * 16
                            pe.matmul(K.ps[0][:, c:c + N_CMP], qT[:, h, t * P:(t + 1) * P], kcT[:, h // 4, :], start=True, stop=True)
                        for n in range(N_CMP):
                            c = (t * N_CMP + n) * GH
                            last = pe.matmul(K.ps[1][:, c:c + GH], hot[:, t, n, :], rel[:, :], start=True, stop=True)
                    last.then_inc(scored, 1)
                    pe.wait_ge(weighted, 1)
                    for b in range(4):
                        for i in range(4):
                            u = 4 * b + i
                            last = pe.transpose(K.ps[2 + b][0:N_CMP, i * P:(i + 1) * P], s[:, u // GH, u % GH, 0:N_CMP], K.ident[:, :])
                        last.then_inc(turned, 1)
                    pe.wait_ge(copied, 4)
                    for b in range(4):
                        for i in range(4):
                            u = 4 * b + i
                            last = pe.matmul(K.ps[2 + b][:, i * P:(i + 1) * P], pT[:, u, :], vc[:, (u % GH) // 4, :], start=True, stop=True)
                        last.then_inc(outed, 1)

                @block.scalar
                def _(act):
                    act.wait_ge(shifted, 1)
                    act.activation(s[:, :, :, 0:N_CMP], s[:, :, :, 0:N_CMP], ACT.Exp).then_inc(exped, 1)
                    for b in range(4):
                        act.wait_ge(turned, b + 1)
                        act.activation(pT[:, 4 * b:4 * b + 4, :], K.ps[2 + b][0:N_CMP, :].rearrange("p (u c) -> p u c", u=4), ACT.Copy).then_inc(copied, 1)
                    for b in range(4):
                        act.wait_ge(outed, b + 1)
                        t, hg = divmod(b, 2)
                        act.activation(cat[:, t, hg * 512:(hg + 1) * 512], K.ps[2 + b][:, :], ACT.Copy)

                @block.vector
                def _(dve):
                    chain = Chain(dve, step)
                    dve.wait_ge(scored, 1)
                    chain(dve.tensor_copy(bc[:, :, :, :].rearrange("p t h n -> p t n h"),
                                          K.ps[1][:, 0:2 * N_CMP * GH].rearrange("p (t n h) -> p t n h", t=2, h=GH)))
                    for t in range(2):
                        sv = s[:, t, :, 0:N_CMP]
                        chain(dve.tensor_tensor(bc[:, t, :, :], bc[:, t, :, :], cm[:, 0, t, :][:, None, :].broadcast_to([P, GH, N_CMP]), ALU.add))
                        chain(dve.scalar_tensor_tensor(out=sv, in0=K.ps[0][:, t * 128:(t + 1) * 128].rearrange("p (h n) -> p h n", n=16)[:, :, 0:N_CMP],
                                                       scalar=SCALE, in1=bc[:, t, :, :], op0=ALU.mult, op1=ALU.add))
                        chain(dve.tensor_reduce(red[:, 0, t, :], sv, AX.X, ALU.max))
                        ins = dve.tensor_tensor(sv, sv, red[:, 0, t, :][:, :, None].broadcast_to([P, GH, N_CMP]), ALU.subtract)
                        if t == 0:
                            chain(ins)
                    ins.then_inc(shifted, 1)
                    dve.wait_ge(exped, 1)
                    for t in range(2):
                        sv = s[:, t, :, 0:N_CMP]
                        chain(dve.tensor_tensor(sv, sv, cm[:, 1, t, :][:, None, :].broadcast_to([P, GH, N_CMP]), ALU.mult))
                        chain(dve.tensor_reduce(red[:, 1, t, :], sv, AX.X, ALU.add))
                        chain(dve.tensor_single_scalar(red[:, 1, t, :], red[:, 1, t, :], 1e-30, ALU.max))
                        chain(dve.reciprocal(red[:, 2, t, :], red[:, 1, t, :]))
                        chain(dve.tensor_tensor(red[:, 2, t, :], red[:, 2, t, :],
                                                gates[:, t, :].rearrange("p (h c) -> p h c", c=3)[:, :, 0], ALU.mult))
                        ins = dve.tensor_tensor(sv, sv, red[:, 2, t, :][:, :, None].broadcast_to([P, GH, N_CMP]), ALU.mult)
                        if t == 0:
                            chain(ins)
                    ins.then_inc(weighted, 1)
        items = []
        for kind in range(2):
            for h in range(GH):
                for t in range(2):
                    n = (t + 1) * P
                    items.append((qT[:, h, t * P:(t + 1) * P], kvT[:, 2 + kind, h // 4, 0:n], bias[:, h, T1 - n:T1],
                                  [vtok[:, kind, c, (h // 4) * P:(h // 4 + 1) * P] for c in range(t + 1)],
                                  cat[:, t, h * P:(h + 1) * P], gates[:, t, 3 * h + 1 + kind:3 * h + 2 + kind], True))
        attend(K, items, SCALE)


def conv_glu(K, l, hT, x):
    nc = K.nc
    J = D_FF // P
    with ExitStack() as mem:
        def sb(name, shape, scope=mem):
            return scope.enter_context(nc.sbuf_tensor(f"gu_{name}{l}", shape, F32))
        actT = sb("actT", [P, J, T1])
        cw, cb = sb("cw", [P, J, 3]), sb("cb", [P, J])
        with ExitStack() as up:
            w = sb("w", [P, 3, 2, KD, T1], up)
            gp, cv = sb("gp", [P, 2, T1 + 2], up), sb("cv", [P, 2, T1], up)
            load(K, (cw[:, :, :], K.dram["ffn_conv_w"][l]), (cb[:, :], K.dram["ffn_conv_b"][l]))
            with stage(K) as (block,):
                @block.vector
                def _(dve):
                    dve.memset(gp[:, :, 0:2], 0.0)
            with stage(K, "w0", "w1", "w2", "gate_psum", "value_psum", "padded", "step", "conved", "acted", "closed") as \
                    (block, w0, w1, w2, gate_psum, value_psum, padded, step, conved, acted, closed):
                loaded = (w0, w1, w2)

                @block.sync
                def _(sp):
                    for n in range(J // 2):
                        if n >= 3:
                            sp.wait_ge(value_psum, 2 * (n - 2))
                        for a in range(2):
                            at = a * D_FF + n * T1
                            sp.dma_start(w[:, n % 3, a, :, :], K.dram["ffn_w_up"][l][:, at:at + T1].rearrange("(k p) n -> p k n", p=P)).then_inc(loaded[n % 3], 16)

                @block.tensor
                def _(pe):
                    for i in range(J):
                        n, o = divmod(i, 2)
                        pe.wait_ge(loaded[n % 3], 32 * (n // 3 + 1))
                        for a, done, free in ((0, gate_psum, padded), (1, value_psum, closed)):
                            if i >= 2:
                                pe.wait_ge(free, i - 1)
                            for k in range(KD):
                                last = pe.matmul(K.ps[2 * a + i % 2][:, 0:T1], w[:, n % 3, a, k, o * P:(o + 1) * P], hT[:, k, :],
                                                 start=k == 0, stop=k == KD - 1)
                            last.then_inc(done, 1)

                @block.scalar
                def _(act):
                    def silu(i):
                        act.wait_ge(conved, i + 1)
                        act.activation(cv[:, i % 2, :], cv[:, i % 2, :], ACT.Silu, bias=cb[:, i:i + 1]).then_inc(acted, 1)

                    for i in range(J):
                        act.wait_ge(gate_psum, i + 1)
                        if i >= 2:
                            act.wait_ge(conved, i - 1)
                        act.activation(gp[:, i % 2, 2:T1 + 2], K.ps[i % 2][:, 0:T1], ACT.Copy).then_inc(padded, 1)
                        if i:
                            silu(i - 1)
                    silu(J - 1)

                @block.vector
                def _(dve):
                    chain = Chain(dve, step)

                    def close(i):
                        dve.wait_ge(acted, i + 1)
                        dve.wait_ge(value_psum, i + 1)
                        dve.tensor_tensor(actT[:, i, :], K.ps[2 + i % 2][:, 0:T1], cv[:, i % 2, :], ALU.mult).then_inc(closed, 1)

                    for i in range(J):
                        dve.wait_ge(padded, i + 1)
                        if i >= 2:
                            dve.wait_ge(closed, i - 1)
                        dst = cv[:, i % 2, :]
                        chain(dve.tensor_scalar(dst, gp[:, i % 2, 0:T1], cw[:, i, 0:1], None, ALU.mult))
                        chain(dve.scalar_tensor_tensor(out=dst, in0=gp[:, i % 2, 1:T1 + 1], scalar=cw[:, i, 1:2], in1=dst, op0=ALU.mult, op1=ALU.add))
                        dve.scalar_tensor_tensor(out=dst, in0=gp[:, i % 2, 2:T1 + 2], scalar=cw[:, i, 2:3], in1=dst,
                                                 op0=ALU.mult, op1=ALU.add).then_inc(conved, 1)
                        if i:
                            close(i - 1)
                    close(J - 1)
        project(K, K.dram["ffn_w_down"][l], J, actT, [(c * 256, 256, False, [0, 1], add_scaled(K, x, None)(c * 256)) for c in range(4)],
                width=256, ring=3, engine="vector")


def second_block(K, x):
    nc = K.nc
    with nc.sbuf_tensor("mem_rows", [P, 2, D], F32) as mem_rows:
        load(K, (mem_rows[:, :, :], K.dram["mem"].rearrange("(t p) d -> p t d", p=P)))
        for l in range(DEPTH):
            def normed(tag, weights, hT):
                with nc.sbuf_tensor(f"b2_gain{tag}", [P, D], F32) as gain, nc.sbuf_tensor(f"b2_h{tag}", [P, 2, D], F32) as h:
                    load(K, (gain[:, :], weights.broadcast_to([P, D])))
                    rms_norm(K, x, [0, 1], lambda t: gain[:, :], None, h, hT)
            with ExitStack() as mix:
                def sb(name, shape):
                    return mix.enter_context(nc.sbuf_tensor(f"b2_{name}{l}", shape, F32))
                cat, qmT = sb("cat", [P, 2, CAT]), sb("qmT", [P, MEM_H, T1])
                with nc.sbuf_tensor(f"b2_hT{l}", [P, KD, T1], F32) as hT:
                    normed(f"m{l}", K.dram["norm_mix_w"][l:l + 1, :], hT)
                    (gdn_layer(K, l, l // 2, hT, cat, qmT) if l % 2 == 0 else sparse_attention(K, l // 2, hT, cat, qmT))
                memory_attention(K, l, mem_rows, qmT, cat)
                catT = sb("catT", [P, CAT // P, T1])
                rows_to_channels(K, cat, catT, [0, 1], CAT)
                project(K, K.dram["w_out_2"][l], CAT // P, catT, [(c * 512, 512, False, [0, 1], add_scaled(K, x, None)(c * 512)) for c in range(2)],
                        engine="vector")
            with nc.sbuf_tensor(f"b2_fT{l}", [P, KD, T1], F32) as hT:
                normed(f"f{l}", K.dram["norm_ffn_w"][l:l + 1, :], hT)
                conv_glu(K, l, hT, x)


def build(nc, K):
    K.nc = nc
    K.uid = K.stages = 0
    K.sems = [[nc.alloc_semaphore(name=f"set{s}_{i}") for i in range(SEMS)] for s in range(2)]
    with ExitStack() as mem:
        def sb(name, shape):
            return mem.enter_context(nc.sbuf_tensor(name, shape, F32))
        K.ps = [mem.enter_context(nc.psum_tensor(f"bank{i}", [P, 512], F32)) for i in range(8)]
        K.ident, K.ones, K.tri, K.iota = sb("ident", [P, P]), sb("ones", [P, P]), sb("tri", [P, P]), sb("iota", [P, P])
        K.pick2, K.pick4, K.ones4 = sb("pick2", [2, 2, P]), sb("pick4", [4, 4, P]), sb("ones4", [4, TALL])
        K.junk, K.small = sb("junk", [P, D]), sb("small", [P, 256])
        x = sb("xrows", [P, 4, D])
        s_cols = sb("s_cols", [P, KD, 2])
        load(K, (K.ident[:, :], K.dram["c_ident"]), (K.ones[:, :], K.dram["c_ones"]), (K.tri[:, :], K.dram["c_tri"]), (K.iota[:, :], K.dram["c_iota"]),
             (K.pick2[:, :, :], K.dram["c_pick2"]), (K.pick4[:, :, :], K.dram["c_pick4"]), (K.ones4[:, :], K.dram["c_ones4"]))
        with nc.sbuf_tensor("grid_pos", [P, 2, D], F32) as pos:
            load(K, (x[:, 0:2, :], K.dram["ctx"].rearrange("(t p) d -> p t d", p=P)), (x[:, 2:4, :], K.dram["x"].rearrange("(t p) d -> p t d", p=P)),
                 (pos[:, :, :], K.dram["grid"].rearrange("(t p) d -> p t d", p=P)), (s_cols[:, :, :], K.dram["cond"]))
            with stage(K) as (block,):
                @block.vector
                def _(dve):
                    dve.tensor_tensor(x[:, 2:4, :], x[:, 2:4, :], pos[:, :, :], ALU.add)

                @block.scalar
                def _(act):
                    act.activation(s_cols[:, :, :], s_cols[:, :, :], ACT.Silu)
        for l in range(DEPTH):
            first_layer(K, l, x, s_cols)
        x2 = x[:, 2:4, :]
        with nc.sbuf_tensor("mid_gain", [P, D], F32) as gain:
            load(K, (gain[:, :], K.dram["final_norm_g"].broadcast_to([P, D])))
            rms_norm(K, x2, [0, 1], lambda t: gain[:, :], None, x2)
        second_block(K, x2)
        with nc.sbuf_tensor("fin_gain", [P, D], F32) as gain, nc.sbuf_tensor("fin_rows", [P, 2, D], F32) as rows:
            load(K, (gain[:, :], K.dram["final_norm_w"].broadcast_to([P, D])))
            rms_norm(K, x2, [0, 1], lambda t: gain[:, :], None, rows)
            with stage(K, "stored") as (block, stored):
                @block.sync
                def _(sp):
                    sp.dma_start(K.out.rearrange("(t p) d -> p t d", p=P), rows[:, :, :]).then_inc(stored, 16)
                    sp.wait_ge(stored, 16)



def buckets(dist):
    n = np.maximum(dist, 0)
    logv = np.log(np.maximum(n, 1).astype(np.float32) / np.float32(16)) / np.float32(np.log(8.0))
    large = np.minimum(16 + (logv * 16).astype(np.int32), 31)
    return np.where(n < 16, n, large)


def constants():
    f = np.float32
    c = {}
    i = np.arange(P)
    c["c_ident"] = np.eye(P, dtype=f)
    c["c_ones"] = np.ones((P, P), f)
    c["c_tri"] = (i[:, None] <= i[None, :]).astype(f)
    c["c_iota"] = np.tile(i.astype(f), (P, 1))
    c["c_pick2"] = np.repeat(np.eye(2, dtype=f)[:, :, None], P, 2)
    c["c_pick4"] = np.repeat(np.eye(4, dtype=f)[:, :, None], P, 2)
    c["c_ones4"] = np.ones((4, TALL), f)
    n_freq = D // 4
    freq = f(1.0) / (f(10000.0) ** (np.arange(n_freq, dtype=f) / f(n_freq)))
    ar = np.repeat(np.arange(T1 // 64, dtype=f), 64)[:, None] * freq
    ac = np.tile(np.arange(64, dtype=f), T1 // 64)[:, None] * freq
    c["grid"] = np.concatenate([np.sin(ar), np.cos(ar), np.sin(ac), np.cos(ac)], -1).astype(f)
    t = np.arange(TALL)
    m = np.zeros((P, 2, 4, TALL), f)
    for s in range(4):
        src = s * P + i[:, None]
        same = (t[None, :] // CTX) == s // 2
        m[:, 0, s, :] = np.where(same & (src > t[None, :]), f(MASKED), f(0))
        m[:, 1, s, :] = np.where(same & (src < t[None, :]), f(MASKED), f(0))
    c["ml_mask"] = m
    a = 2 * np.pi * np.outer(np.arange(CTX), np.arange(CTX)) / CTX
    c["dft_t"] = np.stack([np.cos(a), np.sin(a)]).reshape(2, 2, P, CTX).transpose(2, 0, 1, 3).astype(f)
    b = 2 * np.pi * np.outer(np.arange(DH), np.arange(DH)) / DH
    k = 1.0 / np.sqrt(CTX * DH)
    c["dft_c"] = np.stack([np.kron(np.eye(2), np.cos(b)) * k, -np.kron(np.eye(2), np.sin(b)) * k], 1).astype(f)
    c["gd_masks"] = np.stack([np.where(i[:, None] > i[None, :], f(0), f(-MASKED)), np.where(i[:, None] <= i[None, :], f(0), f(MASKED))], 1)
    lv = [((i[:, None] // (2 * s) == i[None, :] // (2 * s)) & (i[:, None] // s % 2 == 1) & (i[None, :] // s % 2 == 0)) for s in 2 ** np.arange(7)]
    c["gd_levels"] = np.stack(lv, 1).astype(f)
    c["bucket_rev"] = (np.arange(32)[:, None] == buckets(T1 - 1 - np.arange(3 * P))[None, :]).astype(f)
    dist = np.arange(T1).reshape(2, 1, P) - (np.arange(N_CMP) * 16 + 31).reshape(1, N_CMP, 1)
    c["bucket_cmp"] = (np.arange(32)[:, None, None, None] == buckets(dist)[None]).astype(f)
    ok = (dist >= 0).transpose(2, 0, 1)
    c["cmp_masks"] = np.stack([np.where(ok, f(0), f(MASKED)), ok.astype(f)], 1)
    c["causal"] = np.where(i[:, None] >= i[None, :], f(0), f(MASKED))
    return c


def kernel(**inputs):
    import concourse.bacc as _bacc
    from concourse.bass_utils import run_bass_kernel_spmd as _run

    n = {k: np.asarray(v) for k, v in inputs.items()}

    def cols(a):
        a = np.moveaxis(a, -1, 1)
        a = a.reshape(a.shape[0], a.shape[1] // P, P, *a.shape[2:])
        return np.swapaxes(a, 1, 2)

    data = dict(constants())
    data.update({
        "x": n["x"][0], "ctx": n["ctx"][0],
        "cond": np.stack([n["c_ctx"], n["c"][0]], -1).reshape(KD, P, 2).transpose(1, 0, 2),
        "w_ada": n["w_ada"], "b_ada": n["b_ada"], "norm1_g": n["norm1_g"], "norm2_g": n["norm2_g"], "w_in": n["w_in"],
        "ml_conv_w": cols(n["ml_conv_w"]), "ml_conv_b": cols(n["ml_conv_b"]), "ml_gate_b": n["ml_gate_b"],
        "ml_norm_g": n["ml_norm_g"].reshape(DEPTH, MIX), "gm_ln_g": n["gm_ln_g"], "gm_ln_b": n["gm_ln_b"],
        "gm_w_s": n["gm_w_s"].transpose(0, 3, 1, 2), "gm_b_s": n["gm_b_s"].transpose(0, 2, 1),
        "cv_dw_w": cols(n["cv_dw_w"]), "cv_dw_b": cols(n["cv_dw_b"]), "cv_ln_g": n["cv_ln_g"], "cv_ln_b": n["cv_ln_b"],
        "w_branch": n["w_branch"].reshape(DEPTH, 4 * MIX, D), "w_out": n["w_out"], "peer_w_q": n["peer_w_q"],
        "peer_keys": n["peer_keys"].transpose(0, 3, 1, 2), "peer_u": n["peer_u"].transpose(0, 2, 1), "peer_v": n["peer_v"],
        "final_norm_g": n["final_norm_g"][None], "mem": n["mem_2"][0], "rel_bias": n["rel_bias_2"], "norm_mix_w": n["norm_mix_w_2"], "norm_ffn_w": n["norm_ffn_w_2"],
        "final_norm_w": n["final_norm_w_2"][None], "mem_norm_w": n["mem_norm_w_2"], "mem_w_kv": n["mem_w_kv_2"],
        "w_out_2": n["w_out_2"], "gdn_w_in": n["gdn_w_in_2"], "gdn_conv_w": cols(n["gdn_conv_w_2"]),
        "gdn_a_log": n["gdn_a_log_2"], "gdn_dt_bias": n["gdn_dt_bias_2"], "gdn_norm_w": n["gdn_norm_w_2"],
        "nsa_w_in": n["nsa_w_in_2"], "pos_k": n["nsa_cmp_pos_k_2"].transpose(0, 2, 1), "w1_k": n["nsa_cmp_w1_k_2"],
        "w2_k": n["nsa_cmp_w2_k_2"], "pos_v": n["nsa_cmp_pos_v_2"].transpose(0, 2, 1), "w1_v": n["nsa_cmp_w1_v_2"],
        "w2_v": n["nsa_cmp_w2_v_2"], "ffn_w_up": n["ffn_w_up_2"], "ffn_conv_w": cols(n["ffn_conv_w_2"]),
        "ffn_conv_b": cols(n["ffn_conv_b_2"]), "ffn_w_down": n["ffn_w_down_2"],
    })
    nc = _bacc.Bacc("TRN2", target_bir_lowering=False, num_devices=1)
    arrays, dram = {}, {}
    for name, a in data.items():
        arrays[name + "_in"] = np.ascontiguousarray(a)
        dram[name] = nc.dram_tensor(name + "_in", a.shape, F32, kind="ExternalInput").ap()
    dense = nc.dram_tensor("dense_weights", (TALL // 64, P, P * 64), F32, kind="Internal").ap()
    skew = nc.dram_tensor("skewed_bias", (GH, P, 3 * P), F32, kind="Internal").ap()
    out = nc.dram_tensor("out_rows", (T1, D), F32, kind="ExternalOutput").ap()
    build(nc, Core(nc, dram, dense, skew, out))
    r = _run(nc, [arrays], core_ids=[0])
    return r.results[0]["out_rows"].reshape(1, T1, D)
```

```python
import numpy as np
from contextlib import ExitStack, contextmanager

import concourse.bass as bass
from concourse import mybir

F32 = mybir.dt.float32
U32 = mybir.dt.uint32
F32R = mybir.dt.float32r
ALU = mybir.AluOpType
ACT = mybir.ActivationFunctionType
AX = mybir.AxisListType
ds = bass.ds

P = 128
D = 1024
KD = D // P
T1 = 256
CTX = 256
TALL = T1 + CTX
DEPTH = 2
EPS = 1e-6
MASKED = -1e30
MIX = D // 4
HEADS = 4
DH = MIX // HEADS
V_OFF, GATE_OFF_ML, O_OFF = 2 * MIX, 3 * MIX, 3 * MIX + 16
GM_OFF = 4 * MIX + 16
CV_OFF = GM_OFF + 2 * MIX
FT_OFF = CV_OFF + 2 * MIX
BR_OFF = FT_OFF + MIX
CV_K = 31
PAD = CV_K // 2
PH, TOPK, NKEYS = 8, 16, 128
NEXP = NKEYS * NKEYS
GH = D // P
KV_W = 256
MEM_W = 512
MEM_H = 4
CAT = D + MEM_W
D_FF = 2816
N_CMP = (T1 - 32) // 16 + 1
NB = 4
SCALE = float(P) ** -0.5


SEMS = 16


@contextmanager
def stage(K, *names):
    nc = K.nc
    turn = K.stages % 2
    K.stages += 1
    sems = K.sems[turn][0:len(names)]
    retired = K.sems[1 - turn]
    with nc.Block(no_gpsimd_drain=True) as block:
        @block.gpsimd
        def _(pool):
            pool.sem_clear(range(retired[0].num, retired[-1].num + 1))
        yield (block, *sems)


class Core:

    def __init__(self, nc, dram, dense, skew, out):
        self.nc, self.dram, self.dense, self.skew, self.out = nc, dram, dense, skew, out


class Chain:

    def __init__(self, engine, sem):
        self.engine, self.sem, self.count = engine, sem, 0

    def __call__(self, instruction):
        self.count += 1
        instruction.then_inc(self.sem, 1)
        self.engine.wait_ge(self.sem, self.count)


def load(K, *pairs):
    with stage(K, "loaded") as (block, loaded):
        @block.sync
        def _(sp):
            for dst, src in pairs:
                sp.dma_start(dst, src).then_inc(loaded, 16)
            sp.wait_ge(loaded, 16 * len(pairs))


def is_pair(acts):
    return type(acts) is tuple


def products_of(pe, psum, stationary, moving, first=True, last=True):
    if is_pair(stationary):
        terms = [(stationary[0], moving[0]), (stationary[0], moving[1]), (stationary[1], moving[0])]
    else:
        terms = [(stationary, moving)]
    for i, (a, b) in enumerate(terms):
        ins = pe.matmul(psum, a, b, start=first and i == 0, stop=last and i == len(terms) - 1)
    return ins


def both(pair, *index):
    if is_pair(pair):
        return pair[0][index], pair[1][index]
    return pair[index]


def project(K, weights, k_tiles, acts, jobs, width=256, ring=3, engine="scalar"):
    nc = K.nc
    split = is_pair(acts)
    parts = [(c0 + o, min(width, cw - o), by_channel, where, evacuate, o)
             for c0, cw, by_channel, where, evacuate in jobs for o in range(0, cw, width)]
    items = []
    for n, (c0, cw, by_channel, where, evacuate, base) in enumerate(parts):
        if by_channel:
            items += [(n, o, min(P, cw - o), None) for o in range(0, cw, P)]
        else:
            items += [(n, 0, cw, t) for t in where]
    ends = [max(i for i, it in enumerate(items) if it[0] == n) + 1 for n in range(len(parts))]
    of_part = [[i for i, it in enumerate(items) if it[0] == n] for n in range(len(parts))]
    names = ["psum_ready", "psum_free", "step", "hi_ready", "lo_ready"] + [f"weights{r}" for r in range(ring)]
    K.uid += 1
    with ExitStack() as mem:
        wt = mem.enter_context(nc.sbuf_tensor(f"wring{K.uid}", [P, ring, k_tiles, width], F32))
        if split:
            halves = [mem.enter_context(nc.sbuf_tensor(f"w{h}{K.uid}", [P, 2, k_tiles, width], F32R)) for h in ("hi", "lo")]
        block, ready, free, step, hi_ready, lo_ready, *loaded = mem.enter_context(stage(K, *names))

        @block.sync
        def _(sp):
            for n, (c0, cw, _b, _w, _e, _o) in enumerate(parts):
                if n >= ring:
                    if split:
                        sp.wait_ge(lo_ready, n - ring + 1)
                    else:
                        sp.wait_ge(ready, ends[n - ring])
                sp.dma_start(wt[:, n % ring, :, 0:cw],
                             weights[:, c0:c0 + cw].rearrange("(k p) n -> p k n", p=P)).then_inc(loaded[n % ring], 16)

        @block.tensor
        def _(pe):
            for i, (n, o, w, t) in enumerate(items):
                if split:
                    pe.wait_ge(lo_ready, n + 1)
                    w_of, slot = tuple(halves), n % 2
                else:
                    pe.wait_ge(loaded[n % ring], 16 * (n // ring + 1))
                    w_of, slot = wt, n % ring
                if i >= NB:
                    pe.wait_ge(free, i - NB + 1)
                bank = K.ps[i % NB]
                for k in range(k_tiles):
                    if t is None:
                        t0, t1 = parts[n][3]
                        last = products_of(pe, bank[0:w, 0:t1 - t0], both(w_of, slice(0, P), slot, k, slice(o, o + w)),
                                           both(acts, slice(0, P), k, slice(t0, t1)), k == 0, k == k_tiles - 1)
                    else:
                        last = products_of(pe, bank[:, 0:w], both(acts, slice(0, P), k, slice(t * P, (t + 1) * P)),
                                           both(w_of, slice(0, P), slot, k, slice(0, w)), k == 0, k == k_tiles - 1)
                last.then_inc(ready, 1)

        def split_hi(act, n):
            cw = parts[n][1]
            act.wait_ge(loaded[n % ring], 16 * (n // ring + 1))
            if n >= 2:
                act.wait_ge(ready, ends[n - 2])
            act.activation(halves[0][:, n % 2, :, 0:cw], wt[:, n % ring, :, 0:cw], ACT.Copy).then_inc(hi_ready, 1)

        def split_lo(dve, n):
            cw = parts[n][1]
            dve.wait_ge(hi_ready, n + 1)
            dve.tensor_tensor(halves[1][:, n % 2, :, 0:cw], wt[:, n % ring, :, 0:cw],
                              halves[0][:, n % 2, :, 0:cw].bitcast(F32), ALU.subtract).then_inc(lo_ready, 1)

        def program(split_part, evacuates):
            def run(eng):
                chain = Chain(eng, step) if evacuates else None
                if split:
                    split_part(eng, 0)
                for n in range(len(parts)):
                    if split and n + 1 < len(parts):
                        split_part(eng, n + 1)
                    if not evacuates:
                        continue
                    for i in of_part[n]:
                        _n, o, w, t = items[i]
                        eng.wait_ge(ready, i + 1)
                        if i and engine == "vector":
                            eng.wait_ge(free, i)
                        if t is None:
                            t0, t1 = parts[n][3]
                            tile = K.ps[i % NB][0:w, 0:t1 - t0]
                        else:
                            tile = K.ps[i % NB][:, 0:w]
                        parts[n][4](eng, chain, tile, parts[n][5] + o, t).then_inc(free, 1)
            return run

        block.scalar(program(split_hi, engine == "scalar"))
        block.vector(program(split_lo, engine == "vector"))


def transpose(K, groups):
    nc = K.nc
    with stage(K, "turned", "free_even", "free_odd") as (block, turned, free_even, free_odd):
        frees = (free_even, free_odd)

        def bank(i):
            ins, out = groups[i]
            f, n, p = out.shape
            return K.ps[i % NB][0:f, 0:n * p].rearrange("f (n p) -> f n p", n=n)

        @block.tensor
        def _(pe):
            for i, (ins, out) in enumerate(groups):
                if i >= NB:
                    pe.wait_ge(frees[i % 2], i // 2 - 1)
                for j, a in enumerate(ins):
                    p = a.shape[0]
                    last = pe.transpose(bank(i)[:, j, :], a, K.ident[0:p, 0:p])
                last.then_inc(turned, 1)

        @block.scalar
        def _(act):
            for i in range(0, len(groups), 2):
                act.wait_ge(turned, i + 1)
                act.activation(groups[i][1], bank(i), ACT.Copy).then_inc(free_even, 1)

        @block.vector
        def _(dve):
            for i in range(1, len(groups), 2):
                dve.wait_ge(turned, i + 1)
                dve.tensor_copy(groups[i][1], bank(i)).then_inc(free_odd, 1)


def transpose_to_pair(K, groups):
    with stage(K, "turned", "hi_done", "lo_done") as (block, turned, hi_done, lo_done):
        def bank(i):
            f, n, p = groups[i][1][0].shape
            return K.ps[i % NB][0:f, 0:n * p].rearrange("f (n p) -> f n p", n=n)

        @block.tensor
        def _(pe):
            for i, (ins, out) in enumerate(groups):
                if i >= NB:
                    pe.wait_ge(lo_done, i - NB + 1)
                for j, a in enumerate(ins):
                    last = pe.transpose(bank(i)[:, j, :], a, K.ident[:, :])
                last.then_inc(turned, 1)

        @block.scalar
        def _(act):
            for i in range(len(groups)):
                act.wait_ge(turned, i + 1)
                act.activation(groups[i][1][0], bank(i), ACT.Copy).then_inc(hi_done, 1)

        @block.vector
        def _(dve):
            for i in range(len(groups)):
                hi, lo = groups[i][1]
                dve.wait_ge(hi_done, i + 1)
                dve.tensor_tensor(lo, bank(i), hi.bitcast(F32), ALU.subtract).then_inc(lo_done, 1)


def rows_to_channels(K, rows, out, tiles, channels):
    groups = []
    for t in tiles:
        for c in range(0, channels // P, 4):
            n = min(4, channels // P - c)
            groups.append(([rows[:, t, (c + j) * P:(c + j + 1) * P] for j in range(n)],
                           both(out, slice(0, P), slice(c, c + n), slice(t * P, (t + 1) * P))))
    (transpose_to_pair if is_pair(out) else transpose)(K, groups)


def inverse_root(K, values, add):
    with stage(K, "shifted", "rooted") as (block, shifted, rooted):
        @block.vector
        def _(dve):
            dve.tensor_scalar_add(values, values, add).then_inc(shifted, 1)
            dve.wait_ge(rooted, 1)
            dve.reciprocal(values, values)

        @block.scalar
        def _(act):
            act.wait_ge(shifted, 1)
            act.activation(values, values, ACT.Sqrt).then_inc(rooted, 1)


def rms_norm(K, rows, tiles, gain_of, shift_of, out, chans=None):
    nc = K.nc
    ss = K.small[:, 0:len(tiles)]
    with stage(K, "squared") as (block, squared):
        @block.scalar
        def _(act):
            for i, t in enumerate(tiles):
                if i >= 1:
                    act.wait_ge(squared, i)
                act.activation(K.junk[:, 0:D], rows[:, t, :], ACT.Square, scale=D ** -0.5,
                               accum_out=ss[:, i:i + 1]).then_inc(squared, 1)
    inverse_root(K, ss, EPS)
    with stage(K, "scaled", "shifted") as (block, scaled, shifted):
        @block.vector
        def _(dve):
            for i, t in enumerate(tiles):
                dve.scalar_tensor_tensor(out=out[:, t, :], in0=rows[:, t, :], scalar=ss[:, i:i + 1], in1=gain_of(t),
                                         op0=ALU.mult, op1=ALU.mult).then_inc(scaled, 1)

        @block.gpsimd
        def _(pool):
            if shift_of:
                for i, t in enumerate(tiles):
                    pool.wait_ge(scaled, i + 1)
                    pool.tensor_tensor(out[:, t, :], out[:, t, :], shift_of(t), ALU.add).then_inc(shifted, 1)
                pool.wait_ge(shifted, len(tiles))
    if chans is not None:
        rows_to_channels(K, out, chans, tiles, D)


def layer_norm(K, rows, tiles, width, gain, bias, silu=False):
    nc = K.nc
    n = len(tiles)
    stats = K.small[:, 32:32 + 6 * n].rearrange("p (n s) -> p n s", s=6)
    mv = K.small[:, 0:2 * n].rearrange("p (n s) -> p n s", s=2)
    with stage(K, "step") as (block, step):
        @block.vector
        def _(dve):
            chain = Chain(dve, step)
            for i, t in enumerate(tiles):
                chain(dve.bn_stats(stats[:, i, :], rows[:, t, :]))
            for i, t in enumerate(tiles):
                dve.bn_aggr(mv[:, i, :], stats[:, i, :])
    inverse_root(K, mv[:, :, 1], EPS)
    with stage(K, "step", "normed") as (block, step, normed):
        @block.vector
        def _(dve):
            chain = Chain(dve, step)
            for i, t in enumerate(tiles):
                chain(dve.tensor_scalar(rows[:, t, :], rows[:, t, :], mv[:, i, 0:1], mv[:, i, 1:2],
                                        ALU.subtract, ALU.mult))
                chain(dve.tensor_tensor(rows[:, t, :], rows[:, t, :], gain, ALU.mult))
                dve.tensor_tensor(rows[:, t, :], rows[:, t, :], bias, ALU.add).then_inc(normed, 1)

        @block.scalar
        def _(act):
            if silu:
                for i, t in enumerate(tiles):
                    act.wait_ge(normed, i + 1)
                    act.activation(rows[:, t, :], rows[:, t, :], ACT.Silu)



def modulation(K, l, s_cols, mod):
    nc = K.nc
    w = K.dram["w_ada"][l]
    n_chunks = 6 * D // 512
    with nc.sbuf_tensor(f"ada_w{l}", [P, 2, KD, 512], F32) as wt, nc.sbuf_tensor(f"ada_b{l}", [2, 6 * D], F32) as ball, \
            nc.sbuf_tensor(f"ada_row{l}", [2, 2, 512], F32) as row, nc.sbuf_tensor(f"ada_g{l}", [P, 2, D], F32) as gains:
        load(K, (ball[:, :], K.dram["b_ada"][l:l + 1, :].broadcast_to([2, 6 * D])),
             (gains[:, 0, :], K.dram["norm1_g"][l:l + 1, :].broadcast_to([P, D])),
             (gains[:, 1, :], K.dram["norm2_g"][l:l + 1, :].broadcast_to([P, D])))
        with stage(K, "w0", "w1", "row_ready", "row_sum", "spread", "copied") as (block, w0, w1, row_ready, row_sum, spread, copied):
            loaded = (w0, w1)

            @block.sync
            def _(sp):
                for n in range(n_chunks):
                    if n >= 2:
                        sp.wait_ge(row_ready, n - 1)
                    sp.dma_start(wt[:, n % 2, :, :], w[:, n * 512:(n + 1) * 512].rearrange("(k p) n -> p k n", p=P))\
                      .then_inc(loaded[n % 2], 16)

            @block.tensor
            def _(pe):
                def spread_row(n):
                    pe.wait_ge(row_sum, n + 1)
                    if n >= 1:
                        pe.wait_ge(copied, n)
                    for s in range(2):
                        last = pe.matmul(K.ps[2 + s][:, :], K.pick2[0:2, s, :], row[0:2, n % 2, :], start=True, stop=True)
                    last.then_inc(spread, 1)

                for n in range(n_chunks):
                    pe.wait_ge(loaded[n % 2], 16 * (n // 2 + 1))
                    if n >= 2:
                        pe.wait_ge(row_sum, n - 1)
                    for k in range(KD):
                        last = pe.matmul(K.ps[n % 2][0:2, :], s_cols[:, k, :], wt[:, n % 2, k, :], start=k == 0, stop=k == KD - 1)
                    last.then_inc(row_ready, 1)
                    if n >= 1:
                        spread_row(n - 1)
                spread_row(n_chunks - 1)

            @block.vector
            def _(dve):
                for n in range(n_chunks):
                    dve.wait_ge(row_ready, n + 1)
                    if n >= 2:
                        dve.wait_ge(spread, n - 1)
                    dve.tensor_tensor(row[0:2, n % 2, :], K.ps[n % 2][0:2, :], ball[0:2, n * 512:(n + 1) * 512],
                                      ALU.add).then_inc(row_sum, 1)

            @block.scalar
            def _(act):
                for n in range(n_chunks):
                    act.wait_ge(spread, n + 1)
                    c, half = divmod(n, 2)
                    act.activation(mod[c][:, 0, half * 512:(half + 1) * 512], K.ps[2][:, :], ACT.Copy)
                    act.activation(mod[c][:, 1, half * 512:(half + 1) * 512], K.ps[3][:, :], ACT.Copy).then_inc(copied, 1)
        with stage(K) as (block,):
            @block.vector
            def _(dve):
                for s in range(2):
                    for c, g in ((1, 0), (4, 1)):
                        dve.scalar_tensor_tensor(out=mod[c][:, s, :], in0=mod[c][:, s, :], scalar=1.0, in1=gains[:, g, :],
                                                 op0=ALU.add, op1=ALU.mult)


def copy_to(dst_of, func=ACT.Copy):
    def evacuate(eng, chain, psum, o, t):
        return eng.activation(dst_of(o, t), psum, func)
    return evacuate


def mlstm(K, l, hT, zT, n_lat_only, vones, gates, osig):
    nc = K.nc
    out_tiles = [2, 3] if n_lat_only else [0, 1, 2, 3]
    q0 = CTX if n_lat_only else 0
    with ExitStack() as mem:
        def sb(name, shape):
            return mem.enter_context(nc.sbuf_tensor(f"ml_{name}{l}", shape, F32))
        gcol = sb("gcol", [P, 2, 4, 2, 4])
        neg_run = sb("neg_run", [4, 2, TALL])
        qk = sb("qk", [P, 4, TALL])
        cw = sb("cw", [P, 4, 3])
        cb = sb("cb", [P, 4])
        gb = sb("gb", [P, 16])
        ng = sb("ng", [P, MIX])
        early = ExitStack()
        padded = early.enter_context(nc.sbuf_tensor(f"ml_padded{l}", [P, 4, 2, CTX + 2], F32))
        with stage(K) as (block,):
            @block.vector
            def _(dve):
                dve.memset(padded[:, :, :, 0:1], 0.0)
                dve.memset(padded[:, :, :, CTX + 1:CTX + 2], 0.0)
        load(K, (cw[:, :, :], K.dram["ml_conv_w"][l]), (cb[:, :], K.dram["ml_conv_b"][l]),
             (gb[:, :], K.dram["ml_gate_b"][l:l + 1, :].broadcast_to([P, 16])),
             (ng[:, :], K.dram["ml_norm_g"][l:l + 1, :].broadcast_to([P, MIX])))
        project(K, K.dram["w_in"][l], KD, hT, [
            (0, 512, True, (0, TALL), lambda eng, chain, psum, o, t: eng.activation(
                padded[:, o // P, :, 1:CTX + 1], psum.rearrange("p (s t) -> p s t", s=2), ACT.Copy))])
        with stage(K, "step", "conved") as (block, step, conved):
            @block.vector
            def _(dve):
                chain = Chain(dve, step)
                for j in range(4):
                    dst = qk[:, j, :].rearrange("p (s t) -> p s t", s=2)
                    chain(dve.tensor_scalar(dst, padded[:, j, :, 0:CTX], cw[:, j, 0:1], cb[:, j:j + 1], ALU.mult, ALU.add))
                    chain(dve.scalar_tensor_tensor(out=dst, in0=padded[:, j, :, 1:CTX + 1], scalar=cw[:, j, 1:2], in1=dst,
                                                   op0=ALU.mult, op1=ALU.add))
                    dve.scalar_tensor_tensor(out=dst, in0=padded[:, j, :, 2:CTX + 2], scalar=cw[:, j, 2:3], in1=dst,
                                             op0=ALU.mult, op1=ALU.add).then_inc(conved, 1)

            @block.scalar
            def _(act):
                for j in range(4):
                    act.wait_ge(conved, j + 1)
                    act.activation(qk[:, j, :], qk[:, j, :], ACT.Silu)
        early.close()
        early = ExitStack()
        pick4, ones4 = sb("pick4", [4, 4, P]), sb("ones4", [4, TALL])
        load(K, (pick4[:, :, :], K.dram["c_pick4"]), (ones4[:, :], K.dram["c_ones4"]))

        def sb_early(name, shape):
            return early.enter_context(nc.sbuf_tensor(f"ml_{name}{l}", shape, F32))
        lf = sb_early("lf", [P, 4, 8])
        soft = sb_early("soft", [P, 4, 8])
        with stage(K, "step", "to_act", "softened") as (block, step, to_act, softened):
            @block.vector
            def _(dve):
                chain = Chain(dve, step)
                chain(dve.tensor_tensor(gates[:, :, :], gates[:, :, :], gb[:, None, :].broadcast_to([P, 4, 16]), ALU.add))
                dve.tensor_single_scalar(lf[:, :, :], gates[:, :, 8:16], 0.0, ALU.min).then_inc(to_act, 1)
                dve.wait_ge(softened, 3)
                dve.wait_ge(to_act, 1)
                dve.tensor_tensor(lf[:, :, :], lf[:, :, :], soft[:, :, :], ALU.subtract)

            @block.scalar
            def _(act):
                act.wait_ge(to_act, 1)
                chain = Chain(act, softened)
                chain(act.activation(soft[:, :, :], gates[:, :, 8:16], ACT.Abs))
                chain(act.activation(soft[:, :, :], soft[:, :, :], ACT.Exp, scale=-1.0))
                chain(act.activation(soft[:, :, :], soft[:, :, :], ACT.Ln, bias=1.0))
        li_r, lf_r = sb_early("li_r", [4, 2, TALL]), sb_early("lf_r", [4, 2, TALL])
        cum, run = sb_early("cum", [4, 2, TALL]), sb_early("run", [4, 2, TALL])
        gsrc = sb_early("gsrc", [4, 2, 2, TALL])
        with stage(K, "turned", "copied") as (block, turned, copied):
            @block.tensor
            def _(pe):
                for t in range(4):
                    for b, src in enumerate((gates, lf)):
                        for d in range(2):
                            last = pe.transpose(K.ps[t][0:4, (2 * b + d) * P:(2 * b + d + 1) * P],
                                                src[:, t, 4 * d:4 * d + 4], K.ident[:, :])
                last.then_inc(turned, 1)

            @block.vector
            def _(dve):
                dve.wait_ge(turned, 1)
                for t in range(4):
                    for b, dst in enumerate((li_r, lf_r)):
                        dve.tensor_copy(dst[:, 0, t * P:(t + 1) * P], K.ps[t][0:4, 2 * b * P:(2 * b + 1) * P])
                        at = (t // 2) * CTX + (1 - t % 2) * P
                        rev = dst[:, 1, at:at + P]
                        dve.tensor_copy(rev, K.ps[t][0:4, (2 * b + 1) * P:(2 * b + 2) * P][:, ::-1])
        with stage(K, "step") as (block, step):
            @block.vector
            def _(dve):
                chain = Chain(dve, step)
                for d in range(2):
                    chain(dve.tensor_tensor_scan(cum[:, d, :], ones4[0:4, :], lf_r[:, d, :], 0.0, ALU.mult, ALU.add))
                chain(dve.tensor_tensor(li_r[:, :, :], li_r[:, :, :], cum[:, :, :], ALU.subtract))
                for d in range(2):
                    chain(dve.tensor_tensor_scan(run[:, d, :], li_r[:, d, :], li_r[:, d, :], 0.0, ALU.max, ALU.max))
                chain(dve.tensor_tensor(cum[:, :, :], cum[:, :, :], run[:, :, :], ALU.add))
                for src, dst, sign in ((li_r, gsrc[:, 0], 1.0), (cum, gsrc[:, 1], -1.0), (run, neg_run, -1.0)):
                    dve.tensor_single_scalar(dst[:, 0, :], src[:, 0, :], sign, ALU.mult)
                    for s in range(2):
                        dve.tensor_single_scalar(dst[:, 1, s * CTX:(s + 1) * CTX],
                                                 src[:, 1, s * CTX:(s + 1) * CTX][:, ::-1], sign, ALU.mult)
        with stage(K, "turned") as (block, turned):
            @block.tensor
            def _(pe):
                for d in range(2):
                    for t in range(4):
                        for b in range(2):
                            c = ((d * 4 + t) * 2 + b) * 4
                            last = pe.transpose(K.ps[0][:, c:c + 4], gsrc[:, b, d, t * P:(t + 1) * P], K.ident[0:4, 0:4])
                last.then_inc(turned, 1)

            @block.scalar
            def _(act):
                act.wait_ge(turned, 1)
                view = K.ps[0][:, 0:64].rearrange("p (a b h) -> p a b h", b=2, h=4)
                dst = gcol[:, :, :, :, :].rearrange("p d t b h -> p (d t) b h")
                act.activation(dst[:, :, 0, :], view[:, :, 0, :], ACT.Copy)
                act.activation(dst[:, :, 1, :], view[:, :, 1, :], ACT.Exp)
        early.close()
        hacc = sb("hacc", [P, 4, MIX])
        wts = sb("wts", [P, 2, 4, TALL])
        prod = sb("prod", [P, 2, 4, TALL])
        den = sb("den", [P, 2, 4])
        tmp = sb("tmp", [P, 4, DH])
        mask = sb("mask", [P, 2, 2, TALL])
        load(K, (mask[:, :, :, :], K.dram["ml_mask"]))
        n_it = 2 * HEADS
        begin = [q0, q0, CTX, CTX]

        def sources(qt, d):
            if qt < 2:
                return [s for s in (0, 1) if (s <= qt if d == 0 else s >= qt)]
            return [0, 1] + [s for s in (2, 3) if (s <= qt if d == 0 else s >= qt)]

        with stage(K, "scores", "spread", "gated", "exped", "weighted", "summed", "step", "out_read") as \
                (block, scores, spread, gated, exped, weighted, summed, step, out_read):
            @block.tensor
            def _(pe):
                def sums(i):
                    h, d = divmod(i, 2)
                    pe.wait_ge(weighted, i + 1)
                    if i >= 2:
                        pe.wait_ge(out_read, i - 1)
                    for qt in out_tiles:
                        src = sources(qt, d)
                        for s in src:
                            last = pe.matmul(K.ps[6 + i % 2][:, qt * 65:qt * 65 + 65], prod[:, i % 2, s, qt * P:(qt + 1) * P],
                                             vones[:, s, h, :], start=s == src[0], stop=s == src[-1])
                    last.then_inc(summed, 1)

                for i in range(n_it):
                    h, d = divmod(i, 2)
                    r = (h % 2) * DH
                    if d == 0:
                        if i:
                            pe.wait_ge(weighted, i)
                        for s in range(4):
                            last = pe.matmul(K.ps[s][:, begin[s]:TALL], qk[r:r + DH, 2 + h // 2, s * P:(s + 1) * P],
                                             qk[r:r + DH, h // 2, begin[s]:TALL], start=True, stop=True)
                        last.then_inc(scores, 1)
                    if i >= 2:
                        pe.wait_ge(gated, i - 1)
                    pe.matmul(K.ps[4 + i % 2][:, :], pick4[0:4, h, :], neg_run[:, d, :], start=True, stop=True).then_inc(spread, 1)
                    if i:
                        sums(i - 1)
                sums(n_it - 1)

            @block.scalar
            def _(act):
                for i in range(n_it):
                    act.wait_ge(gated, i + 1)
                    for s in range(4):
                        last = act.activation(wts[:, i % 2, s, begin[s]:TALL], wts[:, i % 2, s, begin[s]:TALL], ACT.Exp)
                    last.then_inc(exped, 1)

            @block.vector
            def _(dve):
                chain = Chain(dve, step)

                def collect(i):
                    h, d = divmod(i, 2)
                    dve.wait_ge(summed, i + 1)
                    o = K.ps[6 + i % 2][:, 0:260].rearrange("p (t c) -> p t c", c=65)
                    lo, n = out_tiles[0], len(out_tiles)
                    o = o[:, lo:4, :]
                    chain(dve.tensor_tensor(den[:, 0, lo:4], o[:, :, 64], gcol[:, d, lo:4, 1, h], ALU.max))
                    chain(dve.scalar_tensor_tensor(out=den[:, 1, lo:4], in0=o[:, :, 64], scalar=-1.0, in1=den[:, 0, lo:4],
                                                   op0=ALU.mult, op1=ALU.max))
                    chain(dve.reciprocal(den[:, 1, lo:4], den[:, 1, lo:4]))
                    rd = den[:, 1, lo:4][:, :, None].broadcast_to([P, n, DH])
                    dst = hacc[:, lo:4, h * DH:(h + 1) * DH]
                    if d == 0:
                        ins = dve.tensor_tensor(dst, o[:, :, 0:64], rd, ALU.mult)
                        ins.then_inc(out_read, 1)
                        dve.wait_ge(out_read, i + 1)
                    else:
                        dve.tensor_tensor(tmp[:, lo:4, :], o[:, :, 0:64], rd, ALU.mult).then_inc(out_read, 1)
                        dve.wait_ge(out_read, i + 1)
                        chain(dve.tensor_tensor(dst, dst, tmp[:, lo:4, :], ALU.add))

                for i in range(n_it):
                    h, d = divmod(i, 2)
                    dve.wait_ge(spread, i + 1)
                    for s in range(4):
                        b = begin[s]
                        last = dve.scalar_tensor_tensor(out=wts[:, i % 2, s, b:TALL], in0=K.ps[4 + i % 2][:, b:TALL],
                                                        scalar=gcol[:, d, s, 0, h:h + 1],
                                                        in1=mask[:, d, s % 2, b - (s // 2) * CTX:TALL - (s // 2) * CTX],
                                                        op0=ALU.add, op1=ALU.min)
                    last.then_inc(gated, 1)
                    if i:
                        collect(i - 1)
                    dve.wait_ge(exped, i + 1)
                    dve.wait_ge(scores, h + 1)
                    if i >= 2:
                        dve.wait_ge(summed, i - 1)
                    for s in range(4):
                        b = begin[s]
                        last = dve.scalar_tensor_tensor(out=prod[:, i % 2, s, b:TALL], in0=K.ps[s][:, b:TALL],
                                                        scalar=DH ** -0.5, in1=wts[:, i % 2, s, b:TALL],
                                                        op0=ALU.mult, op1=ALU.mult)
                    last.then_inc(weighted, 1)
                collect(n_it - 1)
        lo, n = out_tiles[0], len(out_tiles)
        ss = sb("ss", [P, 4, 4])
        sq = sb("sq", [P, 4, MIX])
        hv = hacc[:, lo:4, :].rearrange("p t (h d) -> p t h d", h=4)
        with stage(K, "step") as (block, step):
            @block.vector
            def _(dve):
                chain = Chain(dve, step)
                chain(dve.tensor_tensor(sq[:, lo:4, :], hacc[:, lo:4, :], hacc[:, lo:4, :], ALU.mult))
                chain(dve.tensor_reduce(ss[:, lo:4, :], sq[:, lo:4, :].rearrange("p t (h d) -> p t h d", h=4), AX.X, ALU.add))
                dve.tensor_single_scalar(ss[:, lo:4, :], ss[:, lo:4, :], 1.0 / DH, ALU.mult)
        inverse_root(K, ss[:, lo:4, :], EPS)
        with stage(K, "step") as (block, step):
            @block.vector
            def _(dve):
                chain = Chain(dve, step)
                for t in out_tiles:
                    v = hacc[:, t, :].rearrange("p (h d) -> p h d", h=4)
                    chain(dve.tensor_tensor(v, v, ss[:, t, :][:, :, None].broadcast_to([P, 4, DH]), ALU.mult))
                chain(dve.tensor_tensor(hacc[:, lo:4, :], hacc[:, lo:4, :], ng[:, None, :].broadcast_to([P, n, MIX]), ALU.mult))
                dve.tensor_tensor(hacc[:, lo:4, :], hacc[:, lo:4, :], osig[:, lo:4, :], ALU.mult)
        rows_to_channels(K, hacc, zT, out_tiles, MIX)


def gmlp(K, l, zT, gm, tiles):
    nc = K.nc
    lo, n = tiles[0], len(tiles)
    with ExitStack() as mem:
        def sb(name, shape):
            return mem.enter_context(nc.sbuf_tensor(f"gm_{name}{l}", shape, F32))
        ln = sb("ln", [P, 2, MIX])
        ws = sb("ws", [P, 4, P])
        bs = sb("bs", [P, 4])
        mixed = sb("mixed", [P, 4, MIX])
        load(K, (ln[:, 0, :], K.dram["gm_ln_g"][l:l + 1, :].broadcast_to([P, MIX])),
             (ln[:, 1, :], K.dram["gm_ln_b"][l:l + 1, :].broadcast_to([P, MIX])),
             (ws[:, :, :], K.dram["gm_w_s"][l]), (bs[:, :], K.dram["gm_b_s"][l]))
        v = gm[:, :, MIX:2 * MIX]
        layer_norm(K, v, tiles, MIX, ln[:, 0, :], ln[:, 1, :])
        with stage(K, "mixed_s", "step") as (block, done, step):
            @block.tensor
            def _(pe):
                for t in tiles:
                    for g in range(4):
                        last = pe.matmul(K.ps[t][:, g * DH:(g + 1) * DH], ws[:, g, :], v[:, t, g * DH:(g + 1) * DH],
                                         start=True, stop=True)
                    last.then_inc(done, 1)

            @block.vector
            def _(dve):
                chain = Chain(dve, step)
                for i, t in enumerate(tiles):
                    dve.wait_ge(done, i + 1)
                    chain(dve.tensor_tensor(mixed[:, t, :].rearrange("p (g c) -> p g c", g=4),
                                            K.ps[t][:, 0:MIX].rearrange("p (g c) -> p g c", g=4),
                                            bs[:, :][:, :, None].broadcast_to([P, 4, DH]), ALU.add))
                    dve.tensor_tensor(mixed[:, t, :], mixed[:, t, :], gm[:, t, 0:MIX], ALU.mult)
        rows_to_channels(K, mixed, zT, tiles, MIX)


def conv_branch(K, l, hT, zT, streams):
    nc = K.nc
    s0, ns = streams[0], len(streams)
    t0 = s0 * CTX
    tiles = list(range(2 * s0, 4))
    with ExitStack() as mem:
        def sb(name, shape):
            return mem.enter_context(nc.sbuf_tensor(f"cv_{name}{l}", shape, F32))
        a = sb("a", [P, 2, 2, CTX + 2 * PAD])
        b = sb("b", [P, 2, 2, CTX])
        y = sb("y", [P, 2, TALL])
        rows = sb("rows", [P, 4, MIX])
        w = sb("w", [P, 2, CV_K])
        wb = sb("wb", [P, 2])
        ln = sb("ln", [P, 2, MIX])
        with stage(K) as (block,):
            @block.vector
            def _(dve):
                dve.memset(a[:, :, :, :], 0.0)
        load(K, (w[:, :, :], K.dram["cv_dw_w"][l]), (wb[:, :], K.dram["cv_dw_b"][l]),
             (ln[:, 0, :], K.dram["cv_ln_g"][l:l + 1, :].broadcast_to([P, MIX])),
             (ln[:, 1, :], K.dram["cv_ln_b"][l:l + 1, :].broadcast_to([P, MIX])))

        def evac(eng, chain, psum, o, t):
            j = o // P
            src = psum.rearrange("p (s t) -> p s t", s=ns)
            if j < 2:
                return eng.activation(a[:, j, s0:2, PAD:PAD + CTX], src, ACT.Copy)
            return eng.activation(b[:, j - 2, s0:2, :], src, ACT.Sigmoid)
        project(K, K.dram["w_in"][l], KD, hT, [(CV_OFF, 512, True, (t0, TALL), evac)])
        with stage(K, "step", "glu") as (block, step, glu):
            @block.gpsimd
            def _(pool):
                for j in range(2):
                    pool.tensor_tensor(a[:, j, s0:2, PAD:PAD + CTX], a[:, j, s0:2, PAD:PAD + CTX], b[:, j, s0:2, :],
                                       ALU.mult).then_inc(glu, 1)

            @block.vector
            def _(dve):
                chain = Chain(dve, step)
                for j in range(2):
                    dst = y[:, j, t0:TALL].rearrange("p (s t) -> p s t", s=ns)
                    dve.wait_ge(glu, j + 1)
                    chain(dve.tensor_scalar(dst, a[:, j, s0:2, 0:CTX], w[:, j, 0:1], wb[:, j:j + 1], ALU.mult, ALU.add))
                    for tap in range(1, CV_K):
                        chain(dve.scalar_tensor_tensor(out=dst, in0=a[:, j, s0:2, tap:tap + CTX], scalar=w[:, j, tap:tap + 1],
                                                       in1=dst, op0=ALU.mult, op1=ALU.add))
        transpose(K, [([y[:, j, t * P:(t + 1) * P] for j in range(2)],
                       rows[:, t, :].rearrange("p (j c) -> p j c", j=2)) for t in tiles])
        layer_norm(K, rows, tiles, MIX, ln[:, 0, :], ln[:, 1, :], silu=True)
        rows_to_channels(K, rows, zT, tiles, MIX)


def fourier(K, l, zT, ft, streams):
    nc = K.nc
    with nc.sbuf_tensor(f"ft_mid{l}", [P, 2, 2, CTX], F32) as mid, nc.sbuf_tensor(f"ft_t{l}", [P, 2, 2, CTX], F32) as dft_t, \
            nc.sbuf_tensor(f"ft_c{l}", [P, 2, P], F32) as dft_c:
        load(K, (dft_t[:, :, :, :], K.dram["dft_t"]), (dft_c[:, :, :], K.dram["dft_c"]))
        with stage(K, "timed", "copied", "done", "out_copied") as (block, timed, copied, done, out_copied):
            @block.tensor
            def _(pe):
                for i, s in enumerate(streams):
                    if i:
                        pe.wait_ge(copied, i)
                    for c in range(2):
                        for m in range(2):
                            for k in range(2):
                                last = pe.matmul(K.ps[2 * c + m][:, 0:CTX], ft[:, 2 * s + k, c * P:(c + 1) * P],
                                                 dft_t[:, m, k, :], start=k == 0, stop=k == 1)
                    last.then_inc(timed, 1)
                    pe.wait_ge(copied, i + 1)
                    if i:
                        pe.wait_ge(out_copied, i)
                    for c in range(2):
                        for m in range(2):
                            last = pe.matmul(K.ps[4 + c][:, 0:CTX], dft_c[:, m, :], mid[:, c, m, :], start=m == 0, stop=m == 1)
                    last.then_inc(done, 1)

            @block.scalar
            def _(act):
                for i, s in enumerate(streams):
                    act.wait_ge(timed, i + 1)
                    if i:
                        act.wait_ge(done, i)
                    for c in range(2):
                        for m in range(2):
                            last = act.activation(mid[:, c, m, :], K.ps[2 * c + m][:, 0:CTX], ACT.Copy)
                    last.then_inc(copied, 1)

            @block.vector
            def _(dve):
                for i, s in enumerate(streams):
                    dve.wait_ge(done, i + 1)
                    for c in range(2):
                        last = dve.tensor_copy(zT[:, c, s * CTX:(s + 1) * CTX], K.ps[4 + c][:, 0:CTX])
                    last.then_inc(out_copied, 1)


def merge(K, l, hT, zTs, yT, t0):
    nc = K.nc
    tw = TALL - t0
    jobs = [(b, c) for b in range(4) for c in range(4)]
    with ExitStack() as mem:
        wg = mem.enter_context(nc.sbuf_tensor(f"mg_wg{l}", [P, 3, KD, 256], F32))
        wb = mem.enter_context(nc.sbuf_tensor(f"mg_wb{l}", [P, 3, 2, 256], F32))
        halves = tuple(mem.enter_context(nc.sbuf_tensor(f"mg_{h}{l}", [P, 2, KD, 256], F32R)) for h in ("hi", "lo"))
        gate = mem.enter_context(nc.sbuf_tensor(f"mg_gate{l}", [P, 2, tw], F32))
        term = mem.enter_context(nc.sbuf_tensor(f"mg_term{l}", [P, 2, tw], F32))
        with stage(K, "w0", "w1", "w2", "gate_psum", "branch_psum", "gate_done", "termed", "added", "hi_ready", "lo_ready") as \
                (block, w0, w1, w2, gate_psum, branch_psum, gate_done, termed, added, hi_ready, lo_ready):
            loaded = (w0, w1, w2)

            @block.sync
            def _(sp):
                for n, (b, c) in enumerate(jobs):
                    if n >= 3:
                        sp.wait_ge(lo_ready, n - 2)
                        sp.wait_ge(branch_psum, 2 * (n - 2))
                    at = BR_OFF + b * D + c * 256
                    sp.dma_start(wg[:, n % 3, :, :], K.dram["w_in"][l][:, at:at + 256].rearrange("(k p) n -> p k n", p=P)).then_inc(loaded[n % 3], 16)
                    sp.dma_start(wb[:, n % 3, :, :], K.dram["w_branch"][l][b * MIX:(b + 1) * MIX, c * 256:(c + 1) * 256]
                                 .rearrange("(k p) n -> p k n", p=P)).then_inc(loaded[n % 3], 16)

            @block.tensor
            def _(pe):
                for n, (b, c) in enumerate(jobs):
                    pe.wait_ge(loaded[n % 3], 32 * (n // 3 + 1))
                    pe.wait_ge(lo_ready, n + 1)
                    for j in range(2):
                        i = 2 * n + j
                        if i >= 2:
                            pe.wait_ge(gate_done, i - 1)
                        for k in range(KD):
                            last = products_of(pe, K.ps[i % 2][:, 0:tw], both(halves, slice(0, P), n % 2, k, slice(j * P, (j + 1) * P)),
                                               both(hT, slice(0, P), k, slice(t0, TALL)), k == 0, k == KD - 1)
                        last.then_inc(gate_psum, 1)
                        if i >= 2:
                            pe.wait_ge(termed, i - 1)
                        for k in range(2):
                            last = pe.matmul(K.ps[2 + i % 2][:, 0:tw], wb[:, n % 3, k, j * P:(j + 1) * P],
                                             zTs[:, b, k, t0:TALL], start=k == 0, stop=k == 1)
                        last.then_inc(branch_psum, 1)

            @block.scalar
            def _(act):
                def split_hi(n):
                    act.wait_ge(loaded[n % 3], 32 * (n // 3 + 1))
                    if n >= 2:
                        act.wait_ge(gate_psum, 2 * (n - 1))
                    act.activation(halves[0][:, n % 2, :, :], wg[:, n % 3, :, :], ACT.Copy).then_inc(hi_ready, 1)

                split_hi(0)
                for n in range(len(jobs)):
                    if n + 1 < len(jobs):
                        split_hi(n + 1)
                    for i in (2 * n, 2 * n + 1):
                        act.wait_ge(gate_psum, i + 1)
                        if i >= 2:
                            act.wait_ge(termed, i - 1)
                        act.activation(gate[:, i % 2, :], K.ps[i % 2][:, 0:tw], ACT.Sigmoid).then_inc(gate_done, 1)

            @block.vector
            def _(dve):
                def split_lo(n):
                    dve.wait_ge(hi_ready, n + 1)
                    dve.tensor_tensor(halves[1][:, n % 2, :, :], wg[:, n % 3, :, :], halves[0][:, n % 2, :, :].bitcast(F32),
                                      ALU.subtract).then_inc(lo_ready, 1)

                split_lo(0)
                for n, (b, c) in enumerate(jobs):
                    if n + 1 < len(jobs):
                        split_lo(n + 1)
                    for i in (2 * n, 2 * n + 1):
                        dve.wait_ge(gate_done, i + 1)
                        dve.wait_ge(branch_psum, i + 1)
                        dst = yT[:, 2 * c + i % 2, t0:TALL]
                        if b == 0:
                            dve.tensor_tensor(dst, K.ps[2 + i % 2][:, 0:tw], gate[:, i % 2, :], ALU.mult).then_inc(termed, 1)
                        else:
                            if i >= 10:
                                dve.wait_ge(added, i - 9)
                            dve.tensor_tensor(term[:, i % 2, :], K.ps[2 + i % 2][:, 0:tw], gate[:, i % 2, :], ALU.mult).then_inc(termed, 1)
                            dve.wait_ge(termed, i + 1)
                            dve.tensor_tensor(dst, dst, term[:, i % 2, :], ALU.add).then_inc(added, 1)


def add_scaled(K, x, scale_of):
    def evacuate(eng, chain, psum, c, t):
        w = psum.shape[1]
        if scale_of is None:
            return eng.tensor_tensor(x[:, t, c:c + w], x[:, t, c:c + w], psum, ALU.add)
        chain(eng.tensor_tensor(K.junk[:, 0:w], psum, scale_of(t)[:, c:c + w], ALU.mult))
        return eng.tensor_tensor(x[:, t, c:c + w], x[:, t, c:c + w], K.junk[:, 0:w], ALU.add)
    return evacuate


def expert_choice(K, l, qT, tiles, choice):
    nc = K.nc
    with ExitStack() as mem:
        def sb(name, shape, dt=F32):
            return mem.enter_context(nc.sbuf_tensor(f"pc_{name}{l}", shape, dt))
        keys = sb("keys", [P, 2, NKEYS])
        sc = sb("sc", [P, 16, NKEYS])
        sc2 = sb("sc2", [P, 16, NKEYS])
        top = sb("top", [P, 16, TOPK])
        topi = sb("topi", [P, 16, TOPK], U32)
        topf = sb("topf", [P, 16, TOPK])
        best = sb("best", [P, PH, TOPK])
        pos = sb("pos", [P, PH, TOPK], U32)
        half = sb("half", [P, 2, PH, TOPK], U32)
        halff = sb("halff", [P, 2, PH, TOPK])
        rows = sb("rows", [P, 3, P])
        tot = sb("tot", [P, 2, PH])
        cand = sc[:, :, :].rearrange("p (h a) n -> p h (a n)", a=2)
        cand2 = sc2[:, :, :].rearrange("p (h a) n -> p h (a n)", a=2)
        hot = sc2[:, :, :].rearrange("p a n -> p (a n)").rearrange("p (q j) -> p q j", j=TOPK)
        load(K, (keys[:, :, :], K.dram["peer_keys"][l]))
        for t in tiles:
            with stage(K, "scored", "copied", "step", "shifted", "exped", "rows_done", "turned") as \
                    (block, scored, copied, step, shifted, exped, rows_done, turned):
                @block.tensor
                def _(pe):
                    for b in range(4):
                        for j in range(4):
                            hp = 4 * b + j
                            last = pe.matmul(K.ps[b][:, j * P:(j + 1) * P], qT[:, hp, t * P:(t + 1) * P], keys[:, hp % 2, :],
                                             start=True, stop=True)
                        last.then_inc(scored, 1)
                    pe.wait_ge(rows_done, 1)
                    for r in range(3):
                        last = pe.transpose(K.ps[4][:, r * P:(r + 1) * P], rows[:, r, :], K.ident[:, :])
                    last.then_inc(turned, 1)

                @block.scalar
                def _(act):
                    for b in range(4):
                        act.wait_ge(scored, b + 1)
                        act.activation(sc[:, 4 * b:4 * b + 4, :], K.ps[b][:, :].rearrange("p (j n) -> p j n", j=4), ACT.Copy).then_inc(copied, 1)
                    act.wait_ge(shifted, 1)
                    act.activation(rows[:, 2, :], rows[:, 2, :], ACT.Exp).then_inc(exped, 1)
                    act.wait_ge(turned, 1)
                    act.activation(choice[:, :, t * P:(t + 1) * P], K.ps[4][:, 0:3 * P].rearrange("p (r n) -> p r n", r=3), ACT.Copy)

                @block.vector
                def _(dve):
                    chain = Chain(dve, step)

                    def top16(vals, idx, src, scratch, n):
                        for i in range(n):
                            last = dve.max(vals[:, i, 0:8], src[:, i, :])
                        chain(last)
                        for i in range(n):
                            dve.max_index(idx[:, i, 0:8], vals[:, i, 0:8], src[:, i, :])
                            last = dve.match_replace(scratch[:, i, :], vals[:, i, 0:8], src[:, i, :], -3e38)
                        chain(last)
                        for i in range(n):
                            last = dve.max(vals[:, i, 8:16], scratch[:, i, :])
                        chain(last)
                        for i in range(n):
                            last = dve.max_index(idx[:, i, 8:16], vals[:, i, 8:16], scratch[:, i, :])
                        chain(last)

                    dve.wait_ge(copied, 4)
                    top16(top, topi, sc, sc2, 16)
                    chain(dve.tensor_copy(topf[:, :, :], topi[:, :, :]))
                    for h in range(PH):
                        last = dve.tensor_tensor(cand[:, h, :].rearrange("p (a b) -> p a b", a=TOPK),
                                                 top[:, 2 * h, :][:, :, None].broadcast_to([P, TOPK, TOPK]),
                                                 top[:, 2 * h + 1, :][:, None, :].broadcast_to([P, TOPK, TOPK]), ALU.add)
                    chain(last)
                    top16(best, pos, cand, cand2, PH)
                    dve.tensor_single_scalar(half[:, 0, :, :], pos[:, :, :], 4, ALU.logical_shift_right)
                    chain(dve.tensor_single_scalar(half[:, 1, :, :], pos[:, :, :], TOPK - 1, ALU.bitwise_and))
                    chain(dve.tensor_copy(halff[:, :, :, :], half[:, :, :, :]))
                    tf = topf[:, :, :].rearrange("p (h a) j -> p h a j", a=2)
                    for a in range(2):
                        chain(dve.tensor_tensor(hot, halff[:, a, :, :].rearrange("p h k -> p (h k)")[:, :, None].broadcast_to([P, P, TOPK]),
                                                K.iota[:, None, 0:TOPK].broadcast_to([P, P, TOPK]), ALU.is_equal))
                        for h in range(PH):
                            hh = hot[:, h * TOPK:(h + 1) * TOPK, :]
                            last = dve.tensor_tensor(hh, hh, tf[:, h, a, :][:, None, :].broadcast_to([P, TOPK, TOPK]), ALU.mult)
                        chain(last)
                        chain(dve.tensor_reduce(rows[:, a, :], hot, AX.X, ALU.add))
                    g = rows[:, 2, :].rearrange("p (h k) -> p h k", h=PH)
                    dve.tensor_tensor(g, best[:, :, :], best[:, :, 0:1].broadcast_to([P, PH, TOPK]), ALU.subtract).then_inc(shifted, 1)
                    dve.wait_ge(exped, 1)
                    chain(dve.tensor_reduce(tot[:, 0, :], g, AX.X, ALU.add))
                    chain(dve.reciprocal(tot[:, 1, :], tot[:, 0, :]))
                    dve.tensor_tensor(g, g, tot[:, 1, :][:, :, None].broadcast_to([P, PH, TOPK]), ALU.mult).then_inc(rows_done, 1)


def spread_choice(K, l, choice, t0, tw):
    nc = K.nc
    rounds = tw // 128
    with ExitStack() as mem:
        first = mem.enter_context(nc.sbuf_tensor(f"sp_a{l}", [P, 2, 4, P], F32))
        second = mem.enter_context(nc.sbuf_tensor(f"sp_b{l}", [P, 2, 4, P], F32))
        buf = mem.enter_context(nc.sbuf_tensor(f"sp_buf{l}", [P, 2, P, 64], F32))
        with stage(K, "hot", "paired", "copied", "stored0", "stored1") as \
                (block, hot, paired, copied, stored0, stored1):
            stored = (stored0, stored1)

            def groups(eng, work, before_slot=None):
                with eng.Fori(0, rounds) as i:
                    for slot in range(2):
                        if before_slot:
                            before_slot(i, slot)
                        with eng.Fori(0, 8) as g:
                            for u in range(2):
                                work(i * 32 + slot * 16 + g * 2 + u, u, slot, g * 2 + u)

            @block.vector
            def _(dve):
                def work(n, u, slot, q0):
                    dve.wait_ge(copied, n + 1)
                    for q in range(4):
                        t = n * 4 + q + t0
                        dve.tensor_scalar(first[:, u, q, :], K.iota[:, :], choice[:, 0, ds(t, 1)],
                                          choice[:, 2, ds(t, 1)], ALU.is_equal, ALU.mult)
                        last = dve.tensor_scalar(second[:, u, q, :], K.iota[:, :], choice[:, 1, ds(t, 1)], None, ALU.is_equal)
                    last.then_inc(hot, 1)
                groups(dve, work)

            @block.tensor
            def _(pe):
                def work(n, u, slot, q0):
                    pe.wait_ge(hot, n + 1)
                    for q in range(4):
                        last = pe.matmul(K.ps[u][:, q * P:(q + 1) * P], second[:, u, q, :], first[:, u, q, :], start=True, stop=True)
                    last.then_inc(paired, 1)
                groups(pe, work)

            @block.scalar
            def _(act):
                act.sem_inc(copied, 2)

                def work(n, u, slot, q0):
                    act.wait_ge(paired, n + 1)
                    act.activation(buf[:, slot, :, ds(q0 * 4, 4)], K.ps[u][:, :].rearrange("p (q i) -> p i q", q=4),
                                   ACT.Copy).then_inc(copied, 1)
                groups(act, work, lambda i, slot: act.wait_ge(stored[slot], i * 16 + 16))

            @block.sync
            def _(sp):
                for slot in range(2):
                    sp.sem_inc(stored[slot], 16)
                with sp.Fori(0, rounds) as i:
                    for slot in range(2):
                        sp.wait_ge(copied, i * 32 + (slot * 16 + 18))
                        sp.dma_start(K.dense[ds(i * 2 + slot, 1), :, :].rearrange("b j n -> (b j) n"),
                                     buf[:, slot, :, :].rearrange("p i t -> p (i t)")).then_inc(stored[slot], 16)
                for slot in range(2):
                    sp.wait_ge(stored[slot], 16 * (rounds + 1))


def experts(K, l, hT, acc, t0, tw):
    nc = K.nc
    E = 2
    step_e = E * P
    n_steps = NEXP // step_e
    outs = tw // P * 2
    nb = tw // 64
    with ExitStack() as mem:
        def sb(name, shape, dt=F32):
            return mem.enter_context(nc.sbuf_tensor(f"ex_{name}{l}", shape, dt))
        u, v = sb("u", [P, 2, KD, step_e]), sb("v", [P, 2, E, D])
        u2 = sb("uhi", [P, 2, KD, step_e], F32R), sb("ulo", [P, 2, KD, step_e], F32R)
        v2 = sb("vhi", [P, 2, E, D], F32R), sb("vlo", [P, 2, E, D], F32R)
        g = sb("g", [P, 2, nb, E * 64])
        a = sb("a", [P, E, tw])
        a2 = sb("ahi", [P, 2, E, tw], F32R), sb("alo", [P, 2, E, tw], F32R)
        names = ["u0", "u1", "v0", "v1", "g0", "g1", "scored", "gelued", "a_step", "weighted", "outed", "added",
                 "u_hi", "u_lo", "v_hi", "v_lo"]
        with stage(K, *names) as (block, u0, u1, v0, v1, g0, g1, scored, gelued, a_step, weighted, outed, added, u_hi, u_lo, v_hi, v_lo):
            us, vs, gs = (u0, u1), (v0, v1), (g0, g1)
            half = n_steps // 2
            rows = slice(0, P)

            def steps(eng, first, second):
                first(0, 0, 0)
                for n in range(1, 4):
                    first(n, n % 2, n)
                    second(n - 1, (n - 1) % 2, n - 1)
                with eng.Fori(2, half) as i:
                    first(i * 2, 0, None)
                    second(i * 2 - 1, 1, None)
                    first(i * 2 + 1, 1, None)
                    second(i * 2, 0, None)
                second(n_steps - 1, 1, None)

            def later(peeled, least):
                return peeled is None or peeled >= least

            @block.sync
            def _(sp):
                def fetch(n, s, peeled):
                    if later(peeled, 2):
                        sp.wait_ge(u_lo, n - 1)
                    sp.dma_start(u[:, s, :, :], K.dram["peer_u"][l][:, ds(n * step_e, step_e)].rearrange("(k p) e -> p k e", p=P)).then_inc(us[s], 16)
                    if later(peeled, 2):
                        sp.wait_ge(weighted, n * E - E)
                    sp.dma_start(g[:, s, :, :], K.dense[0:nb, :, ds(n * (E * 64), E * 64)].rearrange("b j n -> j b n")).then_inc(gs[s], 16)
                    if later(peeled, 2):
                        sp.wait_ge(v_lo, n - 1)
                    sp.dma_start(v[:, s, :, :], K.dram["peer_v"][l][ds(n * step_e, step_e), :].rearrange("(k p) d -> p k d", p=P)).then_inc(vs[s], 16)
                steps(sp, fetch, lambda n, s, peeled: None)

            @block.gpsimd
            def _(pool):
                def split_u(n, s, peeled):
                    pool.wait_ge(u_hi, n + 1)
                    pool.tensor_tensor(u2[1][:, s, :, :], u[:, s, :, :], u2[0][:, s, :, :].bitcast(F32), ALU.subtract).then_inc(u_lo, 1)
                steps(pool, split_u, lambda n, s, peeled: None)

            @block.tensor
            def _(pe):
                def score(n, s, peeled):
                    pe.wait_ge(u_lo, n + 1)
                    for e in range(E):
                        if later(peeled, 1):
                            pe.wait_ge(gelued, n * E + (e - 1))
                        for k in range(KD):
                            last = products_of(pe, K.ps[e][:, 0:tw], both(u2, rows, s, k, slice(e * P, (e + 1) * P)),
                                               both(hT, rows, k, slice(t0, t0 + tw)), k == 0, k == KD - 1)
                        last.then_inc(scored, 1)

                def combine(n, s, peeled):
                    pe.wait_ge(v_lo, n + 1)
                    pe.wait_ge(weighted, n * E + E)
                    for o in range(outs):
                        t, c = divmod(o, 2)
                        if later(peeled, 1) or o >= 4:
                            pe.wait_ge(added, n * outs + (o - 3))
                        for e in range(E):
                            last = products_of(pe, K.ps[2 + o % 4][:, :], both(a2, rows, s, e, slice(t * P, (t + 1) * P)),
                                               both(v2, rows, s, e, slice(c * 512, (c + 1) * 512)), e == 0, e == E - 1)
                        last.then_inc(outed, 1)
                steps(pe, score, combine)

            @block.scalar
            def _(act):
                def split_u(n, s, peeled):
                    act.wait_ge(us[s], (n - s) * 8 + 16)
                    if later(peeled, 2):
                        act.wait_ge(scored, n * E - E)
                    act.activation(u2[0][:, s, :, :], u[:, s, :, :], ACT.Copy).then_inc(u_hi, 1)

                def values_and_gelu(n, s, peeled):
                    act.wait_ge(vs[s], (n - s) * 8 + 16)
                    if later(peeled, 2):
                        act.wait_ge(outed, n * outs - outs)
                    act.activation(v2[0][:, s, :, :], v[:, s, :, :], ACT.Copy).then_inc(v_hi, 1)
                    for e in range(E):
                        act.wait_ge(scored, n * E + (e + 1))
                        if later(peeled, 1):
                            act.wait_ge(weighted, n * E + (e - 1))
                        act.activation(a[:, e, :], K.ps[e][:, 0:tw], ACT.Gelu_apprx_tanh).then_inc(gelued, 1)
                steps(act, split_u, values_and_gelu)

            @block.vector
            def _(dve):
                def weigh(n, s, peeled):
                    dve.wait_ge(v_hi, n + 1)
                    dve.tensor_tensor(v2[1][:, s, :, :], v[:, s, :, :], v2[0][:, s, :, :].bitcast(F32), ALU.subtract).then_inc(v_lo, 1)
                    dve.wait_ge(gs[s], (n - s) * 8 + 16)
                    if later(peeled, 2):
                        dve.wait_ge(outed, n * outs - outs)
                    for e in range(E):
                        dve.wait_ge(gelued, n * E + (e + 1))
                        av = a[:, e, :].rearrange("p (b t) -> p b t", t=64)
                        dve.tensor_tensor(av, av, g[:, s, :, e * 64:(e + 1) * 64], ALU.mult).then_inc(a_step, 1)
                        dve.wait_ge(a_step, n * (2 * E) + (2 * e + 1))
                        dve.tensor_copy(a2[0][:, s, e, :], a[:, e, :]).then_inc(a_step, 1)
                        dve.wait_ge(a_step, n * (2 * E) + (2 * e + 2))
                        dve.tensor_tensor(a2[1][:, s, e, :], a[:, e, :], a2[0][:, s, e, :].bitcast(F32), ALU.subtract).then_inc(weighted, 1)

                def gather(n, s, peeled):
                    for o in range(outs):
                        t, c = divmod(o, 2)
                        dve.wait_ge(outed, n * outs + (o + 1))
                        dst = acc[:, t, c * 512:(c + 1) * 512]
                        if not later(peeled, 1):
                            dve.tensor_copy(dst, K.ps[2 + o % 4][:, :]).then_inc(added, 1)
                        else:
                            dve.wait_ge(added, n * outs + (o + 1 - outs))
                            dve.tensor_tensor(dst, dst, K.ps[2 + o % 4][:, :], ALU.add).then_inc(added, 1)
                steps(dve, weigh, gather)


def first_layer(K, l, x, s_cols):
    nc = K.nc
    last = l == DEPTH - 1
    all_tiles = [0, 1, 2, 3]
    tiles = [2, 3] if last else all_tiles
    streams = [1] if last else [0, 1]
    t0 = tiles[0] * P
    with ExitStack() as mem:
        def sb(name, shape, scope=mem):
            return scope.enter_context(nc.sbuf_tensor(f"{name}_l{l}", shape, F32))
        mod5 = sb("mod5", [P, 2, D])
        hT = tuple(mem.enter_context(nc.sbuf_tensor(f"hT{h}_l{l}", [P, KD, TALL], F32R)) for h in ("hi", "lo"))
        late = ExitStack()
        mod234 = sb("mod234", [P, 3, 2, D], late)
        with nc.sbuf_tensor(f"mod01_l{l}", [P, 2, 2, D], F32) as mod01, nc.sbuf_tensor(f"h_l{l}", [P, 4, D], F32) as h:
            mod = [mod01[:, 0], mod01[:, 1], mod234[:, 0], mod234[:, 1], mod234[:, 2], mod5[:, :, :]]
            modulation(K, l, s_cols, mod)
            rms_norm(K, x, all_tiles, lambda t: mod[1][:, t // 2, :], lambda t: mod[0][:, t // 2, :], h, hT)
        mix = ExitStack()
        zTs = sb("zTs", [P, 4, 2, TALL], mix)
        with ExitStack() as rows:
            gm = sb("gm", [P, 4, 2 * MIX], rows)
            ft = sb("ft", [P, 4, MIX], rows)
            project(K, K.dram["w_in"][l], KD, hT, [
                (GM_OFF, 2 * MIX, False, tiles, copy_to(lambda o, t: gm[:, t, o:o + 256], ACT.Gelu_apprx_tanh)),
                (FT_OFF, MIX, False, tiles, copy_to(lambda o, t: ft[:, t, :]))])
            gmlp(K, l, zTs[:, 1], gm, tiles)
            fourier(K, l, zTs[:, 3], ft, streams)
        with ExitStack() as rows:
            vones = sb("vones", [P, 4, 4, DH + 1], rows)
            gates = sb("gates", [P, 4, 16], rows)
            osig = sb("osig", [P, 4, MIX], rows)
            with stage(K) as (block,):
                @block.vector
                def _(dve):
                    dve.memset(vones[:, :, :, DH:DH + 1], 1.0)

            def into_v(eng, chain, psum, o, t):
                return eng.activation(vones[:, t, :, 0:DH], psum.rearrange("p (h d) -> p h d", h=4), ACT.Copy)
            project(K, K.dram["w_in"][l], KD, hT, [
                (V_OFF, MIX, False, all_tiles, into_v),
                (GATE_OFF_ML, 16, False, all_tiles, copy_to(lambda o, t: gates[:, t, :])),
                (O_OFF, MIX, False, tiles, copy_to(lambda o, t: osig[:, t, :], ACT.Sigmoid))])
            mlstm(K, l, hT, zTs[:, 0], last, vones, gates, osig)
        conv_branch(K, l, hT, zTs[:, 2], streams)
        yT = sb("yT", [P, KD, TALL], mix)
        merge(K, l, hT, zTs, yT, t0)
        project(K, K.dram["w_out"][l], KD, yT, [(0, D, False, tiles, add_scaled(K, x, lambda t: mod[2][:, t // 2, :]))],
                width=512, ring=2, engine="vector")
        mix.close()
        with nc.sbuf_tensor(f"h2_l{l}", [P, 4, D], F32) as h:
            rms_norm(K, x, tiles, lambda t: mod[4][:, t // 2, :], lambda t: mod[3][:, t // 2, :], h, hT)
        late.close()
        with nc.sbuf_tensor(f"choice_l{l}", [P, 3, TALL], F32) as choice:
            with nc.sbuf_tensor(f"qT_l{l}", [P, 16, TALL], F32) as qT:
                project(K, K.dram["peer_w_q"][l], KD, hT, [(0, 2048, True, (t0, TALL), copy_to(lambda o, t: qT[:, o // P, t0:TALL]))])
                expert_choice(K, l, qT, tiles, choice)
            spread_choice(K, l, choice, t0, TALL - t0)
        with nc.sbuf_tensor(f"peer_l{l}", [P, len(tiles), D], F32) as acc:
            experts(K, l, hT, acc, t0, TALL - t0)
            with stage(K, "step") as (block, step):
                @block.vector
                def _(dve):
                    chain = Chain(dve, step)
                    for i, t in enumerate(tiles):
                        chain(dve.tensor_tensor(acc[:, i, :], acc[:, i, :], mod[5][:, t // 2, :], ALU.mult))
                        dve.tensor_tensor(x[:, t, :], x[:, t, :], acc[:, i, :], ALU.add)



def products(K, jobs, evacuate):
    with stage(K, "done", "step") as (block, done, step):
        @block.tensor
        def _(pe):
            for i, (lhsT, rhs) in enumerate(jobs):
                last = pe.matmul(K.ps[i // 4][:, (i % 4) * P:(i % 4 + 1) * P], lhsT, rhs, start=True, stop=True)
                if i % 4 == 3:
                    last.then_inc(done, 1)

        @block.vector
        def _(dve):
            chain = Chain(dve, step)
            for half in range(len(jobs) // 4):
                dve.wait_ge(done, half + 1)
                evacuate(dve, chain, half, K.ps[half][:, :].rearrange("p (h c) -> p h c", h=4))


def gated_delta(K, j, qkv, ba, z, cat):
    nc = K.nc
    with ExitStack() as mem:
        def sb(name, shape, scope=mem):
            return scope.enter_context(nc.sbuf_tensor(f"gd_{name}", shape, F32))
        beta, g = sb("beta", [P, 2, GH]), sb("g", [P, 2, GH])
        par = sb("par", [P, 3, GH])
        soft = sb("soft", [P, 2, GH])
        gcs = sb("gcs", [P, 2, 2, GH])
        eg = sb("eg", [P, 2, GH])
        kd = sb("kd", [P, 2, GH])
        gain = sb("gain", [P, P])
        load(K, (par[:, 0, :], K.dram["gdn_a_log"][j:j + 1, :].broadcast_to([P, GH])),
             (par[:, 1, :], K.dram["gdn_dt_bias"][j:j + 1, :].broadcast_to([P, GH])),
             (gain[:, :], K.dram["gdn_norm_w"][j:j + 1, :].broadcast_to([P, P])))
        with stage(K, "step", "biased", "act_step") as (block, step, biased, act_step):
            @block.vector
            def _(dve):
                chain = Chain(dve, step)
                dve.tensor_tensor(g[:, :, :], ba[:, :, GH:2 * GH], par[:, 1, :][:, None, :].broadcast_to([P, 2, GH]), ALU.add).then_inc(biased, 1)
                dve.wait_ge(act_step, 5)
                chain(dve.tensor_single_scalar(g[:, :, :], g[:, :, :], 0.0, ALU.max))
                chain(dve.tensor_tensor(g[:, :, :], g[:, :, :], soft[:, :, :], ALU.add))
                chain(dve.tensor_tensor(g[:, :, :], g[:, :, :], par[:, 2, :][:, None, :].broadcast_to([P, 2, GH]), ALU.mult))
                dve.tensor_single_scalar(g[:, :, :], g[:, :, :], -1.0, ALU.mult)

            @block.scalar
            def _(act):
                chain = Chain(act, act_step)
                chain(act.activation(beta[:, :, :], ba[:, :, 0:GH], ACT.Sigmoid))
                chain(act.activation(par[:, 2, :], par[:, 0, :], ACT.Exp))
                act.wait_ge(biased, 1)
                chain(act.activation(soft[:, :, :], g[:, :, :], ACT.Abs))
                chain(act.activation(soft[:, :, :], soft[:, :, :], ACT.Exp, scale=-1.0))
                chain(act.activation(soft[:, :, :], soft[:, :, :], ACT.Ln, bias=1.0))
        with nc.sbuf_tensor("gd_sq", [P, 16, T1], F32) as sq:
            with stage(K, "squared", "summed") as (block, squared, summed):
                @block.scalar
                def _(act):
                    for i in range(16):
                        act.activation(sq[:, i, :], qkv[:, i, :], ACT.Square).then_inc(squared, 1)

                @block.tensor
                def _(pe):
                    for i in range(8):
                        pe.wait_ge(squared, 2 * i + 2)
                        for u in range(2):
                            last = pe.matmul(K.ps[i][:, u * T1:(u + 1) * T1], K.ones[:, :], sq[:, 2 * i + u, :], start=True, stop=True)
                        last.then_inc(summed, 1)

                @block.vector
                def _(dve):
                    for i in range(8):
                        dve.wait_ge(summed, i + 1)
                        dve.tensor_copy(sq[:, 2 * i:2 * i + 2, :], K.ps[i][:, :].rearrange("p (u t) -> p u t", u=2))
            inverse_root(K, sq[:, :, :], EPS)
            with stage(K) as (block,):
                @block.vector
                def _(dve):
                    for i in range(4):
                        dve.tensor_tensor(qkv[:, 4 * i:4 * i + 4, :], qkv[:, 4 * i:4 * i + 4, :], sq[:, 4 * i:4 * i + 4, :], ALU.mult)
        ktok, vtok = sb("ktok", [P, 2, GH, P]), sb("vtok", [P, 2, GH, P])
        transpose(K, [([qkv[:, base + 4 * q + i, t * P:(t + 1) * P] for i in range(4)], dst[:, t, 4 * q:4 * q + 4, :])
                      for base, dst in ((GH, ktok), (2 * GH, vtok)) for t in range(2) for q in range(2)])
        with stage(K, "summed", "copied") as (block, summed, copied):
            @block.tensor
            def _(pe):
                for t in range(2):
                    pe.matmul(K.ps[0][:, t * GH:(t + 1) * GH], K.tri[:, :], g[:, t, :], start=True, stop=True)
                    last = pe.matmul(K.ps[0][:, (2 + t) * GH:(3 + t) * GH], K.ones[:, :], g[:, t, :], start=True, stop=True)
                last.then_inc(summed, 1)

            @block.vector
            def _(dve):
                dve.wait_ge(summed, 1)
                dve.tensor_copy(gcs[:, :, :, :], K.ps[0][:, 0:4 * GH].rearrange("p (a t h) -> p a t h", a=2, t=2)).then_inc(copied, 1)
                dve.wait_ge(copied, 1)
                dve.tensor_tensor(kd[:, :, :], gcs[:, 1, :, :], gcs[:, 0, :, :], ALU.subtract).then_inc(copied, 1)

            @block.scalar
            def _(act):
                act.wait_ge(copied, 2)
                act.activation(eg[:, :, :], gcs[:, 0, :, :], ACT.Exp)
                act.activation(kd[:, :, :], kd[:, :, :], ACT.Exp)
        low, att = sb("low", [P, 4, 4, P]), sb("att", [P, 4, 4, P])
        masks = sb("masks", [P, 2, P])
        load(K, (masks[:, :, :], K.dram["gd_masks"]))
        with stage(K, "pe_done", "ranged", "exped", "read") as (block, pe_done, ranged, exped, read):
            @block.tensor
            def _(pe):
                for n in range(4):
                    t, hg = divmod(n, 2)
                    if n >= 2:
                        pe.wait_ge(read, n - 1)
                    b = 3 * (n % 2)
                    for i in range(4):
                        h = 4 * hg + i
                        cols = slice(i * P, (i + 1) * P)
                        kT, qT = qkv[:, GH + h, t * P:(t + 1) * P], qkv[:, h, t * P:(t + 1) * P]
                        pe.matmul(K.ps[b][:, cols], g[:, t, h:h + 1].broadcast_to([P, P]), K.tri[:, :], start=True, stop=True)
                        pe.matmul(K.ps[b + 1][:, cols], kT, kT, start=True, stop=True)
                        last = pe.matmul(K.ps[b + 2][:, cols], kT, qT, start=True, stop=True)
                    last.then_inc(pe_done, 1)

            @block.vector
            def _(dve):
                for n in range(4):
                    t, hg = divmod(n, 2)
                    dve.wait_ge(pe_done, n + 1)
                    b = 3 * (n % 2)
                    for i in range(4):
                        h = 4 * hg + i
                        row = K.ps[b][:, i * P:(i + 1) * P]
                        dve.scalar_tensor_tensor(out=low[:, n, i, :], in0=row, scalar=gcs[:, 0, t, h:h + 1], in1=masks[:, 0, :],
                                                 op0=ALU.subtract, op1=ALU.max)
                        last = dve.scalar_tensor_tensor(out=att[:, n, i, :], in0=row, scalar=gcs[:, 0, t, h:h + 1], in1=masks[:, 1, :],
                                                        op0=ALU.subtract, op1=ALU.min)
                    last.then_inc(ranged, 1)
                    dve.wait_ge(exped, n + 1)
                    view = [K.ps[b + 1 + i][:, :].rearrange("p (h c) -> p h c", h=4) for i in range(2)]
                    dve.tensor_tensor(low[:, n, :, :], low[:, n, :, :], view[0], ALU.mult)
                    dve.scalar_tensor_tensor(out=att[:, n, :, :], in0=view[1], scalar=SCALE, in1=att[:, n, :, :],
                                             op0=ALU.mult, op1=ALU.mult).then_inc(read, 1)
                    dve.wait_ge(read, n + 1)
                    dve.tensor_tensor(low[:, n, :, :], low[:, n, :, :],
                                      beta[:, t, 4 * hg:4 * hg + 4][:, :, None].broadcast_to([P, 4, P]), ALU.mult)

            @block.scalar
            def _(act):
                for n in range(4):
                    act.wait_ge(ranged, n + 1)
                    act.activation(low[:, n, :, :], low[:, n, :, :], ACT.Exp, scale=-1.0)
                    act.activation(att[:, n, :, :], att[:, n, :, :], ACT.Exp).then_inc(exped, 1)
        inv_t = sb("inv_t", [P, 4, 4, P])
        with ExitStack() as solve:
            inv = sb("inv", [P, 4, 4, P], solve)
            part, mid = sb("part", [P, 4, 4, P], solve), sb("mid", [P, 4, 4, P], solve)
            level = sb("level", [P, 7, P], solve)
            load(K, (level[:, :, :], K.dram["gd_levels"]))
            with stage(K) as (block,):
                @block.vector
                def _(dve):
                    for n in range(4):
                        dve.tensor_copy(inv[:, n, :, :], K.ident[:, None, :].broadcast_to([P, 4, P]))

                @block.scalar
                def _(act):
                    for n in range(4):
                        act.activation(inv_t[:, n, :, :], K.ident[:, None, :].broadcast_to([P, 4, P]), ACT.Copy)
            with stage(K, "parted", "mid_psum", "mid_copied", "joined", "subbed") as (block, parted, mid_psum, mid_copied, joined, subbed):
                @block.gpsimd
                def _(pool):
                    for m in range(28):
                        lv, n = divmod(m, 4)
                        if m >= 4:
                            pool.wait_ge(mid_psum, m - 3)
                        pool.tensor_tensor(part[:, n, :, :], low[:, n, :, :], level[:, lv, :][:, None, :].broadcast_to([P, 4, P]),
                                           ALU.mult).then_inc(parted, 1)

                @block.tensor
                def _(pe):
                    for lv in range(7):
                        for n in range(4):
                            m = 4 * lv + n
                            pe.wait_ge(parted, m + 1)
                            if m >= 4:
                                pe.wait_ge(subbed, m - 3)
                            for i in range(4):
                                last = pe.matmul(K.ps[n][:, i * P:(i + 1) * P], part[:, n, i, :], inv_t[:, n, i, :], start=True, stop=True)
                            last.then_inc(mid_psum, 1)
                        for n in range(4):
                            m = 4 * lv + n
                            pe.wait_ge(mid_copied, m + 1)
                            if m >= 2:
                                pe.wait_ge(subbed, m - 1)
                            b = 4 + 2 * (n % 2)
                            for i in range(4):
                                pe.matmul(K.ps[b][:, i * P:(i + 1) * P], inv[:, n, i, :], mid[:, n, i, :], start=True, stop=True)
                                last = pe.matmul(K.ps[b + 1][:, i * P:(i + 1) * P], mid[:, n, i, :], inv[:, n, i, :], start=True, stop=True)
                            last.then_inc(joined, 1)

                @block.scalar
                def _(act):
                    for m in range(28):
                        n = m % 4
                        act.wait_ge(mid_psum, m + 1)
                        if m >= 4:
                            act.wait_ge(joined, m - 3)
                        act.activation(mid[:, n, :, :], K.ps[n][:, :].rearrange("p (h c) -> p h c", h=4), ACT.Copy).then_inc(mid_copied, 1)

                @block.vector
                def _(dve):
                    for m in range(28):
                        n = m % 4
                        b = 4 + 2 * (n % 2)
                        dve.wait_ge(joined, m + 1)
                        if m >= 4:
                            dve.wait_ge(subbed, m - 3)
                        dve.tensor_tensor(inv_t[:, n, :, :], inv_t[:, n, :, :], K.ps[b][:, :].rearrange("p (h c) -> p h c", h=4), ALU.subtract)
                        dve.tensor_tensor(inv[:, n, :, :], inv[:, n, :, :], K.ps[b + 1][:, :].rearrange("p (h c) -> p h c", h=4),
                                          ALU.subtract).then_inc(subbed, 1)
        vb, vnew = sb("vb", [P, 2, GH, P]), sb("vnew", [P, 2, GH, P])
        state = sb("state", [P, GH, P])
        o = sb("o", [P, 2, GH, P])

        def over(ap, half):
            return ap[:, 4 * half:4 * half + 4][:, :, None].broadcast_to([P, 4, P])
        with stage(K) as (block,):
            @block.vector
            def _(dve):
                for half in range(2):
                    hs = slice(4 * half, 4 * half + 4)
                    dve.tensor_tensor(vb[:, 0, hs, :], vtok[:, 0, hs, :], over(beta[:, 0, :], half), ALU.mult)
                    dve.tensor_tensor(ktok[:, 0, hs, :], ktok[:, 0, hs, :], over(kd[:, 0, :], half), ALU.mult)

        def copy_into(dst):
            def evacuate(dve, chain, half, psum):
                dve.tensor_copy(dst[:, 4 * half:4 * half + 4, :], psum)
            return evacuate
        heads = range(GH)
        products(K, [(inv_t[:, h // 4, h % 4, :], vb[:, 0, h, :]) for h in heads], copy_into(vnew[:, 0]))
        products(K, [(ktok[:, 0, h, :], vnew[:, 0, h, :]) for h in heads], copy_into(state))

        def residual(dve, chain, half, psum):
            hs = slice(4 * half, 4 * half + 4)
            r = vb[:, 1, hs, :]
            chain(dve.tensor_tensor(r, psum, over(eg[:, 1, :], half), ALU.mult))
            chain(dve.tensor_tensor(r, vtok[:, 1, hs, :], r, ALU.subtract))
            chain(dve.tensor_tensor(r, r, over(beta[:, 1, :], half), ALU.mult))
        products(K, [(qkv[:, GH + h, P:2 * P], state[:, h, :]) for h in heads], residual)
        products(K, [(inv_t[:, 2 + h // 4, h % 4, :], vb[:, 1, h, :]) for h in heads], copy_into(vnew[:, 1]))
        for t in range(2):
            products(K, [(att[:, 2 * t + h // 4, h % 4, :], vnew[:, t, h, :]) for h in heads], copy_into(o[:, t]))

        def from_state(dve, chain, half, psum):
            hs = slice(4 * half, 4 * half + 4)
            chain(dve.scalar_tensor_tensor(out=vb[:, 0, hs, :], in0=psum, scalar=SCALE, in1=over(eg[:, 1, :], half),
                                           op0=ALU.mult, op1=ALU.mult))
            dve.tensor_tensor(o[:, 1, hs, :], o[:, 1, hs, :], vb[:, 0, hs, :], ALU.add)
        products(K, [(qkv[:, h, P:2 * P], state[:, h, :]) for h in heads], from_state)
        ss = K.small[:, 0:16].rearrange("p (t h) -> p t h", t=2)
        with stage(K, "step") as (block, step):
            @block.vector
            def _(dve):
                chain = Chain(dve, step)
                for t in range(2):
                    chain(dve.tensor_tensor(vb[:, t, :, :], o[:, t, :, :], o[:, t, :, :], ALU.mult))
                    chain(dve.tensor_reduce(ss[:, t, :], vb[:, t, :, :], AX.X, ALU.add))
                dve.tensor_single_scalar(ss[:, :, :], ss[:, :, :], 1.0 / P, ALU.mult)
        inverse_root(K, K.small[:, 0:16], EPS)
        with stage(K, "step") as (block, step):
            @block.vector
            def _(dve):
                chain = Chain(dve, step)
                for t in range(2):
                    ov = o[:, t, :, :]
                    chain(dve.tensor_tensor(ov, ov, ss[:, t, :][:, :, None].broadcast_to([P, GH, P]), ALU.mult))
                    chain(dve.tensor_tensor(ov, ov, gain[:, None, :].broadcast_to([P, GH, P]), ALU.mult))
                    dve.tensor_tensor(cat[:, t, 0:D].rearrange("p (h c) -> p h c", h=GH), ov,
                                      z[:, t, :].rearrange("p (h c) -> p h c", h=GH), ALU.mult)


def attend(K, items, scale):
    nc = K.nc
    N = len(items)
    K.uid += 1
    with ExitStack() as mem:
        def sb(name, shape):
            return mem.enter_context(nc.sbuf_tensor(f"at_{name}{K.uid}", shape, F32))
        sc, pr, pt = sb("sc", [P, 2, T1]), sb("pr", [P, 2, T1]), sb("pt", [P, 2, T1])
        neg_max, total, weight = sb("max", [P, N]), sb("total", [P, N]), sb("weight", [P, N])
        out_tmp = sb("tmp", [P, 2, P])
        with stage(K, "scored", "scaled", "maxed", "exped", "turned", "pt_ready", "outed", "finished", "step") as \
                (block, scored, scaled, maxed, exped, turned, pt_ready, outed, finished, step):
            @block.tensor
            def _(pe):
                def score(n):
                    q, k = items[n][0:2]
                    if n >= 2:
                        pe.wait_ge(scaled, n - 1)
                    pe.matmul(K.ps[n % 2][:, 0:k.shape[1]], q, k, start=True, stop=True).then_inc(scored, 1)

                score(0)
                for n in range(N):
                    if n + 1 < N:
                        score(n + 1)
                    width = items[n][1].shape[1]
                    pe.wait_ge(exped, n + 1)
                    if n >= 2:
                        pe.wait_ge(pt_ready, n - 1)
                    for c in range(width // P):
                        last = pe.transpose(K.ps[2 + n % 2][:, c * P:(c + 1) * P], pr[:, n % 2, c * P:(c + 1) * P], K.ident[:, :])
                    last.then_inc(turned, 1)
                    pe.wait_ge(pt_ready, n + 1)
                    if n >= 2:
                        pe.wait_ge(finished, n - 1)
                    for c, v in enumerate(items[n][3]):
                        last = pe.matmul(K.ps[4 + n % 2][:, 0:P], pt[:, n % 2, c * P:(c + 1) * P], v, start=c == 0, stop=c == width // P - 1)
                    last.then_inc(outed, 1)

            @block.scalar
            def _(act):
                for n in range(N):
                    width = items[n][1].shape[1]
                    act.wait_ge(maxed, n + 1)
                    if n >= 2:
                        act.wait_ge(turned, n - 1)
                    act.activation(pr[:, n % 2, 0:width], sc[:, n % 2, 0:width], ACT.Exp, bias=neg_max[:, n:n + 1],
                                   accum_out=total[:, n:n + 1]).then_inc(exped, 1)
                    act.wait_ge(turned, n + 1)
                    if n >= 2:
                        act.wait_ge(outed, n - 1)
                    act.activation(pt[:, n % 2, 0:width], K.ps[2 + n % 2][:, 0:width], ACT.Copy).then_inc(pt_ready, 1)

            @block.vector
            def _(dve):
                chain = Chain(dve, step)

                def head(n):
                    bias = items[n][2]
                    width = items[n][1].shape[1]
                    dve.wait_ge(scored, n + 1)
                    if n >= 2:
                        dve.wait_ge(exped, n - 1)
                    s = sc[:, n % 2, 0:width]
                    if bias is None:
                        dve.tensor_single_scalar(s, K.ps[n % 2][:, 0:width], scale, ALU.mult).then_inc(scaled, 1)
                    else:
                        dve.scalar_tensor_tensor(out=s, in0=K.ps[n % 2][:, 0:width], scalar=scale, in1=bias,
                                                 op0=ALU.mult, op1=ALU.add).then_inc(scaled, 1)
                    dve.wait_ge(scaled, n + 1)
                    dve.tensor_reduce(neg_max[:, n:n + 1], s, AX.X, ALU.max, negate=True).then_inc(maxed, 1)

                head(0)
                for n in range(N):
                    if n + 1 < N:
                        head(n + 1)
                    out, gate, add = items[n][4:7]
                    dve.wait_ge(outed, n + 1)
                    chain(dve.reciprocal(weight[:, n:n + 1], total[:, n:n + 1]))
                    if gate is not None:
                        chain(dve.tensor_tensor(weight[:, n:n + 1], weight[:, n:n + 1], gate, ALU.mult))
                    if add:
                        dve.scalar_tensor_tensor(out=out, in0=K.ps[4 + n % 2][:, 0:P], scalar=weight[:, n:n + 1], in1=out,
                                                 op0=ALU.mult, op1=ALU.add).then_inc(finished, 1)
                    else:
                        dve.tensor_scalar(out, K.ps[4 + n % 2][:, 0:P], weight[:, n:n + 1], None, ALU.mult).then_inc(finished, 1)


def memory_attention(K, l, mem_rows, qmT, cat):
    nc = K.nc
    with ExitStack() as mem:
        def sb(name, shape):
            return mem.enter_context(nc.sbuf_tensor(f"ma_{name}{l}", shape, F32))
        mT = tuple(mem.enter_context(nc.sbuf_tensor(f"ma_mT{h}{l}", [P, KD, T1], F32R)) for h in ("hi", "lo"))
        with nc.sbuf_tensor(f"ma_gain{l}", [P, D], F32) as gain, nc.sbuf_tensor(f"ma_h{l}", [P, 2, D], F32) as h:
            load(K, (gain[:, :], K.dram["mem_norm_w"][l:l + 1, :].broadcast_to([P, D])))
            rms_norm(K, mem_rows, [0, 1], lambda t: gain[:, :], None, h, mT)
        kT, v = sb("kT", [P, MEM_H, T1]), sb("v", [P, 2, MEM_W])
        project(K, K.dram["mem_w_kv"][l], KD, mT, [
            (0, MEM_W, True, (0, T1), copy_to(lambda o, t: kT[:, o // P, :])),
            (MEM_W, MEM_W, False, [0, 1], copy_to(lambda o, t: v[:, t, o:o + 256]))])
        attend(K, [(qmT[:, h, t * P:(t + 1) * P], kT[:, h, :], None, [v[:, m, h * P:(h + 1) * P] for m in range(2)],
                    cat[:, t, D + h * P:D + (h + 1) * P], None, False) for h in range(MEM_H) for t in range(2)], SCALE)


def gdn_layer(K, l, j, hT, cat, qmT):
    nc = K.nc
    with ExitStack() as mem:
        def sb(name, shape, scope=mem):
            return scope.enter_context(nc.sbuf_tensor(f"gl_{name}", shape, F32))
        qkv = sb("qkv", [P, 3 * GH, T1])
        ba, z = sb("ba", [P, 2, 2 * GH]), sb("z", [P, 2, D])
        with ExitStack() as conv:
            padded = sb("padded", [P, 3 * GH, T1 + 3], conv)
            w = sb("w", [P, 3 * GH, 4], conv)
            load(K, (w[:, :, :], K.dram["gdn_conv_w"][j]))
            with stage(K) as (block,):
                @block.vector
                def _(dve):
                    dve.memset(padded[:, :, 0:3], 0.0)
            project(K, K.dram["gdn_w_in"][j], KD, hT,
                    [(0, 3 * D, True, (0, T1), copy_to(lambda o, t: padded[:, o // P, 3:T1 + 3]))] +
                    [(3 * D, D, False, [0, 1], copy_to(lambda o, t: z[:, t, o:o + 256], ACT.Silu))] +
                    [(4 * D, 2 * GH, False, [0, 1], copy_to(lambda o, t: ba[:, t, :])),
                     (4 * D + 2 * GH, MEM_W, True, (0, T1), copy_to(lambda o, t: qmT[:, o // P, :]))])
            with stage(K, "step", "conved") as (block, step, conved):
                @block.vector
                def _(dve):
                    chain = Chain(dve, step)
                    for i in range(3 * GH):
                        dst = qkv[:, i, :]
                        chain(dve.tensor_scalar(dst, padded[:, i, 0:T1], w[:, i, 0:1], None, ALU.mult))
                        for tap in range(1, 4):
                            ins = dve.scalar_tensor_tensor(out=dst, in0=padded[:, i, tap:tap + T1], scalar=w[:, i, tap:tap + 1], in1=dst,
                                                           op0=ALU.mult, op1=ALU.add)
                            if tap < 3:
                                chain(ins)
                        ins.then_inc(conved, 1)

                @block.scalar
                def _(act):
                    for i in range(3 * GH):
                        act.wait_ge(conved, i + 1)
                        act.activation(qkv[:, i, :], qkv[:, i, :], ACT.Silu)
        gated_delta(K, j, qkv, ba, z, cat)


def sparse_attention(K, j, hT, cat, qmT):
    nc = K.nc
    with ExitStack() as mem:
        def sb(name, shape, scope=mem):
            return scope.enter_context(nc.sbuf_tensor(f"ns_{name}", shape, F32))
        qT = sb("qT", [P, GH, T1])
        kvT = sb("kvT", [P, 4, 2, T1])
        vtok = sb("vtok", [P, 2, 2, KV_W])
        gates = sb("gates", [P, 2, 3 * GH])

        def kv(n):
            return copy_to(lambda o, t: kvT[:, n, o // P, :])
        base = D
        project(K, K.dram["nsa_w_in"][j], KD, hT,
                [(0, D, True, (0, T1), copy_to(lambda o, t: qT[:, o // P, :]))] +
                [(base + i * KV_W, KV_W, True, (0, T1), kv(n)) for i, n in ((0, 0), (1, 1), (2, 2), (4, 3))] +
                [(base + 3 * KV_W, KV_W, False, [0, 1], copy_to(lambda o, t: vtok[:, 0, t, :])),
                 (base + 5 * KV_W, KV_W, False, [0, 1], copy_to(lambda o, t: vtok[:, 1, t, :])),
                 (base + 6 * KV_W, 3 * GH, False, [0, 1], copy_to(lambda o, t: gates[:, t, :], ACT.Sigmoid)),
                 (base + 6 * KV_W + 3 * GH, MEM_W, True, (0, T1), copy_to(lambda o, t: qmT[:, o // P, :]))])
        rel = sb("rel", [32, GH])
        bias = sb("bias", [P, GH, T1])
        W = 3 * P
        with ExitStack() as tmp:
            hot = sb("hot", [32, W], tmp)
            wide = sb("wide", [P, GH, W], tmp)
            causal = sb("causal", [P, P], tmp)
            load(K, (rel[:, :], K.dram["rel_bias"]), (hot[:, :], K.dram["bucket_rev"]), (causal[:, :], K.dram["causal"]))
            with stage(K, "spread", "copied", "stored", "skewed") as (block, spread, copied, stored, skewed):
                @block.tensor
                def _(pe):
                    for h in range(GH):
                        pe.matmul(K.ps[h][:, 0:W], rel[:, h:h + 1].broadcast_to([32, P]), hot[:, :], start=True, stop=True).then_inc(spread, 1)

                @block.scalar
                def _(act):
                    for h in range(GH):
                        act.wait_ge(spread, h + 1)
                        act.activation(wide[:, h, :], K.ps[h][:, 0:W], ACT.Copy).then_inc(copied, 1)

                @block.sync
                def _(sp):
                    sp.wait_ge(copied, GH)
                    sp.dma_start(K.skew.rearrange("h p w -> p h w"), wide[:, :, :]).then_inc(stored, 16)
                    sp.wait_ge(stored, 16)
                    sp.dma_start(bias[:, :, :], bass.AP(K.skew.tensor, P - 1, [[W - 1, P], [P * W, GH], [1, T1]])).then_inc(skewed, 16)
                    sp.wait_ge(skewed, 16)

                @block.vector
                def _(dve):
                    dve.wait_ge(skewed, 16)
                    dve.tensor_tensor(bias[:, :, P:T1], bias[:, :, P:T1], causal[:, None, :].broadcast_to([P, GH, P]), ALU.add)
        kcT, vc = sb("kcT", [P, 2, N_CMP]), sb("vc", [N_CMP, 2, P])
        for which, (pos_in, w1_in, w2_in) in enumerate(((K.dram["pos_k"], K.dram["w1_k"], K.dram["w2_k"]), (K.dram["pos_v"], K.dram["w1_v"], K.dram["w2_v"]))):
            with ExitStack() as tmp:
                pos, w2 = sb(f"pos{which}", [P, 32], tmp), sb(f"w2{which}", [P, P], tmp)
                w1 = sb(f"w1{which}", [P, 32, P], tmp)
                blk = sb(f"blk{which}", [P, 2, 2, 16, N_CMP], tmp)
                hid = sb(f"hid{which}", [P, 2, N_CMP], tmp)
                load(K, (pos[:, :], pos_in[j]), (w2[:, :], w2_in[j]), (w1[:, :, :], w1_in[j].rearrange("(i p) n -> p i n", p=P)))
                with stage(K, "blocked", "hidden", "acted", "done") as (block, blocked, hidden, acted, done):
                    @block.vector
                    def _(dve):
                        for g in range(2):
                            src = kvT[:, which, g, :].rearrange("p (n i) -> p i n", i=16)
                            for a in range(2):
                                last = dve.tensor_tensor(blk[:, g, a, :, :], src[:, :, a:a + N_CMP],
                                                         pos[:, 16 * a:16 * a + 16][:, :, None].broadcast_to([P, 16, N_CMP]), ALU.add)
                        last.then_inc(blocked, 1)
                        dve.wait_ge(done, 1)
                        if which == 0:
                            dve.tensor_copy(kcT[:, :, :], K.ps[1][:, 0:2 * N_CMP].rearrange("p (g n) -> p g n", g=2))
                        else:
                            dve.tensor_copy(vc[:, :, :], K.ps[1][0:N_CMP, 0:2 * P].rearrange("p (g n) -> p g n", g=2))

                    @block.tensor
                    def _(pe):
                        pe.wait_ge(blocked, 1)
                        for g in range(2):
                            for i in range(32):
                                last = pe.matmul(K.ps[0][:, g * N_CMP:(g + 1) * N_CMP], w1[:, i, :], blk[:, g, i // 16, i % 16, :],
                                                 start=i == 0, stop=i == 31)
                        last.then_inc(hidden, 1)
                        pe.wait_ge(acted, 1)
                        for g in range(2):
                            if which == 0:
                                last = pe.matmul(K.ps[1][:, g * N_CMP:(g + 1) * N_CMP], w2[:, :], hid[:, g, :], start=True, stop=True)
                            else:
                                last = pe.matmul(K.ps[1][0:N_CMP, g * P:(g + 1) * P], hid[:, g, :], w2[:, :], start=True, stop=True)
                        last.then_inc(done, 1)

                    @block.scalar
                    def _(act):
                        act.wait_ge(hidden, 1)
                        act.activation(hid[:, :, :], K.ps[0][:, 0:2 * N_CMP].rearrange("p (g n) -> p g n", g=2), ACT.Silu).then_inc(acted, 1)
        with ExitStack() as tmp:
            hot = sb("chot", [32, 2, N_CMP, P], tmp)
            cm = sb("cmask", [P, 2, 2, N_CMP], tmp)
            s = sb("cs", [P, 2, GH, 16], tmp)
            bc = sb("cb", [P, 2, GH, N_CMP], tmp)
            red = sb("cred", [P, 3, 2, GH], tmp)
            pT = sb("cpT", [N_CMP, 16, P], tmp)
            load(K, (hot[:, :, :, :], K.dram["bucket_cmp"]), (cm[:, :, :, :], K.dram["cmp_masks"]))
            with stage(K, "scored", "shifted", "exped", "step", "weighted", "turned", "copied", "outed") as \
                    (block, scored, shifted, exped, step, weighted, turned, copied, outed):
                @block.tensor
                def _(pe):
                    for t in range(2):
                        for h in range(GH):
                            c = (t * GH + h) * 16
                            pe.matmul(K.ps[0][:, c:c + N_CMP], qT[:, h, t * P:(t + 1) * P], kcT[:, h // 4, :], start=True, stop=True)
                        for n in range(N_CMP):
                            c = (t * N_CMP + n) * GH
                            last = pe.matmul(K.ps[1][:, c:c + GH], hot[:, t, n, :], rel[:, :], start=True, stop=True)
                    last.then_inc(scored, 1)
                    pe.wait_ge(weighted, 1)
                    for b in range(4):
                        for i in range(4):
                            u = 4 * b + i
                            last = pe.transpose(K.ps[2 + b][0:N_CMP, i * P:(i + 1) * P], s[:, u // GH, u % GH, 0:N_CMP], K.ident[:, :])
                        last.then_inc(turned, 1)
                    pe.wait_ge(copied, 4)
                    for b in range(4):
                        for i in range(4):
                            u = 4 * b + i
                            last = pe.matmul(K.ps[2 + b][:, i * P:(i + 1) * P], pT[:, u, :], vc[:, (u % GH) // 4, :], start=True, stop=True)
                        last.then_inc(outed, 1)

                @block.scalar
                def _(act):
                    act.wait_ge(shifted, 1)
                    act.activation(s[:, :, :, 0:N_CMP], s[:, :, :, 0:N_CMP], ACT.Exp).then_inc(exped, 1)
                    for b in range(4):
                        act.wait_ge(turned, b + 1)
                        act.activation(pT[:, 4 * b:4 * b + 4, :], K.ps[2 + b][0:N_CMP, :].rearrange("p (u c) -> p u c", u=4), ACT.Copy).then_inc(copied, 1)
                    for b in range(4):
                        act.wait_ge(outed, b + 1)
                        t, hg = divmod(b, 2)
                        act.activation(cat[:, t, hg * 512:(hg + 1) * 512], K.ps[2 + b][:, :], ACT.Copy)

                @block.vector
                def _(dve):
                    chain = Chain(dve, step)
                    dve.wait_ge(scored, 1)
                    chain(dve.tensor_copy(bc[:, :, :, :].rearrange("p t h n -> p t n h"),
                                          K.ps[1][:, 0:2 * N_CMP * GH].rearrange("p (t n h) -> p t n h", t=2, h=GH)))
                    for t in range(2):
                        sv = s[:, t, :, 0:N_CMP]
                        chain(dve.tensor_tensor(bc[:, t, :, :], bc[:, t, :, :], cm[:, 0, t, :][:, None, :].broadcast_to([P, GH, N_CMP]), ALU.add))
                        chain(dve.scalar_tensor_tensor(out=sv, in0=K.ps[0][:, t * 128:(t + 1) * 128].rearrange("p (h n) -> p h n", n=16)[:, :, 0:N_CMP],
                                                       scalar=SCALE, in1=bc[:, t, :, :], op0=ALU.mult, op1=ALU.add))
                        chain(dve.tensor_reduce(red[:, 0, t, :], sv, AX.X, ALU.max))
                        ins = dve.tensor_tensor(sv, sv, red[:, 0, t, :][:, :, None].broadcast_to([P, GH, N_CMP]), ALU.subtract)
                        if t == 0:
                            chain(ins)
                    ins.then_inc(shifted, 1)
                    dve.wait_ge(exped, 1)
                    for t in range(2):
                        sv = s[:, t, :, 0:N_CMP]
                        chain(dve.tensor_tensor(sv, sv, cm[:, 1, t, :][:, None, :].broadcast_to([P, GH, N_CMP]), ALU.mult))
                        chain(dve.tensor_reduce(red[:, 1, t, :], sv, AX.X, ALU.add))
                        chain(dve.tensor_single_scalar(red[:, 1, t, :], red[:, 1, t, :], 1e-30, ALU.max))
                        chain(dve.reciprocal(red[:, 2, t, :], red[:, 1, t, :]))
                        chain(dve.tensor_tensor(red[:, 2, t, :], red[:, 2, t, :],
                                                gates[:, t, :].rearrange("p (h c) -> p h c", c=3)[:, :, 0], ALU.mult))
                        ins = dve.tensor_tensor(sv, sv, red[:, 2, t, :][:, :, None].broadcast_to([P, GH, N_CMP]), ALU.mult)
                        if t == 0:
                            chain(ins)
                    ins.then_inc(weighted, 1)
        items = []
        for kind in range(2):
            for h in range(GH):
                for t in range(2):
                    n = (t + 1) * P
                    items.append((qT[:, h, t * P:(t + 1) * P], kvT[:, 2 + kind, h // 4, 0:n], bias[:, h, T1 - n:T1],
                                  [vtok[:, kind, c, (h // 4) * P:(h // 4 + 1) * P] for c in range(t + 1)],
                                  cat[:, t, h * P:(h + 1) * P], gates[:, t, 3 * h + 1 + kind:3 * h + 2 + kind], True))
        attend(K, items, SCALE)


def conv_glu(K, l, hT, x):
    nc = K.nc
    J = D_FF // P
    with ExitStack() as mem:
        def sb(name, shape, scope=mem):
            return scope.enter_context(nc.sbuf_tensor(f"gu_{name}{l}", shape, F32))
        actT = tuple(mem.enter_context(nc.sbuf_tensor(f"gu_act{h}{l}", [P, J, T1], F32R)) for h in ("hi", "lo"))
        cw, cb = sb("cw", [P, J, 3]), sb("cb", [P, J])
        with ExitStack() as up:
            w = sb("w", [P, 3, KD, T1], up)
            halves = tuple(up.enter_context(nc.sbuf_tensor(f"gu_w{h}{l}", [P, 2, KD, T1], F32R)) for h in ("hi", "lo"))
            gp, cv, both_sides = sb("gp", [P, 2, T1 + 2], up), sb("cv", [P, 2, T1], up), sb("bs", [P, 2, T1], up)
            load(K, (cw[:, :, :], K.dram["ffn_conv_w"][l]), (cb[:, :], K.dram["ffn_conv_b"][l]))
            with stage(K) as (block,):
                @block.vector
                def _(dve):
                    dve.memset(gp[:, :, 0:2], 0.0)
            with stage(K, "w0", "w1", "w2", "gate_psum", "value_psum", "padded", "step", "conved", "acted", "closed",
                       "hi_ready", "lo_ready", "act_hi", "act_lo") as \
                    (block, w0, w1, w2, gate_psum, value_psum, padded, step, conved, acted, closed, hi_ready, lo_ready, act_hi, act_lo):
                loaded = (w0, w1, w2)

                @block.sync
                def _(sp):
                    for n in range(J):
                        if n >= 3:
                            sp.wait_ge(lo_ready, n - 2)
                        for a in range(2):
                            at = a * D_FF + n * P
                            sp.dma_start(w[:, n % 3, :, a * P:(a + 1) * P], K.dram["ffn_w_up"][l][:, at:at + P].rearrange("(k p) n -> p k n", p=P))\
                              .then_inc(loaded[n % 3], 16)

                @block.tensor
                def _(pe):
                    for i in range(J):
                        pe.wait_ge(lo_ready, i + 1)
                        for a, done, free in ((0, gate_psum, padded), (1, value_psum, closed)):
                            if i >= 2:
                                pe.wait_ge(free, i - 1)
                            for k in range(KD):
                                last = products_of(pe, K.ps[2 * a + i % 2][:, 0:T1],
                                                   both(halves, slice(0, P), i % 2, k, slice(a * P, (a + 1) * P)),
                                                   both(hT, slice(0, P), k, slice(0, T1)), k == 0, k == KD - 1)
                            last.then_inc(done, 1)

                @block.scalar
                def _(act):
                    def split_hi(n):
                        act.wait_ge(loaded[n % 3], 32 * (n // 3 + 1))
                        if n >= 2:
                            act.wait_ge(value_psum, n - 1)
                        act.activation(halves[0][:, n % 2, :, :], w[:, n % 3, :, :], ACT.Copy).then_inc(hi_ready, 1)

                    def silu(i):
                        act.wait_ge(conved, i + 1)
                        act.activation(cv[:, i % 2, :], cv[:, i % 2, :], ACT.Silu, bias=cb[:, i:i + 1]).then_inc(acted, 1)
                        act.wait_ge(closed, i + 1)
                        act.activation(actT[0][:, i, :], both_sides[:, i % 2, :], ACT.Copy).then_inc(act_hi, 1)

                    split_hi(0)
                    for i in range(J):
                        if i + 1 < J:
                            split_hi(i + 1)
                        act.wait_ge(gate_psum, i + 1)
                        if i >= 2:
                            act.wait_ge(conved, i - 1)
                        act.activation(gp[:, i % 2, 2:T1 + 2], K.ps[i % 2][:, 0:T1], ACT.Copy).then_inc(padded, 1)
                        if i:
                            silu(i - 1)
                    silu(J - 1)

                @block.vector
                def _(dve):
                    chain = Chain(dve, step)

                    def split_lo(n):
                        dve.wait_ge(hi_ready, n + 1)
                        dve.tensor_tensor(halves[1][:, n % 2, :, :], w[:, n % 3, :, :], halves[0][:, n % 2, :, :].bitcast(F32),
                                          ALU.subtract).then_inc(lo_ready, 1)

                    def close(i):
                        dve.wait_ge(acted, i + 1)
                        dve.wait_ge(value_psum, i + 1)
                        if i >= 2:
                            dve.wait_ge(act_lo, i - 1)
                        dve.tensor_tensor(both_sides[:, i % 2, :], K.ps[2 + i % 2][:, 0:T1], cv[:, i % 2, :], ALU.mult).then_inc(closed, 1)

                    def close_lo(i):
                        dve.wait_ge(act_hi, i + 1)
                        dve.tensor_tensor(actT[1][:, i, :], both_sides[:, i % 2, :], actT[0][:, i, :].bitcast(F32), ALU.subtract)\
                           .then_inc(act_lo, 1)

                    split_lo(0)
                    for i in range(J):
                        if i + 1 < J:
                            split_lo(i + 1)
                        dve.wait_ge(padded, i + 1)
                        if i >= 2:
                            dve.wait_ge(closed, i - 1)
                            close_lo(i - 2)
                        dst = cv[:, i % 2, :]
                        chain(dve.tensor_scalar(dst, gp[:, i % 2, 0:T1], cw[:, i, 0:1], None, ALU.mult))
                        chain(dve.scalar_tensor_tensor(out=dst, in0=gp[:, i % 2, 1:T1 + 1], scalar=cw[:, i, 1:2], in1=dst, op0=ALU.mult, op1=ALU.add))
                        dve.scalar_tensor_tensor(out=dst, in0=gp[:, i % 2, 2:T1 + 2], scalar=cw[:, i, 2:3], in1=dst,
                                                 op0=ALU.mult, op1=ALU.add).then_inc(conved, 1)
                        if i:
                            close(i - 1)
                    close_lo(J - 2)
                    close(J - 1)
                    close_lo(J - 1)
        down(K, l, actT, J, x)


def down(K, l, actT, J, x):
    nc = K.nc
    with ExitStack() as mem:
        w = mem.enter_context(nc.sbuf_tensor(f"dn_w{l}", [P, 4, D], F32))
        halves = tuple(mem.enter_context(nc.sbuf_tensor(f"dn_{h}{l}", [P, 3, D], F32R)) for h in ("hi", "lo"))
        with stage(K, "w0", "w1", "w2", "w3", "hi_ready", "lo_ready", "used") as (block, w0, w1, w2, w3, hi_ready, lo_ready, used):
            loaded = (w0, w1, w2, w3)

            @block.sync
            def _(sp):
                for k in range(J):
                    if k >= 4:
                        sp.wait_ge(lo_ready, k - 3)
                    sp.dma_start(w[:, k % 4, :], K.dram["ffn_w_down"][l][k * P:(k + 1) * P, :]).then_inc(loaded[k % 4], 16)

            @block.scalar
            def _(act):
                for k in range(J):
                    act.wait_ge(loaded[k % 4], 16 * (k // 4 + 1))
                    if k >= 3:
                        act.wait_ge(used, k - 2)
                    act.activation(halves[0][:, k % 3, :], w[:, k % 4, :], ACT.Copy).then_inc(hi_ready, 1)

            @block.tensor
            def _(pe):
                for k in range(J):
                    pe.wait_ge(lo_ready, k + 1)
                    for t in range(2):
                        for c in range(2):
                            last = products_of(pe, K.ps[2 * t + c][:, :], both(actT, slice(0, P), k, slice(t * P, (t + 1) * P)),
                                               both(halves, slice(0, P), k % 3, slice(c * 512, (c + 1) * 512)), k == 0, k == J - 1)
                    last.then_inc(used, 1)

            @block.vector
            def _(dve):
                for k in range(J):
                    dve.wait_ge(hi_ready, k + 1)
                    dve.tensor_tensor(halves[1][:, k % 3, :], w[:, k % 4, :], halves[0][:, k % 3, :].bitcast(F32), ALU.subtract)\
                       .then_inc(lo_ready, 1)
                dve.wait_ge(used, J)
                for t in range(2):
                    for c in range(2):
                        dst = x[:, t, c * 512:(c + 1) * 512]
                        dve.tensor_tensor(dst, dst, K.ps[2 * t + c][:, :], ALU.add)


def second_block(K, x):
    nc = K.nc
    with nc.sbuf_tensor("mem_rows", [P, 2, D], F32) as mem_rows:
        load(K, (mem_rows[:, :, :], K.dram["mem"].rearrange("(t p) d -> p t d", p=P)))
        for l in range(DEPTH):
            def normed(tag, weights, hT):
                with nc.sbuf_tensor(f"b2_gain{tag}", [P, D], F32) as gain, nc.sbuf_tensor(f"b2_h{tag}", [P, 2, D], F32) as h:
                    load(K, (gain[:, :], weights.broadcast_to([P, D])))
                    rms_norm(K, x, [0, 1], lambda t: gain[:, :], None, h, hT)
            with ExitStack() as mix:
                def sb(name, shape):
                    return mix.enter_context(nc.sbuf_tensor(f"b2_{name}{l}", shape, F32))
                cat, qmT = sb("cat", [P, 2, CAT]), sb("qmT", [P, MEM_H, T1])
                with nc.sbuf_tensor(f"b2_hThi{l}", [P, KD, T1], F32R) as hi, nc.sbuf_tensor(f"b2_hTlo{l}", [P, KD, T1], F32R) as lo:
                    hT = (hi, lo)
                    normed(f"m{l}", K.dram["norm_mix_w"][l:l + 1, :], hT)
                    (gdn_layer(K, l, l // 2, hT, cat, qmT) if l % 2 == 0 else sparse_attention(K, l // 2, hT, cat, qmT))
                memory_attention(K, l, mem_rows, qmT, cat)
                catT = tuple(mix.enter_context(nc.sbuf_tensor(f"b2_catT{h}{l}", [P, CAT // P, T1], F32R)) for h in ("hi", "lo"))
                rows_to_channels(K, cat, catT, [0, 1], CAT)
                project(K, K.dram["w_out_2"][l], CAT // P, catT, [(0, D, False, [0, 1], add_scaled(K, x, None))], ring=2, engine="vector")
            with nc.sbuf_tensor(f"b2_fThi{l}", [P, KD, T1], F32R) as hi, nc.sbuf_tensor(f"b2_fTlo{l}", [P, KD, T1], F32R) as lo:
                hT = (hi, lo)
                normed(f"f{l}", K.dram["norm_ffn_w"][l:l + 1, :], hT)
                conv_glu(K, l, hT, x)


def build(nc, K):
    K.nc = nc
    K.uid = K.stages = 0
    K.sems = [[nc.alloc_semaphore(name=f"set{s}_{i}") for i in range(SEMS)] for s in range(2)]
    with ExitStack() as mem:
        def sb(name, shape):
            return mem.enter_context(nc.sbuf_tensor(name, shape, F32))
        K.ps = [mem.enter_context(nc.psum_tensor(f"bank{i}", [P, 512], F32)) for i in range(8)]
        K.ident, K.ones, K.tri, K.iota = sb("ident", [P, P]), sb("ones", [P, P]), sb("tri", [P, P]), sb("iota", [P, P])
        K.pick2 = sb("pick2", [2, 2, P])
        K.junk, K.small = sb("junk", [P, D]), sb("small", [P, 256])
        x = sb("xrows", [P, 4, D])
        s_cols = sb("s_cols", [P, KD, 2])
        load(K, (K.ident[:, :], K.dram["c_ident"]), (K.ones[:, :], K.dram["c_ones"]), (K.tri[:, :], K.dram["c_tri"]), (K.iota[:, :], K.dram["c_iota"]),
             (K.pick2[:, :, :], K.dram["c_pick2"]))
        with nc.sbuf_tensor("grid_pos", [P, 2, D], F32) as pos:
            load(K, (x[:, 0:2, :], K.dram["ctx"].rearrange("(t p) d -> p t d", p=P)), (x[:, 2:4, :], K.dram["x"].rearrange("(t p) d -> p t d", p=P)),
                 (pos[:, :, :], K.dram["grid"].rearrange("(t p) d -> p t d", p=P)), (s_cols[:, :, :], K.dram["cond"]))
            with stage(K) as (block,):
                @block.vector
                def _(dve):
                    dve.tensor_tensor(x[:, 2:4, :], x[:, 2:4, :], pos[:, :, :], ALU.add)

                @block.scalar
                def _(act):
                    act.activation(s_cols[:, :, :], s_cols[:, :, :], ACT.Silu)
        for l in range(DEPTH):
            first_layer(K, l, x, s_cols)
        x2 = x[:, 2:4, :]
        with nc.sbuf_tensor("mid_gain", [P, D], F32) as gain:
            load(K, (gain[:, :], K.dram["final_norm_g"].broadcast_to([P, D])))
            rms_norm(K, x2, [0, 1], lambda t: gain[:, :], None, x2)
        second_block(K, x2)
        with nc.sbuf_tensor("fin_gain", [P, D], F32) as gain, nc.sbuf_tensor("fin_rows", [P, 2, D], F32) as rows:
            load(K, (gain[:, :], K.dram["final_norm_w"].broadcast_to([P, D])))
            rms_norm(K, x2, [0, 1], lambda t: gain[:, :], None, rows)
            with stage(K, "stored") as (block, stored):
                @block.sync
                def _(sp):
                    sp.dma_start(K.out.rearrange("(t p) d -> p t d", p=P), rows[:, :, :]).then_inc(stored, 16)
                    sp.wait_ge(stored, 16)



def buckets(dist):
    n = np.maximum(dist, 0)
    logv = np.log(np.maximum(n, 1).astype(np.float32) / np.float32(16)) / np.float32(np.log(8.0))
    large = np.minimum(16 + (logv * 16).astype(np.int32), 31)
    return np.where(n < 16, n, large)


def constants():
    f = np.float32
    c = {}
    i = np.arange(P)
    c["c_ident"] = np.eye(P, dtype=f)
    c["c_ones"] = np.ones((P, P), f)
    c["c_tri"] = (i[:, None] <= i[None, :]).astype(f)
    c["c_iota"] = np.tile(i.astype(f), (P, 1))
    c["c_pick2"] = np.repeat(np.eye(2, dtype=f)[:, :, None], P, 2)
    c["c_pick4"] = np.repeat(np.eye(4, dtype=f)[:, :, None], P, 2)
    c["c_ones4"] = np.ones((4, TALL), f)
    n_freq = D // 4
    freq = f(1.0) / (f(10000.0) ** (np.arange(n_freq, dtype=f) / f(n_freq)))
    ar = np.repeat(np.arange(T1 // 64, dtype=f), 64)[:, None] * freq
    ac = np.tile(np.arange(64, dtype=f), T1 // 64)[:, None] * freq
    c["grid"] = np.concatenate([np.sin(ar), np.cos(ar), np.sin(ac), np.cos(ac)], -1).astype(f)
    t = np.arange(TALL)
    m = np.zeros((P, 2, 2, TALL), f)
    for s in range(2):
        src = s * P + i[:, None]
        same = t[None, :] < CTX
        m[:, 0, s, :] = np.where(same & (src > t[None, :]), f(MASKED), f(0))
        m[:, 1, s, :] = np.where(same & (src < t[None, :]), f(MASKED), f(0))
    c["ml_mask"] = m
    a = 2 * np.pi * np.outer(np.arange(CTX), np.arange(CTX)) / CTX
    c["dft_t"] = np.stack([np.cos(a), np.sin(a)]).reshape(2, 2, P, CTX).transpose(2, 0, 1, 3).astype(f)
    b = 2 * np.pi * np.outer(np.arange(DH), np.arange(DH)) / DH
    k = 1.0 / np.sqrt(CTX * DH)
    c["dft_c"] = np.stack([np.kron(np.eye(2), np.cos(b)) * k, -np.kron(np.eye(2), np.sin(b)) * k], 1).astype(f)
    c["gd_masks"] = np.stack([np.where(i[:, None] > i[None, :], f(0), f(-MASKED)), np.where(i[:, None] <= i[None, :], f(0), f(MASKED))], 1)
    lv = [((i[:, None] // (2 * s) == i[None, :] // (2 * s)) & (i[:, None] // s % 2 == 1) & (i[None, :] // s % 2 == 0)) for s in 2 ** np.arange(7)]
    c["gd_levels"] = np.stack(lv, 1).astype(f)
    c["bucket_rev"] = (np.arange(32)[:, None] == buckets(T1 - 1 - np.arange(3 * P))[None, :]).astype(f)
    dist = np.arange(T1).reshape(2, 1, P) - (np.arange(N_CMP) * 16 + 31).reshape(1, N_CMP, 1)
    c["bucket_cmp"] = (np.arange(32)[:, None, None, None] == buckets(dist)[None]).astype(f)
    ok = (dist >= 0).transpose(2, 0, 1)
    c["cmp_masks"] = np.stack([np.where(ok, f(0), f(MASKED)), ok.astype(f)], 1)
    c["causal"] = np.where(i[:, None] >= i[None, :], f(0), f(MASKED))
    return c


def kernel(**inputs):
    import concourse.bacc as _bacc
    from concourse.bass_utils import run_bass_kernel_spmd as _run

    n = {k: np.asarray(v) for k, v in inputs.items()}

    def cols(a):
        a = np.moveaxis(a, -1, 1)
        a = a.reshape(a.shape[0], a.shape[1] // P, P, *a.shape[2:])
        return np.swapaxes(a, 1, 2)

    data = dict(constants())
    data.update({
        "x": n["x"][0], "ctx": n["ctx"][0],
        "cond": np.stack([n["c_ctx"], n["c"][0]], -1).reshape(KD, P, 2).transpose(1, 0, 2),
        "w_ada": n["w_ada"], "b_ada": n["b_ada"], "norm1_g": n["norm1_g"], "norm2_g": n["norm2_g"], "w_in": n["w_in"],
        "ml_conv_w": cols(n["ml_conv_w"]), "ml_conv_b": cols(n["ml_conv_b"]), "ml_gate_b": n["ml_gate_b"],
        "ml_norm_g": n["ml_norm_g"].reshape(DEPTH, MIX), "gm_ln_g": n["gm_ln_g"], "gm_ln_b": n["gm_ln_b"],
        "gm_w_s": n["gm_w_s"].transpose(0, 3, 1, 2), "gm_b_s": n["gm_b_s"].transpose(0, 2, 1),
        "cv_dw_w": cols(n["cv_dw_w"]), "cv_dw_b": cols(n["cv_dw_b"]), "cv_ln_g": n["cv_ln_g"], "cv_ln_b": n["cv_ln_b"],
        "w_branch": n["w_branch"].reshape(DEPTH, 4 * MIX, D), "w_out": n["w_out"], "peer_w_q": n["peer_w_q"],
        "peer_keys": n["peer_keys"].transpose(0, 3, 1, 2), "peer_u": n["peer_u"].transpose(0, 2, 1), "peer_v": n["peer_v"],
        "final_norm_g": n["final_norm_g"][None], "mem": n["mem_2"][0], "rel_bias": n["rel_bias_2"], "norm_mix_w": n["norm_mix_w_2"], "norm_ffn_w": n["norm_ffn_w_2"],
        "final_norm_w": n["final_norm_w_2"][None], "mem_norm_w": n["mem_norm_w_2"], "mem_w_kv": n["mem_w_kv_2"],
        "w_out_2": n["w_out_2"], "gdn_w_in": n["gdn_w_in_2"], "gdn_conv_w": cols(n["gdn_conv_w_2"]),
        "gdn_a_log": n["gdn_a_log_2"], "gdn_dt_bias": n["gdn_dt_bias_2"], "gdn_norm_w": n["gdn_norm_w_2"],
        "nsa_w_in": n["nsa_w_in_2"], "pos_k": n["nsa_cmp_pos_k_2"].transpose(0, 2, 1), "w1_k": n["nsa_cmp_w1_k_2"],
        "w2_k": n["nsa_cmp_w2_k_2"], "pos_v": n["nsa_cmp_pos_v_2"].transpose(0, 2, 1), "w1_v": n["nsa_cmp_w1_v_2"],
        "w2_v": n["nsa_cmp_w2_v_2"], "ffn_w_up": n["ffn_w_up_2"], "ffn_conv_w": cols(n["ffn_conv_w_2"]),
        "ffn_conv_b": cols(n["ffn_conv_b_2"]), "ffn_w_down": n["ffn_w_down_2"],
    })
    nc = _bacc.Bacc("TRN2", target_bir_lowering=False, num_devices=1)
    arrays, dram = {}, {}
    for name, a in data.items():
        arrays[name + "_in"] = np.ascontiguousarray(a)
        dram[name] = nc.dram_tensor(name + "_in", a.shape, F32, kind="ExternalInput").ap()
    dense = nc.dram_tensor("dense_weights", (TALL // 64, P, P * 64), F32, kind="Internal").ap()
    skew = nc.dram_tensor("skewed_bias", (GH, P, 3 * P), F32, kind="Internal").ap()
    out = nc.dram_tensor("out_rows", (T1, D), F32, kind="ExternalOutput").ap()
    build(nc, Core(nc, dram, dense, skew, out))
    r = _run(nc, [arrays], core_ids=[0])
    return r.results[0]["out_rows"].reshape(1, T1, D)
```

```python
import numpy as np
from contextlib import ExitStack, contextmanager

import concourse.bass as bass
from concourse import mybir

F32 = mybir.dt.float32
U32 = mybir.dt.uint32
F32R = mybir.dt.float32r
ALU = mybir.AluOpType
ACT = mybir.ActivationFunctionType
AX = mybir.AxisListType
ds = bass.ds

P = 128
D = 1024
KD = D // P
T1 = 256
CTX = 256
TALL = T1 + CTX
DEPTH = 2
EPS = 1e-6
MASKED = -1e30
MIX = D // 4
HEADS = 4
DH = MIX // HEADS
V_OFF, GATE_OFF_ML, O_OFF = 2 * MIX, 3 * MIX, 3 * MIX + 16
GM_OFF = 4 * MIX + 16
CV_OFF = GM_OFF + 2 * MIX
FT_OFF = CV_OFF + 2 * MIX
BR_OFF = FT_OFF + MIX
CV_K = 31
PAD = CV_K // 2
PH, TOPK, NKEYS = 8, 16, 128
NEXP = NKEYS * NKEYS
GH = D // P
KV_W = 256
MEM_W = 512
MEM_H = 4
CAT = D + MEM_W
D_FF = 2816
N_CMP = (T1 - 32) // 16 + 1
NB = 4
SCALE = float(P) ** -0.5


SEMS = 16


@contextmanager
def stage(K, *names):
    nc = K.nc
    turn = K.stages % 2
    K.stages += 1
    sems = K.sems[turn][0:len(names)]
    retired = K.sems[1 - turn]
    with nc.Block(no_gpsimd_drain=True) as block:
        @block.gpsimd
        def _(pool):
            pool.sem_clear(range(retired[0].num, retired[-1].num + 1))
        yield (block, *sems)


class Core:

    def __init__(self, nc, dram, dense, ada, skew, out):
        self.nc, self.dram, self.dense, self.ada, self.skew, self.out = nc, dram, dense, ada, skew, out


class Chain:

    def __init__(self, engine, sem):
        self.engine, self.sem, self.count = engine, sem, 0

    def __call__(self, instruction):
        self.count += 1
        instruction.then_inc(self.sem, 1)
        self.engine.wait_ge(self.sem, self.count)


def load(K, *pairs):
    with stage(K, "loaded") as (block, loaded):
        @block.sync
        def _(sp):
            for dst, src in pairs:
                sp.dma_start(dst, src).then_inc(loaded, 16)
            sp.wait_ge(loaded, 16 * len(pairs))


def is_pair(acts):
    return type(acts) is tuple


def products_of(pe, psum, stationary, moving, first=True, last=True):
    if is_pair(stationary):
        terms = [(stationary[0], moving[0]), (stationary[0], moving[1]), (stationary[1], moving[0])]
    else:
        terms = [(stationary, moving)]
    for i, (a, b) in enumerate(terms):
        ins = pe.matmul(psum, a, b, start=first and i == 0, stop=last and i == len(terms) - 1)
    return ins


def both(pair, *index):
    if is_pair(pair):
        return pair[0][index], pair[1][index]
    return pair[index]


def part_width(columns, width):
    return columns if columns <= width else width // P * P


def project(K, weights, k_tiles, acts, jobs, width=256, ring=3, engine="scalar", lo_on="gpsimd"):
    nc = K.nc
    split = is_pair(acts)
    parts = [(c0 + o, min(part_width(cw, width), cw - o), by_channel, where, evacuate, o)
             for c0, cw, by_channel, where, evacuate, *_ in jobs for o in range(0, cw, part_width(cw, width))]
    follows = [job[5] if len(job) > 5 else None for job in jobs for o in range(0, job[1], part_width(job[1], width))]
    items = []
    for n, (c0, cw, by_channel, where, evacuate, base) in enumerate(parts):
        if by_channel:
            items += [(n, o, min(P, cw - o), None) for o in range(0, cw, P)]
        else:
            items += [(n, 0, cw, t) for t in where]
    ends = [max(i for i, it in enumerate(items) if it[0] == n) + 1 for n in range(len(parts))]
    of_part = [[i for i, it in enumerate(items) if it[0] == n] for n in range(len(parts))]
    following = any(follows)
    names = ["psum_ready", "psum_free", "step", "hi_ready", "lo_ready", "follow_step", "followed"] + [f"weights{r}" for r in range(ring)]
    K.uid += 1
    with ExitStack() as mem:
        wt = mem.enter_context(nc.sbuf_tensor(f"wring{K.uid}", [P, ring, k_tiles, width], F32))
        if split:
            halves = [mem.enter_context(nc.sbuf_tensor(f"w{h}{K.uid}", [P, 2, k_tiles, width], F32R)) for h in ("hi", "lo")]
        block, ready, free, step, hi_ready, lo_ready, follow_step, followed, *loaded = mem.enter_context(stage(K, *names))

        @block.sync
        def _(sp):
            for n, (c0, cw, _b, _w, _e, _o) in enumerate(parts):
                if n >= ring:
                    if split:
                        sp.wait_ge(lo_ready, n - ring + 1)
                    else:
                        sp.wait_ge(ready, ends[n - ring])
                sp.dma_start(wt[:, n % ring, :, 0:cw],
                             weights[:, c0:c0 + cw].rearrange("(k p) n -> p k n", p=P)).then_inc(loaded[n % ring], 16)

        @block.tensor
        def _(pe):
            for i, (n, o, w, t) in enumerate(items):
                if split:
                    pe.wait_ge(lo_ready, n + 1)
                    w_of, slot = tuple(halves), n % 2
                else:
                    pe.wait_ge(loaded[n % ring], 16 * (n // ring + 1))
                    w_of, slot = wt, n % ring
                if i >= NB:
                    pe.wait_ge(free, i - NB + 1)
                bank = K.ps[i % NB]
                for k in range(k_tiles):
                    if t is None:
                        t0, t1 = parts[n][3]
                        last = products_of(pe, bank[0:w, 0:t1 - t0], both(w_of, slice(0, P), slot, k, slice(o, o + w)),
                                           both(acts, slice(0, P), k, slice(t0, t1)), k == 0, k == k_tiles - 1)
                    else:
                        last = products_of(pe, bank[:, 0:w], both(acts, slice(0, P), k, slice(t * P, (t + 1) * P)),
                                           both(w_of, slice(0, P), slot, k, slice(0, w)), k == 0, k == k_tiles - 1)
                last.then_inc(ready, 1)

        def split_hi(act, n):
            cw = parts[n][1]
            act.wait_ge(loaded[n % ring], 16 * (n // ring + 1))
            if n >= 2:
                act.wait_ge(ready, ends[n - 2])
            act.activation(halves[0][:, n % 2, :, 0:cw], wt[:, n % ring, :, 0:cw], ACT.Copy).then_inc(hi_ready, 1)

        def split_lo(dve, n):
            cw = parts[n][1]
            dve.wait_ge(hi_ready, n + 1)
            dve.tensor_tensor(halves[1][:, n % 2, :, 0:cw], wt[:, n % ring, :, 0:cw],
                              halves[0][:, n % 2, :, 0:cw].bitcast(F32), ALU.subtract).then_inc(lo_ready, 1)

        done = [0]
        for n in range(len(parts)):
            done.append(done[-1] + (len(of_part[n]) if follows[n] and follows[n][1] else 0))

        def follow_parts(dve):
            chain = Chain(dve, follow_step)
            if lo_on == "vector":
                split_lo(dve, 0)
            for n in range(len(parts)):
                if lo_on == "vector" and n + 1 < len(parts):
                    split_lo(dve, n + 1)
                for i in of_part[n] if follows[n] else []:
                    dve.wait_ge(free, i + 1)
                    last = follows[n][0](dve, chain, parts[n][5] + items[i][1])
                    if follows[n][1]:
                        last.then_inc(followed, 1)

        def split_lo_parts(pool):
            for n in range(len(parts)):
                split_lo(pool, n)

        def finish_part(act, n):
            if n >= 0 and follows[n] and follows[n][1]:
                for d, i in enumerate(of_part[n]):
                    act.wait_ge(followed, done[n] + d + 1)
                    follows[n][1](act, parts[n][5] + items[i][1])

        def program(split_part, evacuates):
            def run(eng):
                chain = Chain(eng, step) if evacuates else None
                if split:
                    split_part(eng, 0)
                for n in range(len(parts)):
                    if split and n + 1 < len(parts):
                        split_part(eng, n + 1)
                    if not evacuates:
                        continue
                    for i in of_part[n]:
                        _n, o, w, t = items[i]
                        eng.wait_ge(ready, i + 1)
                        if i and engine == "vector":
                            eng.wait_ge(free, i)
                        if t is None:
                            t0, t1 = parts[n][3]
                            tile = K.ps[i % NB][0:w, 0:t1 - t0]
                        else:
                            tile = K.ps[i % NB][:, 0:w]
                        parts[n][4](eng, chain, tile, parts[n][5] + o, t).then_inc(free, 1)
                    if evacuates:
                        finish_part(eng, n - 1)
                if evacuates:
                    finish_part(eng, len(parts) - 1)
            return run

        block.scalar(program(split_hi, engine == "scalar"))
        if following:
            if lo_on == "gpsimd":
                block.gpsimd(split_lo_parts)
            block.vector(follow_parts)
        else:
            block.vector(program(split_lo, engine == "vector"))


def transpose(K, groups):
    nc = K.nc
    with stage(K, "turned", "free_even", "free_odd") as (block, turned, free_even, free_odd):
        frees = (free_even, free_odd)

        def bank(i):
            ins, out = groups[i]
            f, n, p = out.shape
            return K.ps[i % NB][0:f, 0:n * p].rearrange("f (n p) -> f n p", n=n)

        @block.tensor
        def _(pe):
            for i, (ins, out) in enumerate(groups):
                if i >= NB:
                    pe.wait_ge(frees[i % 2], i // 2 - 1)
                for j, a in enumerate(ins):
                    p = a.shape[0]
                    last = pe.transpose(bank(i)[:, j, :], a, K.ident[0:p, 0:p])
                last.then_inc(turned, 1)

        @block.scalar
        def _(act):
            for i in range(0, len(groups), 2):
                act.wait_ge(turned, i + 1)
                act.activation(groups[i][1], bank(i), ACT.Copy).then_inc(free_even, 1)

        @block.vector
        def _(dve):
            for i in range(1, len(groups), 2):
                dve.wait_ge(turned, i + 1)
                dve.tensor_copy(groups[i][1], bank(i)).then_inc(free_odd, 1)


def transpose_to_pair(K, groups):
    with stage(K, "turned", "hi_done", "lo_done") as (block, turned, hi_done, lo_done):
        def bank(i):
            f, n, p = groups[i][1][0].shape
            return K.ps[i % NB][0:f, 0:n * p].rearrange("f (n p) -> f n p", n=n)

        @block.tensor
        def _(pe):
            for i, (ins, out) in enumerate(groups):
                if i >= NB:
                    pe.wait_ge(lo_done, i - NB + 1)
                for j, a in enumerate(ins):
                    last = pe.transpose(bank(i)[:, j, :], a, K.ident[:, :])
                last.then_inc(turned, 1)

        @block.scalar
        def _(act):
            for i in range(len(groups)):
                act.wait_ge(turned, i + 1)
                act.activation(groups[i][1][0], bank(i), ACT.Copy).then_inc(hi_done, 1)

        @block.vector
        def _(dve):
            for i in range(len(groups)):
                hi, lo = groups[i][1]
                dve.wait_ge(hi_done, i + 1)
                dve.tensor_tensor(lo, bank(i), hi.bitcast(F32), ALU.subtract).then_inc(lo_done, 1)


def rows_to_channels(K, rows, out, tiles, channels):
    groups = []
    for t in tiles:
        for c in range(0, channels // P, 4):
            n = min(4, channels // P - c)
            groups.append(([rows[:, t, (c + j) * P:(c + j + 1) * P] for j in range(n)],
                           both(out, slice(0, P), slice(c, c + n), slice(t * P, (t + 1) * P))))
    (transpose_to_pair if is_pair(out) else transpose)(K, groups)


def inverse_root(K, values, add):
    with stage(K, "shifted", "rooted") as (block, shifted, rooted):
        @block.vector
        def _(dve):
            dve.tensor_scalar_add(values, values, add).then_inc(shifted, 1)
            dve.wait_ge(rooted, 1)
            dve.reciprocal(values, values)

        @block.scalar
        def _(act):
            act.wait_ge(shifted, 1)
            act.activation(values, values, ACT.Sqrt).then_inc(rooted, 1)


def rms_norm(K, rows, tiles, gain_of, shift_of, out, chans=None):
    nc = K.nc
    ss = K.small[:, 0:len(tiles)]
    with stage(K, "squared") as (block, squared):
        @block.scalar
        def _(act):
            for i, t in enumerate(tiles):
                if i >= 1:
                    act.wait_ge(squared, i)
                act.activation(K.junk[:, 0:D], rows[:, t, :], ACT.Square, scale=D ** -0.5,
                               accum_out=ss[:, i:i + 1]).then_inc(squared, 1)
    inverse_root(K, ss, EPS)
    with stage(K, "scaled", "shifted") as (block, scaled, shifted):
        @block.vector
        def _(dve):
            for i, t in enumerate(tiles):
                dve.scalar_tensor_tensor(out=out[:, t, :], in0=rows[:, t, :], scalar=ss[:, i:i + 1], in1=gain_of(t),
                                         op0=ALU.mult, op1=ALU.mult).then_inc(scaled, 1)

        @block.gpsimd
        def _(pool):
            if shift_of:
                for i, t in enumerate(tiles):
                    pool.wait_ge(scaled, i + 1)
                    pool.tensor_tensor(out[:, t, :], out[:, t, :], shift_of(t), ALU.add).then_inc(shifted, 1)
                pool.wait_ge(shifted, len(tiles))
    if chans is not None:
        rows_to_channels(K, out, chans, tiles, D)


def layer_norm(K, rows, tiles, width, gain, bias, silu=False):
    nc = K.nc
    n = len(tiles)
    stats = K.small[:, 32:32 + 6 * n].rearrange("p (n s) -> p n s", s=6)
    mv = K.small[:, 0:2 * n].rearrange("p (n s) -> p n s", s=2)
    with stage(K, "step") as (block, step):
        @block.vector
        def _(dve):
            chain = Chain(dve, step)
            for i, t in enumerate(tiles):
                chain(dve.bn_stats(stats[:, i, :], rows[:, t, :]))
            for i, t in enumerate(tiles):
                dve.bn_aggr(mv[:, i, :], stats[:, i, :])
    inverse_root(K, mv[:, :, 1], EPS)
    with stage(K, "step", "normed") as (block, step, normed):
        @block.vector
        def _(dve):
            chain = Chain(dve, step)
            for i, t in enumerate(tiles):
                chain(dve.tensor_scalar(rows[:, t, :], rows[:, t, :], mv[:, i, 0:1], mv[:, i, 1:2],
                                        ALU.subtract, ALU.mult))
                chain(dve.tensor_tensor(rows[:, t, :], rows[:, t, :], gain, ALU.mult))
                dve.tensor_tensor(rows[:, t, :], rows[:, t, :], bias, ALU.add).then_inc(normed, 1)

        @block.scalar
        def _(act):
            if silu:
                for i, t in enumerate(tiles):
                    act.wait_ge(normed, i + 1)
                    act.activation(rows[:, t, :], rows[:, t, :], ACT.Silu)



def modulation(K, l, s_cols, mod):
    nc = K.nc
    with nc.sbuf_tensor(f"ada_g{l}", [P, 2, D], F32) as gains:
        gain_loads = [(gains[:, i, :], K.dram[f"norm{i + 1}_g"][l:l + 1, :].broadcast_to([P, D])) for i in range(2)]
        if l == 0:
            fresh_modulation(K, l, s_cols, mod, gain_loads)
        else:
            load(K, *[(mod[c][:, s, :], K.ada[s:s + 1, c * D:(c + 1) * D].broadcast_to([P, D])) for s in range(2) for c in range(6)],
                 *gain_loads)
        with stage(K) as (block,):
            @block.vector
            def _(dve):
                for s in range(2):
                    for c, g in ((1, 0), (4, 1)):
                        dve.scalar_tensor_tensor(out=mod[c][:, s, :], in0=mod[c][:, s, :], scalar=1.0, in1=gains[:, g, :],
                                                 op0=ALU.add, op1=ALU.mult)


def fresh_modulation(K, l, s_cols, mod, gain_loads):
    nc = K.nc
    w = K.dram["w_ada"][l]
    n_chunks = 6 * D // 512
    with nc.sbuf_tensor(f"ada_w{l}", [P, 2, KD, 512], F32) as wt, nc.sbuf_tensor(f"ada_b{l}", [2, 6 * D], F32) as ball, \
            nc.sbuf_tensor(f"ada_row{l}", [2, 2, 512], F32) as row:
        with stage(K, "w0", "w1", "bias_in", "gains_in", "row_ready", "row_sum", "row_stored", "mod_in") as \
                (block, w0, w1, bias_in, gains_in, row_ready, row_sum, row_stored, mod_in):
            loaded = (w0, w1)

            @block.sync
            def _(sp):
                for n in range(n_chunks):
                    if n >= 2:
                        sp.wait_ge(row_ready, n - 1)
                    sp.dma_start(wt[:, n % 2, :, :], w[:, n * 512:(n + 1) * 512].rearrange("(k p) n -> p k n", p=P))\
                      .then_inc(loaded[n % 2], 16)
                    if n == 0:
                        sp.dma_start(ball[:, :], K.dram["b_ada"][l:l + 1, :].broadcast_to([2, 6 * D])).then_inc(bias_in, 16)
                for dst, src in gain_loads:
                    sp.dma_start(dst, src).then_inc(gains_in, 16)
                sp.wait_ge(gains_in, 16 * len(gain_loads))

            @block.tensor
            def _(pe):
                for n in range(n_chunks):
                    pe.wait_ge(loaded[n % 2], 16 * (n // 2 + 1))
                    if n >= 2:
                        pe.wait_ge(row_sum, n - 1)
                    for k in range(KD):
                        last = pe.matmul(K.ps[n % 2][0:2, :], s_cols[:, k, :], wt[:, n % 2, k, :], start=k == 0, stop=k == KD - 1)
                    last.then_inc(row_ready, 1)

            @block.vector
            def _(dve):
                dve.wait_ge(bias_in, 16)
                for n in range(n_chunks):
                    dve.wait_ge(row_ready, n + 1)
                    if n >= 2:
                        dve.wait_ge(row_stored, 16 * (n - 1))
                    dve.tensor_tensor(row[0:2, n % 2, :], K.ps[n % 2][0:2, :], ball[0:2, n * 512:(n + 1) * 512],
                                      ALU.add).then_inc(row_sum, 1)

            @block.scalar
            def _(act):
                for n in range(n_chunks):
                    c, half = divmod(n, 2)
                    act.wait_ge(row_sum, n + 1)
                    act.dma_start(K.ada[:, n * 512:(n + 1) * 512], row[0:2, n % 2, :]).then_inc(row_stored, 16)
                    act.wait_ge(row_stored, 16 * (n + 1))
                    for s in range(2 if half else 0):
                        act.dma_start(mod[c][:, s, :], K.ada[s:s + 1, c * D:(c + 1) * D].broadcast_to([P, D])).then_inc(mod_in, 16)
                act.wait_ge(mod_in, 16 * n_chunks)


def copy_to(dst_of, func=ACT.Copy):
    def evacuate(eng, chain, psum, o, t):
        return eng.activation(dst_of(o, t), psum, func)
    return evacuate


def mlstm(K, l, zT, n_lat_only, qk, vones, gates, osig):
    nc = K.nc
    out_tiles = [2, 3] if n_lat_only else [0, 1, 2, 3]
    q0 = CTX if n_lat_only else 0
    with ExitStack() as mem:
        def sb(name, shape):
            return mem.enter_context(nc.sbuf_tensor(f"ml_{name}{l}", shape, F32))
        gcol = sb("gcol", [P, 2, 4, 2, 4])
        neg_run = sb("neg_run", [4, 2, TALL])
        gb = sb("gb", [P, 16])
        ng = sb("ng", [P, MIX])
        early = ExitStack()
        pick4, ones4 = sb("pick4", [4, 4, P]), sb("ones4", [4, TALL])
        load(K, (pick4[:, :, :], K.dram["c_pick4"]), (ones4[:, :], K.dram["c_ones4"]),
             (gb[:, :], K.dram["ml_gate_b"][l:l + 1, :].broadcast_to([P, 16])),
             (ng[:, :], K.dram["ml_norm_g"][l:l + 1, :].broadcast_to([P, MIX])))

        def sb_early(name, shape):
            return early.enter_context(nc.sbuf_tensor(f"ml_{name}{l}", shape, F32))
        lf = sb_early("lf", [P, 4, 8])
        soft = sb_early("soft", [P, 4, 8])
        with stage(K, "step", "to_act", "softened") as (block, step, to_act, softened):
            @block.vector
            def _(dve):
                chain = Chain(dve, step)
                chain(dve.tensor_tensor(gates[:, :, :], gates[:, :, :], gb[:, None, :].broadcast_to([P, 4, 16]), ALU.add))
                dve.tensor_single_scalar(lf[:, :, :], gates[:, :, 8:16], 0.0, ALU.min).then_inc(to_act, 1)
                dve.wait_ge(softened, 3)
                dve.wait_ge(to_act, 1)
                dve.tensor_tensor(lf[:, :, :], lf[:, :, :], soft[:, :, :], ALU.subtract)

            @block.scalar
            def _(act):
                act.wait_ge(to_act, 1)
                chain = Chain(act, softened)
                chain(act.activation(soft[:, :, :], gates[:, :, 8:16], ACT.Abs))
                chain(act.activation(soft[:, :, :], soft[:, :, :], ACT.Exp, scale=-1.0))
                chain(act.activation(soft[:, :, :], soft[:, :, :], ACT.Ln, bias=1.0))
        li_r, lf_r = sb_early("li_r", [4, 2, TALL]), sb_early("lf_r", [4, 2, TALL])
        cum, run = sb_early("cum", [4, 2, TALL]), sb_early("run", [4, 2, TALL])
        gsrc = sb_early("gsrc", [4, 2, 2, TALL])
        with stage(K, "turned", "copied") as (block, turned, copied):
            @block.tensor
            def _(pe):
                for t in range(4):
                    for b, src in enumerate((gates, lf)):
                        for d in range(2):
                            last = pe.transpose(K.ps[t][0:4, (2 * b + d) * P:(2 * b + d + 1) * P],
                                                src[:, t, 4 * d:4 * d + 4], K.ident[:, :])
                last.then_inc(turned, 1)

            @block.vector
            def _(dve):
                dve.wait_ge(turned, 1)
                for t in range(4):
                    for b, dst in enumerate((li_r, lf_r)):
                        dve.tensor_copy(dst[:, 0, t * P:(t + 1) * P], K.ps[t][0:4, 2 * b * P:(2 * b + 1) * P])
                        at = (t // 2) * CTX + (1 - t % 2) * P
                        rev = dst[:, 1, at:at + P]
                        dve.tensor_copy(rev, K.ps[t][0:4, (2 * b + 1) * P:(2 * b + 2) * P][:, ::-1])
        with stage(K, "step") as (block, step):
            @block.vector
            def _(dve):
                chain = Chain(dve, step)
                for d in range(2):
                    chain(dve.tensor_tensor_scan(cum[:, d, :], ones4[0:4, :], lf_r[:, d, :], 0.0, ALU.mult, ALU.add))
                chain(dve.tensor_tensor(li_r[:, :, :], li_r[:, :, :], cum[:, :, :], ALU.subtract))
                for d in range(2):
                    chain(dve.tensor_tensor_scan(run[:, d, :], li_r[:, d, :], li_r[:, d, :], 0.0, ALU.max, ALU.max))
                chain(dve.tensor_tensor(cum[:, :, :], cum[:, :, :], run[:, :, :], ALU.add))
                for src, dst, sign in ((li_r, gsrc[:, 0], 1.0), (cum, gsrc[:, 1], -1.0), (run, neg_run, -1.0)):
                    dve.tensor_single_scalar(dst[:, 0, :], src[:, 0, :], sign, ALU.mult)
                    for s in range(2):
                        dve.tensor_single_scalar(dst[:, 1, s * CTX:(s + 1) * CTX],
                                                 src[:, 1, s * CTX:(s + 1) * CTX][:, ::-1], sign, ALU.mult)
        with stage(K, "turned") as (block, turned):
            @block.tensor
            def _(pe):
                for d in range(2):
                    for t in range(4):
                        for b in range(2):
                            c = ((d * 4 + t) * 2 + b) * 4
                            last = pe.transpose(K.ps[0][:, c:c + 4], gsrc[:, b, d, t * P:(t + 1) * P], K.ident[0:4, 0:4])
                last.then_inc(turned, 1)

            @block.scalar
            def _(act):
                act.wait_ge(turned, 1)
                view = K.ps[0][:, 0:64].rearrange("p (a b h) -> p a b h", b=2, h=4)
                dst = gcol[:, :, :, :, :].rearrange("p d t b h -> p (d t) b h")
                act.activation(dst[:, :, 0, :], view[:, :, 0, :], ACT.Copy)
                act.activation(dst[:, :, 1, :], view[:, :, 1, :], ACT.Exp)
        early.close()
        hacc = sb("hacc", [P, 4, MIX])
        wts = sb("wts", [P, 2, 4, TALL])
        prod = sb("prod", [P, 2, 4, TALL])
        den = sb("den", [P, 2, 4])
        tmp = sb("tmp", [P, 4, DH])
        mask = sb("mask", [P, 2, 2, TALL])
        load(K, (mask[:, :, :, :], K.dram["ml_mask"]))
        n_it = 2 * HEADS
        begin = [q0, q0, CTX, CTX]

        def sources(qt, d):
            if qt < 2:
                return [s for s in (0, 1) if (s <= qt if d == 0 else s >= qt)]
            return [0, 1] + [s for s in (2, 3) if (s <= qt if d == 0 else s >= qt)]

        with stage(K, "scores", "spread", "gated", "exped", "weighted", "summed", "step", "out_read") as \
                (block, scores, spread, gated, exped, weighted, summed, step, out_read):
            @block.tensor
            def _(pe):
                def sums(i):
                    h, d = divmod(i, 2)
                    pe.wait_ge(weighted, i + 1)
                    if i >= 2:
                        pe.wait_ge(out_read, i - 1)
                    for qt in out_tiles:
                        src = sources(qt, d)
                        for s in src:
                            last = pe.matmul(K.ps[6 + i % 2][:, qt * 65:qt * 65 + 65], prod[:, i % 2, s, qt * P:(qt + 1) * P],
                                             vones[:, s, h, :], start=s == src[0], stop=s == src[-1])
                    last.then_inc(summed, 1)

                for i in range(n_it):
                    h, d = divmod(i, 2)
                    r = (h % 2) * DH
                    if d == 0:
                        if i:
                            pe.wait_ge(weighted, i)
                        for s in range(4):
                            last = pe.matmul(K.ps[s][:, begin[s]:TALL], qk[r:r + DH, 2 + h // 2, s * P:(s + 1) * P],
                                             qk[r:r + DH, h // 2, begin[s]:TALL], start=True, stop=True)
                        last.then_inc(scores, 1)
                    if i >= 2:
                        pe.wait_ge(gated, i - 1)
                    pe.matmul(K.ps[4 + i % 2][:, :], pick4[0:4, h, :], neg_run[:, d, :], start=True, stop=True).then_inc(spread, 1)
                    if i:
                        sums(i - 1)
                sums(n_it - 1)

            @block.scalar
            def _(act):
                for i in range(n_it):
                    act.wait_ge(gated, i + 1)
                    for s in range(4):
                        last = act.activation(wts[:, i % 2, s, begin[s]:TALL], wts[:, i % 2, s, begin[s]:TALL], ACT.Exp)
                    last.then_inc(exped, 1)

            @block.vector
            def _(dve):
                chain = Chain(dve, step)

                def collect(i):
                    h, d = divmod(i, 2)
                    dve.wait_ge(summed, i + 1)
                    o = K.ps[6 + i % 2][:, 0:260].rearrange("p (t c) -> p t c", c=65)
                    lo, n = out_tiles[0], len(out_tiles)
                    o = o[:, lo:4, :]
                    chain(dve.tensor_tensor(den[:, 0, lo:4], o[:, :, 64], gcol[:, d, lo:4, 1, h], ALU.max))
                    chain(dve.scalar_tensor_tensor(out=den[:, 1, lo:4], in0=o[:, :, 64], scalar=-1.0, in1=den[:, 0, lo:4],
                                                   op0=ALU.mult, op1=ALU.max))
                    chain(dve.reciprocal(den[:, 1, lo:4], den[:, 1, lo:4]))
                    rd = den[:, 1, lo:4][:, :, None].broadcast_to([P, n, DH])
                    dst = hacc[:, lo:4, h * DH:(h + 1) * DH]
                    if d == 0:
                        ins = dve.tensor_tensor(dst, o[:, :, 0:64], rd, ALU.mult)
                        ins.then_inc(out_read, 1)
                        dve.wait_ge(out_read, i + 1)
                    else:
                        dve.tensor_tensor(tmp[:, lo:4, :], o[:, :, 0:64], rd, ALU.mult).then_inc(out_read, 1)
                        dve.wait_ge(out_read, i + 1)
                        chain(dve.tensor_tensor(dst, dst, tmp[:, lo:4, :], ALU.add))

                for i in range(n_it):
                    h, d = divmod(i, 2)
                    dve.wait_ge(spread, i + 1)
                    for s in range(4):
                        b = begin[s]
                        last = dve.scalar_tensor_tensor(out=wts[:, i % 2, s, b:TALL], in0=K.ps[4 + i % 2][:, b:TALL],
                                                        scalar=gcol[:, d, s, 0, h:h + 1],
                                                        in1=mask[:, d, s % 2, b - (s // 2) * CTX:TALL - (s // 2) * CTX],
                                                        op0=ALU.add, op1=ALU.min)
                    last.then_inc(gated, 1)
                    if i:
                        collect(i - 1)
                    dve.wait_ge(exped, i + 1)
                    dve.wait_ge(scores, h + 1)
                    if i >= 2:
                        dve.wait_ge(summed, i - 1)
                    for s in range(4):
                        b = begin[s]
                        last = dve.scalar_tensor_tensor(out=prod[:, i % 2, s, b:TALL], in0=K.ps[s][:, b:TALL],
                                                        scalar=DH ** -0.5, in1=wts[:, i % 2, s, b:TALL],
                                                        op0=ALU.mult, op1=ALU.mult)
                    last.then_inc(weighted, 1)
                collect(n_it - 1)
        lo, n = out_tiles[0], len(out_tiles)
        ss = sb("ss", [P, 4, 4])
        sq = sb("sq", [P, 4, MIX])
        hv = hacc[:, lo:4, :].rearrange("p t (h d) -> p t h d", h=4)
        with stage(K, "step") as (block, step):
            @block.vector
            def _(dve):
                chain = Chain(dve, step)
                chain(dve.tensor_tensor(sq[:, lo:4, :], hacc[:, lo:4, :], hacc[:, lo:4, :], ALU.mult))
                chain(dve.tensor_reduce(ss[:, lo:4, :], sq[:, lo:4, :].rearrange("p t (h d) -> p t h d", h=4), AX.X, ALU.add))
                dve.tensor_single_scalar(ss[:, lo:4, :], ss[:, lo:4, :], 1.0 / DH, ALU.mult)
        inverse_root(K, ss[:, lo:4, :], EPS)
        with stage(K, "step") as (block, step):
            @block.vector
            def _(dve):
                chain = Chain(dve, step)
                for t in out_tiles:
                    v = hacc[:, t, :].rearrange("p (h d) -> p h d", h=4)
                    chain(dve.tensor_tensor(v, v, ss[:, t, :][:, :, None].broadcast_to([P, 4, DH]), ALU.mult))
                chain(dve.tensor_tensor(hacc[:, lo:4, :], hacc[:, lo:4, :], ng[:, None, :].broadcast_to([P, n, MIX]), ALU.mult))
                dve.tensor_tensor(hacc[:, lo:4, :], hacc[:, lo:4, :], osig[:, lo:4, :], ALU.mult)
        rows_to_channels(K, hacc, zT, out_tiles, MIX)


def gmlp(K, l, zT, gm, tiles):
    nc = K.nc
    lo, n = tiles[0], len(tiles)
    with ExitStack() as mem:
        def sb(name, shape):
            return mem.enter_context(nc.sbuf_tensor(f"gm_{name}{l}", shape, F32))
        ln = sb("ln", [P, 2, MIX])
        ws = sb("ws", [P, 4, P])
        bs = sb("bs", [P, 4])
        mixed = sb("mixed", [P, 4, MIX])
        load(K, (ln[:, 0, :], K.dram["gm_ln_g"][l:l + 1, :].broadcast_to([P, MIX])),
             (ln[:, 1, :], K.dram["gm_ln_b"][l:l + 1, :].broadcast_to([P, MIX])),
             (ws[:, :, :], K.dram["gm_w_s"][l]), (bs[:, :], K.dram["gm_b_s"][l]))
        v = gm[:, :, MIX:2 * MIX]
        layer_norm(K, v, tiles, MIX, ln[:, 0, :], ln[:, 1, :])
        with stage(K, "mixed_s", "step") as (block, done, step):
            @block.tensor
            def _(pe):
                for t in tiles:
                    for g in range(4):
                        last = pe.matmul(K.ps[t][:, g * DH:(g + 1) * DH], ws[:, g, :], v[:, t, g * DH:(g + 1) * DH],
                                         start=True, stop=True)
                    last.then_inc(done, 1)

            @block.vector
            def _(dve):
                chain = Chain(dve, step)
                for i, t in enumerate(tiles):
                    dve.wait_ge(done, i + 1)
                    chain(dve.tensor_tensor(mixed[:, t, :].rearrange("p (g c) -> p g c", g=4),
                                            K.ps[t][:, 0:MIX].rearrange("p (g c) -> p g c", g=4),
                                            bs[:, :][:, :, None].broadcast_to([P, 4, DH]), ALU.add))
                    dve.tensor_tensor(mixed[:, t, :], mixed[:, t, :], gm[:, t, 0:MIX], ALU.mult)
        rows_to_channels(K, mixed, zT, tiles, MIX)


def conv_branch(K, l, zT, y, streams):
    nc = K.nc
    tiles = list(range(2 * streams[0], 4))
    with nc.sbuf_tensor(f"cv_rows{l}", [P, 4, MIX], F32) as rows, nc.sbuf_tensor(f"cv_ln{l}", [P, 2, MIX], F32) as ln:
        load(K, (ln[:, 0, :], K.dram["cv_ln_g"][l:l + 1, :].broadcast_to([P, MIX])),
             (ln[:, 1, :], K.dram["cv_ln_b"][l:l + 1, :].broadcast_to([P, MIX])))
        transpose(K, [([y[:, j, t * P:(t + 1) * P] for j in range(2)],
                       rows[:, t, :].rearrange("p (j c) -> p j c", j=2)) for t in tiles])
        layer_norm(K, rows, tiles, MIX, ln[:, 0, :], ln[:, 1, :], silu=True)
        rows_to_channels(K, rows, zT, tiles, MIX)


def fourier(K, l, zT, ft, streams):
    nc = K.nc
    with nc.sbuf_tensor(f"ft_mid{l}", [P, 2, 2, CTX], F32) as mid, nc.sbuf_tensor(f"ft_t{l}", [P, 2, 2, CTX], F32) as dft_t, \
            nc.sbuf_tensor(f"ft_c{l}", [P, 2, P], F32) as dft_c:
        load(K, (dft_t[:, :, :, :], K.dram["dft_t"]), (dft_c[:, :, :], K.dram["dft_c"]))
        with stage(K, "timed", "copied", "done", "out_copied") as (block, timed, copied, done, out_copied):
            @block.tensor
            def _(pe):
                for i, s in enumerate(streams):
                    if i:
                        pe.wait_ge(copied, i)
                    for c in range(2):
                        for m in range(2):
                            for k in range(2):
                                last = pe.matmul(K.ps[2 * c + m][:, 0:CTX], ft[:, 2 * s + k, c * P:(c + 1) * P],
                                                 dft_t[:, m, k, :], start=k == 0, stop=k == 1)
                    last.then_inc(timed, 1)
                    pe.wait_ge(copied, i + 1)
                    if i:
                        pe.wait_ge(out_copied, i)
                    for c in range(2):
                        for m in range(2):
                            last = pe.matmul(K.ps[4 + c][:, 0:CTX], dft_c[:, m, :], mid[:, c, m, :], start=m == 0, stop=m == 1)
                    last.then_inc(done, 1)

            @block.scalar
            def _(act):
                for i, s in enumerate(streams):
                    act.wait_ge(timed, i + 1)
                    if i:
                        act.wait_ge(done, i)
                    for c in range(2):
                        for m in range(2):
                            last = act.activation(mid[:, c, m, :], K.ps[2 * c + m][:, 0:CTX], ACT.Copy)
                    last.then_inc(copied, 1)

            @block.vector
            def _(dve):
                for i, s in enumerate(streams):
                    dve.wait_ge(done, i + 1)
                    for c in range(2):
                        last = dve.tensor_copy(zT[:, c, s * CTX:(s + 1) * CTX], K.ps[4 + c][:, 0:CTX])
                    last.then_inc(out_copied, 1)


def merge(K, l, hT, zTs, yT, t0):
    nc = K.nc
    tw = TALL - t0
    jobs = [(b, c) for b in range(4) for c in range(4)]
    with ExitStack() as mem:
        wg = mem.enter_context(nc.sbuf_tensor(f"mg_wg{l}", [P, 3, KD, 256], F32))
        wb = mem.enter_context(nc.sbuf_tensor(f"mg_wb{l}", [P, 3, 2, 256], F32))
        halves = tuple(mem.enter_context(nc.sbuf_tensor(f"mg_{h}{l}", [P, 2, KD, 256], F32R)) for h in ("hi", "lo"))
        gate = mem.enter_context(nc.sbuf_tensor(f"mg_gate{l}", [P, 2, tw], F32))
        term = mem.enter_context(nc.sbuf_tensor(f"mg_term{l}", [P, 2, tw], F32))
        with stage(K, "w0", "w1", "w2", "gate_psum", "branch_psum", "gate_done", "termed", "added", "hi_ready", "lo_ready") as \
                (block, w0, w1, w2, gate_psum, branch_psum, gate_done, termed, added, hi_ready, lo_ready):
            loaded = (w0, w1, w2)

            @block.sync
            def _(sp):
                for n, (b, c) in enumerate(jobs):
                    if n >= 3:
                        sp.wait_ge(lo_ready, n - 2)
                        sp.wait_ge(branch_psum, 2 * (n - 2))
                    at = BR_OFF + b * D + c * 256
                    sp.dma_start(wg[:, n % 3, :, :], K.dram["w_in"][l][:, at:at + 256].rearrange("(k p) n -> p k n", p=P)).then_inc(loaded[n % 3], 16)
                    sp.dma_start(wb[:, n % 3, :, :], K.dram["w_branch"][l][b * MIX:(b + 1) * MIX, c * 256:(c + 1) * 256]
                                 .rearrange("(k p) n -> p k n", p=P)).then_inc(loaded[n % 3], 16)

            @block.tensor
            def _(pe):
                for n, (b, c) in enumerate(jobs):
                    pe.wait_ge(loaded[n % 3], 32 * (n // 3 + 1))
                    pe.wait_ge(lo_ready, n + 1)
                    for j in range(2):
                        i = 2 * n + j
                        if i >= 2:
                            pe.wait_ge(gate_done, i - 1)
                        for k in range(KD):
                            last = products_of(pe, K.ps[i % 2][:, 0:tw], both(halves, slice(0, P), n % 2, k, slice(j * P, (j + 1) * P)),
                                               both(hT, slice(0, P), k, slice(t0, TALL)), k == 0, k == KD - 1)
                        last.then_inc(gate_psum, 1)
                        if i >= 2:
                            pe.wait_ge(termed, i - 1)
                        for k in range(2):
                            last = pe.matmul(K.ps[2 + i % 2][:, 0:tw], wb[:, n % 3, k, j * P:(j + 1) * P],
                                             zTs[:, b, k, t0:TALL], start=k == 0, stop=k == 1)
                        last.then_inc(branch_psum, 1)

            @block.scalar
            def _(act):
                def split_hi(n):
                    act.wait_ge(loaded[n % 3], 32 * (n // 3 + 1))
                    if n >= 2:
                        act.wait_ge(gate_psum, 2 * (n - 1))
                    act.activation(halves[0][:, n % 2, :, :], wg[:, n % 3, :, :], ACT.Copy).then_inc(hi_ready, 1)

                split_hi(0)
                for n in range(len(jobs)):
                    if n + 1 < len(jobs):
                        split_hi(n + 1)
                    for i in (2 * n, 2 * n + 1):
                        act.wait_ge(gate_psum, i + 1)
                        if i >= 2:
                            act.wait_ge(termed, i - 1)
                        act.activation(gate[:, i % 2, :], K.ps[i % 2][:, 0:tw], ACT.Sigmoid).then_inc(gate_done, 1)

            @block.vector
            def _(dve):
                def split_lo(n):
                    dve.wait_ge(hi_ready, n + 1)
                    dve.tensor_tensor(halves[1][:, n % 2, :, :], wg[:, n % 3, :, :], halves[0][:, n % 2, :, :].bitcast(F32),
                                      ALU.subtract).then_inc(lo_ready, 1)

                split_lo(0)
                for n, (b, c) in enumerate(jobs):
                    if n + 1 < len(jobs):
                        split_lo(n + 1)
                    for i in (2 * n, 2 * n + 1):
                        dve.wait_ge(gate_done, i + 1)
                        dve.wait_ge(branch_psum, i + 1)
                        dst = yT[:, 2 * c + i % 2, t0:TALL]
                        if b == 0:
                            dve.tensor_tensor(dst, K.ps[2 + i % 2][:, 0:tw], gate[:, i % 2, :], ALU.mult).then_inc(termed, 1)
                        else:
                            if i >= 10:
                                dve.wait_ge(added, i - 9)
                            dve.tensor_tensor(term[:, i % 2, :], K.ps[2 + i % 2][:, 0:tw], gate[:, i % 2, :], ALU.mult).then_inc(termed, 1)
                            dve.wait_ge(termed, i + 1)
                            dve.tensor_tensor(dst, dst, term[:, i % 2, :], ALU.add).then_inc(added, 1)


def add_scaled(K, x, scale_of):
    def evacuate(eng, chain, psum, c, t):
        w = psum.shape[1]
        if scale_of is None:
            return eng.tensor_tensor(x[:, t, c:c + w], x[:, t, c:c + w], psum, ALU.add)
        chain(eng.tensor_tensor(K.junk[:, 0:w], psum, scale_of(t)[:, c:c + w], ALU.mult))
        return eng.tensor_tensor(x[:, t, c:c + w], x[:, t, c:c + w], K.junk[:, 0:w], ALU.add)
    return evacuate


def key_scores(K, l, hT, t0, top, topi):
    nc = K.nc
    tw = TALL - t0
    tiles = tw // P
    width, ring, rows = 2 * P, 3, slice(0, P)
    weights = K.dram["peer_w_q"][l]
    with ExitStack() as mem:
        def sb(name, shape, dt=F32):
            return mem.enter_context(nc.sbuf_tensor(f"ks_{name}{l}", shape, dt))
        keys = sb("keys", [P, 2, NKEYS])
        wt = sb("w", [P, ring, KD, width])
        halves = sb("whi", [P, 2, KD, width], F32R), sb("wlo", [P, 2, KD, width], F32R)
        q = sb("q", [P, 2, 2, tw])
        sc = sb("sc", [P, 2, 2 * tiles, NKEYS])
        sc2 = sb("sc2", [P, 2 * tiles, NKEYS])
        with stage(K, "weights0", "weights1", "weights2", "keys_in", "hi_ready", "lo_ready", "queried", "q_copied",
                   "scored", "sc_copied", "step", "topped") as \
                (block, weights0, weights1, weights2, keys_in, hi_ready, lo_ready, queried, q_copied, scored, sc_copied, step, topped):
            loaded = (weights0, weights1, weights2)

            @block.sync
            def _(sp):
                sp.dma_start(wt[:, 0, :, :], weights[:, 0:width].rearrange("(k p) n -> p k n", p=P)).then_inc(loaded[0], 16)
                sp.dma_start(keys[:, :, :], K.dram["peer_keys"][l]).then_inc(keys_in, 16)
                for n in range(1, PH):
                    if n >= ring:
                        sp.wait_ge(lo_ready, n - ring + 1)
                    sp.dma_start(wt[:, n % ring, :, :], weights[:, n * width:(n + 1) * width].rearrange("(k p) n -> p k n", p=P))\
                      .then_inc(loaded[n % ring], 16)

            @block.tensor
            def _(pe):
                for n in range(PH + 1):
                    if n < PH:
                        pe.wait_ge(lo_ready, n + 1)
                        for j in range(2):
                            if n:
                                pe.wait_ge(q_copied, 2 * n - 1 + j)
                            for k in range(KD):
                                last = products_of(pe, K.ps[j][:, 0:tw], both(halves, rows, n % 2, k, slice(j * P, (j + 1) * P)),
                                                   both(hT, rows, k, slice(t0, TALL)), k == 0, k == KD - 1)
                            last.then_inc(queried, 1)
                    if n == 0:
                        pe.wait_ge(keys_in, 16)
                        continue
                    m = n - 1
                    for j in range(2):
                        pe.wait_ge(q_copied, 2 * m + j + 1)
                        if m:
                            pe.wait_ge(sc_copied, 2 * m - 1 + j)
                        for t in range(tiles):
                            last = pe.matmul(K.ps[2 + j][:, t * P:(t + 1) * P], q[:, m % 2, j, t * P:(t + 1) * P], keys[:, j, :],
                                             start=True, stop=True)
                        last.then_inc(scored, 1)

            @block.scalar
            def _(act):
                def split_hi(n):
                    act.wait_ge(loaded[n % ring], 16 * (n // ring + 1))
                    if n >= 2:
                        act.wait_ge(queried, 2 * n - 2)
                    act.activation(halves[0][:, n % 2, :, :], wt[:, n % ring, :, :], ACT.Copy).then_inc(hi_ready, 1)

                def copy_scores(m):
                    for j in range(2):
                        act.wait_ge(scored, 2 * m + j + 1)
                        if m >= 2:
                            act.wait_ge(topped, m - 1)
                        act.activation(sc[:, m % 2, j * tiles:(j + 1) * tiles, :],
                                       K.ps[2 + j][:, 0:tw].rearrange("p (t n) -> p t n", t=tiles), ACT.Copy).then_inc(sc_copied, 1)
                split_hi(0)
                for n in range(PH):
                    if n + 1 < PH:
                        split_hi(n + 1)
                    for j in range(2):
                        act.wait_ge(queried, 2 * n + j + 1)
                        if n >= 2:
                            act.wait_ge(scored, 2 * n - 3 + j)
                        act.activation(q[:, n % 2, j, :], K.ps[j][:, 0:tw], ACT.Copy).then_inc(q_copied, 1)
                    if n:
                        copy_scores(n - 1)
                copy_scores(PH - 1)

            @block.gpsimd
            def _(pool):
                for n in range(PH):
                    pool.wait_ge(hi_ready, n + 1)
                    pool.tensor_tensor(halves[1][:, n % 2, :, :], wt[:, n % ring, :, :], halves[0][:, n % 2, :, :].bitcast(F32),
                                       ALU.subtract).then_inc(lo_ready, 1)

            @block.vector
            def _(dve):
                chain = Chain(dve, step)
                for n in range(PH):
                    dve.wait_ge(sc_copied, 2 * n + 2)
                    lists = [(top[:, t, 2 * n + j, :], topi[:, t, 2 * n + j, :], sc[:, n % 2, j * tiles + t, :], sc2[:, j * tiles + t, :])
                             for j in range(2) for t in range(tiles)]
                    pick16(dve, chain, lists).then_inc(topped, 1)


def pick16(dve, chain, lists):
    for vals, idx, src, scratch in lists:
        last = dve.max(vals[:, 0:8], src)
    chain(last)
    for vals, idx, src, scratch in lists:
        dve.max_index(idx[:, 0:8], vals[:, 0:8], src)
        last = dve.match_replace(scratch, vals[:, 0:8], src, -3e38)
    chain(last)
    for vals, idx, src, scratch in lists:
        last = dve.max(vals[:, 8:16], scratch)
    chain(last)
    for vals, idx, src, scratch in lists:
        last = dve.max_index(idx[:, 8:16], vals[:, 8:16], scratch)
    return last


def expert_choice(K, l, top, topi, tiles, choice):
    nc = K.nc
    B8 = 8
    CAND = TOPK + (TOPK - 1) * B8
    with ExitStack() as mem:
        def sb(name, shape, dt=F32):
            return mem.enter_context(nc.sbuf_tensor(f"pc_{name}{l}", shape, dt))
        cand = sb("cand", [P, 2, PH, CAND])
        cand2 = sb("cand2", [P, 2, PH, CAND])
        topf = sb("topf", [P, 2, 16, TOPK])
        best = sb("best", [P, 2, PH, TOPK])
        pos = sb("pos", [P, 2, PH, TOPK], U32)
        place = sb("place", [P, 2, 2 * PH * TOPK])
        row_no = sb("row_no", [P, 2, 2 * PH * TOPK], U32)
        half = sb("half", [P, 2, 2 * PH * TOPK])
        hot = sb("hot", [P, 2, P, TOPK])
        rows = sb("rows", [P, 3, 2, P])
        tot = sb("tot", [P, 2, 2 * PH])
        nxt = l + 1 < DEPTH
        chunks = 6 * D // 512 // (len(tiles) // 2)
        if nxt:
            wt, bias, row = sb("ada_w", [P, 2, KD, 512]), sb("ada_b", [1, 2, 512]), sb("ada_row", [2, chunks, 512])
        for ti in range(0, len(tiles), 2):
            with stage(K, "step", "shifted", "exped", "rows_done", "turned", "w0", "w1", "row_ready", "row_copied", "row_stored") as \
                    (block, step, shifted, exped, rows_done, turned, w0, w1, row_ready, row_copied, row_stored):
                loaded = (w0, w1)
                first_chunk = ti // 2 * chunks
                t = tiles[ti]

                @block.sync
                def _(sp):
                    if not nxt:
                        return
                    for n in range(chunks):
                        if n >= 2:
                            sp.wait_ge(row_ready, n - 1)
                        c0 = (first_chunk + n) * 512
                        sp.dma_start(wt[:, n % 2, :, :], K.dram["w_ada"][l + 1][:, c0:c0 + 512].rearrange("(k p) n -> p k n", p=P))\
                          .then_inc(loaded[n % 2], 16)
                        sp.dma_start(bias[:, n % 2, :], K.dram["b_ada"][l + 1:l + 2, c0:c0 + 512]).then_inc(loaded[n % 2], 16)
                    sp.wait_ge(row_copied, chunks)
                    sp.dma_start(K.ada[:, first_chunk * 512:(first_chunk + chunks) * 512], row[:, :, :].rearrange("s c n -> s (c n)"))\
                      .then_inc(row_stored, 16)
                    sp.wait_ge(row_stored, 16)

                @block.tensor
                def _(pe):
                    for n in range(chunks if nxt else 0):
                        pe.wait_ge(loaded[n % 2], 32 * (n // 2 + 1))
                        if n >= 2:
                            pe.wait_ge(row_copied, n - 1)
                        for k in range(KD):
                            pe.matmul(K.ps[n % 2][0:2, :], K.s_cols[:, k, :], wt[:, n % 2, k, :], start=k == 0, stop=False)
                        pe.matmul(K.ps[n % 2][0:2, :], K.ones[0:1, 0:2], bias[:, n % 2, :], start=False, stop=True).then_inc(row_ready, 1)
                    pe.wait_ge(rows_done, 1)
                    for u in range(2):
                        for r in range(3):
                            last = pe.transpose(K.ps[4 + u][:, r * P:(r + 1) * P], rows[:, r, u, :], K.ident[:, :])
                    last.then_inc(turned, 1)

                @block.scalar
                def _(act):
                    for n in range(chunks if nxt else 0):
                        act.wait_ge(row_ready, n + 1)
                        act.activation(row[:, n, :], K.ps[n % 2][0:2, :], ACT.Copy).then_inc(row_copied, 1)
                    act.wait_ge(shifted, 1)
                    act.activation(rows[:, 2, :, :], rows[:, 2, :, :], ACT.Exp).then_inc(exped, 1)
                    act.wait_ge(turned, 1)
                    for u in range(2):
                        act.activation(choice[:, :, (t + u) * P:(t + u + 1) * P], K.ps[4 + u][:, 0:3 * P].rearrange("p (r n) -> p r n", r=3), ACT.Copy)

                @block.vector
                def _(dve):
                    chain = Chain(dve, step)
                    both_tiles = [(u, top[:, ti + u, :, :].rearrange("p (h a) j -> p h a j", a=2)) for u in range(2)]
                    dve.tensor_copy(topf[:, :, :, :], topi[:, ti:ti + 2, :, :])
                    for u, tv in both_tiles:
                        dve.tensor_tensor(cand[:, u, :, 0:TOPK], tv[:, :, 0, 0:1].broadcast_to([P, PH, TOPK]), tv[:, :, 1, :], ALU.add)
                        for h in range(PH):
                            last = dve.tensor_tensor(cand[:, u, h, TOPK:CAND].rearrange("p (a b) -> p a b", b=B8),
                                                     tv[:, h, 0, 1:TOPK][:, :, None].broadcast_to([P, TOPK - 1, B8]),
                                                     tv[:, h, 1, 0:B8][:, None, :].broadcast_to([P, TOPK - 1, B8]), ALU.add)
                    chain(last)
                    chain(pick16(dve, chain, [(best[:, u, h, :], pos[:, u, h, :], cand[:, u, h, :], cand2[:, u, h, :])
                                              for u in range(2) for h in range(PH)]))
                    chain(dve.tensor_copy(place[:, 0, :], pos[:, :, :, :].rearrange("p u h k -> p (u h k)")))
                    chain(dve.tensor_scalar(row_no[:, 0, :], place[:, 0, :], float(B8), float(B8), ALU.max, ALU.subtract))
                    chain(dve.tensor_single_scalar(row_no[:, 1, :], row_no[:, 0, :], 3, ALU.logical_shift_right))
                    chain(dve.tensor_copy(half[:, 0, :], row_no[:, 1, :]))
                    dve.tensor_scalar(place[:, 1, :], half[:, 0, :], 1.0, float(B8), ALU.min, ALU.mult)
                    chain(dve.scalar_tensor_tensor(out=place[:, 0, :], in0=half[:, 0, :], scalar=-float(B8), in1=place[:, 0, :],
                                                   op0=ALU.mult, op1=ALU.add))
                    chain(dve.tensor_tensor(half[:, 1, :], place[:, 0, :], place[:, 1, :], ALU.subtract))
                    hots = hot[:, :, :, :].rearrange("p u q j -> p (u q) j")
                    for a in range(2):
                        chain(dve.tensor_tensor(hots, half[:, a, :][:, :, None].broadcast_to([P, 2 * P, TOPK]),
                                                K.iota[:, None, 0:TOPK].broadcast_to([P, 2 * P, TOPK]), ALU.is_equal))
                        for u in range(2):
                            for h in range(PH):
                                hh = hot[:, u, h * TOPK:(h + 1) * TOPK, :]
                                last = dve.tensor_tensor(hh, hh, topf[:, u, 2 * h + a, :][:, None, :].broadcast_to([P, TOPK, TOPK]), ALU.mult)
                        chain(last)
                        chain(dve.tensor_reduce(rows[:, a, :, :].rearrange("p u q -> p (u q)"), hots, AX.X, ALU.add))
                    g = rows[:, 2, :, :].rearrange("p u (h k) -> p (u h) k", k=TOPK)
                    bests = best[:, :, :, :].rearrange("p u h k -> p (u h) k")
                    dve.tensor_tensor(g, bests, bests[:, :, 0:1].broadcast_to([P, 2 * PH, TOPK]), ALU.subtract).then_inc(shifted, 1)
                    dve.wait_ge(exped, 1)
                    chain(dve.tensor_reduce(tot[:, 0, :], g, AX.X, ALU.add))
                    chain(dve.reciprocal(tot[:, 1, :], tot[:, 0, :]))
                    dve.tensor_tensor(g, g, tot[:, 1, :][:, :, None].broadcast_to([P, 2 * PH, TOPK]), ALU.mult).then_inc(rows_done, 1)


def spread_choice(K, l, choice, t0, tw):
    nc = K.nc
    G = 8
    U = 4
    half_groups = 64 // G
    rounds = tw // 128
    with ExitStack() as mem:
        first = mem.enter_context(nc.sbuf_tensor(f"sp_a{l}", [P, U, G, P], F32))
        second = mem.enter_context(nc.sbuf_tensor(f"sp_b{l}", [P, U, G, P], F32))
        buf = mem.enter_context(nc.sbuf_tensor(f"sp_buf{l}", [P, 2, P, 64], F32))
        with stage(K, "hot1", "hot2", "weighted", "paired", "copied", "stored0", "stored1") as \
                (block, hot1, hot2, weighted, paired, copied, stored0, stored1):
            stored = (stored0, stored1)

            def groups(eng, work, before_slot=None):
                with eng.Fori(0, rounds) as i:
                    for slot in range(2):
                        if before_slot:
                            before_slot(i, slot)
                        with eng.Fori(0, half_groups // U) as g:
                            for u in range(U):
                                work(i * (2 * half_groups) + slot * half_groups + g * U + u, u, g * (U * G) + u * G, slot)

            @block.vector
            def _(dve):
                def work(n, u, q0, slot):
                    dve.wait_ge(paired, n * 2 + 2)
                    for a, (onehot, done) in enumerate(((first, hot1), (second, hot2))):
                        dve.tensor_tensor(onehot[:, u, :, :], choice[:, a, ds(n * G + t0, G)][:, :, None].broadcast_to([P, G, P]),
                                          K.iota[:, None, :].broadcast_to([P, G, P]), ALU.is_equal).then_inc(done, 1)
                groups(dve, work)

            @block.gpsimd
            def _(pool):
                def work(n, u, q0, slot):
                    pool.wait_ge(hot1, n + 1)
                    pool.tensor_tensor(first[:, u, :, :], first[:, u, :, :],
                                       choice[:, 2, ds(n * G + t0, G)][:, :, None].broadcast_to([P, G, P]),
                                       ALU.mult).then_inc(weighted, 1)
                groups(pool, work)

            @block.tensor
            def _(pe):
                pe.sem_inc(paired, 2 * U)

                def work(n, u, q0, slot):
                    pe.wait_ge(hot2, n + 1)
                    pe.wait_ge(weighted, n + 1)
                    for b in range(2):
                        pe.wait_ge(copied, n * 2 + (b + 1))
                        for q in range(4):
                            last = pe.matmul(K.ps[2 * u + b][:, q * P:(q + 1) * P], second[:, u, 4 * b + q, :], first[:, u, 4 * b + q, :],
                                             start=True, stop=True)
                        last.then_inc(paired, 1)
                groups(pe, work)

            @block.scalar
            def _(act):
                act.sem_inc(copied, 2 * U)

                def work(n, u, q0, slot):
                    for b in range(2):
                        act.wait_ge(paired, n * 2 + (b + 1 + 2 * U))
                        act.activation(buf[:, slot, :, ds(q0 + 4 * b, 4)], K.ps[2 * u + b][:, :].rearrange("p (q i) -> p i q", q=4),
                                       ACT.Copy).then_inc(copied, 1)
                groups(act, work, lambda i, slot: act.wait_ge(stored[slot], i * 16 + 16))

            @block.sync
            def _(sp):
                for slot in range(2):
                    sp.sem_inc(stored[slot], 16)
                with sp.Fori(0, rounds) as i:
                    for slot in range(2):
                        sp.wait_ge(copied, i * (4 * half_groups) + (slot + 1) * (2 * half_groups) + 2 * U)
                        sp.dma_start(K.dense[ds(i * 2 + slot, 1), :, :].rearrange("b j n -> (b j) n"),
                                     buf[:, slot, :, :].rearrange("p i t -> p (i t)")).then_inc(stored[slot], 16)
                for slot in range(2):
                    sp.wait_ge(stored[slot], 16 * (rounds + 1))


def experts(K, l, hT, acc, t0, tw):
    nc = K.nc
    E = 2
    step_e = E * P
    n_steps = NEXP // step_e
    outs = tw // P * 2
    nb = tw // 64
    with ExitStack() as mem:
        def sb(name, shape, dt=F32):
            return mem.enter_context(nc.sbuf_tensor(f"ex_{name}{l}", shape, dt))
        u, v = sb("u", [P, 2, KD, step_e]), sb("v", [P, 2, E, D])
        u2 = sb("uhi", [P, 2, KD, step_e], F32R), sb("ulo", [P, 2, KD, step_e], F32R)
        v2 = sb("vhi", [P, 2, E, D], F32R), sb("vlo", [P, 2, E, D], F32R)
        g = sb("g", [P, 2, nb, E * 64])
        a = sb("a", [P, E, tw])
        a2 = sb("ahi", [P, 2, E, tw], F32R), sb("alo", [P, 2, E, tw], F32R)
        names = ["u0", "u1", "v0", "v1", "g0", "g1", "scored", "gelued", "a_step", "weighted", "outed", "added",
                 "u_hi", "u_lo", "v_hi", "v_lo"]
        with stage(K, *names) as (block, u0, u1, v0, v1, g0, g1, scored, gelued, a_step, weighted, outed, added, u_hi, u_lo, v_hi, v_lo):
            us, vs, gs = (u0, u1), (v0, v1), (g0, g1)
            half = n_steps // 2
            rows = slice(0, P)

            def steps(eng, first, second):
                first(0, 0, 0)
                for n in range(1, 4):
                    first(n, n % 2, n)
                    second(n - 1, (n - 1) % 2, n - 1)
                with eng.Fori(2, half) as i:
                    first(i * 2, 0, None)
                    second(i * 2 - 1, 1, None)
                    first(i * 2 + 1, 1, None)
                    second(i * 2, 0, None)
                second(n_steps - 1, 1, None)

            def later(peeled, least):
                return peeled is None or peeled >= least

            @block.sync
            def _(sp):
                def fetch(n, s, peeled):
                    if later(peeled, 2):
                        sp.wait_ge(u_lo, n - 1)
                    sp.dma_start(u[:, s, :, :], K.dram["peer_u"][l][:, ds(n * step_e, step_e)].rearrange("(k p) e -> p k e", p=P)).then_inc(us[s], 16)
                    if later(peeled, 2):
                        sp.wait_ge(weighted, n * E - E)
                    sp.dma_start(g[:, s, :, :], K.dense[0:nb, :, ds(n * (E * 64), E * 64)].rearrange("b j n -> j b n")).then_inc(gs[s], 16)
                    if later(peeled, 2):
                        sp.wait_ge(v_lo, n - 1)
                    sp.dma_start(v[:, s, :, :], K.dram["peer_v"][l][ds(n * step_e, step_e), :].rearrange("(k p) d -> p k d", p=P)).then_inc(vs[s], 16)
                steps(sp, fetch, lambda n, s, peeled: None)

            @block.gpsimd
            def _(pool):
                def split_u(n, s, peeled):
                    pool.wait_ge(u_hi, n + 1)
                    pool.tensor_tensor(u2[1][:, s, :, :], u[:, s, :, :], u2[0][:, s, :, :].bitcast(F32), ALU.subtract).then_inc(u_lo, 1)
                steps(pool, split_u, lambda n, s, peeled: None)

            @block.tensor
            def _(pe):
                def score(n, s, peeled):
                    pe.wait_ge(u_lo, n + 1)
                    for e in range(E):
                        if later(peeled, 1):
                            pe.wait_ge(gelued, n * E + (e - 1))
                        for k in range(KD):
                            last = products_of(pe, K.ps[e][:, 0:tw], both(u2, rows, s, k, slice(e * P, (e + 1) * P)),
                                               both(hT, rows, k, slice(t0, t0 + tw)), k == 0, k == KD - 1)
                        last.then_inc(scored, 1)

                def combine(n, s, peeled):
                    pe.wait_ge(v_lo, n + 1)
                    pe.wait_ge(weighted, n * E + E)
                    for o in range(outs):
                        t, c = divmod(o, 2)
                        if later(peeled, 1) or o >= 4:
                            pe.wait_ge(added, n * outs + (o - 3))
                        for e in range(E):
                            last = products_of(pe, K.ps[2 + o % 4][:, :], both(a2, rows, s, e, slice(t * P, (t + 1) * P)),
                                               both(v2, rows, s, e, slice(c * 512, (c + 1) * 512)), e == 0, e == E - 1)
                        last.then_inc(outed, 1)
                steps(pe, score, combine)

            @block.scalar
            def _(act):
                def split_u(n, s, peeled):
                    act.wait_ge(us[s], (n - s) * 8 + 16)
                    if later(peeled, 2):
                        act.wait_ge(scored, n * E - E)
                    act.activation(u2[0][:, s, :, :], u[:, s, :, :], ACT.Copy).then_inc(u_hi, 1)

                def values_and_gelu(n, s, peeled):
                    act.wait_ge(vs[s], (n - s) * 8 + 16)
                    if later(peeled, 2):
                        act.wait_ge(outed, n * outs - outs)
                    act.activation(v2[0][:, s, :, :], v[:, s, :, :], ACT.Copy).then_inc(v_hi, 1)
                    for e in range(E):
                        act.wait_ge(scored, n * E + (e + 1))
                        if later(peeled, 1):
                            act.wait_ge(weighted, n * E + (e - 1))
                        act.activation(a[:, e, :], K.ps[e][:, 0:tw], ACT.Gelu_apprx_tanh).then_inc(gelued, 1)
                steps(act, split_u, values_and_gelu)

            @block.vector
            def _(dve):
                def weigh(n, s, peeled):
                    dve.wait_ge(v_hi, n + 1)
                    dve.tensor_tensor(v2[1][:, s, :, :], v[:, s, :, :], v2[0][:, s, :, :].bitcast(F32), ALU.subtract).then_inc(v_lo, 1)
                    dve.wait_ge(gs[s], (n - s) * 8 + 16)
                    if later(peeled, 2):
                        dve.wait_ge(outed, n * outs - outs)
                    for e in range(E):
                        dve.wait_ge(gelued, n * E + (e + 1))
                        av = a[:, e, :].rearrange("p (b t) -> p b t", t=64)
                        dve.tensor_tensor(av, av, g[:, s, :, e * 64:(e + 1) * 64], ALU.mult).then_inc(a_step, 1)
                        dve.wait_ge(a_step, n * (2 * E) + (2 * e + 1))
                        dve.tensor_copy(a2[0][:, s, e, :], a[:, e, :]).then_inc(a_step, 1)
                        dve.wait_ge(a_step, n * (2 * E) + (2 * e + 2))
                        dve.tensor_tensor(a2[1][:, s, e, :], a[:, e, :], a2[0][:, s, e, :].bitcast(F32), ALU.subtract).then_inc(weighted, 1)

                def gather(n, s, peeled):
                    for o in range(outs):
                        t, c = divmod(o, 2)
                        dve.wait_ge(outed, n * outs + (o + 1))
                        dst = acc[:, t, c * 512:(c + 1) * 512]
                        if not later(peeled, 1):
                            dve.tensor_copy(dst, K.ps[2 + o % 4][:, :]).then_inc(added, 1)
                        else:
                            dve.wait_ge(added, n * outs + (o + 1 - outs))
                            dve.tensor_tensor(dst, dst, K.ps[2 + o % 4][:, :], ALU.add).then_inc(added, 1)
                steps(dve, weigh, gather)


def branch_inputs(K, l, hT, tiles, streams, qk, vones, gates, osig, y, gm, ft):
    nc = K.nc
    s0, ns = streams[0], len(streams)
    t0 = s0 * CTX
    all_tiles = [0, 1, 2, 3]
    with ExitStack() as mem:
        def sb(name, shape):
            return mem.enter_context(nc.sbuf_tensor(f"bi_{name}{l}", shape, F32))
        padded = sb("padded", [P, 4, 2, CTX + 2])
        a, b = sb("a", [P, 2, 2, CTX + 2 * PAD]), sb("b", [P, 2, 2, CTX])
        cw, cb = sb("cw", [P, 4, 3]), sb("cb", [P, 4])
        w, wb = sb("w", [P, 2, CV_K]), sb("wb", [P, 2])
        with stage(K) as (block,):
            @block.vector
            def _(dve):
                dve.memset(padded[:, :, :, 0:1], 0.0)
                dve.memset(padded[:, :, :, CTX + 1:CTX + 2], 0.0)
                dve.memset(a[:, :, :, :], 0.0)
                dve.memset(vones[:, :, :, DH:DH + 1], 1.0)
        load(K, (cw[:, :, :], K.dram["ml_conv_w"][l]), (cb[:, :], K.dram["ml_conv_b"][l]),
             (w[:, :, :], K.dram["cv_dw_w"][l]), (wb[:, :], K.dram["cv_dw_b"][l]))

        def by_stream(ap, n):
            return ap.rearrange("p (s t) -> p s t", s=n)

        def qk_conv(dve, chain, o):
            j = o // P
            dst = by_stream(qk[:, j, :], 2)
            chain(dve.tensor_scalar(dst, padded[:, j, :, 0:CTX], cw[:, j, 0:1], cb[:, j:j + 1], ALU.mult, ALU.add))
            chain(dve.scalar_tensor_tensor(out=dst, in0=padded[:, j, :, 1:CTX + 1], scalar=cw[:, j, 1:2], in1=dst,
                                           op0=ALU.mult, op1=ALU.add))
            return dve.scalar_tensor_tensor(out=dst, in0=padded[:, j, :, 2:CTX + 2], scalar=cw[:, j, 2:3], in1=dst,
                                            op0=ALU.mult, op1=ALU.add)

        def qk_silu(act, o):
            act.activation(qk[:, o // P, :], qk[:, o // P, :], ACT.Silu)

        def cv_in(eng, chain, psum, o, t):
            j, src = o // P, by_stream(psum, ns)
            if j < 2:
                return eng.activation(a[:, j, s0:2, PAD:PAD + CTX], src, ACT.Copy)
            return eng.activation(b[:, j - 2, s0:2, :], src, ACT.Sigmoid)

        def cv_conv(dve, chain, o):
            j = o // P - 2
            if j < 0:
                return None
            mid = a[:, j, s0:2, PAD:PAD + CTX]
            dst = by_stream(y[:, j, t0:TALL], ns)
            chain(dve.tensor_tensor(mid, mid, b[:, j, s0:2, :], ALU.mult))
            chain(dve.tensor_scalar(dst, a[:, j, s0:2, 0:CTX], w[:, j, 0:1], wb[:, j:j + 1], ALU.mult, ALU.add))
            for tap in range(1, CV_K):
                ins = dve.scalar_tensor_tensor(out=dst, in0=a[:, j, s0:2, tap:tap + CTX], scalar=w[:, j, tap:tap + 1],
                                               in1=dst, op0=ALU.mult, op1=ALU.add)
                if tap < CV_K - 1:
                    chain(ins)
            return ins

        def v_and_gates(eng, chain, psum, o, t):
            eng.activation(vones[:, t, :, 0:DH], psum[:, 0:MIX].rearrange("p (h d) -> p h d", h=4), ACT.Copy)
            return eng.activation(gates[:, t, :], psum[:, MIX:MIX + 16], ACT.Copy)

        def qk_in(eng, chain, psum, o, t):
            return eng.activation(padded[:, o // P, :, 1:CTX + 1], by_stream(psum, 2), ACT.Copy)
        project(K, K.dram["w_in"][l], KD, hT, [
            (0, 2 * MIX, True, (0, TALL), qk_in, (qk_conv, qk_silu)),
            (CV_OFF, 2 * MIX, True, (t0, TALL), cv_in, (cv_conv, None)),
            (V_OFF, MIX + 16, False, all_tiles, v_and_gates),
            (GM_OFF, 2 * MIX, False, tiles, copy_to(lambda o, t: gm[:, t, o:o + 256], ACT.Gelu_apprx_tanh)),
            (FT_OFF, MIX, False, tiles, copy_to(lambda o, t: ft[:, t, :])),
            (O_OFF, MIX, False, tiles, copy_to(lambda o, t: osig[:, t, :], ACT.Sigmoid))], width=MIX + 16, ring=2)


def first_layer(K, l, x, s_cols):
    nc = K.nc
    last = l == DEPTH - 1
    all_tiles = [0, 1, 2, 3]
    tiles = [2, 3] if last else all_tiles
    streams = [1] if last else [0, 1]
    t0 = tiles[0] * P
    with ExitStack() as mem:
        def sb(name, shape, scope=mem):
            return scope.enter_context(nc.sbuf_tensor(f"{name}_l{l}", shape, F32))
        mod5 = sb("mod5", [P, 2, D])
        hT = tuple(mem.enter_context(nc.sbuf_tensor(f"hT{h}_l{l}", [P, KD, TALL], F32R)) for h in ("hi", "lo"))
        late = ExitStack()
        mod234 = sb("mod234", [P, 3, 2, D], late)
        with nc.sbuf_tensor(f"mod01_l{l}", [P, 2, 2, D], F32) as mod01, nc.sbuf_tensor(f"h_l{l}", [P, 4, D], F32) as h:
            mod = [mod01[:, 0], mod01[:, 1], mod234[:, 0], mod234[:, 1], mod234[:, 2], mod5[:, :, :]]
            modulation(K, l, s_cols, mod)
            rms_norm(K, x, all_tiles, lambda t: mod[1][:, t // 2, :], lambda t: mod[0][:, t // 2, :], h, hT)
        mix = ExitStack()
        zTs = sb("zTs", [P, 4, 2, TALL], mix)
        with ExitStack() as rows:
            qk, vones = sb("qk", [P, 4, TALL], rows), sb("vones", [P, 4, 4, DH + 1], rows)
            gates, osig = sb("gates", [P, 4, 16], rows), sb("osig", [P, 4, MIX], rows)
            y = sb("conv_y", [P, 2, TALL], rows)
            gm, ft = sb("gm", [P, 4, 2 * MIX], rows), sb("ft", [P, 4, MIX], rows)
            branch_inputs(K, l, hT, tiles, streams, qk, vones, gates, osig, y, gm, ft)
            gmlp(K, l, zTs[:, 1], gm, tiles)
            fourier(K, l, zTs[:, 3], ft, streams)
            conv_branch(K, l, zTs[:, 2], y, streams)
            mlstm(K, l, zTs[:, 0], last, qk, vones, gates, osig)
        yT = sb("yT", [P, KD, TALL], mix)
        merge(K, l, hT, zTs, yT, t0)
        project(K, K.dram["w_out"][l], KD, yT, [(0, D, False, tiles, add_scaled(K, x, lambda t: mod[2][:, t // 2, :]))],
                width=512, ring=2, engine="vector")
        mix.close()
        with nc.sbuf_tensor(f"h2_l{l}", [P, 4, D], F32) as h:
            rms_norm(K, x, tiles, lambda t: mod[4][:, t // 2, :], lambda t: mod[3][:, t // 2, :], h, hT)
        late.close()
        with nc.sbuf_tensor(f"choice_l{l}", [P, 3, TALL], F32) as choice:
            with nc.sbuf_tensor(f"top_l{l}", [P, len(tiles), 16, TOPK], F32) as top, \
                    nc.sbuf_tensor(f"topi_l{l}", [P, len(tiles), 16, TOPK], U32) as topi:
                key_scores(K, l, hT, t0, top, topi)
                expert_choice(K, l, top, topi, tiles, choice)
            spread_choice(K, l, choice, t0, TALL - t0)
        with nc.sbuf_tensor(f"peer_l{l}", [P, len(tiles), D], F32) as acc:
            experts(K, l, hT, acc, t0, TALL - t0)
            with stage(K, "step") as (block, step):
                @block.vector
                def _(dve):
                    chain = Chain(dve, step)
                    for i, t in enumerate(tiles):
                        chain(dve.tensor_tensor(acc[:, i, :], acc[:, i, :], mod[5][:, t // 2, :], ALU.mult))
                        dve.tensor_tensor(x[:, t, :], x[:, t, :], acc[:, i, :], ALU.add)



def products(K, jobs, evacuate):
    with stage(K, "done", "step") as (block, done, step):
        @block.tensor
        def _(pe):
            for i, (lhsT, rhs) in enumerate(jobs):
                last = pe.matmul(K.ps[i // 4][:, (i % 4) * P:(i % 4 + 1) * P], lhsT, rhs, start=True, stop=True)
                if i % 4 == 3:
                    last.then_inc(done, 1)

        @block.vector
        def _(dve):
            chain = Chain(dve, step)
            for half in range(len(jobs) // 4):
                dve.wait_ge(done, half + 1)
                evacuate(dve, chain, half, K.ps[half][:, :].rearrange("p (h c) -> p h c", h=4))


def gated_delta(K, j, qkv, ba, z, cat):
    nc = K.nc
    with ExitStack() as mem:
        def sb(name, shape, scope=mem):
            return scope.enter_context(nc.sbuf_tensor(f"gd_{name}", shape, F32))
        beta, g = sb("beta", [P, 2, GH]), sb("g", [P, 2, GH])
        par = sb("par", [P, 3, GH])
        soft = sb("soft", [P, 2, GH])
        gcs = sb("gcs", [P, 2, 2, GH])
        eg = sb("eg", [P, 2, GH])
        kd = sb("kd", [P, 2, GH])
        gain = sb("gain", [P, P])
        load(K, (par[:, 0, :], K.dram["gdn_a_log"][j:j + 1, :].broadcast_to([P, GH])),
             (par[:, 1, :], K.dram["gdn_dt_bias"][j:j + 1, :].broadcast_to([P, GH])),
             (gain[:, :], K.dram["gdn_norm_w"][j:j + 1, :].broadcast_to([P, P])))
        with stage(K, "step", "biased", "act_step") as (block, step, biased, act_step):
            @block.vector
            def _(dve):
                chain = Chain(dve, step)
                dve.tensor_tensor(g[:, :, :], ba[:, :, GH:2 * GH], par[:, 1, :][:, None, :].broadcast_to([P, 2, GH]), ALU.add).then_inc(biased, 1)
                dve.wait_ge(act_step, 5)
                chain(dve.tensor_single_scalar(g[:, :, :], g[:, :, :], 0.0, ALU.max))
                chain(dve.tensor_tensor(g[:, :, :], g[:, :, :], soft[:, :, :], ALU.add))
                chain(dve.tensor_tensor(g[:, :, :], g[:, :, :], par[:, 2, :][:, None, :].broadcast_to([P, 2, GH]), ALU.mult))
                dve.tensor_single_scalar(g[:, :, :], g[:, :, :], -1.0, ALU.mult)

            @block.scalar
            def _(act):
                chain = Chain(act, act_step)
                chain(act.activation(beta[:, :, :], ba[:, :, 0:GH], ACT.Sigmoid))
                chain(act.activation(par[:, 2, :], par[:, 0, :], ACT.Exp))
                act.wait_ge(biased, 1)
                chain(act.activation(soft[:, :, :], g[:, :, :], ACT.Abs))
                chain(act.activation(soft[:, :, :], soft[:, :, :], ACT.Exp, scale=-1.0))
                chain(act.activation(soft[:, :, :], soft[:, :, :], ACT.Ln, bias=1.0))
        n_u = 2 * GH
        with nc.sbuf_tensor("gd_sq", [P, n_u, T1], F32) as sq, nc.sbuf_tensor("gd_unit", [P, n_u, n_u], F32) as unit, \
                nc.sbuf_tensor("gd_inv_norm", [n_u, T1], F32) as inv_norm:
            load(K, (unit[:, :, :], K.dram["c_unit16"]))
            with stage(K, "squared", "summed") as (block, squared, summed):
                @block.scalar
                def _(act):
                    for i in range(0, n_u, 4):
                        act.activation(sq[:, i:i + 4, :], qkv[:, i:i + 4, :], ACT.Square).then_inc(squared, 1)

                @block.tensor
                def _(pe):
                    for i in range(n_u):
                        pe.wait_ge(squared, i // 4 + 1)
                        last = pe.matmul(K.ps[0][0:n_u, 0:T1], unit[:, i, :], sq[:, i, :], start=i == 0, stop=i == n_u - 1)
                    last.then_inc(summed, 1)

                @block.vector
                def _(dve):
                    dve.wait_ge(summed, 1)
                    dve.tensor_copy(inv_norm[:, :], K.ps[0][0:n_u, 0:T1])
            inverse_root(K, inv_norm[:, :], EPS)
            with stage(K, "spread") as (block, spread):
                @block.tensor
                def _(pe):
                    for i in range(n_u):
                        ins = pe.matmul(K.ps[i // 2][:, (i % 2) * T1:(i % 2 + 1) * T1], K.ident[0:n_u, i:i + 1].broadcast_to([n_u, P]),
                                        inv_norm[:, :], start=True, stop=True)
                        if i % 2:
                            ins.then_inc(spread, 1)

                @block.vector
                def _(dve):
                    for i in range(n_u // 2):
                        dve.wait_ge(spread, i + 1)
                        dve.tensor_tensor(qkv[:, 2 * i:2 * i + 2, :], qkv[:, 2 * i:2 * i + 2, :],
                                          K.ps[i][:, :].rearrange("p (u t) -> p u t", u=2), ALU.mult)
        ktok, vtok = sb("ktok", [P, 2, GH, P]), sb("vtok", [P, 2, GH, P])
        transpose(K, [([qkv[:, base + 4 * q + i, t * P:(t + 1) * P] for i in range(4)], dst[:, t, 4 * q:4 * q + 4, :])
                      for base, dst in ((GH, ktok), (2 * GH, vtok)) for t in range(2) for q in range(2)])
        with stage(K, "summed", "copied") as (block, summed, copied):
            @block.tensor
            def _(pe):
                for t in range(2):
                    pe.matmul(K.ps[0][:, t * GH:(t + 1) * GH], K.tri[:, :], g[:, t, :], start=True, stop=True)
                    last = pe.matmul(K.ps[0][:, (2 + t) * GH:(3 + t) * GH], K.ones[:, :], g[:, t, :], start=True, stop=True)
                last.then_inc(summed, 1)

            @block.vector
            def _(dve):
                dve.wait_ge(summed, 1)
                dve.tensor_copy(gcs[:, :, :, :], K.ps[0][:, 0:4 * GH].rearrange("p (a t h) -> p a t h", a=2, t=2)).then_inc(copied, 1)
                dve.wait_ge(copied, 1)
                dve.tensor_tensor(kd[:, :, :], gcs[:, 1, :, :], gcs[:, 0, :, :], ALU.subtract).then_inc(copied, 1)

            @block.scalar
            def _(act):
                act.wait_ge(copied, 2)
                act.activation(eg[:, :, :], gcs[:, 0, :, :], ACT.Exp)
                act.activation(kd[:, :, :], kd[:, :, :], ACT.Exp)
        low, att = sb("low", [P, 4, 4, P]), sb("att", [P, 4, 4, P])
        masks = sb("masks", [P, 2, P])
        load(K, (masks[:, :, :], K.dram["gd_masks"]))
        with stage(K, "pe_done", "ranged", "exped", "read") as (block, pe_done, ranged, exped, read):
            @block.tensor
            def _(pe):
                for n in range(4):
                    t, hg = divmod(n, 2)
                    if n >= 2:
                        pe.wait_ge(read, n - 1)
                    b = 3 * (n % 2)
                    for i in range(4):
                        h = 4 * hg + i
                        cols = slice(i * P, (i + 1) * P)
                        kT, qT = qkv[:, GH + h, t * P:(t + 1) * P], qkv[:, h, t * P:(t + 1) * P]
                        pe.matmul(K.ps[b][:, cols], g[:, t, h:h + 1].broadcast_to([P, P]), K.tri[:, :], start=True, stop=True)
                        pe.matmul(K.ps[b + 1][:, cols], kT, kT, start=True, stop=True)
                        last = pe.matmul(K.ps[b + 2][:, cols], kT, qT, start=True, stop=True)
                    last.then_inc(pe_done, 1)

            @block.vector
            def _(dve):
                for n in range(4):
                    t, hg = divmod(n, 2)
                    dve.wait_ge(pe_done, n + 1)
                    b = 3 * (n % 2)
                    for i in range(4):
                        h = 4 * hg + i
                        row = K.ps[b][:, i * P:(i + 1) * P]
                        dve.scalar_tensor_tensor(out=low[:, n, i, :], in0=row, scalar=gcs[:, 0, t, h:h + 1], in1=masks[:, 0, :],
                                                 op0=ALU.subtract, op1=ALU.max)
                        last = dve.scalar_tensor_tensor(out=att[:, n, i, :], in0=row, scalar=gcs[:, 0, t, h:h + 1], in1=masks[:, 1, :],
                                                        op0=ALU.subtract, op1=ALU.min)
                    last.then_inc(ranged, 1)
                    dve.wait_ge(exped, n + 1)
                    view = [K.ps[b + 1 + i][:, :].rearrange("p (h c) -> p h c", h=4) for i in range(2)]
                    dve.tensor_tensor(low[:, n, :, :], low[:, n, :, :], view[0], ALU.mult)
                    dve.scalar_tensor_tensor(out=att[:, n, :, :], in0=view[1], scalar=SCALE, in1=att[:, n, :, :],
                                             op0=ALU.mult, op1=ALU.mult).then_inc(read, 1)
                    dve.wait_ge(read, n + 1)
                    dve.tensor_tensor(low[:, n, :, :], low[:, n, :, :],
                                      beta[:, t, 4 * hg:4 * hg + 4][:, :, None].broadcast_to([P, 4, P]), ALU.mult)

            @block.scalar
            def _(act):
                for n in range(4):
                    act.wait_ge(ranged, n + 1)
                    act.activation(low[:, n, :, :], low[:, n, :, :], ACT.Exp, scale=-1.0)
                    act.activation(att[:, n, :, :], att[:, n, :, :], ACT.Exp).then_inc(exped, 1)
        inv_t = sb("inv_t", [P, 4, 4, P])
        with ExitStack() as solve:
            inv = sb("inv", [P, 4, 4, P], solve)
            part, mid = sb("part", [P, 4, 4, P], solve), sb("mid", [P, 4, 4, P], solve)
            level = sb("level", [P, 7, P], solve)
            load(K, (level[:, :, :], K.dram["gd_levels"]))
            with stage(K) as (block,):
                @block.vector
                def _(dve):
                    for n in range(4):
                        dve.tensor_copy(inv[:, n, :, :], K.ident[:, None, :].broadcast_to([P, 4, P]))

                @block.scalar
                def _(act):
                    for n in range(4):
                        act.activation(inv_t[:, n, :, :], K.ident[:, None, :].broadcast_to([P, 4, P]), ACT.Copy)
            with stage(K, "parted", "mid_psum", "mid_copied", "joined", "subbed") as (block, parted, mid_psum, mid_copied, joined, subbed):
                @block.gpsimd
                def _(pool):
                    for m in range(28):
                        lv, n = divmod(m, 4)
                        if m >= 4:
                            pool.wait_ge(mid_psum, m - 3)
                        pool.tensor_tensor(part[:, n, :, :], low[:, n, :, :], level[:, lv, :][:, None, :].broadcast_to([P, 4, P]),
                                           ALU.mult).then_inc(parted, 1)

                @block.tensor
                def _(pe):
                    for lv in range(7):
                        for n in range(4):
                            m = 4 * lv + n
                            pe.wait_ge(parted, m + 1)
                            if m >= 4:
                                pe.wait_ge(subbed, m - 3)
                            for i in range(4):
                                last = pe.matmul(K.ps[n][:, i * P:(i + 1) * P], part[:, n, i, :], inv_t[:, n, i, :], start=True, stop=True)
                            last.then_inc(mid_psum, 1)
                        for n in range(4):
                            m = 4 * lv + n
                            pe.wait_ge(mid_copied, m + 1)
                            if m >= 2:
                                pe.wait_ge(subbed, m - 1)
                            b = 4 + 2 * (n % 2)
                            for i in range(4):
                                pe.matmul(K.ps[b][:, i * P:(i + 1) * P], inv[:, n, i, :], mid[:, n, i, :], start=True, stop=True)
                                last = pe.matmul(K.ps[b + 1][:, i * P:(i + 1) * P], mid[:, n, i, :], inv[:, n, i, :], start=True, stop=True)
                            last.then_inc(joined, 1)

                @block.scalar
                def _(act):
                    for m in range(28):
                        n = m % 4
                        act.wait_ge(mid_psum, m + 1)
                        if m >= 4:
                            act.wait_ge(joined, m - 3)
                        act.activation(mid[:, n, :, :], K.ps[n][:, :].rearrange("p (h c) -> p h c", h=4), ACT.Copy).then_inc(mid_copied, 1)

                @block.vector
                def _(dve):
                    for m in range(28):
                        n = m % 4
                        b = 4 + 2 * (n % 2)
                        dve.wait_ge(joined, m + 1)
                        if m >= 4:
                            dve.wait_ge(subbed, m - 3)
                        dve.tensor_tensor(inv_t[:, n, :, :], inv_t[:, n, :, :], K.ps[b][:, :].rearrange("p (h c) -> p h c", h=4), ALU.subtract)
                        dve.tensor_tensor(inv[:, n, :, :], inv[:, n, :, :], K.ps[b + 1][:, :].rearrange("p (h c) -> p h c", h=4),
                                          ALU.subtract).then_inc(subbed, 1)
        vb, vnew = sb("vb", [P, 2, GH, P]), sb("vnew", [P, 2, GH, P])
        state = sb("state", [P, GH, P])
        o = sb("o", [P, 2, GH, P])

        def over(ap, half):
            return ap[:, 4 * half:4 * half + 4][:, :, None].broadcast_to([P, 4, P])
        with stage(K) as (block,):
            @block.vector
            def _(dve):
                for half in range(2):
                    hs = slice(4 * half, 4 * half + 4)
                    dve.tensor_tensor(vb[:, 0, hs, :], vtok[:, 0, hs, :], over(beta[:, 0, :], half), ALU.mult)
                    dve.tensor_tensor(ktok[:, 0, hs, :], ktok[:, 0, hs, :], over(kd[:, 0, :], half), ALU.mult)

        def copy_into(dst):
            def evacuate(dve, chain, half, psum):
                dve.tensor_copy(dst[:, 4 * half:4 * half + 4, :], psum)
            return evacuate
        heads = range(GH)
        products(K, [(inv_t[:, h // 4, h % 4, :], vb[:, 0, h, :]) for h in heads], copy_into(vnew[:, 0]))
        products(K, [(ktok[:, 0, h, :], vnew[:, 0, h, :]) for h in heads], copy_into(state))

        def residual(dve, chain, half, psum):
            hs = slice(4 * half, 4 * half + 4)
            r = vb[:, 1, hs, :]
            chain(dve.tensor_tensor(r, psum, over(eg[:, 1, :], half), ALU.mult))
            chain(dve.tensor_tensor(r, vtok[:, 1, hs, :], r, ALU.subtract))
            chain(dve.tensor_tensor(r, r, over(beta[:, 1, :], half), ALU.mult))
        products(K, [(qkv[:, GH + h, P:2 * P], state[:, h, :]) for h in heads], residual)
        products(K, [(inv_t[:, 2 + h // 4, h % 4, :], vb[:, 1, h, :]) for h in heads], copy_into(vnew[:, 1]))
        for t in range(2):
            products(K, [(att[:, 2 * t + h // 4, h % 4, :], vnew[:, t, h, :]) for h in heads], copy_into(o[:, t]))

        def from_state(dve, chain, half, psum):
            hs = slice(4 * half, 4 * half + 4)
            chain(dve.scalar_tensor_tensor(out=vb[:, 0, hs, :], in0=psum, scalar=SCALE, in1=over(eg[:, 1, :], half),
                                           op0=ALU.mult, op1=ALU.mult))
            dve.tensor_tensor(o[:, 1, hs, :], o[:, 1, hs, :], vb[:, 0, hs, :], ALU.add)
        products(K, [(qkv[:, h, P:2 * P], state[:, h, :]) for h in heads], from_state)
        ss = K.small[:, 0:16].rearrange("p (t h) -> p t h", t=2)
        with stage(K, "step") as (block, step):
            @block.vector
            def _(dve):
                chain = Chain(dve, step)
                for t in range(2):
                    chain(dve.tensor_tensor(vb[:, t, :, :], o[:, t, :, :], o[:, t, :, :], ALU.mult))
                    chain(dve.tensor_reduce(ss[:, t, :], vb[:, t, :, :], AX.X, ALU.add))
                dve.tensor_single_scalar(ss[:, :, :], ss[:, :, :], 1.0 / P, ALU.mult)
        inverse_root(K, K.small[:, 0:16], EPS)
        with stage(K, "step") as (block, step):
            @block.vector
            def _(dve):
                chain = Chain(dve, step)
                for t in range(2):
                    ov = o[:, t, :, :]
                    chain(dve.tensor_tensor(ov, ov, ss[:, t, :][:, :, None].broadcast_to([P, GH, P]), ALU.mult))
                    chain(dve.tensor_tensor(ov, ov, gain[:, None, :].broadcast_to([P, GH, P]), ALU.mult))
                    dve.tensor_tensor(cat[:, t, 0:D].rearrange("p (h c) -> p h c", h=GH), ov,
                                      z[:, t, :].rearrange("p (h c) -> p h c", h=GH), ALU.mult)


def attend(K, items, scale):
    nc = K.nc
    N = len(items)
    K.uid += 1
    with ExitStack() as mem:
        def sb(name, shape):
            return mem.enter_context(nc.sbuf_tensor(f"at_{name}{K.uid}", shape, F32))
        sc, pr, pt = sb("sc", [P, 2, T1]), sb("pr", [P, 2, T1]), sb("pt", [P, 2, T1])
        neg_max, total, weight = sb("max", [P, N]), sb("total", [P, N]), sb("weight", [P, N])
        out_tmp = sb("tmp", [P, 2, P])
        with stage(K, "scored", "scaled", "maxed", "exped", "turned", "pt_ready", "outed", "finished", "step") as \
                (block, scored, scaled, maxed, exped, turned, pt_ready, outed, finished, step):
            @block.tensor
            def _(pe):
                def score(n):
                    q, k = items[n][0:2]
                    if n >= 2:
                        pe.wait_ge(scaled, n - 1)
                    pe.matmul(K.ps[n % 2][:, 0:k.shape[1]], q, k, start=True, stop=True).then_inc(scored, 1)

                score(0)
                for n in range(N):
                    if n + 1 < N:
                        score(n + 1)
                    width = items[n][1].shape[1]
                    pe.wait_ge(exped, n + 1)
                    if n >= 2:
                        pe.wait_ge(pt_ready, n - 1)
                    for c in range(width // P):
                        last = pe.transpose(K.ps[2 + n % 2][:, c * P:(c + 1) * P], pr[:, n % 2, c * P:(c + 1) * P], K.ident[:, :])
                    last.then_inc(turned, 1)
                    pe.wait_ge(pt_ready, n + 1)
                    if n >= 2:
                        pe.wait_ge(finished, n - 1)
                    for c, v in enumerate(items[n][3]):
                        last = pe.matmul(K.ps[4 + n % 2][:, 0:P], pt[:, n % 2, c * P:(c + 1) * P], v, start=c == 0, stop=c == width // P - 1)
                    last.then_inc(outed, 1)

            @block.scalar
            def _(act):
                for n in range(N):
                    width = items[n][1].shape[1]
                    act.wait_ge(maxed, n + 1)
                    if n >= 2:
                        act.wait_ge(turned, n - 1)
                    act.activation(pr[:, n % 2, 0:width], sc[:, n % 2, 0:width], ACT.Exp, bias=neg_max[:, n:n + 1],
                                   accum_out=total[:, n:n + 1]).then_inc(exped, 1)
                    act.wait_ge(turned, n + 1)
                    if n >= 2:
                        act.wait_ge(outed, n - 1)
                    act.activation(pt[:, n % 2, 0:width], K.ps[2 + n % 2][:, 0:width], ACT.Copy).then_inc(pt_ready, 1)

            @block.vector
            def _(dve):
                chain = Chain(dve, step)

                def head(n):
                    bias = items[n][2]
                    width = items[n][1].shape[1]
                    dve.wait_ge(scored, n + 1)
                    if n >= 2:
                        dve.wait_ge(exped, n - 1)
                    s = sc[:, n % 2, 0:width]
                    if bias is None:
                        dve.tensor_single_scalar(s, K.ps[n % 2][:, 0:width], scale, ALU.mult).then_inc(scaled, 1)
                    else:
                        dve.scalar_tensor_tensor(out=s, in0=K.ps[n % 2][:, 0:width], scalar=scale, in1=bias,
                                                 op0=ALU.mult, op1=ALU.add).then_inc(scaled, 1)
                    dve.wait_ge(scaled, n + 1)
                    dve.tensor_reduce(neg_max[:, n:n + 1], s, AX.X, ALU.max, negate=True).then_inc(maxed, 1)

                head(0)
                for n in range(N):
                    if n + 1 < N:
                        head(n + 1)
                    out, gate, add = items[n][4:7]
                    dve.wait_ge(outed, n + 1)
                    chain(dve.reciprocal(weight[:, n:n + 1], total[:, n:n + 1]))
                    if gate is not None:
                        chain(dve.tensor_tensor(weight[:, n:n + 1], weight[:, n:n + 1], gate, ALU.mult))
                    if add:
                        dve.scalar_tensor_tensor(out=out, in0=K.ps[4 + n % 2][:, 0:P], scalar=weight[:, n:n + 1], in1=out,
                                                 op0=ALU.mult, op1=ALU.add).then_inc(finished, 1)
                    else:
                        dve.tensor_scalar(out, K.ps[4 + n % 2][:, 0:P], weight[:, n:n + 1], None, ALU.mult).then_inc(finished, 1)


def memory_attention(K, l, mem_rows, qmT, cat):
    nc = K.nc
    with ExitStack() as mem:
        def sb(name, shape):
            return mem.enter_context(nc.sbuf_tensor(f"ma_{name}{l}", shape, F32))
        mT = tuple(mem.enter_context(nc.sbuf_tensor(f"ma_mT{h}{l}", [P, KD, T1], F32R)) for h in ("hi", "lo"))
        with nc.sbuf_tensor(f"ma_gain{l}", [P, D], F32) as gain, nc.sbuf_tensor(f"ma_h{l}", [P, 2, D], F32) as h:
            load(K, (gain[:, :], K.dram["mem_norm_w"][l:l + 1, :].broadcast_to([P, D])))
            rms_norm(K, mem_rows, [0, 1], lambda t: gain[:, :], None, h, mT)
        kT, v = sb("kT", [P, MEM_H, T1]), sb("v", [P, 2, MEM_W])
        project(K, K.dram["mem_w_kv"][l], KD, mT, [
            (0, MEM_W, True, (0, T1), copy_to(lambda o, t: kT[:, o // P, :])),
            (MEM_W, MEM_W, False, [0, 1], copy_to(lambda o, t: v[:, t, o:o + 256]))])
        attend(K, [(qmT[:, h, t * P:(t + 1) * P], kT[:, h, :], None, [v[:, m, h * P:(h + 1) * P] for m in range(2)],
                    cat[:, t, D + h * P:D + (h + 1) * P], None, False) for h in range(MEM_H) for t in range(2)], SCALE)


def gdn_layer(K, l, j, hT, cat, qmT):
    nc = K.nc
    with ExitStack() as mem:
        def sb(name, shape, scope=mem):
            return scope.enter_context(nc.sbuf_tensor(f"gl_{name}", shape, F32))
        qkv = sb("qkv", [P, 3 * GH, T1])
        ba, z = sb("ba", [P, 2, 2 * GH]), sb("z", [P, 2, D])
        with ExitStack() as conv:
            padded = sb("padded", [P, 3 * GH, T1 + 3], conv)
            w = sb("w", [P, 3 * GH, 4], conv)
            load(K, (w[:, :, :], K.dram["gdn_conv_w"][j]))
            with stage(K) as (block,):
                @block.vector
                def _(dve):
                    dve.memset(padded[:, :, 0:3], 0.0)

            def conv_taps(dve, chain, o):
                i = o // P
                dst = qkv[:, i, :]
                chain(dve.tensor_scalar(dst, padded[:, i, 0:T1], w[:, i, 0:1], None, ALU.mult))
                for tap in range(1, 4):
                    ins = dve.scalar_tensor_tensor(out=dst, in0=padded[:, i, tap:tap + T1], scalar=w[:, i, tap:tap + 1], in1=dst,
                                                   op0=ALU.mult, op1=ALU.add)
                    if tap < 3:
                        chain(ins)
                return ins

            def conv_silu(act, o):
                act.activation(qkv[:, o // P, :], qkv[:, o // P, :], ACT.Silu)

            def last_z_and_ba(eng, chain, psum, o, t):
                eng.activation(z[:, t, D - 256:D], psum[:, 0:256], ACT.Silu)
                return eng.activation(ba[:, t, :], psum[:, 256:256 + 2 * GH], ACT.Copy)
            project(K, K.dram["gdn_w_in"][j], KD, hT,
                    [(0, 3 * D, True, (0, T1), copy_to(lambda o, t: padded[:, o // P, 3:T1 + 3]), (conv_taps, conv_silu))] +
                    [(3 * D, D - 256, False, [0, 1], copy_to(lambda o, t: z[:, t, o:o + 256], ACT.Silu)),
                     (4 * D - 256, 256 + 2 * GH, False, [0, 1], last_z_and_ba),
                     (4 * D + 2 * GH, MEM_W, True, (0, T1), copy_to(lambda o, t: qmT[:, o // P, :]))], lo_on="vector", width=256 + 2 * GH)
        gated_delta(K, j, qkv, ba, z, cat)


def sparse_attention(K, j, hT, cat, qmT):
    nc = K.nc
    with ExitStack() as mem:
        def sb(name, shape, scope=mem):
            return scope.enter_context(nc.sbuf_tensor(f"ns_{name}", shape, F32))
        qT = sb("qT", [P, GH, T1])
        kvT = sb("kvT", [P, 4, 2, T1])
        vtok = sb("vtok", [P, 2, 2, KV_W])
        gates = sb("gates", [P, 2, 3 * GH])

        def kv(n):
            return copy_to(lambda o, t: kvT[:, n, o // P, :])
        base = D

        def window_v_and_gates(eng, chain, psum, o, t):
            eng.activation(vtok[:, 1, t, :], psum[:, 0:KV_W], ACT.Copy)
            return eng.activation(gates[:, t, :], psum[:, KV_W:KV_W + 3 * GH], ACT.Sigmoid)
        project(K, K.dram["nsa_w_in"][j], KD, hT,
                [(0, D, True, (0, T1), copy_to(lambda o, t: qT[:, o // P, :]))] +
                [(base + i * KV_W, KV_W, True, (0, T1), kv(n)) for i, n in ((0, 0), (1, 1), (2, 2), (4, 3))] +
                [(base + 3 * KV_W, KV_W, False, [0, 1], copy_to(lambda o, t: vtok[:, 0, t, :])),
                 (base + 5 * KV_W, KV_W + 3 * GH, False, [0, 1], window_v_and_gates),
                 (base + 6 * KV_W + 3 * GH, MEM_W, True, (0, T1), copy_to(lambda o, t: qmT[:, o // P, :]))], width=KV_W + 3 * GH)
        rel = sb("rel", [32, GH])
        bias = sb("bias", [P, GH, T1])
        W = 3 * P
        with ExitStack() as tmp:
            hot = sb("hot", [32, W], tmp)
            wide = sb("wide", [P, GH, W], tmp)
            causal = sb("causal", [P, P], tmp)
            load(K, (rel[:, :], K.dram["rel_bias"]), (hot[:, :], K.dram["bucket_rev"]), (causal[:, :], K.dram["causal"]))
            with stage(K, "spread", "copied", "stored", "skewed") as (block, spread, copied, stored, skewed):
                @block.tensor
                def _(pe):
                    for h in range(GH):
                        pe.matmul(K.ps[h][:, 0:W], rel[:, h:h + 1].broadcast_to([32, P]), hot[:, :], start=True, stop=True).then_inc(spread, 1)

                @block.scalar
                def _(act):
                    for h in range(GH):
                        act.wait_ge(spread, h + 1)
                        act.activation(wide[:, h, :], K.ps[h][:, 0:W], ACT.Copy).then_inc(copied, 1)

                @block.sync
                def _(sp):
                    sp.wait_ge(copied, GH)
                    sp.dma_start(K.skew.rearrange("h p w -> p h w"), wide[:, :, :]).then_inc(stored, 16)
                    sp.wait_ge(stored, 16)
                    sp.dma_start(bias[:, :, :], bass.AP(K.skew.tensor, P - 1, [[W - 1, P], [P * W, GH], [1, T1]])).then_inc(skewed, 16)
                    sp.wait_ge(skewed, 16)

                @block.vector
                def _(dve):
                    dve.wait_ge(skewed, 16)
                    dve.tensor_tensor(bias[:, :, P:T1], bias[:, :, P:T1], causal[:, None, :].broadcast_to([P, GH, P]), ALU.add)
        kcT, vc = sb("kcT", [P, 2, N_CMP]), sb("vc", [N_CMP, 2, P])
        for which, (pos_in, w1_in, w2_in) in enumerate(((K.dram["pos_k"], K.dram["w1_k"], K.dram["w2_k"]), (K.dram["pos_v"], K.dram["w1_v"], K.dram["w2_v"]))):
            with ExitStack() as tmp:
                pos, w2 = sb(f"pos{which}", [P, 32], tmp), sb(f"w2{which}", [P, P], tmp)
                w1 = sb(f"w1{which}", [P, 32, P], tmp)
                blk = sb(f"blk{which}", [P, 2, 16, 2, N_CMP], tmp)
                hid = sb(f"hid{which}", [P, 2, N_CMP], tmp)
                load(K, (pos[:, :], pos_in[j]), (w2[:, :], w2_in[j]), (w1[:, :, :], w1_in[j].rearrange("(i p) n -> p i n", p=P)))
                with stage(K, "blocked", "hidden", "acted", "done") as (block, blocked, hidden, acted, done):
                    @block.vector
                    def _(dve):
                        for g in range(2):
                            src = kvT[:, which, g, :].rearrange("p (n i) -> p i n", i=16)
                            for a in range(2):
                                last = dve.tensor_tensor(blk[:, a, :, g, :], src[:, :, a:a + N_CMP],
                                                         pos[:, 16 * a:16 * a + 16][:, :, None].broadcast_to([P, 16, N_CMP]), ALU.add)
                        last.then_inc(blocked, 1)
                        dve.wait_ge(done, 1)
                        if which == 0:
                            dve.tensor_copy(kcT[:, :, :], K.ps[1][:, 0:2 * N_CMP].rearrange("p (g n) -> p g n", g=2))
                        else:
                            dve.tensor_copy(vc[:, :, :], K.ps[1][0:N_CMP, 0:2 * P].rearrange("p (g n) -> p g n", g=2))

                    @block.tensor
                    def _(pe):
                        pe.wait_ge(blocked, 1)
                        for i in range(32):
                            last = pe.matmul(K.ps[0][:, 0:2 * N_CMP], w1[:, i, :], blk[:, i // 16, i % 16, :, :].rearrange("p g n -> p (g n)"),
                                             start=i == 0, stop=i == 31)
                        last.then_inc(hidden, 1)
                        pe.wait_ge(acted, 1)
                        for g in range(2):
                            if which == 0:
                                last = pe.matmul(K.ps[1][:, g * N_CMP:(g + 1) * N_CMP], w2[:, :], hid[:, g, :], start=True, stop=True)
                            else:
                                last = pe.matmul(K.ps[1][0:N_CMP, g * P:(g + 1) * P], hid[:, g, :], w2[:, :], start=True, stop=True)
                        last.then_inc(done, 1)

                    @block.scalar
                    def _(act):
                        act.wait_ge(hidden, 1)
                        act.activation(hid[:, :, :], K.ps[0][:, 0:2 * N_CMP].rearrange("p (g n) -> p g n", g=2), ACT.Silu).then_inc(acted, 1)
        with ExitStack() as tmp:
            hot = sb("chot", [32, 2, N_CMP, P], tmp)
            cm = sb("cmask", [P, 2, 2, N_CMP], tmp)
            s = sb("cs", [P, 2, GH, 16], tmp)
            bc = sb("cb", [P, 2, GH, N_CMP], tmp)
            red = sb("cred", [P, 3, 2, GH], tmp)
            pT = sb("cpT", [N_CMP, 16, P], tmp)
            load(K, (hot[:, :, :, :], K.dram["bucket_cmp"]), (cm[:, :, :, :], K.dram["cmp_masks"]))
            with stage(K, "scored", "shifted", "exped", "step", "weighted", "turned", "copied", "outed") as \
                    (block, scored, shifted, exped, step, weighted, turned, copied, outed):
                @block.tensor
                def _(pe):
                    for t in range(2):
                        for h in range(GH):
                            c = (t * GH + h) * 16
                            pe.matmul(K.ps[0][:, c:c + N_CMP], qT[:, h, t * P:(t + 1) * P], kcT[:, h // 4, :], start=True, stop=True)
                        for n in range(N_CMP):
                            c = (t * N_CMP + n) * GH
                            last = pe.matmul(K.ps[1][:, c:c + GH], hot[:, t, n, :], rel[:, :], start=True, stop=True)
                    last.then_inc(scored, 1)
                    pe.wait_ge(weighted, 1)
                    for b in range(4):
                        for i in range(4):
                            u = 4 * b + i
                            last = pe.transpose(K.ps[2 + b][0:N_CMP, i * P:(i + 1) * P], s[:, u // GH, u % GH, 0:N_CMP], K.ident[:, :])
                        last.then_inc(turned, 1)
                    pe.wait_ge(copied, 4)
                    for b in range(4):
                        for i in range(4):
                            u = 4 * b + i
                            last = pe.matmul(K.ps[2 + b][:, i * P:(i + 1) * P], pT[:, u, :], vc[:, (u % GH) // 4, :], start=True, stop=True)
                        last.then_inc(outed, 1)

                @block.scalar
                def _(act):
                    act.wait_ge(shifted, 1)
                    act.activation(s[:, :, :, 0:N_CMP], s[:, :, :, 0:N_CMP], ACT.Exp).then_inc(exped, 1)
                    for b in range(4):
                        act.wait_ge(turned, b + 1)
                        act.activation(pT[:, 4 * b:4 * b + 4, :], K.ps[2 + b][0:N_CMP, :].rearrange("p (u c) -> p u c", u=4), ACT.Copy).then_inc(copied, 1)
                    for b in range(4):
                        act.wait_ge(outed, b + 1)
                        t, hg = divmod(b, 2)
                        act.activation(cat[:, t, hg * 512:(hg + 1) * 512], K.ps[2 + b][:, :], ACT.Copy)

                @block.vector
                def _(dve):
                    chain = Chain(dve, step)
                    dve.wait_ge(scored, 1)
                    chain(dve.tensor_copy(bc[:, :, :, :].rearrange("p t h n -> p t n h"),
                                          K.ps[1][:, 0:2 * N_CMP * GH].rearrange("p (t n h) -> p t n h", t=2, h=GH)))
                    for t in range(2):
                        sv = s[:, t, :, 0:N_CMP]
                        chain(dve.tensor_tensor(bc[:, t, :, :], bc[:, t, :, :], cm[:, 0, t, :][:, None, :].broadcast_to([P, GH, N_CMP]), ALU.add))
                        chain(dve.scalar_tensor_tensor(out=sv, in0=K.ps[0][:, t * 128:(t + 1) * 128].rearrange("p (h n) -> p h n", n=16)[:, :, 0:N_CMP],
                                                       scalar=SCALE, in1=bc[:, t, :, :], op0=ALU.mult, op1=ALU.add))
                        chain(dve.tensor_reduce(red[:, 0, t, :], sv, AX.X, ALU.max))
                        ins = dve.tensor_tensor(sv, sv, red[:, 0, t, :][:, :, None].broadcast_to([P, GH, N_CMP]), ALU.subtract)
                        if t == 0:
                            chain(ins)
                    ins.then_inc(shifted, 1)
                    dve.wait_ge(exped, 1)
                    for t in range(2):
                        sv = s[:, t, :, 0:N_CMP]
                        chain(dve.tensor_tensor(sv, sv, cm[:, 1, t, :][:, None, :].broadcast_to([P, GH, N_CMP]), ALU.mult))
                        chain(dve.tensor_reduce(red[:, 1, t, :], sv, AX.X, ALU.add))
                        chain(dve.tensor_single_scalar(red[:, 1, t, :], red[:, 1, t, :], 1e-30, ALU.max))
                        chain(dve.reciprocal(red[:, 2, t, :], red[:, 1, t, :]))
                        chain(dve.tensor_tensor(red[:, 2, t, :], red[:, 2, t, :],
                                                gates[:, t, :].rearrange("p (h c) -> p h c", c=3)[:, :, 0], ALU.mult))
                        ins = dve.tensor_tensor(sv, sv, red[:, 2, t, :][:, :, None].broadcast_to([P, GH, N_CMP]), ALU.mult)
                        if t == 0:
                            chain(ins)
                    ins.then_inc(weighted, 1)
        items = []
        for kind in range(2):
            for h in range(GH):
                for t in range(2):
                    n = (t + 1) * P
                    items.append((qT[:, h, t * P:(t + 1) * P], kvT[:, 2 + kind, h // 4, 0:n], bias[:, h, T1 - n:T1],
                                  [vtok[:, kind, c, (h // 4) * P:(h // 4 + 1) * P] for c in range(t + 1)],
                                  cat[:, t, h * P:(h + 1) * P], gates[:, t, 3 * h + 1 + kind:3 * h + 2 + kind], True))
        attend(K, items, SCALE)


def conv_glu(K, l, hT, x):
    nc = K.nc
    J = D_FF // P
    with ExitStack() as mem:
        def sb(name, shape, scope=mem):
            return scope.enter_context(nc.sbuf_tensor(f"gu_{name}{l}", shape, F32))
        actT = tuple(mem.enter_context(nc.sbuf_tensor(f"gu_act{h}{l}", [P, J, T1], F32R)) for h in ("hi", "lo"))
        cw, cb = sb("cw", [P, J, 3]), sb("cb", [P, J])
        with ExitStack() as up:
            w = sb("w", [P, 3, KD, T1], up)
            halves = tuple(up.enter_context(nc.sbuf_tensor(f"gu_w{h}{l}", [P, 2, KD, T1], F32R)) for h in ("hi", "lo"))
            gp, cv, both_sides = sb("gp", [P, 2, T1 + 2], up), sb("cv", [P, 2, T1], up), sb("bs", [P, 2, T1], up)
            load(K, (cw[:, :, :], K.dram["ffn_conv_w"][l]), (cb[:, :], K.dram["ffn_conv_b"][l]))
            with stage(K) as (block,):
                @block.vector
                def _(dve):
                    dve.memset(gp[:, :, 0:2], 0.0)
            with stage(K, "w0", "w1", "w2", "gate_psum", "value_psum", "padded", "step", "conved", "acted", "closed",
                       "hi_ready", "lo_ready", "act_hi", "act_lo") as \
                    (block, w0, w1, w2, gate_psum, value_psum, padded, step, conved, acted, closed, hi_ready, lo_ready, act_hi, act_lo):
                loaded = (w0, w1, w2)

                @block.sync
                def _(sp):
                    for n in range(J):
                        if n >= 3:
                            sp.wait_ge(lo_ready, n - 2)
                        for a in range(2):
                            at = a * D_FF + n * P
                            sp.dma_start(w[:, n % 3, :, a * P:(a + 1) * P], K.dram["ffn_w_up"][l][:, at:at + P].rearrange("(k p) n -> p k n", p=P))\
                              .then_inc(loaded[n % 3], 16)

                @block.tensor
                def _(pe):
                    for i in range(J):
                        pe.wait_ge(lo_ready, i + 1)
                        for a, done, free in ((0, gate_psum, padded), (1, value_psum, closed)):
                            if i >= 2:
                                pe.wait_ge(free, i - 1)
                            for k in range(KD):
                                last = products_of(pe, K.ps[2 * a + i % 2][:, 0:T1],
                                                   both(halves, slice(0, P), i % 2, k, slice(a * P, (a + 1) * P)),
                                                   both(hT, slice(0, P), k, slice(0, T1)), k == 0, k == KD - 1)
                            last.then_inc(done, 1)

                @block.scalar
                def _(act):
                    def split_hi(n):
                        act.wait_ge(loaded[n % 3], 32 * (n // 3 + 1))
                        if n >= 2:
                            act.wait_ge(value_psum, n - 1)
                        act.activation(halves[0][:, n % 2, :, :], w[:, n % 3, :, :], ACT.Copy).then_inc(hi_ready, 1)

                    def silu(i):
                        act.wait_ge(conved, i + 1)
                        act.activation(cv[:, i % 2, :], cv[:, i % 2, :], ACT.Silu, bias=cb[:, i:i + 1]).then_inc(acted, 1)

                    def act_split_hi(i):
                        act.wait_ge(closed, i + 1)
                        act.activation(actT[0][:, i, :], both_sides[:, i % 2, :], ACT.Copy).then_inc(act_hi, 1)

                    split_hi(0)
                    for i in range(J):
                        if i + 1 < J:
                            split_hi(i + 1)
                        if i:
                            silu(i - 1)
                        act.wait_ge(gate_psum, i + 1)
                        if i >= 2:
                            act.wait_ge(conved, i - 1)
                        act.activation(gp[:, i % 2, 2:T1 + 2], K.ps[i % 2][:, 0:T1], ACT.Copy).then_inc(padded, 1)
                        if i:
                            act_split_hi(i - 1)
                    silu(J - 1)
                    act_split_hi(J - 1)

                @block.vector
                def _(dve):
                    chain = Chain(dve, step)

                    def split_lo(n):
                        dve.wait_ge(hi_ready, n + 1)
                        dve.tensor_tensor(halves[1][:, n % 2, :, :], w[:, n % 3, :, :], halves[0][:, n % 2, :, :].bitcast(F32),
                                          ALU.subtract).then_inc(lo_ready, 1)

                    def close(i):
                        dve.wait_ge(acted, i + 1)
                        dve.wait_ge(value_psum, i + 1)
                        if i >= 2:
                            dve.wait_ge(act_lo, i - 1)
                        dve.tensor_tensor(both_sides[:, i % 2, :], K.ps[2 + i % 2][:, 0:T1], cv[:, i % 2, :], ALU.mult).then_inc(closed, 1)

                    def close_lo(i):
                        dve.wait_ge(act_hi, i + 1)
                        dve.tensor_tensor(actT[1][:, i, :], both_sides[:, i % 2, :], actT[0][:, i, :].bitcast(F32), ALU.subtract)\
                           .then_inc(act_lo, 1)

                    split_lo(0)
                    for i in range(J):
                        if i + 1 < J:
                            split_lo(i + 1)
                        if i:
                            close(i - 1)
                        if i >= 2:
                            dve.wait_ge(closed, i - 1)
                            close_lo(i - 2)
                        dve.wait_ge(padded, i + 1)
                        dst = cv[:, i % 2, :]
                        chain(dve.tensor_scalar(dst, gp[:, i % 2, 0:T1], cw[:, i, 0:1], None, ALU.mult))
                        chain(dve.scalar_tensor_tensor(out=dst, in0=gp[:, i % 2, 1:T1 + 1], scalar=cw[:, i, 1:2], in1=dst, op0=ALU.mult, op1=ALU.add))
                        dve.scalar_tensor_tensor(out=dst, in0=gp[:, i % 2, 2:T1 + 2], scalar=cw[:, i, 2:3], in1=dst,
                                                 op0=ALU.mult, op1=ALU.add).then_inc(conved, 1)
                    close(J - 1)
                    close_lo(J - 2)
                    close_lo(J - 1)
        down(K, l, actT, J, x)


def down(K, l, actT, J, x):
    nc = K.nc
    with ExitStack() as mem:
        w = mem.enter_context(nc.sbuf_tensor(f"dn_w{l}", [P, 4, D], F32))
        halves = tuple(mem.enter_context(nc.sbuf_tensor(f"dn_{h}{l}", [P, 3, D], F32R)) for h in ("hi", "lo"))
        with stage(K, "w0", "w1", "w2", "w3", "hi_ready", "lo_ready", "used") as (block, w0, w1, w2, w3, hi_ready, lo_ready, used):
            loaded = (w0, w1, w2, w3)

            @block.sync
            def _(sp):
                for k in range(J):
                    if k >= 4:
                        sp.wait_ge(lo_ready, k - 3)
                    sp.dma_start(w[:, k % 4, :], K.dram["ffn_w_down"][l][k * P:(k + 1) * P, :]).then_inc(loaded[k % 4], 16)

            @block.scalar
            def _(act):
                for k in range(J):
                    act.wait_ge(loaded[k % 4], 16 * (k // 4 + 1))
                    if k >= 3:
                        act.wait_ge(used, k - 2)
                    act.activation(halves[0][:, k % 3, :], w[:, k % 4, :], ACT.Copy).then_inc(hi_ready, 1)

            @block.tensor
            def _(pe):
                for k in range(J):
                    pe.wait_ge(lo_ready, k + 1)
                    for t in range(2):
                        for c in range(2):
                            last = products_of(pe, K.ps[2 * t + c][:, :], both(actT, slice(0, P), k, slice(t * P, (t + 1) * P)),
                                               both(halves, slice(0, P), k % 3, slice(c * 512, (c + 1) * 512)), k == 0, k == J - 1)
                    last.then_inc(used, 1)

            @block.vector
            def _(dve):
                for k in range(J):
                    dve.wait_ge(hi_ready, k + 1)
                    dve.tensor_tensor(halves[1][:, k % 3, :], w[:, k % 4, :], halves[0][:, k % 3, :].bitcast(F32), ALU.subtract)\
                       .then_inc(lo_ready, 1)
                dve.wait_ge(used, J)
                for t in range(2):
                    for c in range(2):
                        dst = x[:, t, c * 512:(c + 1) * 512]
                        dve.tensor_tensor(dst, dst, K.ps[2 * t + c][:, :], ALU.add)


def second_block(K, x):
    nc = K.nc
    with nc.sbuf_tensor("mem_rows", [P, 2, D], F32) as mem_rows:
        load(K, (mem_rows[:, :, :], K.dram["mem"].rearrange("(t p) d -> p t d", p=P)))
        for l in range(DEPTH):
            def normed(tag, weights, hT):
                with nc.sbuf_tensor(f"b2_gain{tag}", [P, D], F32) as gain, nc.sbuf_tensor(f"b2_h{tag}", [P, 2, D], F32) as h:
                    load(K, (gain[:, :], weights.broadcast_to([P, D])))
                    rms_norm(K, x, [0, 1], lambda t: gain[:, :], None, h, hT)
            with ExitStack() as mix:
                def sb(name, shape):
                    return mix.enter_context(nc.sbuf_tensor(f"b2_{name}{l}", shape, F32))
                cat, qmT = sb("cat", [P, 2, CAT]), sb("qmT", [P, MEM_H, T1])
                with nc.sbuf_tensor(f"b2_hThi{l}", [P, KD, T1], F32R) as hi, nc.sbuf_tensor(f"b2_hTlo{l}", [P, KD, T1], F32R) as lo:
                    hT = (hi, lo)
                    normed(f"m{l}", K.dram["norm_mix_w"][l:l + 1, :], hT)
                    (gdn_layer(K, l, l // 2, hT, cat, qmT) if l % 2 == 0 else sparse_attention(K, l // 2, hT, cat, qmT))
                memory_attention(K, l, mem_rows, qmT, cat)
                catT = tuple(mix.enter_context(nc.sbuf_tensor(f"b2_catT{h}{l}", [P, CAT // P, T1], F32R)) for h in ("hi", "lo"))
                rows_to_channels(K, cat, catT, [0, 1], CAT)
                project(K, K.dram["w_out_2"][l], CAT // P, catT, [(0, D, False, [0, 1], add_scaled(K, x, None))], ring=2, engine="vector")
            with nc.sbuf_tensor(f"b2_fThi{l}", [P, KD, T1], F32R) as hi, nc.sbuf_tensor(f"b2_fTlo{l}", [P, KD, T1], F32R) as lo:
                hT = (hi, lo)
                normed(f"f{l}", K.dram["norm_ffn_w"][l:l + 1, :], hT)
                conv_glu(K, l, hT, x)


def build(nc, K):
    K.nc = nc
    K.uid = K.stages = 0
    K.sems = [[nc.alloc_semaphore(name=f"set{s}_{i}") for i in range(SEMS)] for s in range(2)]
    with ExitStack() as mem:
        def sb(name, shape):
            return mem.enter_context(nc.sbuf_tensor(name, shape, F32))
        K.ps = [mem.enter_context(nc.psum_tensor(f"bank{i}", [P, 512], F32)) for i in range(8)]
        K.ident, K.ones, K.tri, K.iota = sb("ident", [P, P]), sb("ones", [P, P]), sb("tri", [P, P]), sb("iota", [P, P])
        K.junk, K.small = sb("junk", [P, D]), sb("small", [P, 256])
        x = sb("xrows", [P, 4, D])
        s_cols = K.s_cols = sb("s_cols", [P, KD, 2])
        load(K, (K.ident[:, :], K.dram["c_ident"]), (K.ones[:, :], K.dram["c_ones"]), (K.tri[:, :], K.dram["c_tri"]), (K.iota[:, :], K.dram["c_iota"]))
        with nc.sbuf_tensor("grid_pos", [P, 2, D], F32) as pos:
            load(K, (x[:, 0:2, :], K.dram["ctx"].rearrange("(t p) d -> p t d", p=P)), (x[:, 2:4, :], K.dram["x"].rearrange("(t p) d -> p t d", p=P)),
                 (pos[:, :, :], K.dram["grid"].rearrange("(t p) d -> p t d", p=P)), (s_cols[:, :, :], K.dram["cond"]))
            with stage(K) as (block,):
                @block.vector
                def _(dve):
                    dve.tensor_tensor(x[:, 2:4, :], x[:, 2:4, :], pos[:, :, :], ALU.add)

                @block.scalar
                def _(act):
                    act.activation(s_cols[:, :, :], s_cols[:, :, :], ACT.Silu)
        for l in range(DEPTH):
            first_layer(K, l, x, s_cols)
        x2 = x[:, 2:4, :]
        with nc.sbuf_tensor("mid_gain", [P, D], F32) as gain:
            load(K, (gain[:, :], K.dram["final_norm_g"].broadcast_to([P, D])))
            rms_norm(K, x2, [0, 1], lambda t: gain[:, :], None, x2)
        second_block(K, x2)
        with nc.sbuf_tensor("fin_gain", [P, D], F32) as gain, nc.sbuf_tensor("fin_rows", [P, 2, D], F32) as rows:
            load(K, (gain[:, :], K.dram["final_norm_w"].broadcast_to([P, D])))
            rms_norm(K, x2, [0, 1], lambda t: gain[:, :], None, rows)
            with stage(K, "stored") as (block, stored):
                @block.sync
                def _(sp):
                    sp.dma_start(K.out.rearrange("(t p) d -> p t d", p=P), rows[:, :, :]).then_inc(stored, 16)
                    sp.wait_ge(stored, 16)



def buckets(dist):
    n = np.maximum(dist, 0)
    logv = np.log(np.maximum(n, 1).astype(np.float32) / np.float32(16)) / np.float32(np.log(8.0))
    large = np.minimum(16 + (logv * 16).astype(np.int32), 31)
    return np.where(n < 16, n, large)


def constants():
    f = np.float32
    c = {}
    i = np.arange(P)
    c["c_ident"] = np.eye(P, dtype=f)
    c["c_ones"] = np.ones((P, P), f)
    c["c_tri"] = (i[:, None] <= i[None, :]).astype(f)
    c["c_iota"] = np.tile(i.astype(f), (P, 1))
    c["c_unit16"] = np.tile(np.eye(2 * GH, dtype=f), (P, 1, 1))
    c["c_pick4"] = np.repeat(np.eye(4, dtype=f)[:, :, None], P, 2)
    c["c_ones4"] = np.ones((4, TALL), f)
    n_freq = D // 4
    freq = f(1.0) / (f(10000.0) ** (np.arange(n_freq, dtype=f) / f(n_freq)))
    ar = np.repeat(np.arange(T1 // 64, dtype=f), 64)[:, None] * freq
    ac = np.tile(np.arange(64, dtype=f), T1 // 64)[:, None] * freq
    c["grid"] = np.concatenate([np.sin(ar), np.cos(ar), np.sin(ac), np.cos(ac)], -1).astype(f)
    t = np.arange(TALL)
    m = np.zeros((P, 2, 2, TALL), f)
    for s in range(2):
        src = s * P + i[:, None]
        same = t[None, :] < CTX
        m[:, 0, s, :] = np.where(same & (src > t[None, :]), f(MASKED), f(0))
        m[:, 1, s, :] = np.where(same & (src < t[None, :]), f(MASKED), f(0))
    c["ml_mask"] = m
    a = 2 * np.pi * np.outer(np.arange(CTX), np.arange(CTX)) / CTX
    c["dft_t"] = np.stack([np.cos(a), np.sin(a)]).reshape(2, 2, P, CTX).transpose(2, 0, 1, 3).astype(f)
    b = 2 * np.pi * np.outer(np.arange(DH), np.arange(DH)) / DH
    k = 1.0 / np.sqrt(CTX * DH)
    c["dft_c"] = np.stack([np.kron(np.eye(2), np.cos(b)) * k, -np.kron(np.eye(2), np.sin(b)) * k], 1).astype(f)
    c["gd_masks"] = np.stack([np.where(i[:, None] > i[None, :], f(0), f(-MASKED)), np.where(i[:, None] <= i[None, :], f(0), f(MASKED))], 1)
    lv = [((i[:, None] // (2 * s) == i[None, :] // (2 * s)) & (i[:, None] // s % 2 == 1) & (i[None, :] // s % 2 == 0)) for s in 2 ** np.arange(7)]
    c["gd_levels"] = np.stack(lv, 1).astype(f)
    c["bucket_rev"] = (np.arange(32)[:, None] == buckets(T1 - 1 - np.arange(3 * P))[None, :]).astype(f)
    dist = np.arange(T1).reshape(2, 1, P) - (np.arange(N_CMP) * 16 + 31).reshape(1, N_CMP, 1)
    c["bucket_cmp"] = (np.arange(32)[:, None, None, None] == buckets(dist)[None]).astype(f)
    ok = (dist >= 0).transpose(2, 0, 1)
    c["cmp_masks"] = np.stack([np.where(ok, f(0), f(MASKED)), ok.astype(f)], 1)
    c["causal"] = np.where(i[:, None] >= i[None, :], f(0), f(MASKED))
    return c


def kernel(**inputs):
    import concourse.bacc as _bacc
    from concourse.bass_utils import run_bass_kernel_spmd as _run

    n = {k: np.asarray(v) for k, v in inputs.items()}

    def cols(a):
        a = np.moveaxis(a, -1, 1)
        a = a.reshape(a.shape[0], a.shape[1] // P, P, *a.shape[2:])
        return np.swapaxes(a, 1, 2)

    data = dict(constants())
    data.update({
        "x": n["x"][0], "ctx": n["ctx"][0],
        "cond": np.stack([n["c_ctx"], n["c"][0]], -1).reshape(KD, P, 2).transpose(1, 0, 2),
        "w_ada": n["w_ada"], "b_ada": n["b_ada"], "norm1_g": n["norm1_g"], "norm2_g": n["norm2_g"], "w_in": n["w_in"],
        "ml_conv_w": cols(n["ml_conv_w"]), "ml_conv_b": cols(n["ml_conv_b"]), "ml_gate_b": n["ml_gate_b"],
        "ml_norm_g": n["ml_norm_g"].reshape(DEPTH, MIX), "gm_ln_g": n["gm_ln_g"], "gm_ln_b": n["gm_ln_b"],
        "gm_w_s": n["gm_w_s"].transpose(0, 3, 1, 2), "gm_b_s": n["gm_b_s"].transpose(0, 2, 1),
        "cv_dw_w": cols(n["cv_dw_w"]), "cv_dw_b": cols(n["cv_dw_b"]), "cv_ln_g": n["cv_ln_g"], "cv_ln_b": n["cv_ln_b"],
        "w_branch": n["w_branch"].reshape(DEPTH, 4 * MIX, D), "w_out": n["w_out"], "peer_w_q": n["peer_w_q"],
        "peer_keys": n["peer_keys"].transpose(0, 3, 1, 2), "peer_u": n["peer_u"].transpose(0, 2, 1), "peer_v": n["peer_v"],
        "final_norm_g": n["final_norm_g"][None], "mem": n["mem_2"][0], "rel_bias": n["rel_bias_2"], "norm_mix_w": n["norm_mix_w_2"], "norm_ffn_w": n["norm_ffn_w_2"],
        "final_norm_w": n["final_norm_w_2"][None], "mem_norm_w": n["mem_norm_w_2"], "mem_w_kv": n["mem_w_kv_2"],
        "w_out_2": n["w_out_2"], "gdn_w_in": n["gdn_w_in_2"], "gdn_conv_w": cols(n["gdn_conv_w_2"]),
        "gdn_a_log": n["gdn_a_log_2"], "gdn_dt_bias": n["gdn_dt_bias_2"], "gdn_norm_w": n["gdn_norm_w_2"],
        "nsa_w_in": n["nsa_w_in_2"], "pos_k": n["nsa_cmp_pos_k_2"].transpose(0, 2, 1), "w1_k": n["nsa_cmp_w1_k_2"],
        "w2_k": n["nsa_cmp_w2_k_2"], "pos_v": n["nsa_cmp_pos_v_2"].transpose(0, 2, 1), "w1_v": n["nsa_cmp_w1_v_2"],
        "w2_v": n["nsa_cmp_w2_v_2"], "ffn_w_up": n["ffn_w_up_2"], "ffn_conv_w": cols(n["ffn_conv_w_2"]),
        "ffn_conv_b": cols(n["ffn_conv_b_2"]), "ffn_w_down": n["ffn_w_down_2"],
    })
    nc = _bacc.Bacc("TRN2", target_bir_lowering=False, num_devices=1)
    arrays, dram = {}, {}
    for name, a in data.items():
        arrays[name + "_in"] = np.ascontiguousarray(a)
        dram[name] = nc.dram_tensor(name + "_in", a.shape, F32, kind="ExternalInput").ap()
    dense = nc.dram_tensor("dense_weights", (TALL // 64, P, P * 64), F32, kind="Internal").ap()
    ada = nc.dram_tensor("modulation_rows", (2, 6 * D), F32, kind="Internal").ap()
    skew = nc.dram_tensor("skewed_bias", (GH, P, 3 * P), F32, kind="Internal").ap()
    out = nc.dram_tensor("out_rows", (T1, D), F32, kind="ExternalOutput").ap()
    build(nc, Core(nc, dram, dense, ada, skew, out))
    r = _run(nc, [arrays], core_ids=[0])
    return r.results[0]["out_rows"].reshape(1, T1, D)
```
